# Optimizing a Trainium2 kernel written in Bass

```python
import math
import jax, jax.numpy as jnp
from jax import lax
import numpy as np

D_MODEL = 1024
BATCH = 1
SEQ = 256
DEPTH = 2
DEC_BATCH = 8
DEC_SEQ = 8
PAST_LEN = 2048
PAGE_SIZE = 128

A_HEADS = 4
A_DK = 128
A_DV = 128
CONV_W = 4
A_CONV_DIM = A_HEADS * (2 * A_DK + A_DV)
A_GATE = A_HEADS * A_DV
B_HEADS = 4
B_DK = 128
B_DV = 128
B_QK = B_HEADS * B_DK
B_VD = B_HEADS * B_DV
ROPE_BASE = 10000.0
CHUNK = 64
C_HD = 64
C_HEADS = D_MODEL // C_HD
C_DECAY_LORA = 64
C_AAA_LORA = 64
C_GATE_LORA = 128
RWKV_GN_EPS = 64e-5
MEM_LEN = 256
X_HEADS = 4
X_HD = D_MODEL // X_HEADS
X_DIM = X_HEADS * X_HD
N_GROUPS = 4
EXP_PER_GROUP = 8
TOP_K_IN_GROUP = 2
EXP_FF = 256
N_AB = (DEPTH + 1) // 2
N_C = DEPTH // 2
AB_IN = A_CONV_DIM + 2 * A_HEADS + A_GATE + 2 * B_QK + 2 * B_VD
AB_MIX = A_HEADS * A_DV + B_HEADS * B_DV
DEEPNORM_ALPHA = (2.0 * DEPTH) ** 0.25
DEEPNORM_BETA = (8.0 * DEPTH) ** -0.25
LN_EPS = 1e-5
RMS_EPS = 1e-6

kernel_name = 'hybrid_deltanet_retention_rwkv7_hmoe_step'

F32 = jnp.float32

def layer_norm(x, w, b):
    xf = x.astype(F32)
    mu = jnp.mean(xf, -1, keepdims=True)
    var = jnp.mean(jnp.square(xf - mu), -1, keepdims=True)
    return ((xf - mu) * lax.rsqrt(var + LN_EPS) * w + b).astype(x.dtype)

def head_norm(x, eps):
    mu = jnp.mean(x, -1, keepdims=True)
    var = jnp.mean(jnp.square(x - mu), -1, keepdims=True)
    return (x - mu) * lax.rsqrt(var + eps)

def rms_norm(x, w):
    return x * lax.rsqrt(jnp.mean(jnp.square(x), -1, keepdims=True) + RMS_EPS) * w

def l2norm(x):
    return x * lax.rsqrt(jnp.sum(jnp.square(x), -1, keepdims=True) + 1e-6)

def rotary(x, pos):
    half = x.shape[-1] // 2
    inv = ROPE_BASE ** (-jnp.linspace(0.0, 1.0, half, dtype=F32))
    ang = pos[:, None] * inv[None, :]
    cos = jnp.cos(ang)[None, :, None, :]
    sin = jnp.sin(ang)[None, :, None, :]
    x1, x2 = x[..., :half], x[..., half:]
    return jnp.concatenate([x1 * cos - x2 * sin, x1 * sin + x2 * cos], -1)

def causal_conv(u, buf, w):
    L = u.shape[1]
    xp = jnp.concatenate([buf.astype(u.dtype), u], axis=1)
    out = sum(xp[:, j:j + L] * w[j] for j in range(CONV_W))
    return out, xp[:, -(CONV_W - 1):]

def to_chunks(x, c):
    b, L = x.shape[:2]
    xr = x.reshape((b, L // c, c) + x.shape[2:])
    return xr.transpose((1, 0, 3, 2) + tuple(range(4, xr.ndim)))

def from_chunks(o):
    n, b, h, c, v = o.shape
    return o.transpose(1, 0, 3, 2, 4).reshape(b, n * c, h, v)

def gated_delta_rule(q, k, v, g, beta, s0):
    L = q.shape[1]
    c = math.gcd(L, CHUNK)
    q = to_chunks(q * (A_DK ** -0.5), c)
    k = to_chunks(k, c)
    v = to_chunks(v, c)
    g = to_chunks(g, c)
    beta = to_chunks(beta, c)
    gc = jnp.cumsum(g, -1)
    incl = jnp.tril(jnp.ones((c, c), bool))
    strict = jnp.tril(jnp.ones((c, c), bool), -1)
    diff = gc[..., :, None] - gc[..., None, :]
    decay = jnp.where(incl, jnp.exp(jnp.where(incl, diff, 0.0)), 0.0)
    kb = k * beta[..., None]
    m = jnp.where(strict, jnp.einsum('nbhik,nbhjk->nbhij', kb, k) * decay, 0.0)
    eye = jnp.eye(c, dtype=m.dtype)
    t_inv = lax.linalg.triangular_solve(eye + m, jnp.broadcast_to(eye, m.shape), left_side=True, lower=True, unit_diagonal=True)
    u = jnp.einsum('nbhij,nbhjv->nbhiv', t_inv, v * beta[..., None])
    w = jnp.einsum('nbhij,nbhjk->nbhik', t_inv, kb * jnp.exp(gc)[..., None])
    qk = jnp.einsum('nbhik,nbhjk->nbhij', q, k) * decay
    qg = q * jnp.exp(gc)[..., None]
    glast = gc[..., -1]
    kd = k * jnp.exp(glast[..., None] - gc)[..., None]

    def step(s, inp):
        qg_c, w_c, u_c, qk_c, kd_c, gl_c = inp
        v_new = u_c - jnp.einsum('bhck,bhkv->bhcv', w_c, s)
        o = jnp.einsum('bhck,bhkv->bhcv', qg_c, s) + jnp.einsum('bhij,bhjv->bhiv', qk_c, v_new)
        s = s * jnp.exp(gl_c)[..., None, None] + jnp.einsum('bhck,bhcv->bhkv', kd_c, v_new)
        return s, o

    s, o = lax.scan(step, s0, (qg, w, u, qk, kd, glast))
    return from_chunks(o), s

def retention(q, k, v, log_gamma, s0):
    L = q.shape[1]
    c = math.gcd(L, CHUNK)
    q = to_chunks(q, c)
    k = to_chunks(k, c)
    v = to_chunks(v, c)
    idx = jnp.arange(c, dtype=F32)
    diff = idx[:, None] - idx[None, :]
    decay = jnp.where(diff >= 0, jnp.exp(log_gamma[:, None, None] * jnp.maximum(diff, 0.0)), 0.0)
    inner = jnp.einsum('nbhij,nbhjv->nbhiv', jnp.einsum('nbhik,nbhjk->nbhij', q, k) * decay, v)
    qd = q * jnp.exp(log_gamma[:, None] * (idx + 1.0))[:, :, None]
    kd = k * jnp.exp(log_gamma[:, None] * (c - 1.0 - idx))[:, :, None]
    chunk_decay = jnp.exp(log_gamma * c)[:, None, None]

    def step(s, inp):
        qd_c, kd_c, v_c, in_c = inp
        o = in_c + jnp.einsum('bhck,bhkv->bhcv', qd_c, s)
        s = s * chunk_decay + jnp.einsum('bhck,bhcv->bhkv', kd_c, v_c)
        return s, o

    s, o = lax.scan(step, s0, (qd, kd, v, inner))
    return from_chunks(o), s

def ab_mix(x, pos0, conv_buf, s_delta, s_ret, w_in, conv_w, a_log, dt_bias, norm_w, w_out):
    bsz, L, _ = x.shape
    h = x @ w_in
    sizes = (A_CONV_DIM, A_HEADS, A_HEADS, A_GATE, B_QK, B_QK, B_VD, B_VD)
    qkv_raw, a_raw, b_raw, gate_a, q_b, k_b, v_b, gate_b = jnp.split(h, np.cumsum(sizes)[:-1].tolist(), axis=-1)
    u, new_buf = causal_conv(qkv_raw, conv_buf, conv_w)
    u = jax.nn.silu(u).astype(F32)
    q_a, k_a, v_a = jnp.split(u, [A_HEADS * A_DK, 2 * A_HEADS * A_DK], axis=-1)
    q_a = l2norm(q_a.reshape(bsz, L, A_HEADS, A_DK))
    k_a = l2norm(k_a.reshape(bsz, L, A_HEADS, A_DK))
    v_a = v_a.reshape(bsz, L, A_HEADS, A_DV)
    g = -jnp.exp(a_log.astype(F32)) * jax.nn.softplus(a_raw.astype(F32) + dt_bias.astype(F32))
    beta = jax.nn.sigmoid(b_raw.astype(F32))
    o_a, s_delta = gated_delta_rule(q_a, k_a, v_a, g, beta, s_delta.astype(F32))
    z_a = jax.nn.silu(gate_a.astype(F32)).reshape(bsz, L, A_HEADS, A_DV)
    o_a = rms_norm(o_a, norm_w.astype(F32)) * z_a
    pos = pos0 + jnp.arange(L, dtype=F32)
    q_b = rotary(q_b.astype(F32).reshape(bsz, L, B_HEADS, B_DK), pos)
    k_b = rotary(k_b.astype(F32).reshape(bsz, L, B_HEADS, B_DK), pos) * (B_DK ** -0.5)
    v_b = v_b.astype(F32).reshape(bsz, L, B_HEADS, B_DV)
    log_gamma = jnp.log(1.0 - 2.0 ** (-5.0 - jnp.arange(B_HEADS, dtype=F32)))
    o_b, s_ret = retention(q_b, k_b, v_b, log_gamma, s_ret.astype(F32))
    z_b = jax.nn.silu(gate_b.astype(F32)).reshape(bsz, L, B_HEADS, B_DV)
    o_b = head_norm(o_b, LN_EPS) * z_b
    mixed = jnp.concatenate([o_a.reshape(bsz, L, -1), o_b.reshape(bsz, L, -1)], -1).astype(x.dtype)
    return mixed @ w_out, new_buf, s_delta, s_ret

def rwkv7_scan(r, w, k, v, kk, a, s0):
    xs = tuple(jnp.moveaxis(t, 1, 0) for t in (r, w, k, v, kk, a))

    def step(s, inp):
        r_t, w_t, k_t, v_t, kk_t, a_t = inp
        sa = jnp.einsum('bhvk,bhk->bhv', s, -kk_t)
        s = s * w_t[:, :, None, :] + sa[..., None] * (kk_t * a_t)[:, :, None, :] + v_t[..., None] * k_t[:, :, None, :]
        return s, jnp.einsum('bhvk,bhk->bhv', s, r_t)

    s, y = lax.scan(step, s0, xs)
    return jnp.moveaxis(y, 0, 1), s

def rwkv7_mix(x, shift, s0, mu, w_r, w_k, w_v, w0, w_w1, w_w2, a0, w_a1, w_a2, w_g1, w_g2, k_k, k_a, r_k, ln_w, ln_b, w_out):
    bsz, L, _ = x.shape
    prev = jnp.concatenate([shift[:, None].astype(x.dtype), x[:, :-1]], axis=1)
    xx = prev - x
    xr, xw, xk, xv, xa, xg = [x + xx * mu[i] for i in range(6)]
    r = xr @ w_r
    k = xk @ w_k
    v = xv @ w_v
    w_log = -jax.nn.softplus(-(w0 + jnp.tanh(xw @ w_w1) @ w_w2).astype(F32)) - 0.5
    decay = jnp.exp(-jnp.exp(w_log))
    a = jax.nn.sigmoid((a0 + (xa @ w_a1) @ w_a2).astype(F32))
    g = jax.nn.sigmoid(xg @ w_g1) @ w_g2

    def heads(t):
        return t.astype(F32).reshape(bsz, L, C_HEADS, C_HD)

    r_h, v_h, a_h, w_h = heads(r), heads(v), heads(a), heads(decay)
    kk = l2norm(heads(k * k_k))
    k_h = heads(k) * (1.0 + (a_h - 1.0) * k_a.astype(F32).reshape(C_HEADS, C_HD))
    y, s = rwkv7_scan(r_h, w_h, k_h, v_h, kk, a_h, s0.astype(F32))
    y = head_norm(y, RWKV_GN_EPS).reshape(bsz, L, D_MODEL) * ln_w + ln_b
    bonus = jnp.sum(r_h * k_h * r_k.astype(F32), -1, keepdims=True) * v_h
    y = (y + bonus.reshape(bsz, L, D_MODEL)) * g
    return y.astype(x.dtype) @ w_out, x[:, -1], s

def cross_attn(x, mem_k, mem_v, w_q, w_o):
    bsz, L, _ = x.shape
    q = (x @ w_q).reshape(bsz, L, X_HEADS, X_HD)
    s = jnp.einsum('blhd,bmhd->bhlm', q, mem_k).astype(F32) * (X_HD ** -0.5)
    p = jax.nn.softmax(s, -1).astype(mem_v.dtype)
    o = jnp.einsum('bhlm,bmhd->blhd', p, mem_v).reshape(bsz, L, X_DIM)
    return o @ w_o

def hier_moe(x, w_grp, b_grp, w_exp, b_exp, w1, w3, w2):
    bsz, L, d = x.shape
    xt = x.reshape(-1, d)
    p_grp = jax.nn.softmax((xt @ w_grp + b_grp).astype(F32), -1)
    g_sel = jnp.argmax(p_grp, -1)
    g_onehot = jax.nn.one_hot(g_sel, N_GROUPS, dtype=F32)
    p_grp_sel = jnp.max(p_grp, -1, keepdims=True)
    logits_e = (jnp.einsum('nd,gde->nge', xt, w_exp) + b_exp).astype(F32)
    p_e = jax.nn.softmax(jnp.einsum('nge,ng->ne', logits_e, g_onehot), -1)
    top_p, top_i = lax.top_k(p_e, TOP_K_IN_GROUP)
    top_p = top_p / jnp.sum(top_p, -1, keepdims=True)
    w_in_group = jnp.sum(jax.nn.one_hot(top_i, EXP_PER_GROUP, dtype=F32) * top_p[..., None], 1)
    gates = (g_onehot[:, :, None] * (p_grp_sel * w_in_group)[:, None, :]).astype(x.dtype)
    out = jnp.zeros_like(xt)
    for gi in range(N_GROUPS):
        hdn = jax.nn.silu(jnp.einsum('nd,edf->nef', xt, w1[gi])) * jnp.einsum('nd,edf->nef', xt, w3[gi])
        out = out + jnp.einsum('nef,efd->nd', hdn * gates[:, gi, :, None], w2[gi])
    return out.reshape(bsz, L, d)

def trunk(x, pos0, conv_a, s_delta, s_ret, s_shift, s_wkv, mem_k, mem_v, ab_p, c_p, x_w_q, x_w_o, moe_p, ln_w, ln_b):
    new_conv, new_delta, new_ret, new_shift, new_wkv = [], [], [], [], []
    for layer in range(DEPTH):
        i = layer // 2
        if layer % 2 == 0:
            f, cb, sd, sr = ab_mix(x, pos0, conv_a[i], s_delta[i], s_ret[i], *[p[i] for p in ab_p])
            new_conv.append(cb)
            new_delta.append(sd)
            new_ret.append(sr)
        else:
            f, sh, sw = rwkv7_mix(x, s_shift[i], s_wkv[i], *[p[i] for p in c_p])
            new_shift.append(sh)
            new_wkv.append(sw)
        x = layer_norm(DEEPNORM_ALPHA * x + f, ln_w[layer, 0], ln_b[layer, 0])
        x = layer_norm(DEEPNORM_ALPHA * x + cross_attn(x, mem_k[layer], mem_v[layer], x_w_q[layer], x_w_o[layer]), ln_w[layer, 1], ln_b[layer, 1])
        x = layer_norm(DEEPNORM_ALPHA * x + hier_moe(x, *[p[layer] for p in moe_p]), ln_w[layer, 2], ln_b[layer, 2])
    dt = x.dtype
    return (x, jnp.stack(new_conv).astype(dt), jnp.stack(new_delta).astype(dt), jnp.stack(new_ret).astype(dt),
            jnp.stack(new_shift).astype(dt), jnp.stack(new_wkv).astype(dt))

def setup_inputs(seed: int = 0) -> dict:
    key = jax.random.key(seed)
    ks = iter(jax.random.split(key, 64))

    def nrm(shape, scale=1.0):
        return jax.random.normal(next(ks), shape, F32) * scale

    def unif(shape, lo, hi):
        return jax.random.uniform(next(ks), shape, F32, lo, hi)

    inv_d = D_MODEL ** -0.5
    dt = jnp.exp(unif((N_AB, A_HEADS), math.log(1e-3), math.log(1e-1)))
    return {
        'x_prompt': nrm((BATCH, SEQ, D_MODEL)),
        'x_sample': nrm((DEC_BATCH, DEC_SEQ, D_MODEL)),
        'mem_prompt': nrm((BATCH, MEM_LEN, D_MODEL)),
        'cache_mem_k': nrm((DEPTH, DEC_BATCH, MEM_LEN, X_HEADS, X_HD)),
        'cache_mem_v': nrm((DEPTH, DEC_BATCH, MEM_LEN, X_HEADS, X_HD)),
        'state_conv_a': nrm((N_AB, DEC_BATCH, CONV_W - 1, A_CONV_DIM)),
        'state_delta': nrm((N_AB, DEC_BATCH, A_HEADS, A_DK, A_DV), 0.1),
        'state_ret': nrm((N_AB, DEC_BATCH, B_HEADS, B_DK, B_DV), 0.5),
        'state_shift_c': nrm((N_C, DEC_BATCH, D_MODEL)),
        'state_wkv': nrm((N_C, DEC_BATCH, C_HEADS, C_HD, C_HD), 0.5),
        'ab_w_in': nrm((N_AB, D_MODEL, AB_IN), inv_d),
        'ab_conv_w': nrm((N_AB, CONV_W, A_CONV_DIM), 0.5),
        'ab_a_log': jnp.log(unif((N_AB, A_HEADS), 1.0, 16.0)),
        'ab_dt_bias': dt + jnp.log(-jnp.expm1(-dt)),
        'ab_norm_w': 1.0 + nrm((N_AB, A_DV), 0.02),
        'ab_w_out': nrm((N_AB, AB_MIX, D_MODEL), AB_MIX ** -0.5 * DEEPNORM_BETA),
        'c_mu': unif((N_C, 6, D_MODEL), 0.0, 1.0),
        'c_w_r': nrm((N_C, D_MODEL, D_MODEL), inv_d),
        'c_w_k': nrm((N_C, D_MODEL, D_MODEL), inv_d),
        'c_w_v': nrm((N_C, D_MODEL, D_MODEL), inv_d),
        'c_w0': unif((N_C, D_MODEL), -6.5, -1.5),
        'c_w_w1': nrm((N_C, D_MODEL, C_DECAY_LORA), 0.1 * inv_d),
        'c_w_w2': nrm((N_C, C_DECAY_LORA, D_MODEL), 0.1 * C_DECAY_LORA ** -0.5),
        'c_a0': nrm((N_C, D_MODEL), 0.1),
        'c_w_a1': nrm((N_C, D_MODEL, C_AAA_LORA), inv_d),
        'c_w_a2': nrm((N_C, C_AAA_LORA, D_MODEL), C_AAA_LORA ** -0.5),
        'c_w_g1': nrm((N_C, D_MODEL, C_GATE_LORA), inv_d),
        'c_w_g2': nrm((N_C, C_GATE_LORA, D_MODEL), C_GATE_LORA ** -0.5),
        'c_k_k': 0.85 + nrm((N_C, D_MODEL), 0.02),
        'c_k_a': 1.0 + nrm((N_C, D_MODEL), 0.02),
        'c_r_k': nrm((N_C, C_HEADS, C_HD), 0.1),
        'c_ln_w': 1.0 + nrm((N_C, D_MODEL), 0.02),
        'c_ln_b': nrm((N_C, D_MODEL), 0.02),
        'c_w_out': nrm((N_C, D_MODEL, D_MODEL), inv_d * DEEPNORM_BETA),
        'x_w_q': nrm((DEPTH, D_MODEL, X_DIM), inv_d),
        'x_w_k': nrm((DEPTH, D_MODEL, X_DIM), inv_d),
        'x_w_v': nrm((DEPTH, D_MODEL, X_DIM), inv_d),
        'x_w_o': nrm((DEPTH, X_DIM, D_MODEL), X_DIM ** -0.5 * DEEPNORM_BETA),
        'moe_w_grp': nrm((DEPTH, D_MODEL, N_GROUPS), inv_d),
        'moe_b_grp': nrm((DEPTH, N_GROUPS), 0.01),
        'moe_w_exp': nrm((DEPTH, N_GROUPS, D_MODEL, EXP_PER_GROUP), inv_d),
        'moe_b_exp': nrm((DEPTH, N_GROUPS, EXP_PER_GROUP), 0.01),
        'moe_w1': nrm((DEPTH, N_GROUPS, EXP_PER_GROUP, D_MODEL, EXP_FF), inv_d),
        'moe_w3': nrm((DEPTH, N_GROUPS, EXP_PER_GROUP, D_MODEL, EXP_FF), inv_d),
        'moe_w2': nrm((DEPTH, N_GROUPS, EXP_PER_GROUP, EXP_FF, D_MODEL), EXP_FF ** -0.5 * DEEPNORM_BETA),
        'ln_w': 1.0 + nrm((DEPTH, 3, D_MODEL), 0.02),
        'ln_b': nrm((DEPTH, 3, D_MODEL), 0.02),
    }

def reference(x_prompt, x_sample, mem_prompt, cache_mem_k, cache_mem_v, state_conv_a, state_delta, state_ret, state_shift_c, state_wkv,
              ab_w_in, ab_conv_w, ab_a_log, ab_dt_bias, ab_norm_w, ab_w_out,
              c_mu, c_w_r, c_w_k, c_w_v, c_w0, c_w_w1, c_w_w2, c_a0, c_w_a1, c_w_a2, c_w_g1, c_w_g2, c_k_k, c_k_a, c_r_k, c_ln_w, c_ln_b, c_w_out,
              x_w_q, x_w_k, x_w_v, x_w_o, moe_w_grp, moe_b_grp, moe_w_exp, moe_b_exp, moe_w1, moe_w3, moe_w2, ln_w, ln_b):
    ab_p = (ab_w_in, ab_conv_w, ab_a_log, ab_dt_bias, ab_norm_w, ab_w_out)
    c_p = (c_mu, c_w_r, c_w_k, c_w_v, c_w0, c_w_w1, c_w_w2, c_a0, c_w_a1, c_w_a2, c_w_g1, c_w_g2, c_k_k, c_k_a, c_r_k, c_ln_w, c_ln_b, c_w_out)
    moe_p = (moe_w_grp, moe_b_grp, moe_w_exp, moe_b_exp, moe_w1, moe_w3, moe_w2)

    bp = x_prompt.shape[0]
    dt = x_prompt.dtype
    mem_k_prompt = jnp.einsum('bmd,ldk->lbmk', mem_prompt, x_w_k).reshape(DEPTH, bp, MEM_LEN, X_HEADS, X_HD)
    mem_v_prompt = jnp.einsum('bmd,ldk->lbmk', mem_prompt, x_w_v).reshape(DEPTH, bp, MEM_LEN, X_HEADS, X_HD)
    y_prompt, conv_p, delta_p, ret_p, shift_p, wkv_p = trunk(
        x_prompt, 0,
        jnp.zeros((N_AB, bp, CONV_W - 1, A_CONV_DIM), dt),
        jnp.zeros((N_AB, bp, A_HEADS, A_DK, A_DV), dt),
        jnp.zeros((N_AB, bp, B_HEADS, B_DK, B_DV), dt),
        jnp.zeros((N_C, bp, D_MODEL), dt),
        jnp.zeros((N_C, bp, C_HEADS, C_HD, C_HD), dt),
        mem_k_prompt, mem_v_prompt, ab_p, c_p, x_w_q, x_w_o, moe_p, ln_w, ln_b)

    y_sample, conv_s, delta_s, ret_s, shift_s, wkv_s = trunk(
        x_sample, PAST_LEN, state_conv_a, state_delta, state_ret, state_shift_c, state_wkv,
        cache_mem_k, cache_mem_v, ab_p, c_p, x_w_q, x_w_o, moe_p, ln_w, ln_b)

    return (y_prompt, y_sample, mem_k_prompt, mem_v_prompt, conv_p, delta_p, ret_p, shift_p, wkv_p,
            conv_s, delta_s, ret_s, shift_s, wkv_s)


_drawn_inputs = setup_inputs


def setup_inputs(seed=0):
    import zlib

    import numpy as np

    out = dict(_drawn_inputs(seed))
    spreads = {}
    factors = {'ab_norm_w': 6.322,
     'c_w_w1': 8.0,
     'c_w_w2': 8.0,
     'c_ln_w': 24.635,
     'c_ln_b': 23.602,
     'moe_b_grp': 8.0,
     'moe_b_exp': 5.899,
     'c_r_k': 4.725}
    for name, (base, spread) in spreads.items():
        noise = np.random.default_rng([zlib.crc32(name.encode()), seed]).standard_normal(out[name].shape)
        drawn = base * np.exp(spread * noise) if base else spread * noise
        out[name] = __import__('jax').numpy.asarray(drawn.astype(out[name].dtype))
    for name, factor in factors.items():
        out[name] = (out[name] * factor).astype(out[name].dtype)
    return out
```

```python
import contextlib

import numpy as np

import concourse.bass as bass
from concourse import mybir

F32 = mybir.dt.float32
I32 = mybir.dt.int32
ALU = mybir.AluOpType
ACT = mybir.ActivationFunctionType
AX = mybir.AxisListType.X

D = 1024
KT = D // 128
SEQ, SEQS, STEPS = 256, 8, 8
SAMPLE = SEQS * STEPS
TOK = SEQ + SAMPLE
TILES = 3
ROWS = [128, 128, SAMPLE]
AT = [0, 128, 256]
MEM = 256
CONV = 4
QKV = 1536
XH = 4
GROUPS, PER_GROUP, FF = 4, 8, 256
EXPERTS = GROUPS * PER_GROUP
CHUNK = 64
ALPHA = 4.0 ** 0.25
LN_EPS, RMS_EPS, GN_EPS = 1e-5, 1e-6, 64e-5
WIDE = TOK + 24
RING, SLOT = 4, 4096
PAST = 2048


def constants():
    i = np.arange(128)
    parts = {}
    parts["ident"] = np.eye(128)
    parts["ones"] = np.ones((128, 128))
    for kind, c in (("p", CHUNK), ("s", STEPS)):
        same = i[:, None] // c == i[None, :] // c
        parts["upto_" + kind] = same & (i[:, None] <= i[None, :])
        parts["below_" + kind] = same & (i[:, None] > i[None, :])
        parts["above_" + kind] = same & (i[:, None] < i[None, :])
        parts["of_chunk_" + kind] = i[:, None] // c == np.arange(8)[None, :]
    for s in (1, 2, 4, 8, 16, 32):
        same = i[:, None] // (2 * s) == i[None, :] // (2 * s)
        parts[f"level{s}"] = same & (i[:, None] // s % 2 == 1) & (i[None, :] // s % 2 == 0)
    parts["pair"] = i[:, None] // 64 == i[None, :] // 64
    half = 64
    inv = np.float32(10000.0) ** (-np.linspace(0.0, 1.0, half, dtype=np.float32))
    pos = np.concatenate([np.arange(256), PAST + np.arange(64) % 8, np.zeros(64)]).astype(np.float32)
    ang = (pos[:, None] * inv[None, :]).astype(np.float32).reshape(3, 128, half)
    parts["cos"] = np.cos(ang).transpose(1, 0, 2).reshape(128, -1)
    parts["sin"] = np.sin(ang).transpose(1, 0, 2).reshape(128, -1)
    lg = np.log(1.0 - 2.0 ** (-5.0 - np.arange(4)))
    scale = 128.0 ** -0.5
    for kind, c in (("p", CHUNK), ("s", STEPS)):
        d = i[None, :] - i[:, None]
        same = (i[:, None] // c == i[None, :] // c) & (d >= 0)
        dec = np.exp(lg[None, :, None] * np.maximum(d, 0)[:, None, :]) * same[:, None, :] * scale
        parts["retdecay_" + kind] = dec.reshape(128, -1)
        parts["retq_" + kind] = np.exp(lg[None, :] * (i[:, None] % c + 1.0))
        parts["retk_" + kind] = np.exp(lg[None, :] * (c - 1.0 - i[:, None] % c)) * scale
    parts["descend"] = np.tile(8.0 - np.arange(8), (128, 1))
    at, cols = {}, 0
    for name, a in parts.items():
        a = np.asarray(a, np.float32).reshape(128, -1)
        parts[name] = a
        at[name] = (cols, a.shape[1])
        cols += a.shape[1]
    return np.concatenate(list(parts.values()), 1), at


CHUNK_DECAY = {c: [float((1.0 - 2.0 ** (-5.0 - h)) ** c) for h in range(4)] for c in (CHUNK, STEPS)}


class Signal:

    def __init__(self, sem):
        self.sem, self.sent, self.base = sem, 0, 0

    def up(self, by=1):
        self.sent += by
        return self.sem, by

    def at(self, n):
        return self.sem, self.base + n


class Kernel:

    def __init__(self, nc, ins, outs, at, stack):
        self.nc, self.ins, self.outs, self.at, self.stack = nc, ins, outs, at, stack
        self.signals = {}
        self.uid = 0

    def sem(self, name):
        if name not in self.signals:
            self.signals[name] = Signal(self.stack.enter_context(self.nc.semaphore(name)))
        return self.signals[name]

    @contextlib.contextmanager
    def phase(self, *names):
        got = [self.sem(n) for n in names]
        for s in got:
            s.base = s.sent
        with self.nc.Block() as block:
            yield (block, *got)

    def sb(self, stack, name, shape, dt=F32):
        self.uid += 1
        return stack.enter_context(self.nc.sbuf_tensor(f"{name}_{self.uid}", shape, dt))

    def const(self, name, rows=128):
        a, n = self.at[name]
        return self.cst[0:rows, a:a + n]


def chain(eng, sig):

    def link(ins):
        ins.then_inc(*sig.up())
        eng.wait_ge(sig.sem, sig.sent)

    return link


def tile_kind(t):
    return "p" if t < 2 else "s"


def cols_of(t):
    return slice(AT[t], AT[t] + ROWS[t])



def weight_chunks(K):
    I = K.ins
    chunks, first = [], {}

    def dense(name, w, c0s):
        first[name] = len(chunks)
        for c0 in c0s:
            chunks.append([(lambda s: s.rearrange("p (k n) -> p k n", k=KT),
                            w[:, c0:c0 + 512].rearrange("(k p) n -> p k n", p=128))])

    def experts(name, layer):
        first[name] = len(chunks)
        for e in range(EXPERTS):
            for c in expert_chunks(K, layer, e // PER_GROUP, e % PER_GROUP):
                chunks.append(c)

    w_in = I["ab_w_in"][0]
    dense("ab_qkv", w_in, [0, 512, 1024])
    dense("ab_rest", w_in, [1544 + 512 * n for n in range(5)])
    dense("ab_out", I["ab_w_out"][0], [0, 512])
    for layer in range(2):
        if layer:
            for n in ("r", "k", "v"):
                dense("c_" + n, I["c_w_" + n][0], [0, 512])
            dense("c_out", I["c_w_out"][0], [0, 512])
        for n in ("k", "v", "q", "o"):
            dense(f"x_{n}{layer}", I["x_w_" + n][layer], [0, 512])
        experts(f"moe{layer}", layer)
    return chunks, first


def expert_chunks(K, layer, g, e):
    I = K.ins
    up = [(lambda s, j=j: s.rearrange("p (k j f) -> p k j f", k=KT, j=2)[:, :, j, :],
           I[w][layer, g, e].rearrange("(k p) f -> p k f", p=128)) for j, w in enumerate(("moe_w1", "moe_w3"))]
    down = [(lambda s: s[:, 0:2 * D].rearrange("p (k n) -> p k n", k=2),
             I["moe_w2"][layer, g, e].rearrange("(k p) n -> p k n", p=128))]
    return [up, down]


def load_chunk(K, sp, g):
    if g >= len(K.chunks):
        return
    for view, src in K.chunks[g]:
        sp.dma_start(view(K.ring[:, g % RING, :]), src).then_inc(K.arrived[g % RING], 16)


def run_ahead(K, sp, first, full, counts):
    for n, count in enumerate(counts):
        sp.wait_ge(*full.at(count))
        load_chunk(K, sp, first + n + RING)


def await_chunk(K, pe, g):
    pe.wait_ge(K.arrived[g % RING], K.arrival[g])


def slot8(K, g):
    return K.ring[:, g % RING, :].rearrange("p (k n) -> p k n", k=KT)



def transpose_phase(K, groups):
    nc = K.nc
    with K.phase("tr_full", "tr_act", "tr_dve") as (block, full, by_act, by_dve):
        def view(n):
            srcs, dst = groups[n]
            p, c = srcs[0].shape[0], srcs[0].shape[1]
            return K.ps[n % 4][0:c, 0:len(srcs) * p].rearrange("c (n p) -> c n p", p=p)

        @block.tensor
        def _(pe):
            for n, (srcs, dst) in enumerate(groups):
                if n >= 4:
                    pe.wait_ge(*(by_act if n % 2 == 0 else by_dve).at((n - 4) // 2 + 1))
                for j, s in enumerate(srcs):
                    last = nc.tensor.transpose(view(n)[:, j, :], s, K.const("ident")[0:s.shape[0], 0:s.shape[0]])
                last.then_inc(*full.up())

        @block.scalar
        def _(act):
            for n in range(0, len(groups), 2):
                act.wait_ge(*full.at(n + 1))
                nc.scalar.copy(groups[n][1], view(n)).then_inc(*by_act.up())

        @block.vector
        def _(dve):
            for n in range(1, len(groups), 2):
                dve.wait_ge(*full.at(n + 1))
                nc.vector.tensor_copy(groups[n][1], view(n)).then_inc(*by_dve.up())


def token_major_phase(K, first, n_chunks, xT, tiles, dest, stores=()):
    nc = K.nc
    units = [(g, t) for g in range(n_chunks) for t in range(len(tiles))]
    with K.phase("mm_full", "mm_act", "mm_dve", "mm_store") as (block, full, by_act, by_dve, stored):
        @block.sync
        def _(sp):
            run_ahead(K, sp, first, full, [len(tiles) * (g + 1) for g in range(n_chunks)])
            for n, (dst, src) in enumerate(stores):
                if n == 0:
                    sp.wait_ge(*by_act.at((len(units) + 1) // 2))
                    sp.wait_ge(*by_dve.at(len(units) // 2))
                sp.dma_start(dst, src).then_inc(*stored.up(16))
            if stores:
                sp.wait_ge(*stored.at(16 * len(stores)))

        @block.tensor
        def _(pe):
            for n, (g, t) in enumerate(units):
                if t == 0:
                    await_chunk(K, pe, first + g)
                if n >= 4:
                    pe.wait_ge(*(by_act if n % 2 == 0 else by_dve).at((n - 4) // 2 + 1))
                c, rows = tiles[t]
                w = slot8(K, first + g)
                for k in range(KT):
                    last = nc.tensor.matmul(K.ps[n % 4][0:rows, :], xT[:, k, c:c + rows], w[:, k, :],
                                            start=(k == 0), stop=(k == KT - 1))
                last.then_inc(*full.up())

        @block.scalar
        def _(act):
            for n in range(0, len(units), 2):
                act.wait_ge(*full.at(n + 1))
                g, t = units[n]
                nc.scalar.copy(dest(g, t), K.ps[n % 4][0:tiles[t][1], :]).then_inc(*by_act.up())

        @block.vector
        def _(dve):
            for n in range(1, len(units), 2):
                dve.wait_ge(*full.at(n + 1))
                g, t = units[n]
                nc.vector.tensor_copy(dest(g, t), K.ps[n % 4][0:tiles[t][1], :]).then_inc(*by_dve.up())


def feature_major_phase(K, first, n_chunks, xT, n_tok, dest):
    nc = K.nc
    with K.phase("mm_full", "mm_act", "mm_dve") as (block, full, by_act, by_dve):
        @block.sync
        def _(sp):
            run_ahead(K, sp, first, full, [4 * (g + 1) for g in range(n_chunks)])

        @block.tensor
        def _(pe):
            for f in range(4 * n_chunks):
                g = first + f // 4
                if f % 4 == 0:
                    await_chunk(K, pe, g)
                if f >= 4:
                    pe.wait_ge(*(by_act if f % 2 == 0 else by_dve).at((f - 4) // 2 + 1))
                w = slot8(K, g)
                for k in range(KT):
                    last = nc.tensor.matmul(K.ps[f % 4][:, 0:n_tok], w[:, k, (f % 4) * 128:(f % 4 + 1) * 128],
                                            xT[:, k, 0:n_tok], start=(k == 0), stop=(k == KT - 1))
                last.then_inc(*full.up())

        @block.scalar
        def _(act):
            for f in range(0, 4 * n_chunks, 2):
                act.wait_ge(*full.at(f + 1))
                for dst, src in dest(f, K.ps[f % 4]):
                    last = nc.scalar.copy(dst, src)
                last.then_inc(*by_act.up())

        @block.vector
        def _(dve):
            for f in range(1, 4 * n_chunks, 2):
                dve.wait_ge(*full.at(f + 1))
                for dst, src in dest(f, K.ps[f % 4]):
                    last = nc.vector.tensor_copy(dst, src)
                last.then_inc(*by_dve.up())


def transpose_x(K):
    groups = []
    for t in range(TILES):
        for q in range(2):
            groups.append(([K.x[0:ROWS[t], t, (4 * q + j) * 128:(4 * q + j + 1) * 128] for j in range(4)],
                           K.xT[:, 4 * q:4 * q + 4, cols_of(t)]))
    transpose_phase(K, groups)


def row_broadcast(ap, rows=128):
    return ap.rearrange("(a n) -> a n", a=1).broadcast_to([rows, ap.shape[0]])


def norm_tile(K, dve, link, act_sig, sq, t, rows, stats, mv, lnw, lnb):
    nc = K.nc
    x = K.x[0:rows, t, :]
    for h in range(2):
        last = nc.vector.bn_stats(stats[0:rows, h, :], K.x[0:rows, t, h * 512:(h + 1) * 512])
    link(last)
    link(nc.vector.bn_aggr(mv[0:rows, t, 0:2], stats[0:rows, :, :].rearrange("p a b -> p (a b)")))
    nc.vector.tensor_scalar(mv[0:rows, t, 1:2], mv[0:rows, t, 1:2], LN_EPS, None, ALU.add).then_inc(*sq.up())
    dve.wait_ge(*act_sig.at(t + 1))
    link(nc.vector.reciprocal(mv[0:rows, t, 3:4], mv[0:rows, t, 2:3]))
    link(nc.vector.tensor_scalar(x, x, mv[0:rows, t, 0:1], mv[0:rows, t, 3:4], ALU.subtract, ALU.mult))
    link(nc.vector.tensor_tensor(x, x, lnw[0:rows, :], ALU.mult))
    link(nc.vector.tensor_tensor(x, x, lnb[0:rows, :], ALU.add))


def add_and_norm_phase(K, first, srcT, layer, which):
    nc = K.nc
    with contextlib.ExitStack() as st:
        lnw, lnb = K.sb(st, "lnw", [128, D]), K.sb(st, "lnb", [128, D])
        stats, mv = K.sb(st, "stats", [128, 2, 6]), K.sb(st, "mv", [128, TILES, 4])
        with K.phase("mm_full", "ln_rows", "ln_free", "ln_var", "ln_std", "ln_step") as (
                block, full, rows_in, free, var, std, step):
            @block.gpsimd
            def _(pool):
                pool.dma_start(lnw[:, :], row_broadcast(K.ins["ln_w"][layer, which])).then_inc(*rows_in.up(16))
                pool.dma_start(lnb[:, :], row_broadcast(K.ins["ln_b"][layer, which])).then_inc(*rows_in.up(16))

            @block.sync
            def _(sp):
                run_ahead(K, sp, first, full, [TILES, TILES])

            @block.tensor
            def _(pe):
                for g in range(2):
                    await_chunk(K, pe, first + g)
                for t in range(TILES):
                    if t == 2:
                        pe.wait_ge(*free.at(1))
                    for g in range(2):
                        w = slot8(K, first + g)
                        for k in range(KT):
                            last = nc.tensor.matmul(K.ps[2 * (t % 2) + g][0:ROWS[t], :], srcT[:, k, cols_of(t)],
                                                    w[:, k, :], start=(k == 0), stop=(k == KT - 1))
                    last.then_inc(*full.up())

            @block.scalar
            def _(act):
                for t in range(TILES):
                    act.wait_ge(*var.at(t + 1))
                    nc.scalar.activation(mv[0:ROWS[t], t, 2:3], mv[0:ROWS[t], t, 1:2], ACT.Sqrt).then_inc(*std.up())

            @block.vector
            def _(dve):
                link = chain(dve, step)
                for t in range(TILES):
                    rows = ROWS[t]
                    dve.wait_ge(*full.at(t + 1))
                    for g in range(2):
                        xs = K.x[0:rows, t, g * 512:(g + 1) * 512]
                        last = nc.vector.scalar_tensor_tensor(xs, xs, ALPHA, K.ps[2 * (t % 2) + g][0:rows, :],
                                                              ALU.mult, ALU.add)
                    last.then_inc(*free.up())
                    dve.wait_ge(*free.at(t + 1))
                    if t == 0:
                        dve.wait_ge(*rows_in.at(32))
                    norm_tile(K, dve, link, std, var, t, rows, stats, mv, lnw, lnb)
    transpose_x(K)



def hist(b):
    return 3 + SEQ + b * (CONV - 1 + STEPS)


RAW = 3 + SEQ + SEQS * (CONV - 1 + STEPS)


def ab_mixer(K):
    with contextlib.ExitStack() as outer:
        o = K.sb(outer, "o", [128, TILES, 8, 128])
        ab_heads(K, o)
        ab_finish(K, o)


def ab_heads(K, o):
    with contextlib.ExitStack() as st:
        kq = K.sb(st, "kq", [128, 2, 8, TOK])
        v = K.sb(st, "v", [128, TILES, 8, 128])
        kd = K.sb(st, "kd", [128, TILES, 8, 128])
        ab = K.sb(st, "ab", [128, TILES, 8])
        with contextlib.ExitStack() as s1:
            ab_project(K, s1, kq, v, kd, ab)
        ab_scan(K, st, kq, v, kd, ab, o)


def ab_project(K, st, kq, v, kd, ab):
    nc, I, O = K.nc, K.ins, K.outs
    raw = K.sb(st, "raw", [128, 12, RAW])
    u_v = K.sb(st, "u_v", [128, 4, TOK])
    cwT = K.sb(st, "cwT", [128, CONV, 12])
    small = contextlib.ExitStack()
    past = K.sb(small, "past", [24, QKV])
    cw = K.sb(small, "cw", [48, 128])
    wab = K.sb(small, "wab", [128, KT, 8])
    with K.phase("small_in", "ab_full") as (block, loaded, full):
        @block.scalar
        def _(act):
            act.dma_start(past[:, :], I["state_conv_a"][0].rearrange("b j n -> (b j) n")).then_inc(*loaded.up(16))
            act.dma_start(cw[:, :], I["ab_conv_w"][0].rearrange("j (k p) -> (j k) p", p=128)).then_inc(*loaded.up(16))
            act.dma_start(wab[:, :, :], I["ab_w_in"][0][:, QKV:QKV + 8].rearrange("(k p) n -> p k n", p=128)
                          ).then_inc(*loaded.up(16))
            act.wait_ge(*full.at(1))
            for t in range(TILES):
                last = nc.scalar.copy(ab[0:ROWS[t], t, :], K.ps[4][0:ROWS[t], 8 * t:8 * t + 8])

        @block.vector
        def _(dve):
            nc.vector.memset(raw[:, :, 0:3], 0.0)

        @block.tensor
        def _(pe):
            pe.wait_ge(*loaded.at(48))
            for t in range(TILES):
                for k in range(KT):
                    last = nc.tensor.matmul(K.ps[4][0:ROWS[t], 8 * t:8 * t + 8], K.xT[:, k, cols_of(t)],
                                            wab[:, k, :], start=(k == 0), stop=(k == KT - 1))
            last.then_inc(*full.up())
    samples = raw[:, :, hist(0):RAW].rearrange("p f (b j) -> p f b j", b=SEQS)
    groups = [([past[:, f * 128:(f + 1) * 128]],
               samples[:, f:f + 1, :, 0:3]) for f in range(12)]
    transpose_history(K, groups)
    transpose_phase(K, [([cw[:, :]], cwT[:, :, :].rearrange("p j f -> p (j f)").unsqueeze(1))])
    small.close()
    qk = K.sb(st, "qk", [128, TILES, D])
    gates = contextlib.ExitStack()
    gate = K.sb(gates, "gate", [128, TILES, D])

    def raw_dest(f, bank):
        return [(raw[:, f, 3:3 + SEQ], bank[:, 0:SEQ]),
                (samples[:, f, :, 3:3 + STEPS], bank[:, SEQ:TOK].rearrange("p (b s) -> p b s", b=SEQS))]

    feature_major_phase(K, K.first["ab_qkv"], 3, K.xT, TOK, raw_dest)
    tiles = [(AT[t], ROWS[t]) for t in range(TILES)]

    def rest_dest(g, t):
        r = slice(0, ROWS[t])
        if g in (0, 4):
            return gate[r, t, g // 4 * 512:g // 4 * 512 + 512]
        if g in (1, 2):
            return qk[r, t, (g - 1) * 512:g * 512]
        return v[r, t, 4:8, :].rearrange("p h d -> p (h d)")

    token_major_phase(K, K.first["ab_rest"], 5, K.xT, tiles, rest_dest,
                      stores=[(K.scratch["gate"][cols_of(t), :], gate[0:ROWS[t], t, :]) for t in range(TILES)])
    gates.close()
    ab_conv(K, st, raw, samples, cwT, kq, u_v)
    ab_rotary(K, st, qk, kq)
    groups = []
    for t in range(TILES):
        c = cols_of(t)
        groups.append(([u_v[:, h, c] for h in range(4)], v[0:ROWS[t], t, 0:4, :]))
        groups.append(([kq[:, 0, h, c] for h in range(4)], kd[0:ROWS[t], t, 0:4, :]))
        groups.append(([kq[:, 0, 4 + h, c] for h in range(4)], kd[0:ROWS[t], t, 4:8, :]))
    transpose_phase(K, groups)


def transpose_history(K, groups):
    nc = K.nc
    with K.phase("tr_full") as (block, full):
        @block.tensor
        def _(pe):
            for f, (srcs, dst) in enumerate(groups):
                last = nc.tensor.transpose(K.ps[f % 4][:, f // 4 * 24:f // 4 * 24 + 24], srcs[0],
                                           K.const("ident")[0:24, 0:24])
            last.then_inc(*full.up())

        @block.vector
        def _(dve):
            dve.wait_ge(*full.at(1))
            for f, (srcs, dst) in enumerate(groups):
                src = K.ps[f % 4][:, f // 4 * 24:f // 4 * 24 + 24].rearrange("p (a b j) -> p a b j", a=1, b=SEQS)
                nc.vector.tensor_copy(dst, src)


def ab_conv(K, st, raw, samples, cwT, kq, u_v):
    nc, O = K.nc, K.outs
    with contextlib.ExitStack() as tmp:
        last3 = K.sb(tmp, "last3", [128, 12, 32])
        tail = K.sb(tmp, "tail", [32, QKV])

        def place(f):
            return kq[:, 1, f, :] if f < 4 else kq[:, 0, f - 4, :] if f < 8 else u_v[:, f - 8, :]

        with K.phase("conv_done", "silu_done", "conv_step") as (block, conv, silu, step):
            @block.vector
            def _(dve):
                link = chain(dve, step)
                for f in range(12):
                    o = place(f)
                    os = o[:, SEQ:TOK].rearrange("p (b s) -> p b s", b=SEQS)
                    for j in range(CONV):
                        w = cwT[:, j, f:f + 1]
                        if j == 0:
                            nc.vector.tensor_scalar(o[:, 0:SEQ], raw[:, f, 0:SEQ], w, None, ALU.mult)
                            last = nc.vector.tensor_scalar(os, samples[:, f, :, 0:STEPS], w, None, ALU.mult)
                        else:
                            nc.vector.scalar_tensor_tensor(o[:, 0:SEQ], raw[:, f, j:j + SEQ], w, o[:, 0:SEQ],
                                                           ALU.mult, ALU.add)
                            last = nc.vector.scalar_tensor_tensor(os, samples[:, f, :, j:j + STEPS], w, os,
                                                                  ALU.mult, ALU.add)
                        if j < CONV - 1:
                            link(last)
                    last.then_inc(*conv.up())

            @block.gpsimd
            def _(pool):
                nc.gpsimd.tensor_copy(last3[:, :, 0:3], raw[:, :, SEQ:SEQ + 3])
                nc.gpsimd.tensor_copy(last3[:, :, 3:27].rearrange("p f (b j) -> p f b j", b=SEQS),
                                      samples[:, :, :, STEPS:STEPS + 3])

            @block.scalar
            def _(act):
                for f in range(12):
                    act.wait_ge(*conv.at(f + 1))
                    nc.scalar.activation(place(f), place(f), ACT.Silu)
        transpose_phase(K, [([last3[:, 4 * q + j, 0:27] for j in range(4)],
                             tail[0:27, 512 * q:512 * q + 512].rearrange("c (n p) -> c n p", n=4)) for q in range(3)])
        sq = K.sb(tmp, "sq", [128, 2, TOK])
        root = K.sb(tmp, "root", [128, 2, TOK])
        inv = K.sb(tmp, "inv", [128, 2, TOK])
        with K.phase("sq_done", "sum_done", "root_done", "inv_done", "scaled", "tail_out") as (
                block, sqd, summed, rooted, inved, scaled, stored):
            heads = [(i, h) for i in range(2) for h in range(4)]

            @block.sync
            def _(sp):
                sp.dma_start(O[4][0, 0], tail[0:3, :]).then_inc(*stored.up(16))
                sp.dma_start(O[9][0].rearrange("b j n -> (b j) n"), tail[3:27, :]).then_inc(*stored.up(16))
                sp.wait_ge(*stored.at(32))

            @block.gpsimd
            def _(pool):
                for n, (i, h) in enumerate(heads):
                    if n >= 2:
                        pool.wait_ge(*summed.at(n - 1))
                    nc.gpsimd.tensor_tensor(sq[:, n % 2, :], kq[:, i, h, :], kq[:, i, h, :], ALU.mult
                                            ).then_inc(*sqd.up())

            @block.tensor
            def _(pe):
                for n in range(8):
                    pe.wait_ge(*sqd.at(n + 1))
                    if n >= 2:
                        pe.wait_ge(*rooted.at(n - 1))
                    nc.tensor.matmul(K.ps[n % 2][:, 0:TOK], K.const("ones"), sq[:, n % 2, :], start=True, stop=True
                                     ).then_inc(*summed.up())

            @block.scalar
            def _(act):
                for n in range(8):
                    act.wait_ge(*summed.at(n + 1))
                    if n >= 2:
                        act.wait_ge(*inved.at(n - 1))
                    nc.scalar.activation(root[:, n % 2, :], K.ps[n % 2][:, 0:TOK], ACT.Sqrt, bias=K.eps6[:, 0:1]
                                         ).then_inc(*rooted.up())

            @block.vector
            def _(dve):
                for n, (i, h) in enumerate(heads):
                    dve.wait_ge(*rooted.at(n + 1))
                    if n >= 2:
                        dve.wait_ge(*scaled.at(n - 1))
                    nc.vector.reciprocal(inv[:, n % 2, :], root[:, n % 2, :]).then_inc(*inved.up())
                    dve.wait_ge(*inved.at(n + 1))
                    if i == 1:
                        nc.vector.scalar_tensor_tensor(kq[:, i, h, :], kq[:, i, h, :], 128.0 ** -0.5, inv[:, n % 2, :],
                                                       ALU.mult, ALU.mult).then_inc(*scaled.up())
                    else:
                        nc.vector.tensor_tensor(kq[:, i, h, :], kq[:, i, h, :], inv[:, n % 2, :], ALU.mult
                                                ).then_inc(*scaled.up())


def ab_rotary(K, st, qk, kq):
    nc = K.nc
    with contextlib.ExitStack() as tmp:
        t1 = K.sb(tmp, "t1", [128, 8, 64])
        t2 = K.sb(tmp, "t2", [128, 8, 64])
        with K.phase("rot_a", "rot_b") as (block, first, step):
            @block.vector
            def _(dve):
                link = chain(dve, step)
                for t in range(TILES):
                    r = slice(0, ROWS[t])
                    h = qk[r, t, :].rearrange("p (h d) -> p h d", h=8)
                    x1, x2 = h[:, :, 0:64], h[:, :, 64:128]
                    cos = K.const("cos")[r, t * 64:(t + 1) * 64].unsqueeze(1).broadcast_to([ROWS[t], 8, 64])
                    sin = K.const("sin")[r, t * 64:(t + 1) * 64].unsqueeze(1).broadcast_to([ROWS[t], 8, 64])
                    nc.vector.tensor_tensor(t1[r], x1, sin, ALU.mult)
                    link(nc.vector.tensor_tensor(t2[r], x2, sin, ALU.mult))
                    nc.vector.tensor_tensor(x1, x1, cos, ALU.mult)
                    link(nc.vector.tensor_tensor(x2, x2, cos, ALU.mult))
                    nc.vector.tensor_tensor(x1, x1, t2[r], ALU.subtract)
                    link(nc.vector.tensor_tensor(x2, x2, t1[r], ALU.add))
        groups = []
        for t in range(TILES):
            for i, o in ((1, 0), (0, 4)):
                groups.append(([qk[0:ROWS[t], t, (o + h) * 128:(o + h + 1) * 128] for h in range(4)],
                               kq[:, i, 4:8, cols_of(t)]))
        transpose_phase(K, groups)


def invert_phase(K, low, T, R, work, units, levels):
    nc = K.nc
    c, y = work
    with K.phase("inv_cut", "inv_y", "inv_yc", "inv_d", "inv_t", "inv_r") as (block, cut, ys, yc, ds, ts, rs):
        steps = [(s, n) for s in levels for n in range(len(units)) if s in units[n][2]]
        prior = {}
        for m, (s, n) in enumerate(steps):
            prior[m] = max([j for j in range(m) if steps[j][1] == n], default=-1)

        @block.gpsimd
        def _(pool):
            for m, (s, n) in enumerate(steps):
                i, rows, _ = units[n]
                if m >= 2:
                    pool.wait_ge(*ys.at(m - 1))
                mask = K.const(f"level{s}")[0:rows, 0:rows].unsqueeze(1).broadcast_to([rows, 4, rows])
                nc.gpsimd.tensor_tensor(c[0:rows, m % 2, :, 0:rows], low[0:rows, i, :, 0:rows], mask, ALU.mult
                                        ).then_inc(*cut.up())

        @block.tensor
        def _(pe):
            for m, (s, n) in enumerate(steps):
                i, rows, _ = units[n]
                b = m % 2
                pe.wait_ge(*cut.at(m + 1))
                if prior[m] >= 0:
                    pe.wait_ge(*ts.at(prior[m] + 1))
                    pe.wait_ge(*rs.at(prior[m] + 1))
                if m >= 2:
                    pe.wait_ge(*yc.at(m - 1))
                for h in range(4):
                    last = nc.tensor.matmul(K.ps[b][0:rows, h * rows:(h + 1) * rows], c[0:rows, b, h, 0:rows],
                                            R[0:rows, i, h, 0:rows], start=True, stop=True)
                last.then_inc(*ys.up())
                pe.wait_ge(*yc.at(m + 1))
                if m >= 2:
                    pe.wait_ge(*ts.at(m - 1))
                    pe.wait_ge(*rs.at(m - 1))
                for h in range(4):
                    nc.tensor.matmul(K.ps[2 + b][0:rows, h * rows:(h + 1) * rows], y[0:rows, b, h, 0:rows],
                                     T[0:rows, i, h, 0:rows], start=True, stop=True)
                for h in range(4):
                    last = nc.tensor.matmul(K.ps[4 + b][0:rows, h * rows:(h + 1) * rows], T[0:rows, i, h, 0:rows],
                                            y[0:rows, b, h, 0:rows], start=True, stop=True)
                last.then_inc(*ds.up())

        @block.scalar
        def _(act):
            for m, (s, n) in enumerate(steps):
                i, rows, _ = units[n]
                act.wait_ge(*ys.at(m + 1))
                if m >= 2:
                    act.wait_ge(*ds.at(m - 1))
                nc.scalar.copy(y[0:rows, m % 2, :, 0:rows],
                               K.ps[m % 2][0:rows, 0:4 * rows].rearrange("p (h n) -> p h n", h=4)).then_inc(*yc.up())

        @block.vector
        def _(dve):
            for m, (s, n) in enumerate(steps):
                i, rows, _ = units[n]
                dve.wait_ge(*ds.at(m + 1))
                for dst, bank, sig in ((T, 2, ts), (R, 4, rs)):
                    d = dst[0:rows, i, :, 0:rows]
                    nc.vector.tensor_tensor(d, d, K.ps[bank + m % 2][0:rows, 0:4 * rows].rearrange(
                        "p (h n) -> p h n", h=4), ALU.subtract).then_inc(*sig.up())


def first_level(K, low, T, R, units):
    nc = K.nc
    with K.phase("inv_first") as (block, step):
        @block.vector
        def _(dve):
            link = chain(dve, step)
            for i, rows, _ in units:
                d = T[0:rows, i, :, 0:rows]
                mask = K.const("level1")[0:rows, 0:rows].unsqueeze(1).broadcast_to([rows, 4, rows])
                ident = K.const("ident")[0:rows, 0:rows].unsqueeze(1).broadcast_to([rows, 4, rows])
                link(nc.vector.tensor_tensor(d, low[0:rows, i, :, 0:rows], mask, ALU.mult))
                link(nc.vector.tensor_tensor(d, ident, d, ALU.subtract))
    transpose_phase(K, [([T[0:rows, i, h, 0:rows] for h in range(4)], R[0:rows, i, :, 0:rows])
                        for i, rows, _ in units])


LEVELS = [2, 4, 8, 16, 32]


def ab_scan(K, st, kq, v, kd, ab, o):
    nc, I, O = K.nc, K.ins, K.outs
    qkd = K.sb(st, "qkd", [128, TILES, 8, 128])
    R = K.sb(st, "R", [128, TILES, 4, 128])
    beta = K.sb(st, "beta", [128, TILES, 4])
    gcol = K.sb(st, "gcol", [128, TILES, 8])
    egc = K.sb(st, "egc", [128, TILES, 8])
    ekd = K.sb(st, "ekd", [128, TILES, 8])
    nbeg = K.sb(st, "nbeg", [128, TILES, 4])
    total = K.sb(st, "total", [128, 4 + SEQS, 8])
    with contextlib.ExitStack() as tmp:
        arow = K.sb(tmp, "arow", [128, 8])
        g = K.sb(tmp, "g", [128, TILES, 4])
        s1 = K.sb(tmp, "s1", [128, TILES, 4])
        s2 = K.sb(tmp, "s2", [128, TILES, 4])
        gup = K.sb(tmp, "gup", [128, TILES, 4, 128])
        gp = K.sb(tmp, "gp", [128, 4, 4])
        gb = K.sb(tmp, "gb", [128, SEQS, 4])
        low = K.sb(tmp, "low", [128, TILES, 4, 128])
        T = K.sb(tmp, "T", [128, TILES, 4, 128])
        c = K.sb(tmp, "c", [128, 2, 4, 128])
        y = K.sb(tmp, "y", [128, 2, 4, 128])
        with K.phase("g_in", "g_act", "g_dve") as (block, loaded, by_act, by_dve):
            full = [(slice(0, 128), slice(0, 2)), (slice(0, SAMPLE), slice(2, 3))]

            @block.sync
            def _(sp):
                sp.dma_start(arow[:, 0:4], row_broadcast(I["ab_a_log"][0])).then_inc(*loaded.up(16))
                sp.dma_start(arow[:, 4:8], row_broadcast(I["ab_dt_bias"][0])).then_inc(*loaded.up(16))

            @block.scalar
            def _(act):
                link = chain(act, by_act)
                act.wait_ge(*loaded.at(32))
                link(nc.scalar.activation(arow[:, 0:4], arow[:, 0:4], ACT.Exp))
                act.wait_ge(*by_dve.at(2))
                for r, t in full:
                    nc.scalar.activation(beta[r, t, :], ab[r, t, 4:8], ACT.Sigmoid)
                for r, t in full:
                    last = nc.scalar.activation(s2[r, t, :], s1[r, t, :], ACT.Exp)
                link(last)
                for r, t in full:
                    last = nc.scalar.activation(s2[r, t, :], s2[r, t, :], ACT.Ln, bias=1.0)
                link(last)

            @block.vector
            def _(dve):
                link = chain(dve, by_dve)
                dve.wait_ge(*loaded.at(32))
                for r, t in full:
                    n = t.stop - t.start
                    last = nc.vector.tensor_tensor(g[r, t, :], ab[r, t, 0:4], arow[r, 4:8].unsqueeze(1).broadcast_to(
                        [r.stop, n, 4]), ALU.add)
                link(last)
                for r, t in full:
                    last = nc.vector.scalar_tensor_tensor(s1[r, t, :], g[r, t, :], -1.0, g[r, t, :], ALU.mult, ALU.min)
                link(last)
                dve.wait_ge(*by_act.at(3))
                for r, t in full:
                    last = nc.vector.scalar_tensor_tensor(g[r, t, :], g[r, t, :], 0.0, s2[r, t, :], ALU.max, ALU.add)
                link(last)
                for r, t in full:
                    n = t.stop - t.start
                    last = nc.vector.scalar_tensor_tensor(
                        g[r, t, :], g[r, t, :], -1.0, arow[r, 0:4].unsqueeze(1).broadcast_to([r.stop, n, 4]),
                        ALU.mult, ALU.mult)
                link(last)
                for t in range(TILES):
                    r = ROWS[t]
                    for h in range(4):
                        nc.vector.tensor_scalar(gup[0:r, t, h, 0:r], K.const("upto_" + tile_kind(t))[0:r, 0:r],
                                                g[0:r, t, h:h + 1], None, ALU.mult)
                for n in range(4):
                    nc.vector.tensor_scalar(gp[:, n, :], g[:, n // 2, :], K.const("of_chunk_p")[:, n % 2:n % 2 + 1],
                                            None, ALU.mult)
                nc.vector.tensor_tensor(
                    gb[0:SAMPLE], g[0:SAMPLE, 2, :].unsqueeze(1).broadcast_to([SAMPLE, SEQS, 4]),
                    K.const("of_chunk_s")[0:SAMPLE, :].unsqueeze(2).broadcast_to([SAMPLE, SEQS, 4]), ALU.mult)
        with K.phase("sum_full", "low_done", "dec_act", "dec_dve", "dec_pool") as (
                block, full, low_done, by_act, by_dve, by_pool):
            tot = K.ps[3][:, 32:80].rearrange("p (c h) -> p c h", h=4)

            @block.tensor
            def _(pe):
                for t in range(TILES):
                    r, kind = ROWS[t], tile_kind(t)
                    nc.tensor.matmul(K.ps[t][0:r, 0:4 * r], K.const("ones")[0:r, 0:r],
                                     gup[0:r, t, :, 0:r], start=True, stop=True)
                    nc.tensor.matmul(K.ps[3][0:r, 8 * t:8 * t + 4], K.const("upto_" + kind)[0:r, 0:r], g[0:r, t, :],
                                     start=True, stop=True)
                    nc.tensor.matmul(K.ps[3][0:r, 8 * t + 4:8 * t + 8], K.const("below_" + kind)[0:r, 0:r],
                                     g[0:r, t, :], start=True, stop=True)
                nc.tensor.matmul(tot[:, 0:4, :], K.const("ones"), gp[:, :, :], start=True, stop=True)
                nc.tensor.matmul(tot[:, 4:12, :], K.const("ones")[0:SAMPLE, :], gb[0:SAMPLE, :, :],
                                 start=True, stop=True).then_inc(*full.up())
                for t in range(TILES):
                    r = ROWS[t]
                    if t >= 1:
                        pe.wait_ge(*low_done.at(3 * t))
                    for h in range(4):
                        nc.tensor.matmul(K.ps[4][0:r, h * r:(h + 1) * r], kq[:, 0, h, cols_of(t)],
                                         kq[:, 0, h, cols_of(t)], start=True, stop=True)
                    for h in range(8):
                        last = nc.tensor.matmul(K.ps[5 + h // 4][0:r, h % 4 * r:(h % 4 + 1) * r],
                                                kq[:, 0, h, cols_of(t)], kq[:, 1, h, cols_of(t)],
                                                start=True, stop=True)
                    last.then_inc(*full.up())

            @block.vector
            def _(dve):
                link = chain(dve, by_dve)
                dve.wait_ge(*full.at(1))
                for t in range(TILES):
                    r = ROWS[t]
                    last = nc.vector.tensor_copy(gcol[0:r, t, :], K.ps[3][0:r, 8 * t:8 * t + 8])
                link(last)
                for t in range(TILES):
                    r = ROWS[t]
                    for h in range(4):
                        s = K.ps[t][0:r, h * r:(h + 1) * r]
                        gc = gcol[0:r, t, h:h + 1]
                        nc.vector.tensor_scalar(low[0:r, t, h, 0:r], s, gc, 0.0, ALU.subtract, ALU.max)
                        last = nc.vector.tensor_scalar(qkd[0:r, t, h, 0:r], s, gc, 0.0, ALU.subtract, ALU.min)
                link(last)
                dve.wait_ge(*by_act.at(1))
                for t in range(TILES):
                    r, kind = ROWS[t], tile_kind(t)
                    below = K.const("below_" + kind)[0:r, 0:r].unsqueeze(1).broadcast_to([r, 4, r])
                    upto = K.const("upto_" + kind)[0:r, 0:r].unsqueeze(1).broadcast_to([r, 4, r])
                    nc.vector.tensor_tensor(low[0:r, t, :, 0:r], low[0:r, t, :, 0:r], below, ALU.mult)
                    last = nc.vector.tensor_tensor(qkd[0:r, t, 0:4, 0:r], qkd[0:r, t, 0:4, 0:r], upto, ALU.mult)
                link(last)
                for t in range(TILES):
                    r, kind = ROWS[t], tile_kind(t)
                    dve.wait_ge(*full.at(t + 2))
                    for h in range(4):
                        last = nc.vector.scalar_tensor_tensor(
                            low[0:r, t, h, 0:r], K.ps[4][0:r, h * r:(h + 1) * r], beta[0:r, t, h:h + 1],
                            low[0:r, t, h, 0:r], ALU.mult, ALU.mult)
                    last.then_inc(*low_done.up())
                    nc.vector.tensor_tensor(qkd[0:r, t, 0:4, 0:r], qkd[0:r, t, 0:4, 0:r],
                                            K.ps[5][0:r, 0:4 * r].rearrange("p (h n) -> p h n", h=4), ALU.mult
                                            ).then_inc(*low_done.up())
                    ret = K.const("retdecay_" + kind)[0:r].rearrange("p (h n) -> p h n", h=4)[:, :, 0:r]
                    nc.vector.tensor_tensor(qkd[0:r, t, 4:8, 0:r], ret,
                                            K.ps[6][0:r, 0:4 * r].rearrange("p (h n) -> p h n", h=4), ALU.mult
                                            ).then_inc(*low_done.up())
                    nc.vector.tensor_copy(egc[0:r, t, 4:8], K.const("retq_" + kind)[0:r])
                    nc.vector.tensor_copy(ekd[0:r, t, 4:8], K.const("retk_" + kind)[0:r])
                    link(nc.vector.scalar_tensor_tensor(nbeg[0:r, t, :], egc[0:r, t, 0:4], -1.0, beta[0:r, t, :],
                                                   ALU.mult, ALU.mult))
                    for h in range(8):
                        nc.vector.tensor_scalar(kd[0:r, t, h, :], kd[0:r, t, h, :], ekd[0:r, t, h:h + 1], None,
                                                ALU.mult)
                        if h < 4:
                            nc.vector.tensor_scalar(v[0:r, t, h, :], v[0:r, t, h, :], beta[0:r, t, h:h + 1], None,
                                                    ALU.mult)
                for h in range(4):
                    nc.vector.memset(total[:, 0:4, 4 + h], CHUNK_DECAY[CHUNK][h])
                    nc.vector.memset(total[:, 4:12, 4 + h], CHUNK_DECAY[STEPS][h])

            @block.scalar
            def _(act):
                act.wait_ge(*by_dve.at(2))
                for t in range(TILES):
                    r = ROWS[t]
                    nc.scalar.activation(low[0:r, t, :, 0:r], low[0:r, t, :, 0:r], ACT.Exp, scale=-1.0)
                    nc.scalar.activation(qkd[0:r, t, 0:4, 0:r], qkd[0:r, t, 0:4, 0:r], ACT.Exp)
                    nc.scalar.activation(egc[0:r, t, 0:4], gcol[0:r, t, 0:4], ACT.Exp)
                    nc.scalar.activation(ekd[0:r, t, 0:4], gcol[0:r, t, 4:8], ACT.Exp)
                nc.scalar.activation(total[:, :, 0:4], tot, ACT.Exp).then_inc(*by_act.up())
        units = [(t, ROWS[t], LEVELS if t < 2 else [2, 4]) for t in range(TILES)]
        first_level(K, low, T, R, units)
        invert_phase(K, low, T, R, (c, y), units, LEVELS)
    ab_chunks(K, kq, v, kd, qkd, R, egc, nbeg, total, o)


def ab_chunks(K, kq, v, kd, qkd, R, egc, nbeg, total, o):
    nc, I, O = K.nc, K.ins, K.outs
    with contextlib.ExitStack() as tmp:
        S = K.sb(tmp, "S", [128, 8, 128])
        vn = K.sb(tmp, "vn", [128, 4, 128])
        r_ = K.sb(tmp, "r", [128, 4, 128])
        for n in range(5):
            ab_chunk(K, n, kq, v, kd, qkd, R, egc, nbeg, total, o, S, vn, r_)


def ab_chunk(K, n, kq, v, kd, qkd, R, egc, nbeg, total, o, S, vn, r_):
    nc, I, O = K.nc, K.ins, K.outs
    sample = n == 4
    t, off = (2, 0) if sample else (n // 2, 64 * (n % 2))
    sl = slice(off, off + 64)
    c = slice(AT[t] + off, AT[t] + off + 64)
    with contextlib.ExitStack() as tmp:
        if sample:
            ab_sample_states(K, tmp, kq)
        with K.phase("ks_full", "r_done", "vn_full", "vn_done", "o_full", "o_scaled", "o_done", "su_full",
                     "s_done", "s_out") as (
                block, ks, rd, vf, vd, of, osc, od, sf, sd, out):
            @block.tensor
            def _(pe):
                if not sample and n:
                    for h in range(4):
                        nc.tensor.matmul(K.ps[0][sl, h * 128:(h + 1) * 128], kq[:, 0, h, c], S[:, h, :],
                                         start=True, stop=True)
                    for h in range(8):
                        last = nc.tensor.matmul(K.ps[1 + h // 4][sl, h % 4 * 128:(h % 4 + 1) * 128], kq[:, 1, h, c],
                                                S[:, h, :], start=True, stop=True)
                    last.then_inc(*ks.up())
                elif sample:
                    for h in range(4):
                        nc.tensor.matmul(K.ps[0][sl, h * 128:(h + 1) * 128], K.byst[:, h, 0, :], K.const("ident"),
                                         start=True, stop=True)
                    for h in range(8):
                        last = nc.tensor.matmul(K.ps[1 + h // 4][sl, h % 4 * 128:(h % 4 + 1) * 128],
                                                K.byst[:, h, 1, :], K.const("ident"), start=True, stop=True)
                    last.then_inc(*ks.up())
                if n:
                    pe.wait_ge(*rd.at(1))
                src = r_ if n else v[:, 0, 0:4, :]
                for h in range(4):
                    last = nc.tensor.matmul(K.ps[3][sl, h * 128:(h + 1) * 128], R[sl, t, h, sl], src[sl, h, :],
                                            start=True, stop=True)
                last.then_inc(*vf.up())
                pe.wait_ge(*vd.at(1))
                for h in range(8):
                    vals = vn[sl, h, :] if h < 4 else v[sl, t, h, :]
                    last = nc.tensor.matmul(K.ps[4 + h // 4][sl, h % 4 * 128:(h % 4 + 1) * 128], qkd[sl, t, h, sl],
                                            vals, start=True, stop=True)
                last.then_inc(*of.up())
                if not sample:
                    for h in range(8):
                        vals = vn[sl, h, :] if h < 4 else v[sl, t, h, :]
                        last = nc.tensor.matmul(K.ps[6 + h // 4][:, h % 4 * 128:(h % 4 + 1) * 128], kd[sl, t, h, :],
                                                vals, start=True, stop=True)
                    last.then_inc(*sf.up())

            @block.scalar
            def _(act):
                act.wait_ge(*vf.at(1))
                nc.scalar.copy(vn[sl, :, :], K.ps[3][sl, :].rearrange("p (h n) -> p h n", h=4)).then_inc(*vd.up())
                if n:
                    for h in range(8):
                        last = nc.scalar.mul(o[sl, t, h, :], K.ps[1 + h // 4][sl, h % 4 * 128:(h % 4 + 1) * 128],
                                             egc[sl, t, h:h + 1])
                    last.then_inc(*osc.up())

            @block.vector
            def _(dve):
                if n:
                    dve.wait_ge(*ks.at(1))
                    for h in range(4):
                        last = nc.vector.scalar_tensor_tensor(
                            r_[sl, h, :], K.ps[0][sl, h * 128:(h + 1) * 128], nbeg[sl, t, h:h + 1], v[sl, t, h, :],
                            ALU.mult, ALU.add)
                    last.then_inc(*rd.up())
                if not sample:
                    dve.wait_ge(*sf.at(1))
                    for h in range(8):
                        up = K.ps[6 + h // 4][:, h % 4 * 128:(h % 4 + 1) * 128]
                        if n:
                            last = nc.vector.scalar_tensor_tensor(S[:, h, :], S[:, h, :], total[:, n, h:h + 1], up,
                                                                  ALU.mult, ALU.add)
                        else:
                            last = nc.vector.tensor_copy(S[:, h, :], up)
                    last.then_inc(*sd.up())
                dve.wait_ge(*of.at(1))
                if n:
                    dve.wait_ge(*osc.at(1))
                for q in range(2):
                    ops = K.ps[4 + q][sl, :].rearrange("p (h n) -> p h n", h=4)
                    dst = o[sl, t, 4 * q:4 * q + 4, :]
                    if n:
                        nc.vector.tensor_tensor(dst, dst, ops, ALU.add)
                    else:
                        nc.vector.tensor_copy(dst, ops)

            if n == 3:
                @block.sync
                def _(sp):
                    sp.wait_ge(*sd.at(1))
                    for q, i in ((0, 5), (1, 6)):
                        sp.dma_start(O[i][0, 0].rearrange("h k v -> k h v"), S[:, 4 * q:4 * q + 4, :]
                                     ).then_inc(*out.up(16))
                    sp.wait_ge(*out.at(32))
        if sample:
            ab_sample_update(K, tmp, kd, v, vn, total)


def ab_sample_states(K, tmp, kq):
    nc, I = K.nc, K.ins
    K.byst = K.sb(tmp, "byst", [128, 8, 2, SAMPLE])
    K.state = K.sb(tmp, "state", [128, 2, SEQS, 128])
    with K.phase("st_in0", "st_in1", "st_full", "st_done") as (block, in0, in1, full, done):
        ins = (in0, in1)

        @block.sync
        def _(sp):
            for h in range(8):
                if h >= 2:
                    sp.wait_ge(*full.at(h - 1))
                src = I["state_delta" if h < 4 else "state_ret"][0, :, h % 4].rearrange("b k v -> k b v")
                sp.dma_start(K.state[:, h % 2, :, :], src).then_inc(*ins[h % 2].up(16))

        @block.tensor
        def _(pe):
            for h in range(8):
                pe.wait_ge(*ins[h % 2].at(16 * (h // 2 + 1)))
                if h >= 2:
                    pe.wait_ge(*done.at(h - 1))
                bank = K.ps[h % 2][:, 0:2 * SAMPLE].rearrange("p (i c) -> p i c", i=2)
                for b in range(SEQS):
                    c = slice(SEQ + 8 * b, SEQ + 8 * b + 8)
                    last = nc.tensor.matmul(bank[:, :, 8 * b:8 * b + 8], K.state[:, h % 2, b, :], kq[:, :, h, c],
                                            start=True, stop=True)
                last.then_inc(*full.up())

        @block.scalar
        def _(act):
            for h in range(8):
                act.wait_ge(*full.at(h + 1))
                nc.scalar.copy(K.byst[:, h, :, :], K.ps[h % 2][:, 0:2 * SAMPLE].rearrange("p (i c) -> p i c", i=2)
                               ).then_inc(*done.up())


def ab_sample_update(K, tmp, kd, v, vn, total):
    nc, I, O = K.nc, K.ins, K.outs
    spread = K.sb(tmp, "spread", [SAMPLE, 2, SEQS, 128])
    with K.phase("st_in0", "st_in1", "spread_done", "su_full", "su_done", "su_out0", "su_out1") as (
            block, in0, in1, sp_done, full, done, out0, out1):
        ins, outs = (in0, in1), (out0, out1)

        def store(sp, h):
            sp.wait_ge(*done.at(h + 1))
            dst = O[10 if h < 4 else 11][0, :, h % 4].rearrange("b k v -> k b v")
            sp.dma_start(dst, K.state[:, h % 2, :, :]).then_inc(*outs[h % 2].up(16))

        @block.sync
        def _(sp):
            for h in range(8):
                if h >= 2:
                    sp.wait_ge(*outs[h % 2].at(16 * (h // 2)))
                src = I["state_delta" if h < 4 else "state_ret"][0, :, h % 4].rearrange("b k v -> k b v")
                sp.dma_start(K.state[:, h % 2, :, :], src).then_inc(*ins[h % 2].up(16))
                if h >= 1:
                    store(sp, h - 1)
            store(sp, 7)
            for q in range(2):
                sp.wait_ge(*outs[q].at(64))

        @block.gpsimd
        def _(pool):
            for h in range(8):
                if h >= 2:
                    pool.wait_ge(*full.at(h - 1))
                vals = vn[0:SAMPLE, h, :] if h < 4 else v[0:SAMPLE, 2, h, :]
                nc.gpsimd.tensor_tensor(
                    spread[:, h % 2, :, :], vals.unsqueeze(1).broadcast_to([SAMPLE, SEQS, 128]),
                    K.const("of_chunk_s")[0:SAMPLE, :].unsqueeze(2).broadcast_to([SAMPLE, SEQS, 128]), ALU.mult
                ).then_inc(*sp_done.up())

        @block.tensor
        def _(pe):
            for h in range(8):
                pe.wait_ge(*sp_done.at(h + 1))
                if h >= 2:
                    pe.wait_ge(*done.at(h - 1))
                for q in range(2):
                    last = nc.tensor.matmul(K.ps[2 * (h % 2) + q][:, :], kd[0:SAMPLE, 2, h, :],
                                            spread[:, h % 2, 4 * q:4 * q + 4, :], start=True, stop=True)
                last.then_inc(*full.up())

        @block.vector
        def _(dve):
            for h in range(8):
                dve.wait_ge(*full.at(h + 1))
                dve.wait_ge(*ins[h % 2].at(16 * (h // 2 + 1)))
                for b in range(SEQS):
                    s = K.state[:, h % 2, b, :]
                    last = nc.vector.scalar_tensor_tensor(
                        s, s, total[:, 4 + b, h:h + 1], K.ps[2 * (h % 2) + b // 4][:, b % 4 * 128:(b % 4 + 1) * 128],
                        ALU.mult, ALU.add)
                last.then_inc(*done.up())


def ab_finish(K, o):
    nc, I = K.nc, K.ins
    with contextlib.ExitStack() as tmp:
        gate = K.sb(tmp, "gate", [128, TILES, D])
        nw = K.sb(tmp, "nw", [128, 128])
        sq = K.sb(tmp, "sq", [128, D])
        mean = K.sb(tmp, "mean", [128, TILES, 8])
        ms = K.sb(tmp, "ms", [128, TILES, 8])
        with K.phase("fin_in", "fin_act", "fin_var", "fin_step", "fin_silu") as (block, loaded, std, var, step, silu):
            @block.sync
            def _(sp):
                for t in range(TILES):
                    sp.dma_start(gate[0:ROWS[t], t, :], K.scratch["gate"][cols_of(t), :]).then_inc(*loaded.up(16))
                sp.dma_start(nw[:, :], row_broadcast(I["ab_norm_w"][0])).then_inc(*loaded.up(16))

            @block.scalar
            def _(act):
                act.wait_ge(*loaded.at(64))
                for t in range(TILES):
                    nc.scalar.activation(gate[0:ROWS[t], t, :], gate[0:ROWS[t], t, :], ACT.Silu).then_inc(*silu.up())
                for t in range(TILES):
                    act.wait_ge(*var.at(t + 1))
                    r = ROWS[t]
                    nc.scalar.activation(ms[0:r, t, 0:4], ms[0:r, t, 0:4], ACT.Sqrt, scale=1.0 / 128,
                                         bias=K.eps6[0:r, 0:1])
                    nc.scalar.activation(ms[0:r, t, 4:8], ms[0:r, t, 4:8], ACT.Sqrt, scale=1.0 / 128,
                                         bias=K.eps5[0:r, 0:1]).then_inc(*std.up())

            @block.vector
            def _(dve):
                link = chain(dve, step)
                dve.wait_ge(*loaded.at(64))
                for t in range(TILES):
                    r = ROWS[t]
                    ot = o[0:r, t, :, :]
                    link(nc.vector.tensor_reduce(mean[0:r, t, 4:8], ot[:, 4:8, :], AX, ALU.add))
                    link(nc.vector.tensor_scalar(mean[0:r, t, 4:8], mean[0:r, t, 4:8], 1.0 / 128, None, ALU.mult))
                    link(nc.vector.tensor_tensor(ot[:, 4:8, :], ot[:, 4:8, :], mean[0:r, t, 4:8].unsqueeze(2
                                                 ).broadcast_to([r, 4, 128]), ALU.subtract))
                    sqv = sq[0:r, :].rearrange("p (h n) -> p h n", h=8)
                    link(nc.vector.tensor_tensor(sqv, ot, ot, ALU.mult))
                    nc.vector.tensor_reduce(ms[0:r, t, :], sqv, AX, ALU.add).then_inc(*var.up())
                    dve.wait_ge(*var.at(t + 1))
                for t in range(TILES):
                    r = ROWS[t]
                    ot = o[0:r, t, :, :]
                    dve.wait_ge(*std.at(t + 1))
                    link(nc.vector.reciprocal(ms[0:r, t, :], ms[0:r, t, :]))
                    link(nc.vector.tensor_tensor(ot, ot, ms[0:r, t, :].unsqueeze(2).broadcast_to([r, 8, 128]),
                                                 ALU.mult))
                    link(nc.vector.tensor_tensor(ot[:, 0:4, :], ot[:, 0:4, :], nw[0:r, :].unsqueeze(1).broadcast_to(
                        [r, 4, 128]), ALU.mult))
                    dve.wait_ge(*silu.at(t + 1))
                    link(nc.vector.tensor_tensor(ot, ot, gate[0:r, t, :].rearrange("p (h n) -> p h n", h=8),
                                                 ALU.mult))
        outT = K.sb(tmp, "outT", [128, KT, TOK])
        transpose_phase(K, [([o[0:ROWS[t], t, 4 * q + j, :] for j in range(4)],
                             outT[:, 4 * q:4 * q + 4, cols_of(t)]) for t in range(TILES) for q in range(2)])
        add_and_norm_phase(K, K.first["ab_out"], outT, 0, 0)



def cross_attention(K, layer):
    nc, I, O = K.nc, K.ins, K.outs
    with contextlib.ExitStack() as st:
        oT = K.sb(st, "oT", [128, KT, TOK])
        with contextlib.ExitStack() as tmp:
            kT = K.sb(tmp, "kT", [128, KT, MEM])
            v = K.sb(tmp, "v", [128, 2, D])
            qT = K.sb(tmp, "qT", [128, KT, WIDE])
            with contextlib.ExitStack() as t1:
                mem = K.sb(t1, "mem", [128, 2, D])
                memT = K.sb(t1, "memT", [128, KT, MEM])
                k = K.sb(t1, "k", [128, 2, D])
                with K.phase("mem_in") as (block, loaded):
                    @block.scalar
                    def _(act):
                        act.dma_start(mem[:, :, :], I["mem_prompt"][0].rearrange("(t p) n -> p t n", p=128)
                                      ).then_inc(*loaded.up(16))
                        act.wait_ge(*loaded.at(16))
                transpose_phase(K, [([mem[:, t, (4 * q + j) * 128:(4 * q + j + 1) * 128] for j in range(4)],
                                     memT[:, 4 * q:4 * q + 4, t * 128:(t + 1) * 128])
                                    for t in range(2) for q in range(2)])
                tiles = [(0, 128), (128, 128)]
                token_major_phase(
                    K, K.first[f"x_k{layer}"], 4, memT, tiles,
                    lambda g, t: (k, v)[g // 2][:, t, g % 2 * 512:g % 2 * 512 + 512],
                    stores=[(O[2][layer, 0].rearrange("(t p) h d -> p t (h d)", p=128), k[:, :, :]),
                            (O[3][layer, 0].rearrange("(t p) h d -> p t (h d)", p=128), v[:, :, :])])
                transpose_phase(K, [([k[:, t, (4 * q + j) * 128:(4 * q + j + 1) * 128] for j in range(4)],
                                     kT[:, 4 * q:4 * q + 4, t * 128:(t + 1) * 128])
                                    for t in range(2) for q in range(2)])
            feature_major_phase(K, K.first[f"x_q{layer}"], 2, K.xT, TOK,
                                lambda f, bank: [(qT[:, f, 0:TOK], bank[:, 0:TOK])])
            attend_prompt(K, qT, kT, v, oT)
            attend_samples(K, layer, qT, oT)
        add_and_norm_phase(K, K.first[f"x_o{layer}"], oT, layer, 1)


XSCALE = float(D // XH) ** -0.5


def attend_prompt(K, qT, kT, v, oT):
    nc = K.nc
    with contextlib.ExitStack() as tmp:
        p = K.sb(tmp, "p", [128, 8, MEM])
        pT = K.sb(tmp, "pT", [128, 2, 8, 128])
        col = K.sb(tmp, "col", [128, 3, 8])
        pairs = [(h, t) for h in range(XH) for t in range(2)]
        with K.phase("sc_full", "max_done", "exp_done", "p_step") as (block, full, maxed, exped, step):
            @block.gpsimd
            def _(pool):
                nc.gpsimd.memset(qT[:, :, TOK:WIDE], 0.0)

            @block.tensor
            def _(pe):
                for n, (h, t) in enumerate(pairs):
                    for j in range(2):
                        last = nc.tensor.matmul(K.ps[n][:, 0:MEM],
                                                qT[:, 2 * h + j, t * 128:(t + 1) * 128], kT[:, 2 * h + j, :],
                                                start=(j == 0), stop=(j == 1))
                    last.then_inc(*full.up())

            @block.vector
            def _(dve):
                link = chain(dve, step)
                for n in range(8):
                    dve.wait_ge(*full.at(n + 1))
                    link(nc.vector.reduce_max(col[:, 0, n:n + 1], K.ps[n][:, 0:MEM], AX))
                    nc.vector.tensor_scalar(col[:, 1, n:n + 1], col[:, 0, n:n + 1], -XSCALE, None, ALU.mult
                                            ).then_inc(*maxed.up())
                dve.wait_ge(*exped.at(8))
                link(nc.vector.reciprocal(col[:, 2, :], col[:, 2, :]))
                nc.vector.tensor_tensor(p[:, :, :], p[:, :, :], col[:, 2, :].unsqueeze(2).broadcast_to([128, 8, MEM]),
                                        ALU.mult)

            @block.scalar
            def _(act):
                for n in range(8):
                    act.wait_ge(*maxed.at(n + 1))
                    nc.scalar.activation(p[:, n, :], K.ps[n][:, 0:MEM], ACT.Exp,
                                         scale=XSCALE, bias=col[:, 1, n:n + 1], accum_out=col[:, 2, n:n + 1]
                                         ).then_inc(*exped.up())
        transpose_phase(K, [([p[:, 4 * q + j, m * 128:(m + 1) * 128] for j in range(4)],
                             pT[:, m, 4 * q:4 * q + 4, :]) for m in range(2) for q in range(2)])
        with K.phase("mm_full", "mm_act") as (block, full, by_act):
            @block.tensor
            def _(pe):
                for f in range(KT):
                    if f >= 4:
                        pe.wait_ge(*by_act.at(f - 3))
                    h = f // 2
                    for m in range(2):
                        last = nc.tensor.matmul(K.ps[f % 4][:, 0:SEQ], v[:, m, f * 128:(f + 1) * 128],
                                                pT[:, m, 2 * h:2 * h + 2, :], start=(m == 0), stop=(m == 1))
                    last.then_inc(*full.up())

            @block.scalar
            def _(act):
                for f in range(KT):
                    act.wait_ge(*full.at(f + 1))
                    nc.scalar.copy(oT[:, f, 0:SEQ], K.ps[f % 4][:, 0:SEQ]).then_inc(*by_act.up())


def attend_samples(K, layer, qT, oT):
    nc, I = K.nc, K.ins
    with contextlib.ExitStack() as tmp:
        kc = K.sb(tmp, "kc", [128, 2, 2, D])
        vc = K.sb(tmp, "vc", [128, 2, 2, D])
        kcT = K.sb(tmp, "kcT", [128, KT, MEM])
        p = K.sb(tmp, "p", [128, MEM])
        pT = K.sb(tmp, "pT", [128, 2, 128])
        col = K.sb(tmp, "col", [128, SEQS, 4])
        with K.phase("kc_in0", "kc_in1", "vc_in0", "vc_in1", "kt_full", "kt_act", "kt_dve", "sc_full", "max_done",
                     "exp_done", "p_done", "pt_full", "pt_done", "o_full", "o_done", "p_step") as (
                block, kin0, kin1, vin0, vin1, ktf, kta, ktd, scf, maxed, exped, pd, ptf, ptd, of, od, step):
            kin, vin = (kin0, kin1), (vin0, vin1)

            @block.sync
            def _(sp):
                for b in range(SEQS):
                    if b >= 2:
                        sp.wait_ge(*ktf.at(4 * (b - 1)))
                        sp.wait_ge(*of.at(b - 1))
                    for dst, name, sig in ((kc, "cache_mem_k", kin), (vc, "cache_mem_v", vin)):
                        sp.dma_start(dst[:, b % 2, :, :], I[name][layer, b].rearrange("(t p) h d -> p t (h d)", p=128)
                                     ).then_inc(*sig[b % 2].up(16))

            @block.tensor
            def _(pe):
                for b in range(SEQS):
                    pe.wait_ge(*kin[b % 2].at(16 * (b // 2 + 1)))
                    for n in range(4):
                        t, q = n // 2, n % 2
                        if b:
                            pe.wait_ge(*(kta if n % 2 == 0 else ktd).at(2 * (b - 1) + n // 2 + 1))
                        for j in range(4):
                            f = 4 * q + j
                            last = nc.tensor.transpose(K.ps[n][:, j * 128:(j + 1) * 128],
                                                       kc[:, b % 2, t, f * 128:(f + 1) * 128], K.const("ident"))
                        last.then_inc(*ktf.up())
                    pe.wait_ge(*kta.at(2 * (b + 1)))
                    pe.wait_ge(*ktd.at(2 * (b + 1)))
                    c = slice(SEQ + 8 * b, SEQ + 8 * b + 32)
                    if b:
                        pe.wait_ge(*exped.at(b))
                    for h in range(XH):
                        for j in range(2):
                            last = nc.tensor.matmul(K.ps[4][32 * h:32 * h + 32, 0:MEM], qT[:, 2 * h + j, c],
                                                    kcT[:, 2 * h + j, :], start=(j == 0), stop=(j == 1))
                    last.then_inc(*scf.up())
                    pe.wait_ge(*pd.at(b + 1))
                    if b:
                        pe.wait_ge(*ptd.at(b))
                    for m in range(2):
                        last = nc.tensor.transpose(K.ps[5][:, m * 128:(m + 1) * 128], p[:, m * 128:(m + 1) * 128],
                                                   K.const("ident"))
                    last.then_inc(*ptf.up())
                    pe.wait_ge(*ptd.at(b + 1))
                    pe.wait_ge(*vin[b % 2].at(16 * (b // 2 + 1)))
                    if b >= 2:
                        pe.wait_ge(*od.at(b - 1))
                    for f in range(KT):
                        h = f // 2
                        for m in range(2):
                            last = nc.tensor.matmul(K.ps[6 + b % 2][:, 8 * f:8 * f + 8],
                                                    vc[:, b % 2, m, f * 128:(f + 1) * 128],
                                                    pT[:, m, 32 * h:32 * h + 8], start=(m == 0), stop=(m == 1))
                    last.then_inc(*of.up())

            @block.scalar
            def _(act):
                for b in range(SEQS):
                    for n in (0, 2):
                        act.wait_ge(*ktf.at(4 * b + n + 1))
                        if b and n == 0:
                            act.wait_ge(*scf.at(b))
                        nc.scalar.copy(kcT[:, 0:4, n // 2 * 128:(n // 2 + 1) * 128],
                                       K.ps[n][:, :].rearrange("p (j n) -> p j n", j=4)).then_inc(*kta.up())
                    act.wait_ge(*maxed.at(b + 1))
                    if b:
                        act.wait_ge(*ptf.at(b))
                    nc.scalar.activation(p[:, :], K.ps[4][:, 0:MEM], ACT.Exp, scale=XSCALE, bias=col[:, b, 1:2],
                                         accum_out=col[:, b, 2:3]).then_inc(*exped.up())
                    act.wait_ge(*ptf.at(b + 1))
                    if b:
                        act.wait_ge(*of.at(b))
                    nc.scalar.copy(pT[:, :, :], K.ps[5][:, 0:2 * 128].rearrange("p (m n) -> p m n", m=2)
                                   ).then_inc(*ptd.up())

            @block.vector
            def _(dve):
                link = chain(dve, step)
                for b in range(SEQS):
                    for n in (1, 3):
                        dve.wait_ge(*ktf.at(4 * b + n + 1))
                        if b and n == 1:
                            dve.wait_ge(*scf.at(b))
                        nc.vector.tensor_copy(kcT[:, 4:8, n // 2 * 128:(n // 2 + 1) * 128],
                                              K.ps[n][:, :].rearrange("p (j n) -> p j n", j=4)).then_inc(*ktd.up())
                    dve.wait_ge(*scf.at(b + 1))
                    link(nc.vector.reduce_max(col[:, b, 0:1], K.ps[4][:, 0:MEM], AX))
                    nc.vector.tensor_scalar(col[:, b, 1:2], col[:, b, 0:1], -XSCALE, None, ALU.mult
                                            ).then_inc(*maxed.up())
                    dve.wait_ge(*exped.at(b + 1))
                    link(nc.vector.reciprocal(col[:, b, 3:4], col[:, b, 2:3]))
                    nc.vector.tensor_scalar(p[:, :], p[:, :], col[:, b, 3:4], None, ALU.mult).then_inc(*pd.up())
                    dve.wait_ge(*of.at(b + 1))
                    nc.vector.tensor_copy(oT[:, :, SEQ + 8 * b:SEQ + 8 * b + 8],
                                          K.ps[6 + b % 2][:, 0:64].rearrange("p (f s) -> p f s", f=8)
                                          ).then_inc(*od.up())



def moe(K, layer):
    nc, I = K.nc, K.ins
    with contextlib.ExitStack() as st:
        gates = K.sb(st, "gates", [128, TILES, EXPERTS])
        with contextlib.ExitStack() as tmp:
            route(K, tmp, layer, gates)
        moe_dense(K, st, layer)
        moe_norm(K, st, layer)
    if layer == 0:
        transpose_x(K)


def route(K, tmp, layer, gates):
    nc, I = K.nc, K.ins
    w = K.sb(tmp, "w", [128, KT, 36])
    bias = K.sb(tmp, "bias", [128, 36])
    lg = K.sb(tmp, "lg", [128, TILES, 36])
    a = K.sb(tmp, "a", [128, TILES, 8])
    e8 = K.sb(tmp, "e8", [128, TILES, 8])
    o1 = K.sb(tmp, "o1", [128, TILES, 8])
    o2 = K.sb(tmp, "o2", [128, TILES, 8])
    og = K.sb(tmp, "og", [128, TILES, 4])
    m = K.sb(tmp, "m", [128, TILES, 8])
    prod = K.sb(tmp, "prod", [128, TILES, 8, 4])
    gT = K.sb(tmp, "gT", [EXPERTS, TOK])
    with K.phase("r_in", "r_full", "r_exp", "r_step", "r_sub") as (block, loaded, full, exped, step, sub):
        @block.sync
        def _(sp):
            sp.dma_start(w[:, :, 0:4], I["moe_w_grp"][layer].rearrange("(k p) n -> p k n", p=128)
                         ).then_inc(*loaded.up(16))
            for g in range(GROUPS):
                sp.dma_start(w[:, :, 4 + 8 * g:12 + 8 * g], I["moe_w_exp"][layer, g].rearrange(
                    "(k p) n -> p k n", p=128)).then_inc(*loaded.up(16))
            sp.dma_start(bias[:, 0:4], row_broadcast(I["moe_b_grp"][layer])).then_inc(*loaded.up(16))
            sp.dma_start(bias[:, 4:36], row_broadcast(I["moe_b_exp"][layer].rearrange("g e -> (g e)"))
                         ).then_inc(*loaded.up(16))

        @block.tensor
        def _(pe):
            pe.wait_ge(*loaded.at(16 * 7))
            for t in range(TILES):
                for k in range(KT):
                    last = nc.tensor.matmul(K.ps[0][0:ROWS[t], 36 * t:36 * t + 36], K.xT[:, k, cols_of(t)], w[:, k, :],
                                            start=(k == 0), stop=(k == KT - 1))
            last.then_inc(*full.up())

        @block.scalar
        def _(act):
            for t in range(TILES):
                r = ROWS[t]
                act.wait_ge(*sub.at(t + 1))
                nc.scalar.activation(a[0:r, t, 0:4], a[0:r, t, 0:4], ACT.Exp)
                nc.scalar.activation(m[0:r, t, 5:6], m[0:r, t, 4:5], ACT.Exp).then_inc(*exped.up())

        @block.vector
        def _(dve):
            link = chain(dve, step)

            def first(r, t, val, mx, eq, tmp8, n):
                link(nc.vector.reduce_max(mx, val, AX))
                link(nc.vector.tensor_scalar(eq, val, mx, None, ALU.is_equal))
                link(nc.vector.tensor_tensor(eq, eq, K.const("descend")[0:r, 0:n], ALU.mult))
                link(nc.vector.reduce_max(tmp8, eq, AX))
                link(nc.vector.tensor_scalar(eq, K.const("descend")[0:r, 0:n], tmp8, None, ALU.is_equal))

            dve.wait_ge(*loaded.at(16 * 7))
            dve.wait_ge(*full.at(1))
            for t in range(TILES):
                r = ROWS[t]
                c = lambda i: m[0:r, t, i:i + 1]
                l = lg[0:r, t, :]
                link(nc.vector.tensor_tensor(l, K.ps[0][0:r, 36 * t:36 * t + 36], bias[0:r, :], ALU.add))
                first(r, t, l[:, 0:4], c(0), og[0:r, t, :], c(1), 4)
                link(nc.vector.tensor_scalar(a[0:r, t, 0:4], l[:, 0:4], c(0), None, ALU.subtract))
                link(nc.vector.tensor_tensor(prod[0:r, t], l[:, 4:36].rearrange("p (g e) -> p e g", g=4),
                                             og[0:r, t, :].unsqueeze(1).broadcast_to([r, 8, 4]), ALU.mult))
                link(nc.vector.tensor_reduce(e8[0:r, t, :], prod[0:r, t], AX, ALU.add))
                first(r, t, e8[0:r, t, :], c(2), o1[0:r, t, :], c(1), 8)
                link(nc.vector.scalar_tensor_tensor(e8[0:r, t, :], o1[0:r, t, :], -1e30, e8[0:r, t, :],
                                                    ALU.mult, ALU.add))
                first(r, t, e8[0:r, t, :], c(3), o2[0:r, t, :], c(1), 8)
                nc.vector.tensor_tensor(c(4), c(3), c(2), ALU.subtract).then_inc(*sub.up())
                dve.wait_ge(*exped.at(t + 1))
                link(nc.vector.tensor_reduce(c(6), a[0:r, t, 0:4], AX, ALU.add))
                link(nc.vector.scalar_tensor_tensor(c(6), c(5), 1.0, c(6), ALU.add, ALU.mult))
                link(nc.vector.reciprocal(c(6), c(6)))
                link(nc.vector.scalar_tensor_tensor(o2[0:r, t, :], o2[0:r, t, :], c(5), o1[0:r, t, :],
                                                    ALU.mult, ALU.add))
                link(nc.vector.tensor_scalar(o2[0:r, t, :], o2[0:r, t, :], c(6), None, ALU.mult))
                link(nc.vector.tensor_tensor(
                    gates[0:r, t, :].rearrange("p (g e) -> p g e", g=4),
                    og[0:r, t, :].unsqueeze(2).broadcast_to([r, 4, 8]),
                    o2[0:r, t, :].unsqueeze(1).broadcast_to([r, 4, 8]), ALU.mult))
    with K.phase("gt_full", "gt_done", "gt_out") as (block, full, done, out):
        @block.tensor
        def _(pe):
            for t in range(TILES):
                r = ROWS[t]
                last = nc.tensor.transpose(K.ps[0][0:EXPERTS, cols_of(t)], gates[0:r, t, :],
                                           K.const("ident")[0:r, 0:r])
            last.then_inc(*full.up())

        @block.vector
        def _(dve):
            dve.wait_ge(*full.at(1))
            nc.vector.tensor_copy(gT[:, :], K.ps[0][0:EXPERTS, 0:TOK]).then_inc(*done.up())

        @block.sync
        def _(sp):
            sp.wait_ge(*done.at(1))
            sp.dma_start(K.scratch["gates"], gT[:, :]).then_inc(*out.up(16))
            sp.wait_ge(*out.at(16))


def moe_dense(K, st, layer):
    nc, I = K.nc, K.ins
    first = K.first[f"moe{layer}"]
    w1 = I["moe_w1"][layer].rearrange("g e d f -> (g e) d f")
    w3 = I["moe_w3"][layer].rearrange("g e d f -> (g e) d f")
    w2 = I["moe_w2"][layer].rearrange("g e f d -> (g e) f d")
    with contextlib.ExitStack() as tmp:
        zero = K.sb(tmp, "zero", [128, 512])
        grow = K.sb(tmp, "grow", [128, 2, TOK])
        hs = K.sb(tmp, "hs", [128, 2, TOK])
        hT = K.sb(tmp, "hT", [128, 2, TOK])
        with K.phase("zeroed", "grow_in0", "grow_in1", "h_full", "silu_done", "h_raw", "h_done", "y_full",
                     "w13_read") as (
                block, zeroed, gin0, gin1, hf, sd, hr, hd, yf, w13):
            gin = (gin0, gin1)
            for sig in (hr, hd, yf):
                sig.base += 1
                sig.sent += 1
            slot = [(first + j) % RING for j in range(RING)]
            base = [K.arrival[first + j] for j in range(RING)]
            inc = [32, 16, 32, 16]

            @block.sync
            def _(sp):
                with sp.Fori(0, EXPERTS // 2 - 1) as it:
                    for j in range(2):
                        sp.wait_ge(w13.sem, it * 2 + (w13.base + j + 1))
                        up = K.ring[:, slot[2 * j], :].rearrange("p (k i f) -> p k i f", k=KT, i=2)
                        for i, w in enumerate((w1, w3)):
                            sp.dma_start(up[:, :, i, :], w[it * 2 + (2 + j)].rearrange("(k p) f -> p k f", p=128)
                                         ).then_inc(K.arrived[slot[2 * j]], 16)
                        sp.wait_ge(yf.sem, it * 2 + (yf.base + j + 1))
                        sp.dma_start(K.ring[:, slot[2 * j + 1], 0:2 * D].rearrange("p (k n) -> p k n", k=2),
                                     w2[it * 2 + (2 + j)].rearrange("(k p) n -> p k n", p=128)
                                     ).then_inc(K.arrived[slot[2 * j + 1]], 16)
                for j in range(2):
                    e = EXPERTS - 2 + j
                    sp.wait_ge(*w13.at(e + 1))
                    load_chunk(K, sp, first + 2 * e + RING)
                    sp.wait_ge(*yf.at(e + 1))
                    load_chunk(K, sp, first + 2 * e + 1 + RING)

            @block.gpsimd
            def _(pool):
                nc.gpsimd.memset(zero[:, :], 0.0).then_inc(*zeroed.up())
                for j in range(2):
                    pool.dma_start(grow[:, j, :], K.scratch["gates"][j, :].rearrange("(a n) -> a n", a=1
                                   ).broadcast_to([128, TOK])).then_inc(gin[j].sem, 16)
                with pool.Fori(0, EXPERTS // 2 - 1) as it:
                    for j in range(2):
                        pool.wait_ge(hd.sem, it * 4 + (hd.base + 2 * j + 2))
                        pool.dma_start(grow[:, j, :], K.scratch["gates"][bass.ds(it * 2 + (2 + j), 1), :
                                       ].broadcast_to([128, TOK])).then_inc(gin[j].sem, 16)
                gin[0].sent += 16 * EXPERTS // 2
                gin[1].sent += 16 * EXPERTS // 2

            @block.tensor
            def _(pe):
                pe.sem_inc(yf.sem, 1)
                pe.wait_ge(*zeroed.at(1))
                for b in range(6):
                    nc.tensor.matmul(K.ps[b][0:ROWS[b // 2], :], zero[:, 0:ROWS[b // 2]], zero[:, :],
                                     start=True, stop=False, skip_group_check=True)
                with pe.Fori(0, EXPERTS // 2) as it:
                    for j in range(2):
                        pe.wait_ge(K.arrived[slot[2 * j]], it * inc[2 * j] + base[2 * j])
                        w = K.ring[:, slot[2 * j], :].rearrange("p (k i f) -> p k i f", k=KT, i=2)
                        for f in range(2):
                            pe.wait_ge(hr.sem, it * 4 + (hr.base + 2 * j + f))
                            for i in range(2):
                                for k in range(KT):
                                    last = nc.tensor.matmul(K.ps[6 + i][:, 0:TOK], w[:, k, i, f * 128:(f + 1) * 128],
                                                            K.xT[:, k, 0:TOK], start=(k == 0), stop=(k == KT - 1))
                            last.then_inc(hf.sem, 1)
                        pe.wait_ge(hf.sem, it * 4 + (hf.base + 2 * j + 2))
                        pe.sem_inc(w13.sem, 1)
                        pe.wait_ge(K.arrived[slot[2 * j + 1]], it * inc[2 * j + 1] + base[2 * j + 1])
                        w = K.ring[:, slot[2 * j + 1], 0:2 * D].rearrange("p (k n) -> p k n", k=2)
                        pe.wait_ge(hd.sem, it * 4 + (hd.base + 2 * j + 2))
                        for b in range(6):
                            t = b // 2
                            for f in range(2):
                                last = nc.tensor.matmul(K.ps[b][0:ROWS[t], :], hT[:, f, cols_of(t)],
                                                        w[:, f, b % 2 * 512:(b % 2 + 1) * 512],
                                                        start=False, stop=False, skip_group_check=True)
                        last.then_inc(yf.sem, 1)
                for b in range(6):
                    nc.tensor.matmul(K.ps[b][0:ROWS[b // 2], :], zero[:, 0:ROWS[b // 2]], zero[:, :],
                                     start=False, stop=True, skip_group_check=True)

            @block.scalar
            def _(act):
                with act.Fori(0, EXPERTS // 2) as it:
                    for j in range(2):
                        for f in range(2):
                            act.wait_ge(hf.sem, it * 4 + (hf.base + 2 * j + f + 1))
                            if f == 0:
                                act.wait_ge(hd.sem, it * 4 + (hd.base + 2 * j))
                            nc.scalar.activation(hs[:, f, :], K.ps[6][:, 0:TOK], ACT.Silu).then_inc(sd.sem, 1)

            @block.vector
            def _(dve):
                dve.sem_inc(hr.sem, 1)
                dve.sem_inc(hd.sem, 1)
                with dve.Fori(0, EXPERTS // 2) as it:
                    for j in range(2):
                        dve.wait_ge(gin[j].sem, it * 16 + (gin[j].base + 16))
                        for f in range(2):
                            dve.wait_ge(sd.sem, it * 4 + (sd.base + 2 * j + f + 1))
                            if f == 0:
                                dve.wait_ge(yf.sem, it * 2 + (yf.base + j))
                            nc.vector.tensor_tensor(hT[:, f, :], hs[:, f, :], K.ps[7][:, 0:TOK], ALU.mult
                                                    ).then_inc(hr.sem, 1)
                            dve.wait_ge(hr.sem, it * 4 + (hr.base + 2 * j + f + 1))
                            nc.vector.tensor_tensor(hT[:, f, :], hT[:, f, :], grow[:, j, :], ALU.mult
                                                    ).then_inc(hd.sem, 1)

            for s in (hf, sd, hr, hd):
                s.sent += 2 * EXPERTS
            yf.sent += EXPERTS
            w13.sent += EXPERTS


def moe_norm(K, st, layer):
    nc, I = K.nc, K.ins
    with contextlib.ExitStack() as tmp:
        lnw, lnb = K.sb(tmp, "lnw", [128, D]), K.sb(tmp, "lnb", [128, D])
        stats, mv = K.sb(tmp, "stats", [128, 2, 6]), K.sb(tmp, "mv", [128, TILES, 4])
        with K.phase("norm_rows", "ln_var", "ln_std", "ln_step") as (block, rows_in, var, std, step):
            @block.sync
            def _(sp):
                sp.dma_start(lnw[:, :], row_broadcast(I["ln_w"][layer, 2])).then_inc(*rows_in.up(16))
                sp.dma_start(lnb[:, :], row_broadcast(I["ln_b"][layer, 2])).then_inc(*rows_in.up(16))

            @block.scalar
            def _(act):
                for t in range(TILES):
                    act.wait_ge(*var.at(t + 1))
                    nc.scalar.activation(mv[0:ROWS[t], t, 2:3], mv[0:ROWS[t], t, 1:2], ACT.Sqrt).then_inc(*std.up())

            @block.vector
            def _(dve):
                link = chain(dve, step)
                for t in range(TILES):
                    for g in range(2):
                        xs = K.x[0:ROWS[t], t, g * 512:(g + 1) * 512]
                        last = nc.vector.scalar_tensor_tensor(xs, xs, ALPHA, K.ps[2 * t + g][0:ROWS[t], :],
                                                              ALU.mult, ALU.add)
                    link(last)
                    if t == 0:
                        dve.wait_ge(*rows_in.at(32))
                    norm_tile(K, dve, link, std, var, t, ROWS[t], stats, mv, lnw, lnb)



C_HEADS = 16


def rwkv_mixer(K):
    nc, I, O = K.nc, K.ins, K.outs
    rwkv_project(K)
    with contextlib.ExitStack() as st:
        yT = K.sb(st, "yT", [128, KT, TOK])
        H = K.sb(st, "H", [128, KT, 128])
        for t in range(TILES):
            with contextlib.ExitStack() as tt:
                rwkv_tile(K, tt, t, H, yT)
        add_and_norm_phase(K, K.first["c_out"], yT, 1, 0)


def rwkv_project(K):
    nc, I, O = K.nc, K.ins, K.outs
    tiles = [(AT[t], ROWS[t]) for t in range(TILES)]
    with contextlib.ExitStack() as st:
        shift = K.sb(st, "shift", [SEQS, D])
        cols = K.sb(st, "cols", [48, 128])
        shT = K.sb(st, "shT", [128, KT, SEQS])
        mu = K.sb(st, "mu", [128, 6, KT])
        xx = K.sb(st, "xx", [128, KT, TOK])
        mix = K.sb(st, "mix", [128, KT, TOK])
        out = K.sb(st, "out", [128, TILES, D])
        hT = K.sb(st, "hT", [128, TOK])
        l1 = {"w": K.sb(st, "w1", [128, KT, 64]), "a": K.sb(st, "a1", [128, KT, 64]),
              "g": K.sb(st, "g1", [128, KT, 128])}
        l2 = {"w": K.sb(st, "w2", [64, D]), "a": K.sb(st, "a2", [64, D]), "g": K.sb(st, "g2", [128, D])}
        row = {"w": K.sb(st, "w0", [128, D]), "a": K.sb(st, "a0", [128, D])}
        with K.phase("c_in", "c_shift") as (block, loaded, shifted):
            @block.sync
            def _(sp):
                sp.dma_start(shift[:, :], I["state_shift_c"][0]).then_inc(*loaded.up(16))
                sp.dma_start(cols[:, :], I["c_mu"][0].rearrange("i (k p) -> (i k) p", p=128)).then_inc(*loaded.up(16))
                for n in "wag":
                    sp.dma_start(l1[n][:, :, :], I[f"c_w_{n}1"][0].rearrange("(k p) n -> p k n", p=128)
                                 ).then_inc(*loaded.up(16))
                    sp.dma_start(l2[n][:, :], I[f"c_w_{n}2"][0]).then_inc(*loaded.up(16))
                sp.dma_start(row["w"][:, :], row_broadcast(I["c_w0"][0])).then_inc(*loaded.up(16))
                sp.dma_start(row["a"][:, :], row_broadcast(I["c_a0"][0])).then_inc(*loaded.up(16))
                sp.dma_start(O[7][0], K.x[127:128, 1, :]).then_inc(*shifted.up(16))
                for b in range(SEQS):
                    sp.dma_start(O[12][0, b:b + 1], K.x[8 * b + 7:8 * b + 8, 2, :]).then_inc(*shifted.up(16))
                sp.wait_ge(*loaded.at(160))
                sp.wait_ge(*shifted.at(16 * 9))
        transpose_phase(K, [([shift[:, (4 * q + j) * 128:(4 * q + j + 1) * 128] for j in range(4)],
                             shT[:, 4 * q:4 * q + 4, :]) for q in range(2)]
                        + [([cols[:, :]], mu[:, :, :].rearrange("p i k -> p (i k)").unsqueeze(1))])
        with K.phase("xx_done") as (block, done):
            @block.vector
            def _(dve):
                x = K.xT
                nc.vector.tensor_tensor(xx[:, :, 1:SEQ], x[:, :, 0:SEQ - 1], x[:, :, 1:SEQ], ALU.subtract)
                nc.vector.tensor_scalar(xx[:, :, 0:1], x[:, :, 0:1], -1.0, None, ALU.mult)
                xs = x[:, :, SEQ:TOK].rearrange("p k (b s) -> p k b s", b=SEQS)
                ds = xx[:, :, SEQ:TOK].rearrange("p k (b s) -> p k b s", b=SEQS)
                for k in range(KT):
                    nc.vector.tensor_tensor(ds[:, k, :, 1:8], xs[:, k, :, 0:7], xs[:, k, :, 1:8], ALU.subtract)
                nc.vector.tensor_tensor(ds[:, :, :, 0], shT[:, :, :], xs[:, :, :, 0], ALU.subtract)

        def mixture(i):
            with K.phase("mix_done") as (block, done):
                @block.vector
                def _(dve):
                    for k in range(KT):
                        nc.vector.scalar_tensor_tensor(mix[:, k, :], xx[:, k, :], mu[:, i, k:k + 1],
                                                       K.xT[:, k, 0:TOK], ALU.mult, ALU.add)

        def stores(name):
            return [(K.scratch[name][cols_of(t), :], out[0:ROWS[t], t, :]) for t in range(TILES)]

        for i, n in ((0, "r"), (2, "k"), (3, "v")):
            mixture(i)
            token_major_phase(K, K.first["c_" + n], 2, mix, tiles,
                              lambda g, t: out[0:ROWS[t], t, g * 512:(g + 1) * 512], stores=stores(n))
        for i, n, inner in ((1, "w", ACT.Tanh), (4, "a", ACT.Copy), (5, "g", ACT.Sigmoid)):
            mixture(i)
            m = 128 if n == "g" else 64
            with K.phase("l1_full", "l1_done", "l2_full", "l2_done", "l2_out", "l2_step") as (
                    block, f1, d1, f2, d2, stored, step):
                @block.tensor
                def _(pe):
                    for k in range(KT):
                        last = nc.tensor.matmul(K.ps[0][0:m, 0:TOK], l1[n][:, k, :], mix[:, k, :],
                                                start=(k == 0), stop=(k == KT - 1))
                    last.then_inc(*f1.up())
                    pe.wait_ge(*d1.at(1))
                    for t in range(TILES):
                        for g in range(2):
                            last = nc.tensor.matmul(K.ps[1 + 2 * t + g][0:ROWS[t], :], hT[0:m, cols_of(t)],
                                                    l2[n][:, g * 512:(g + 1) * 512], start=True, stop=True)
                        last.then_inc(*f2.up())

                @block.scalar
                def _(act):
                    act.wait_ge(*f1.at(1))
                    nc.scalar.activation(hT[0:m, :], K.ps[0][0:m, 0:TOK], inner).then_inc(*d1.up())
                    for t in range(TILES):
                        r = ROWS[t]
                        if n == "g":
                            act.wait_ge(*f2.at(t + 1))
                            for g in range(2):
                                last = nc.scalar.copy(out[0:r, t, g * 512:(g + 1) * 512], K.ps[1 + 2 * t + g][0:r, :])
                            last.then_inc(*d2.up())
                        else:
                            act.wait_ge(*step.at(t + 1))
                            nc.scalar.activation(out[0:r, t, :], out[0:r, t, :], ACT.Sigmoid).then_inc(*d2.up())

                if n != "g":
                    @block.vector
                    def _(dve):
                        for t in range(TILES):
                            r = ROWS[t]
                            dve.wait_ge(*f2.at(t + 1))
                            for g in range(2):
                                c = slice(g * 512, (g + 1) * 512)
                                last = nc.vector.tensor_tensor(out[0:r, t, c], K.ps[1 + 2 * t + g][0:r, :],
                                                               row[n][0:r, c], ALU.add)
                            last.then_inc(*step.up())

                @block.sync
                def _(sp):
                    sp.wait_ge(*d2.at(TILES))
                    for dst, src in stores(n):
                        sp.dma_start(dst, src).then_inc(*stored.up(16))
                    sp.wait_ge(*stored.at(16 * TILES))


def rwkv_tile(K, st, t, H, yT):
    nc, I, O = K.nc, K.ins, K.outs
    rows, kind = ROWS[t], tile_kind(t)
    r = slice(0, rows)
    names = ["r", "k", "v", "w", "a"]
    d = {n: K.sb(st, "in_" + n, [128, D]) for n in names}
    bonus = K.sb(st, "bonus", [128, C_HEADS])
    ec = K.sb(st, "ec", [128, KT, 8])
    y = K.sb(st, "y", [128, D])
    with contextlib.ExitStack() as outer:
        ktr = K.sb(outer, "ktr", [128, KT, 2, rows])
        bkn = K.sb(outer, "bkn", [128, KT, 2, rows])
        with contextlib.ExitStack() as tmp:
            rwkv_factors(K, tmp, t, d, bonus, ec, ktr, bkn)
        if t == 2:
            byst = rwkv_sample_states(K, outer, ktr)
        for half in range(2):
            with contextlib.ExitStack() as tmp:
                rwkv_half(K, tmp, t, half, d, ec, ktr, bkn, H, y, byst if t == 2 else None)
        if t == 2:
            rwkv_sample_update(K, outer, d, ec)
    if t == 1:
        rwkv_prompt_state(K, H)
    rwkv_output(K, t, d, bonus, y, yT)


def rwkv_factors(K, tmp, t, d, bonus, ec, ktr, bkn):
    nc, I = K.nc, K.ins
    rows, kind = ROWS[t], tile_kind(t)
    r = slice(0, rows)
    kt = K.sb(tmp, "kt", [128, D])
    t1 = K.sb(tmp, "t1", [128, D])
    t2 = K.sb(tmp, "t2", [128, D])
    vec = {n: K.sb(tmp, "vec_" + n, [128, D]) for n in ("k_k", "k_a", "r_k")}
    ss = K.sb(tmp, "ss", [128, 3, C_HEADS])
    y_neg, y_pos = K.sb(tmp, "neg", [128, D]), K.sb(tmp, "pos", [128, D])
    h3 = lambda a: a[r, :].rearrange("p (h n) -> p h n", h=C_HEADS)
    with K.phase("f_in", "f_lw", "f_sum", "f_kk", "f_act", "f_dve", "f_root") as (
            block, loaded, lw, summed, kkd, by_act, by_dve, rooted):
        @block.sync
        def _(sp):
            for n in d:
                sp.dma_start(d[n][r, :], K.scratch[n][cols_of(t), :]).then_inc(*loaded.up(16))
            for n, src in (("k_k", I["c_k_k"][0]), ("k_a", I["c_k_a"][0]),
                           ("r_k", I["c_r_k"][0].rearrange("h n -> (h n)"))):
                sp.dma_start(vec[n][:, :], row_broadcast(src)).then_inc(*loaded.up(16))

        @block.tensor
        def _(pe):
            pe.wait_ge(*lw.at(1))
            for g in range(2):
                nc.tensor.matmul(K.ps[g][r, :], K.const("upto_" + kind)[r, 0:rows], d["w"][r, g * 512:(g + 1) * 512],
                                 start=True, stop=True)
            for f in range(KT):
                last = nc.tensor.matmul(K.ps[2][:, 8 * f:8 * f + 8], d["w"][r, f * 128:(f + 1) * 128],
                                        K.const("of_chunk_" + kind)[r, :], start=True, stop=True)
            last.then_inc(*summed.up())

        @block.scalar
        def _(act):
            act.wait_ge(*rooted.at(1))
            nc.scalar.activation(ss[r, 1, :], ss[r, 0, :], ACT.Sqrt, bias=K.eps6[r, 0:1]).then_inc(*by_act.up())
            act.wait_ge(*summed.at(1))
            nc.scalar.activation(ec[:, :, :], K.ps[2][:, 0:64].rearrange("p (f c) -> p f c", f=KT), ACT.Exp
                                 ).then_inc(*by_act.up())
            for g in range(2):
                c = slice(g * 512, (g + 1) * 512)
                nc.scalar.activation(y_neg[r, c], K.ps[g][r, :], ACT.Exp, scale=-1.0)
                last = nc.scalar.activation(y_pos[r, c], K.ps[g][r, :], ACT.Exp)
            last.then_inc(*by_act.up())
            act.wait_ge(*kkd.at(1))
            nc.scalar.activation(d["w"][r, :], d["w"][r, :], ACT.Exp).then_inc(*by_act.up())

        @block.vector
        def _(dve):
            link = chain(dve, by_dve)
            dve.wait_ge(*loaded.at(128))
            nc.vector.tensor_scalar(d["w"][r, :], d["w"][r, :], -float(np.exp(-0.5)), None, ALU.mult
                                    ).then_inc(*lw.up())
            link(nc.vector.tensor_tensor(kt[r, :], d["k"][r, :], vec["k_k"][r, :], ALU.mult))
            link(nc.vector.tensor_tensor(t1[r, :], kt[r, :], kt[r, :], ALU.mult))
            nc.vector.tensor_reduce(ss[r, 0, :], h3(t1), AX, ALU.add).then_inc(*rooted.up())
            nc.vector.scalar_tensor_tensor(t2[r, :], d["a"][r, :], -1.0, vec["k_a"][r, :], ALU.add, ALU.mult)
            dve.wait_ge(*by_act.at(1))
            link(nc.vector.reciprocal(ss[r, 2, :], ss[r, 1, :]))
            link(nc.vector.scalar_tensor_tensor(d["k"][r, :], t2[r, :], 1.0, d["k"][r, :], ALU.add, ALU.mult))
            link(nc.vector.tensor_tensor(h3(kt), h3(kt), ss[r, 2, :].unsqueeze(2).broadcast_to([rows, C_HEADS, 64]),
                                         ALU.mult))
            link(nc.vector.tensor_tensor(t1[r, :], d["r"][r, :], d["k"][r, :], ALU.mult))
            link(nc.vector.tensor_tensor(t1[r, :], t1[r, :], vec["r_k"][r, :], ALU.mult))
            nc.vector.tensor_reduce(bonus[r, :], h3(t1), AX, ALU.add)
            link(nc.vector.scalar_tensor_tensor(d["a"][r, :], d["a"][r, :], -1.0, kt[r, :], ALU.mult, ALU.mult))
            dve.wait_ge(*by_act.at(3))
            for g in range(2):
                c = slice(g * 512, (g + 1) * 512)
                last = nc.vector.scalar_tensor_tensor(d["w"][r, c], d["w"][r, c], -1.0, K.ps[g][r, :],
                                                      ALU.mult, ALU.add)
            last.then_inc(*kkd.up())
            nc.vector.tensor_tensor(d["a"][r, :], d["a"][r, :], y_neg[r, :], ALU.mult)
            nc.vector.tensor_tensor(d["k"][r, :], d["k"][r, :], y_neg[r, :], ALU.mult)
            nc.vector.tensor_tensor(d["r"][r, :], d["r"][r, :], y_pos[r, :], ALU.mult)
            dve.wait_ge(*by_act.at(4))
            nc.vector.tensor_tensor(kt[r, :], kt[r, :], d["w"][r, :], ALU.mult)
    groups = []
    for q in range(2):
        for src, dst, i in ((kt, ktr, 0), (d["r"], ktr, 1), (d["a"], bkn, 0), (d["k"], bkn, 1)):
            groups.append(([src[r, (4 * q + j) * 128:(4 * q + j + 1) * 128] for j in range(4)],
                           dst[:, 4 * q:4 * q + 4, i, :]))
    transpose_phase(K, groups)


def rwkv_half(K, tmp, t, half, d, ec, ktr, bkn, H, y, byst):
    nc = K.nc
    rows, kind = ROWS[t], tile_kind(t)
    r = slice(0, rows)
    mats = {n: K.sb(tmp, "m_" + n, [128, 2, 4, 128]) for n in ("low", "n", "rb", "rk", "T", "R")}
    with contextlib.ExitStack() as t2:
        work = (K.sb(t2, "c", [128, 2, 4, 128]), K.sb(t2, "y", [128, 2, 4, 128]))
        with K.phase("int_full", "int_done") as (block, full, done):
            @block.tensor
            def _(pe):
                for i in range(2):
                    if i:
                        pe.wait_ge(*done.at(4))
                    for h in range(4):
                        f = 4 * half + 2 * i + h // 2
                        k = slice(64 * (h % 2), 64 * (h % 2) + 64)
                        c = slice(h * rows, (h + 1) * rows)
                        kt, rt, bn, kn = ktr[k, f, 0, :], ktr[k, f, 1, :], bkn[k, f, 0, :], bkn[k, f, 1, :]
                        nc.tensor.matmul(K.ps[h % 2 * 4 + 0][r, h // 2 * rows:(h // 2 + 1) * rows], kt, bn, start=True, stop=True)
                        nc.tensor.matmul(K.ps[h % 2 * 4 + 1][r, h // 2 * rows:(h // 2 + 1) * rows], kn, kt, start=True, stop=True)
                        nc.tensor.matmul(K.ps[h % 2 * 4 + 2][r, h // 2 * rows:(h // 2 + 1) * rows], bn, rt, start=True, stop=True)
                        last = nc.tensor.matmul(K.ps[h % 2 * 4 + 3][r, h // 2 * rows:(h // 2 + 1) * rows], kn, rt, start=True, stop=True)
                    last.then_inc(*full.up())

            @block.vector
            def _(dve):
                for i in range(2):
                    dve.wait_ge(*full.at(i + 1))
                    for b, (n, mask) in enumerate((("low", "below_"), ("n", "above_"), ("rb", "upto_"),
                                                   ("rk", "upto_"))):
                        m = K.const(mask + kind)[r, 0:rows].unsqueeze(1).broadcast_to([rows, 2, rows])
                        for e in range(2):
                            src = K.ps[4 * e + b][r, 0:2 * rows].rearrange("p (h n) -> p h n", h=2)
                            dst = mats[n][r, i, e::2, 0:rows]
                            if b == 0:
                                last = nc.vector.scalar_tensor_tensor(dst, src, -1.0, m, ALU.mult, ALU.mult)
                            else:
                                last = nc.vector.tensor_tensor(dst, src, m, ALU.mult)
                        last.then_inc(*done.up())
        units = [(i, rows, LEVELS if t < 2 else [2, 4]) for i in range(2)]
        first_level(K, mats["low"], mats["T"], mats["R"], units)
        invert_phase(K, mats["low"], mats["T"], mats["R"], work, units, LEVELS)
    for chunk in range(2 if t < 2 else 1):
        rwkv_chunk(K, tmp, t, half, chunk, d, ec, ktr, mats, H, y, byst)


def rwkv_chunk(K, tmp, t, half, chunk, d, ec, ktr, mats, H, y, byst):
    nc = K.nc
    first = t == 0 and chunk == 0
    o = 64 * chunk
    sl = slice(o, o + 64)
    fs = slice(4 * half, 4 * half + 4)
    hs = slice(512 * half, 512 * half + 512)
    with contextlib.ExitStack() as t2:
        u = K.sb(t2, "u", [128, 512])
        s = K.s_all if t == 2 else K.sb(t2, "s", [128, D])
        change = K.sb(t2, "change", [128, 4, 128])
        with K.phase("u_full", "u_done", "s_full", "s_done", "y_full", "h_full", "h_step", "h_done") as (
                block, uf, ud, sf, sd, yf, hf, step, hdone):
            def from_state(bank, p, i):
                f = 4 * half + p
                out = bank[sl, p * 128:(p + 1) * 128]
                if byst is not None:
                    nc.tensor.matmul(out, byst[:, f, i, :], K.const("ident"), start=True, stop=False,
                                     skip_group_check=True)
                elif not first:
                    nc.tensor.matmul(out, ktr[:, f, i, sl], H[:, f, :], start=True, stop=False,
                                     skip_group_check=True)

            def head(h):
                return mats_at(h), slice(512 * half + 64 * h, 512 * half + 64 * h + 64)

            def mats_at(h):
                return h // 4, h % 4

            @block.tensor
            def _(pe):
                for p in range(4):
                    from_state(K.ps[0], p, 0)
                    for h in (2 * p, 2 * p + 1):
                        (i, j), c = head(h)
                        last = nc.tensor.matmul(K.ps[0][sl, h * 64:h * 64 + 64], mats["n"][sl, i, j, sl],
                                                d["v"][sl, c], start=first, stop=True, skip_group_check=True)
                last.then_inc(*uf.up())
                pe.wait_ge(*ud.at(1))
                for h in range(8):
                    (i, j), c = head(h)
                    last = nc.tensor.matmul(K.ps[1][sl, h * 64:h * 64 + 64], mats["R"][sl, i, j, sl],
                                            u[sl, h * 64:h * 64 + 64], start=True, stop=True)
                last.then_inc(*sf.up())
                pe.wait_ge(*sd.at(1))
                if t < 2:
                    for p in range(4):
                        c = slice(512 * half + p * 128, 512 * half + p * 128 + 128)
                        nc.tensor.matmul(K.ps[3][:, p * 128:(p + 1) * 128], d["a"][sl, c], s[sl, c],
                                         start=True, stop=False)
                        last = nc.tensor.matmul(K.ps[3][:, p * 128:(p + 1) * 128], d["k"][sl, c], d["v"][sl, c],
                                                start=False, stop=True)
                    last.then_inc(*hf.up())
                for p in range(4):
                    from_state(K.ps[2], p, 1)
                    for h in (2 * p, 2 * p + 1):
                        (i, j), c = head(h)
                        nc.tensor.matmul(K.ps[2][sl, h * 64:h * 64 + 64], mats["rb"][sl, i, j, sl], s[sl, c],
                                         start=first, stop=False, skip_group_check=True)
                        last = nc.tensor.matmul(K.ps[2][sl, h * 64:h * 64 + 64], mats["rk"][sl, i, j, sl],
                                                d["v"][sl, c], start=False, stop=True, skip_group_check=True)
                last.then_inc(*yf.up())

            @block.scalar
            def _(act):
                act.wait_ge(*uf.at(1))
                nc.scalar.copy(u[sl, :], K.ps[0][sl, :]).then_inc(*ud.up())
                act.wait_ge(*sf.at(1))
                nc.scalar.copy(s[sl, hs], K.ps[1][sl, :]).then_inc(*sd.up())
                act.wait_ge(*yf.at(1))
                nc.scalar.copy(y[sl, hs], K.ps[2][sl, :])

            if t < 2:
                @block.vector
                def _(dve):
                    link = chain(dve, step)
                    dve.wait_ge(*hf.at(1))
                    pair = K.const("pair").unsqueeze(1).broadcast_to([128, 4, 128])
                    link(nc.vector.tensor_tensor(change[:, :, :], K.ps[3][:, :].rearrange("p (f n) -> p f n", f=4),
                                                 pair, ALU.mult))
                    if not first:
                        link(nc.vector.tensor_tensor(change[:, :, :], change[:, :, :], H[:, fs, :], ALU.add))
                    dve.wait_ge(*yf.at(1))
                    nc.vector.tensor_tensor(H[:, fs, :], change[:, :, :],
                                            ec[:, fs, chunk:chunk + 1].broadcast_to([128, 4, 128]), ALU.mult)


def load_states(K, sp, buf, b, sig):
    for e in range(2):
        src = K.ins["state_wkv"][0, b].rearrange("(f e) v k -> e v f k", e=2)[e]
        sp.dma_start(buf[64 * e:64 * e + 64, :, 64 * e:64 * e + 64], src).then_inc(*sig.up(16))


def rwkv_sample_states(K, outer, ktr):
    nc, I = K.nc, K.ins
    byst = K.sb(outer, "byst", [128, KT, 2, SAMPLE])
    K.s_all = K.sb(outer, "s_all", [128, D])
    with contextlib.ExitStack() as tmp:
        S = K.sb(tmp, "S", [128, 2, KT, 128])
        HT = K.sb(tmp, "HT", [128, KT, 128])
        with K.phase("z_done") as (block, z):
            @block.vector
            def _(dve):
                nc.vector.memset(S[:, :, :, :], 0.0)
        with K.phase("sin0", "sin1", "st_full", "st_act", "st_dve", "by_full", "by_done") as (
                block, in0, in1, full, by_act, by_dve, byf, byd):
            ins = (in0, in1)

            @block.sync
            def _(sp):
                for b in range(SEQS):
                    if b >= 2:
                        sp.wait_ge(*full.at(2 * (b - 1)))
                    load_states(K, sp, S[:, b % 2, :, :], b, ins[b % 2])

            @block.tensor
            def _(pe):
                for b in range(SEQS):
                    pe.wait_ge(*ins[b % 2].at(32 * (b // 2 + 1)))
                    if b:
                        pe.wait_ge(*by_act.at(b))
                        pe.wait_ge(*by_dve.at(b))
                    for q in range(2):
                        for j in range(4):
                            last = nc.tensor.transpose(K.ps[q][:, j * 128:(j + 1) * 128], S[:, b % 2, 4 * q + j, :],
                                                       K.const("ident"))
                        last.then_inc(*full.up())
                    pe.wait_ge(*by_act.at(b + 1))
                    pe.wait_ge(*by_dve.at(b + 1))
                    if b >= 2:
                        pe.wait_ge(*byd.at(b - 1))
                    for f in range(KT):
                        last = nc.tensor.matmul(K.ps[2 + b % 2][:, 16 * f:16 * f + 16], HT[:, f, :],
                                                ktr[:, f, :, 8 * b:8 * b + 8], start=True, stop=True)
                    last.then_inc(*byf.up())

            @block.scalar
            def _(act):
                for b in range(SEQS):
                    act.wait_ge(*full.at(2 * b + 1))
                    if b:
                        act.wait_ge(*byf.at(b))
                    nc.scalar.copy(HT[:, 0:4, :], K.ps[0][:, :].rearrange("p (f n) -> p f n", f=4)
                                   ).then_inc(*by_act.up())
                    act.wait_ge(*byf.at(b + 1))
                    nc.scalar.copy(byst[:, :, :, 8 * b:8 * b + 8],
                                   K.ps[2 + b % 2][:, 0:128].rearrange("p (f i s) -> p f i s", f=KT, i=2)
                                   ).then_inc(*byd.up())

            @block.vector
            def _(dve):
                for b in range(SEQS):
                    dve.wait_ge(*full.at(2 * b + 2))
                    if b:
                        dve.wait_ge(*byf.at(b))
                    nc.vector.tensor_copy(HT[:, 4:8, :], K.ps[1][:, :].rearrange("p (f n) -> p f n", f=4)
                                          ).then_inc(*by_dve.up())
    return byst


def rwkv_sample_update(K, outer, d, ec):
    nc, I, O = K.nc, K.ins, K.outs
    with contextlib.ExitStack() as tmp:
        S = K.sb(tmp, "S", [128, 2, KT, 128])
        cut = K.sb(tmp, "cut", [SAMPLE, 2, 2, D])
        HT = K.sb(tmp, "HT", [128, KT, 128])
        with K.phase("z_done") as (block, z):
            @block.vector
            def _(dve):
                nc.vector.memset(S[:, :, :, :], 0.0)
        with K.phase("sin0", "sin1", "cut_done", "ch_full", "ch_done", "sout0", "sout1", "ch_step", "tr_full",
                     "tr_done", "back_full", "back_done", "hn_done") as (
                block, in0, in1, cd, chf, chd, out0, out1, step, trf, trd, bf, bd, hnd):
            ins, outs = (in0, in1), (out0, out1)

            def store(sp, b):
                sp.wait_ge(*bd.at(b + 1))
                for e in range(2):
                    dst = O[13][0, b].rearrange("(f e) v k -> e v f k", e=2)[e]
                    sp.dma_start(dst, S[64 * e:64 * e + 64, b % 2, :, 64 * e:64 * e + 64]
                                 ).then_inc(*outs[b % 2].up(16))

            @block.sync
            def _(sp):
                for b in range(SEQS):
                    if b >= 2:
                        sp.wait_ge(*outs[b % 2].at(32 * (b // 2)))
                    load_states(K, sp, S[:, b % 2, :, :], b, ins[b % 2])
                    if b:
                        store(sp, b - 1)
                store(sp, SEQS - 1)
                for q in range(2):
                    sp.wait_ge(*outs[q].at(32 * SEQS // 2))

            @block.gpsimd
            def _(pool):
                for b in range(SEQS):
                    if b >= 2:
                        pool.wait_ge(*chf.at(b - 1))
                    m = K.const("of_chunk_s")[0:SAMPLE, b:b + 1]
                    nc.gpsimd.tensor_scalar(cut[:, b % 2, 0, :], K.s_all[0:SAMPLE, :], m, None, ALU.mult)
                    nc.gpsimd.tensor_scalar(cut[:, b % 2, 1, :], d["v"][0:SAMPLE, :], m, None, ALU.mult
                                            ).then_inc(*cd.up())

            @block.tensor
            def _(pe):
                r = slice(0, SAMPLE)
                for b in range(SEQS):
                    pe.wait_ge(*ins[b % 2].at(32 * (b // 2 + 1)))
                    pe.wait_ge(*cd.at(b + 1))
                    if b:
                        pe.wait_ge(*hnd.at(b))
                    for f in range(KT):
                        q, j = f // 4, f % 4
                        nc.tensor.transpose(K.ps[q][:, j * 128:(j + 1) * 128], S[:, b % 2, f, :], K.const("ident"))
                    for f in range(KT):
                        q, j = f // 4, f % 4
                        c = slice(f * 128, (f + 1) * 128)
                        nc.tensor.matmul(K.ps[2 + q][:, j * 128:(j + 1) * 128], d["a"][r, c], cut[:, b % 2, 0, c],
                                         start=True, stop=False)
                        last = nc.tensor.matmul(K.ps[2 + q][:, j * 128:(j + 1) * 128], d["k"][r, c],
                                                cut[:, b % 2, 1, c], start=False, stop=True)
                    last.then_inc(*chf.up())
                    pe.wait_ge(*hnd.at(b + 1))
                    if b:
                        pe.wait_ge(*bd.at(b))
                    for f in range(KT):
                        q, j = f // 4, f % 4
                        last = nc.tensor.transpose(K.ps[4 + q][:, j * 128:(j + 1) * 128], HT[:, f, :],
                                                   K.const("ident"))
                    last.then_inc(*bf.up())

            @block.vector
            def _(dve):
                link = chain(dve, step)
                pair = K.const("pair").unsqueeze(1).broadcast_to([128, 4, 128])
                for b in range(SEQS):
                    dve.wait_ge(*chf.at(b + 1))
                    if b:
                        dve.wait_ge(*bf.at(b))
                    for q in range(2):
                        last = nc.vector.tensor_tensor(HT[:, 4 * q:4 * q + 4, :], K.ps[2 + q][:, :].rearrange(
                            "p (f n) -> p f n", f=4), pair, ALU.mult)
                    link(last)
                    for q in range(2):
                        h = HT[:, 4 * q:4 * q + 4, :]
                        last = nc.vector.tensor_tensor(h, h, K.ps[q][:, :].rearrange("p (f n) -> p f n", f=4),
                                                       ALU.add)
                    link(last)
                    nc.vector.tensor_tensor(HT[:, :, :], HT[:, :, :], ec[:, :, b:b + 1].broadcast_to([128, KT, 128]),
                                            ALU.mult).then_inc(*hnd.up())

            @block.scalar
            def _(act):
                for b in range(SEQS):
                    act.wait_ge(*bf.at(b + 1))
                    for q in range(2):
                        last = nc.scalar.copy(S[:, b % 2, 4 * q:4 * q + 4, :],
                                              K.ps[4 + q][:, :].rearrange("p (f n) -> p f n", f=4))
                    last.then_inc(*bd.up())


def rwkv_prompt_state(K, H):
    nc, O = K.nc, K.outs
    with contextlib.ExitStack() as tmp:
        S = K.sb(tmp, "S", [128, KT, 128])
        transpose_phase(K, [([H[:, 4 * q + j, :] for j in range(4)], S[:, 4 * q:4 * q + 4, :]) for q in range(2)])
        with K.phase("sout0") as (block, out):
            @block.sync
            def _(sp):
                for e in range(2):
                    dst = O[8][0, 0].rearrange("(f e) v k -> e v f k", e=2)[e]
                    sp.dma_start(dst, S[64 * e:64 * e + 64, :, 64 * e:64 * e + 64]).then_inc(*out.up(16))
                sp.wait_ge(*out.at(32))


def rwkv_output(K, t, d, bonus, y, yT):
    nc, I = K.nc, K.ins
    rows = ROWS[t]
    r = slice(0, rows)
    h3 = lambda a: a[r, :].rearrange("p (h n) -> p h n", h=C_HEADS)
    bc = lambda a: a.unsqueeze(2).broadcast_to([rows, C_HEADS, 64])
    with contextlib.ExitStack() as tmp:
        g, w, b, sq = (K.sb(tmp, n, [128, D]) for n in ("g", "lw", "lb", "sq"))
        s = K.sb(tmp, "s", [128, 3, C_HEADS])
        with K.phase("f_in", "fin_var", "fin_std", "fin_step") as (block, loaded, var, std, step):
            @block.sync
            def _(sp):
                sp.dma_start(g[r, :], K.scratch["g"][cols_of(t), :]).then_inc(*loaded.up(16))
                sp.dma_start(w[:, :], row_broadcast(I["c_ln_w"][0])).then_inc(*loaded.up(16))
                sp.dma_start(b[:, :], row_broadcast(I["c_ln_b"][0])).then_inc(*loaded.up(16))

            @block.scalar
            def _(act):
                act.wait_ge(*var.at(1))
                nc.scalar.activation(s[r, 1, :], s[r, 1, :], ACT.Sqrt, scale=1.0 / 64, bias=K.epsg[r, 0:1]
                                     ).then_inc(*std.up())

            @block.vector
            def _(dve):
                link = chain(dve, step)
                link(nc.vector.tensor_reduce(s[r, 0, :], h3(y), AX, ALU.add))
                link(nc.vector.tensor_scalar(s[r, 0, :], s[r, 0, :], 1.0 / 64, None, ALU.mult))
                link(nc.vector.tensor_tensor(h3(y), h3(y), bc(s[r, 0, :]), ALU.subtract))
                link(nc.vector.tensor_tensor(sq[r, :], y[r, :], y[r, :], ALU.mult))
                nc.vector.tensor_reduce(s[r, 1, :], h3(sq), AX, ALU.add).then_inc(*var.up())
                dve.wait_ge(*std.at(1))
                link(nc.vector.reciprocal(s[r, 2, :], s[r, 1, :]))
                link(nc.vector.tensor_tensor(h3(y), h3(y), bc(s[r, 2, :]), ALU.mult))
                dve.wait_ge(*loaded.at(48))
                link(nc.vector.tensor_tensor(y[r, :], y[r, :], w[r, :], ALU.mult))
                link(nc.vector.tensor_tensor(y[r, :], y[r, :], b[r, :], ALU.add))
                link(nc.vector.tensor_tensor(h3(sq), h3(d["v"]), bc(bonus[r, :]), ALU.mult))
                link(nc.vector.tensor_tensor(y[r, :], y[r, :], sq[r, :], ALU.add))
                link(nc.vector.tensor_tensor(y[r, :], y[r, :], g[r, :], ALU.mult))
        transpose_phase(K, [([y[r, (4 * q + j) * 128:(4 * q + j + 1) * 128] for j in range(4)],
                             yT[:, 4 * q:4 * q + 4, cols_of(t)]) for q in range(2)])



INPUTS = ["x_prompt", "x_sample", "mem_prompt", "cache_mem_k", "cache_mem_v", "state_conv_a", "state_delta",
          "state_ret", "state_shift_c", "state_wkv", "ab_w_in", "ab_conv_w", "ab_a_log", "ab_dt_bias", "ab_norm_w",
          "ab_w_out", "c_mu", "c_w_r", "c_w_k", "c_w_v", "c_w0", "c_w_w1", "c_w_w2", "c_a0", "c_w_a1", "c_w_a2",
          "c_w_g1", "c_w_g2", "c_k_k", "c_k_a", "c_r_k", "c_ln_w", "c_ln_b", "c_w_out", "x_w_q", "x_w_k", "x_w_v",
          "x_w_o", "moe_w_grp", "moe_b_grp", "moe_w_exp", "moe_b_exp", "moe_w1", "moe_w3", "moe_w2", "ln_w", "ln_b"]
OUTPUTS = [(1, 256, 1024), (8, 8, 1024), (2, 1, 256, 4, 256), (2, 1, 256, 4, 256), (1, 1, 3, 1536),
           (1, 1, 4, 128, 128), (1, 1, 4, 128, 128), (1, 1, 1024), (1, 1, 16, 64, 64), (1, 8, 3, 1536),
           (1, 8, 4, 128, 128), (1, 8, 4, 128, 128), (1, 8, 1024), (1, 8, 16, 64, 64)]


def inference_step(nc, ins, outs, at, probe=None):
    stack = contextlib.ExitStack()
    with stack:
        K = Kernel(nc, ins, outs, at, stack)
        K.scratch = {n: nc.dram_tensor("scratch_" + n, (TOK, D), F32, kind="Internal").ap()
                     for n in ("gate", "r", "k", "v", "w", "a", "g")}
        K.scratch["gates"] = nc.dram_tensor("scratch_gates", (EXPERTS, TOK), F32, kind="Internal").ap()
        K.cst = K.sb(stack, "cst", [128, ins["constants"].shape[1]])
        K.x = K.sb(stack, "x", [128, TILES, D])
        K.xT = K.sb(stack, "xT", [128, KT, TOK])
        K.ring = K.sb(stack, "ring", [128, RING, SLOT])
        K.eps6, K.eps5, K.epsg = (K.sb(stack, "eps", [128, 1]) for _ in range(3))
        K.ps = [stack.enter_context(nc.psum_tensor(f"bank{b}", [128, 512], F32)) for b in range(8)]
        K.arrived = [stack.enter_context(nc.semaphore(f"weights_arrived{b}")) for b in range(RING)]
        K.chunks, K.first = weight_chunks(K)
        total = [0] * RING
        K.arrival = []
        for g, chunk in enumerate(K.chunks):
            total[g % RING] += 16 * len(chunk)
            K.arrival.append(total[g % RING])
        with K.phase("x_in") as (block, loaded):
            @block.sync
            def _(sp):
                sp.dma_start(K.cst[:, :], ins["constants"]).then_inc(*loaded.up(16))
                for t in range(2):
                    sp.dma_start(K.x[:, t, :], ins["x_prompt"][0, t * 128:(t + 1) * 128, :]).then_inc(*loaded.up(16))
                sp.dma_start(K.x[0:SAMPLE, 2, :], ins["x_sample"].rearrange("b s d -> (b s) d")
                             ).then_inc(*loaded.up(16))
                for g in range(RING):
                    load_chunk(K, sp, g)
                sp.wait_ge(*loaded.at(64))

            @block.vector
            def _(dve):
                nc.vector.memset(K.eps6[:, :], 1e-6)
                nc.vector.memset(K.eps5[:, :], LN_EPS)
                nc.vector.memset(K.epsg[:, :], GN_EPS)
        transpose_x(K)
        ab_mixer(K)
        if probe == "ab":
            return finish(K)
        cross_attention(K, 0)
        if probe == "x0":
            return finish(K)
        moe(K, 0)
        if probe == "moe0":
            return finish(K)
        rwkv_mixer(K)
        if probe == "c":
            return finish(K)
        cross_attention(K, 1)
        moe(K, 1)
        finish(K)


def finish(K):
    with K.phase("y_out") as (block, out):
        @block.sync
        def _(sp):
            for t in range(2):
                sp.dma_start(K.outs[0][0, t * 128:(t + 1) * 128, :], K.x[:, t, :]).then_inc(*out.up(16))
            sp.dma_start(K.outs[1].rearrange("b s d -> (b s) d"), K.x[0:SAMPLE, 2, :]).then_inc(*out.up(16))
            sp.wait_ge(*out.at(48))


def kernel(**inputs):
    import concourse.bacc as bacc
    from concourse.bass_utils import run_bass_kernel_spmd

    nc = bacc.Bacc("TRN2", target_bir_lowering=False, num_devices=1)
    table, at = constants()
    arrays = {"in_" + n: np.ascontiguousarray(inputs[n]) for n in INPUTS}
    arrays["in_constants"] = table
    ins = {n[3:]: nc.dram_tensor(n, a.shape, F32, kind="ExternalInput").ap() for n, a in arrays.items()}
    outs = [nc.dram_tensor(f"out_{i}", s, F32, kind="ExternalOutput").ap() for i, s in enumerate(OUTPUTS)]
    inference_step(nc, ins, outs, at)
    r = run_bass_kernel_spmd(nc, [arrays], core_ids=[0])
    return tuple(r.results[0][f"out_{i}"] for i in range(len(OUTPUTS)))
```

```python
import contextlib

import numpy as np

import concourse.bass as bass
from concourse import mybir

F32 = mybir.dt.float32
I32 = mybir.dt.int32
ALU = mybir.AluOpType
ACT = mybir.ActivationFunctionType
AX = mybir.AxisListType.X

D = 1024
KT = D // 128
SEQ, SEQS, STEPS = 256, 8, 8
SAMPLE = SEQS * STEPS
TOK = SEQ + SAMPLE
TILES = 3
ROWS = [128, 128, SAMPLE]
AT = [0, 128, 256]
MEM = 256
CONV = 4
QKV = 1536
XH = 4
GROUPS, PER_GROUP, FF = 4, 8, 256
EXPERTS = GROUPS * PER_GROUP
CHUNK = 64
ALPHA = 4.0 ** 0.25
LN_EPS, RMS_EPS, GN_EPS = 1e-5, 1e-6, 64e-5
WIDE = TOK + 24
RING, SLOT = 4, 4096
PAST = 2048


def constants():
    i = np.arange(128)
    parts = {}
    parts["ident"] = np.eye(128)
    parts["ones"] = np.ones((128, 128))
    for kind, c in (("p", CHUNK), ("s", STEPS)):
        same = i[:, None] // c == i[None, :] // c
        parts["upto_" + kind] = same & (i[:, None] <= i[None, :])
        parts["below_" + kind] = same & (i[:, None] > i[None, :])
        parts["above_" + kind] = same & (i[:, None] < i[None, :])
        parts["of_chunk_" + kind] = i[:, None] // c == np.arange(8)[None, :]
    for s in (1, 2, 4, 8, 16, 32):
        same = i[:, None] // (2 * s) == i[None, :] // (2 * s)
        parts[f"level{s}"] = same & (i[:, None] // s % 2 == 1) & (i[None, :] // s % 2 == 0)
    parts["pair"] = i[:, None] // 64 == i[None, :] // 64
    half = 64
    inv = np.float32(10000.0) ** (-np.linspace(0.0, 1.0, half, dtype=np.float32))
    pos = np.concatenate([np.arange(256), PAST + np.arange(64) % 8, np.zeros(64)]).astype(np.float32)
    ang = (pos[:, None] * inv[None, :]).astype(np.float32).reshape(3, 128, half)
    parts["cos"] = np.cos(ang).transpose(1, 0, 2).reshape(128, -1)
    parts["sin"] = np.sin(ang).transpose(1, 0, 2).reshape(128, -1)
    lg = np.log(1.0 - 2.0 ** (-5.0 - np.arange(4)))
    scale = 128.0 ** -0.5
    for kind, c in (("p", CHUNK), ("s", STEPS)):
        d = i[None, :] - i[:, None]
        same = (i[:, None] // c == i[None, :] // c) & (d >= 0)
        dec = np.exp(lg[None, :, None] * np.maximum(d, 0)[:, None, :]) * same[:, None, :] * scale
        parts["retdecay_" + kind] = dec.reshape(128, -1)
        parts["retq_" + kind] = np.exp(lg[None, :] * (i[:, None] % c + 1.0))
        parts["retk_" + kind] = np.exp(lg[None, :] * (c - 1.0 - i[:, None] % c)) * scale
    parts["descend"] = np.tile(8.0 - np.arange(8), (128, 1))
    parts["upto_all"] = i[:, None] <= i[None, :]
    parts["slot_base"] = np.tile(64.0 * np.arange(32) - 1.0, (128, 1))
    parts["slots"] = np.tile(i, (128, 1))
    parts["row"] = i[:, None]
    at, cols = {}, 0
    for name, a in parts.items():
        a = np.asarray(a, np.float32).reshape(128, -1)
        parts[name] = a
        at[name] = (cols, a.shape[1])
        cols += a.shape[1]
    return np.concatenate(list(parts.values()), 1), at


CHUNK_DECAY = {c: [float((1.0 - 2.0 ** (-5.0 - h)) ** c) for h in range(4)] for c in (CHUNK, STEPS)}


class Signal:

    def __init__(self, sem):
        self.sem, self.sent, self.base = sem, 0, 0

    def up(self, by=1):
        self.sent += by
        return self.sem, by

    def at(self, n):
        return self.sem, self.base + n


class Kernel:

    def __init__(self, nc, ins, outs, at, stack):
        self.nc, self.ins, self.outs, self.at, self.stack = nc, ins, outs, at, stack
        self.signals = {}
        self.uid = 0

    def sem(self, name):
        if name not in self.signals:
            self.signals[name] = Signal(self.stack.enter_context(self.nc.semaphore(name)))
        return self.signals[name]

    @contextlib.contextmanager
    def phase(self, *names):
        got = [self.sem(n) for n in names]
        for s in got:
            s.base = s.sent
        with self.nc.Block() as block:
            yield (block, *got)

    def sb(self, stack, name, shape, dt=F32):
        self.uid += 1
        return stack.enter_context(self.nc.sbuf_tensor(f"{name}_{self.uid}", shape, dt))

    def const(self, name, rows=128):
        a, n = self.at[name]
        return self.cst[0:rows, a:a + n]


def chain(eng, sig):

    def link(ins):
        ins.then_inc(*sig.up())
        eng.wait_ge(sig.sem, sig.sent)

    return link


def tile_kind(t):
    return "p" if t < 2 else "s"


def cols_of(t):
    return slice(AT[t], AT[t] + ROWS[t])



def weight_chunks(K):
    I = K.ins
    chunks, first = [], {}

    def dense(name, w, c0s):
        first[name] = len(chunks)
        for c0 in c0s:
            chunks.append([(lambda s: s.rearrange("p (k n) -> p k n", k=KT),
                            w[:, c0:c0 + 512].rearrange("(k p) n -> p k n", p=128))])

    def experts(name, layer):
        first[name] = len(chunks)
        for e in range(EXPERTS):
            for c in expert_chunks(K, layer, e // PER_GROUP, e % PER_GROUP):
                chunks.append(c)

    w_in = I["ab_w_in"][0]
    dense("ab_qkv", w_in, [0, 512, 1024])
    dense("ab_rest", w_in, [1544 + 512 * n for n in range(5)])
    dense("ab_out", I["ab_w_out"][0], [0, 512])
    for layer in range(2):
        if layer:
            for n in ("r", "k", "v"):
                dense("c_" + n, I["c_w_" + n][0], [0, 512])
            dense("c_out", I["c_w_out"][0], [0, 512])
        for n in ("k", "v", "q", "o"):
            dense(f"x_{n}{layer}", I["x_w_" + n][layer], [0, 512])
        experts(f"moe{layer}", layer)
    return chunks, first


def expert_chunks(K, layer, g, e):
    I = K.ins
    up = [(lambda s, j=j: s.rearrange("p (k j f) -> p k j f", k=KT, j=2)[:, :, j, :],
           I[w][layer, g, e].rearrange("(k p) f -> p k f", p=128)) for j, w in enumerate(("moe_w1", "moe_w3"))]
    down = [(lambda s: s[:, 0:2 * D].rearrange("p (k n) -> p k n", k=2),
             I["moe_w2"][layer, g, e].rearrange("(k p) n -> p k n", p=128))]
    return [up, down]


def load_chunk(K, sp, g):
    if g >= len(K.chunks):
        return
    for view, src in K.chunks[g]:
        sp.dma_start(view(K.ring[:, g % RING, :]), src).then_inc(K.arrived[g % RING], 16)


def run_ahead(K, sp, first, full, counts):
    for n, count in enumerate(counts):
        sp.wait_ge(*full.at(count))
        load_chunk(K, sp, first + n + RING)


def await_chunk(K, pe, g):
    pe.wait_ge(K.arrived[g % RING], K.arrival[g])


def slot8(K, g):
    return K.ring[:, g % RING, :].rearrange("p (k n) -> p k n", k=KT)



def transpose_phase(K, groups):
    nc = K.nc
    with K.phase("tr_full", "tr_act", "tr_dve") as (block, full, by_act, by_dve):
        def view(n):
            srcs, dst = groups[n]
            p, c = srcs[0].shape[0], srcs[0].shape[1]
            return K.ps[n % 4][0:c, 0:len(srcs) * p].rearrange("c (n p) -> c n p", p=p)

        @block.tensor
        def _(pe):
            for n, (srcs, dst) in enumerate(groups):
                if n >= 4:
                    pe.wait_ge(*(by_act if n % 2 == 0 else by_dve).at((n - 4) // 2 + 1))
                for j, s in enumerate(srcs):
                    last = nc.tensor.transpose(view(n)[:, j, :], s, K.const("ident")[0:s.shape[0], 0:s.shape[0]])
                last.then_inc(*full.up())

        @block.scalar
        def _(act):
            for n in range(0, len(groups), 2):
                act.wait_ge(*full.at(n + 1))
                nc.scalar.copy(groups[n][1], view(n)).then_inc(*by_act.up())

        @block.vector
        def _(dve):
            for n in range(1, len(groups), 2):
                dve.wait_ge(*full.at(n + 1))
                nc.vector.tensor_copy(groups[n][1], view(n)).then_inc(*by_dve.up())


def token_major_phase(K, first, n_chunks, xT, tiles, dest, stores=(), stored_later=None,
                      aside=None, last_wait=None):
    nc = K.nc
    units = [(g, t) for g in range(n_chunks) for t in range(len(tiles))]
    with K.phase("mm_full", "mm_act", "mm_dve", "stored", "aside_step") as (
            block, full, by_act, by_dve, stored, scaled):
        @block.sync
        def _(sp):
            run_ahead(K, sp, first, full, [len(tiles) * (g + 1) for g in range(n_chunks)])
            for n, (dst, src) in enumerate(stores):
                if n == 0:
                    sp.wait_ge(*by_act.at((len(units) + 1) // 2))
                    sp.wait_ge(*by_dve.at(len(units) // 2))
                sp.dma_start(dst, src).then_inc(*(stored_later or stored).up(16))
            if stores and not stored_later:
                sp.wait_ge(*stored.at(16 * len(stores)))
            if last_wait:
                last_wait(sp)

        if aside:
            @block.gpsimd
            def _(pool):
                aside(pool, scaled)

        @block.tensor
        def _(pe):
            for n, (g, t) in enumerate(units):
                if t == 0:
                    await_chunk(K, pe, first + g)
                if n >= 4:
                    pe.wait_ge(*(by_act if n % 2 == 0 else by_dve).at((n - 4) // 2 + 1))
                c, rows = tiles[t]
                w = slot8(K, first + g)
                for k in range(KT):
                    last = nc.tensor.matmul(K.ps[n % 4][0:rows, :], xT[:, k, c:c + rows], w[:, k, :],
                                            start=(k == 0), stop=(k == KT - 1))
                last.then_inc(*full.up())

        @block.scalar
        def _(act):
            for n in range(0, len(units), 2):
                act.wait_ge(*full.at(n + 1))
                g, t = units[n]
                nc.scalar.copy(dest(g, t), K.ps[n % 4][0:tiles[t][1], :]).then_inc(*by_act.up())

        @block.vector
        def _(dve):
            for n in range(1, len(units), 2):
                dve.wait_ge(*full.at(n + 1))
                g, t = units[n]
                nc.vector.tensor_copy(dest(g, t), K.ps[n % 4][0:tiles[t][1], :]).then_inc(*by_dve.up())


def feature_major_phase(K, first, n_chunks, xT, n_tok, dest):
    nc = K.nc
    with K.phase("mm_full", "mm_act", "mm_dve") as (block, full, by_act, by_dve):
        @block.sync
        def _(sp):
            run_ahead(K, sp, first, full, [4 * (g + 1) for g in range(n_chunks)])

        @block.tensor
        def _(pe):
            for f in range(4 * n_chunks):
                g = first + f // 4
                if f % 4 == 0:
                    await_chunk(K, pe, g)
                if f >= 4:
                    pe.wait_ge(*(by_act if f % 2 == 0 else by_dve).at((f - 4) // 2 + 1))
                w = slot8(K, g)
                for k in range(KT):
                    last = nc.tensor.matmul(K.ps[f % 4][:, 0:n_tok], w[:, k, (f % 4) * 128:(f % 4 + 1) * 128],
                                            xT[:, k, 0:n_tok], start=(k == 0), stop=(k == KT - 1))
                last.then_inc(*full.up())

        @block.scalar
        def _(act):
            for f in range(0, 4 * n_chunks, 2):
                act.wait_ge(*full.at(f + 1))
                for dst, src in dest(f, K.ps[f % 4]):
                    last = nc.scalar.copy(dst, src)
                last.then_inc(*by_act.up())

        @block.vector
        def _(dve):
            for f in range(1, 4 * n_chunks, 2):
                dve.wait_ge(*full.at(f + 1))
                for dst, src in dest(f, K.ps[f % 4]):
                    last = nc.vector.tensor_copy(dst, src)
                last.then_inc(*by_dve.up())


def transpose_x(K):
    groups = []
    for t in range(TILES):
        for q in range(2):
            groups.append(([K.x[0:ROWS[t], t, (4 * q + j) * 128:(4 * q + j + 1) * 128] for j in range(4)],
                           K.xT[:, 4 * q:4 * q + 4, cols_of(t)]))
    transpose_phase(K, groups)


def row_broadcast(ap, rows=128):
    return ap.rearrange("(a n) -> a n", a=1).broadcast_to([rows, ap.shape[0]])


def norm_tile(K, dve, link, act_sig, sq, t, rows, stats, mv, lnw, lnb):
    nc = K.nc
    x = K.x[0:rows, t, :]
    for h in range(2):
        last = nc.vector.bn_stats(stats[0:rows, h, :], K.x[0:rows, t, h * 512:(h + 1) * 512])
    link(last)
    link(nc.vector.bn_aggr(mv[0:rows, t, 0:2], stats[0:rows, :, :].rearrange("p a b -> p (a b)")))
    nc.vector.tensor_scalar(mv[0:rows, t, 1:2], mv[0:rows, t, 1:2], LN_EPS, None, ALU.add).then_inc(*sq.up())
    dve.wait_ge(*act_sig.at(t + 1))
    link(nc.vector.reciprocal(mv[0:rows, t, 3:4], mv[0:rows, t, 2:3]))
    link(nc.vector.tensor_scalar(x, x, mv[0:rows, t, 0:1], mv[0:rows, t, 3:4], ALU.subtract, ALU.mult))
    link(nc.vector.tensor_tensor(x, x, lnw[0:rows, :], ALU.mult))
    link(nc.vector.tensor_tensor(x, x, lnb[0:rows, :], ALU.add))


def add_and_norm_phase(K, first, srcT, layer, which):
    nc = K.nc
    with contextlib.ExitStack() as st:
        lnw, lnb = K.sb(st, "lnw", [128, D]), K.sb(st, "lnb", [128, D])
        stats, mv = K.sb(st, "stats", [128, 2, 6]), K.sb(st, "mv", [128, TILES, 4])
        with K.phase("mm_full", "loaded", "ln_free", "ln_var", "ln_std", "vector_step") as (
                block, full, rows_in, free, var, std, step):
            @block.sync
            def _(sp):
                sp.dma_start(lnw[:, :], row_broadcast(K.ins["ln_w"][layer, which])).then_inc(*rows_in.up(16))
                sp.dma_start(lnb[:, :], row_broadcast(K.ins["ln_b"][layer, which])).then_inc(*rows_in.up(16))
                run_ahead(K, sp, first, full, [TILES, TILES])

            @block.tensor
            def _(pe):
                for g in range(2):
                    await_chunk(K, pe, first + g)
                for t in range(TILES):
                    if t == 2:
                        pe.wait_ge(*free.at(1))
                    for g in range(2):
                        w = slot8(K, first + g)
                        for k in range(KT):
                            last = nc.tensor.matmul(K.ps[2 * (t % 2) + g][0:ROWS[t], :], srcT[:, k, cols_of(t)],
                                                    w[:, k, :], start=(k == 0), stop=(k == KT - 1))
                    last.then_inc(*full.up())

            @block.scalar
            def _(act):
                for t in range(TILES):
                    act.wait_ge(*var.at(t + 1))
                    nc.scalar.activation(mv[0:ROWS[t], t, 2:3], mv[0:ROWS[t], t, 1:2], ACT.Sqrt).then_inc(*std.up())

            @block.vector
            def _(dve):
                link = chain(dve, step)
                for t in range(TILES):
                    rows = ROWS[t]
                    dve.wait_ge(*full.at(t + 1))
                    for g in range(2):
                        xs = K.x[0:rows, t, g * 512:(g + 1) * 512]
                        last = nc.vector.scalar_tensor_tensor(xs, xs, ALPHA, K.ps[2 * (t % 2) + g][0:rows, :],
                                                              ALU.mult, ALU.add)
                    last.then_inc(*free.up())
                    dve.wait_ge(*free.at(t + 1))
                    if t == 0:
                        dve.wait_ge(*rows_in.at(32))
                    norm_tile(K, dve, link, std, var, t, rows, stats, mv, lnw, lnb)
    transpose_x(K)



def hist(b):
    return 3 + SEQ + b * (CONV - 1 + STEPS)


RAW = 3 + SEQ + SEQS * (CONV - 1 + STEPS)


def ab_mixer(K):
    with contextlib.ExitStack() as outer:
        o = K.sb(outer, "o", [128, TILES, 8, 128])
        ab_heads(K, o)
        ab_finish(K, o)


def ab_heads(K, o):
    with contextlib.ExitStack() as st:
        kq = K.sb(st, "kq", [128, 2, 8, TOK])
        v = K.sb(st, "v", [128, TILES, 8, 128])
        kd = K.sb(st, "kd", [128, TILES, 8, 128])
        ab = K.sb(st, "ab", [128, TILES, 8])
        with contextlib.ExitStack() as s1:
            ab_project(K, s1, kq, v, kd, ab)
        ab_scan(K, st, kq, v, kd, ab, o)


def ab_project(K, st, kq, v, kd, ab):
    nc, I, O = K.nc, K.ins, K.outs
    raw = K.sb(st, "raw", [128, 12, RAW])
    u_v = K.sb(st, "u_v", [128, 4, TOK])
    cwT = K.sb(st, "cwT", [128, CONV, 12])
    small = contextlib.ExitStack()
    past = K.sb(small, "past", [24, QKV])
    cw = K.sb(small, "cw", [48, 128])
    wab = K.sb(small, "wab", [128, KT, 8])
    with K.phase("loaded", "ab_full") as (block, loaded, full):
        @block.scalar
        def _(act):
            act.dma_start(past[:, :], I["state_conv_a"][0].rearrange("b j n -> (b j) n")).then_inc(*loaded.up(16))
            act.dma_start(cw[:, :], I["ab_conv_w"][0].rearrange("j (k p) -> (j k) p", p=128)).then_inc(*loaded.up(16))
            act.dma_start(wab[:, :, :], I["ab_w_in"][0][:, QKV:QKV + 8].rearrange("(k p) n -> p k n", p=128)
                          ).then_inc(*loaded.up(16))
            act.wait_ge(*full.at(1))
            for t in range(TILES):
                last = nc.scalar.copy(ab[0:ROWS[t], t, :], K.ps[4][0:ROWS[t], 8 * t:8 * t + 8])

        @block.vector
        def _(dve):
            nc.vector.memset(raw[:, :, 0:3], 0.0)

        @block.tensor
        def _(pe):
            pe.wait_ge(*loaded.at(48))
            for t in range(TILES):
                for k in range(KT):
                    last = nc.tensor.matmul(K.ps[4][0:ROWS[t], 8 * t:8 * t + 8], K.xT[:, k, cols_of(t)],
                                            wab[:, k, :], start=(k == 0), stop=(k == KT - 1))
            last.then_inc(*full.up())
    samples = raw[:, :, hist(0):RAW].rearrange("p f (b j) -> p f b j", b=SEQS)
    groups = [([past[:, f * 128:(f + 1) * 128]],
               samples[:, f:f + 1, :, 0:3]) for f in range(12)]
    transpose_history(K, groups)
    transpose_phase(K, [([cw[:, :]], cwT[:, :, :].rearrange("p j f -> p (j f)").unsqueeze(1))])
    small.close()
    qk = K.sb(st, "qk", [128, TILES, D])
    gates = contextlib.ExitStack()
    gate = K.sb(gates, "gate", [128, TILES, D])

    def raw_dest(f, bank):
        return [(raw[:, f, 3:3 + SEQ], bank[:, 0:SEQ]),
                (samples[:, f, :, 3:3 + STEPS], bank[:, SEQ:TOK].rearrange("p (b s) -> p b s", b=SEQS))]

    feature_major_phase(K, K.first["ab_qkv"], 3, K.xT, TOK, raw_dest)
    tiles = [(AT[t], ROWS[t]) for t in range(TILES)]

    def rest_dest(g, t):
        r = slice(0, ROWS[t])
        if g in (0, 4):
            return gate[r, t, g // 4 * 512:g // 4 * 512 + 512]
        if g in (1, 2):
            return qk[r, t, (g - 1) * 512:g * 512]
        return v[r, t, 4:8, :].rearrange("p h d -> p (h d)")

    token_major_phase(K, K.first["ab_rest"], 5, K.xT, tiles, rest_dest,
                      stores=[(K.scratch["gate"][cols_of(t), :], gate[0:ROWS[t], t, :]) for t in range(TILES)])
    gates.close()
    ab_conv(K, st, raw, samples, cwT, kq, u_v)
    ab_rotary(K, st, qk, kq)
    groups = []
    for t in range(TILES):
        c = cols_of(t)
        groups.append(([u_v[:, h, c] for h in range(4)], v[0:ROWS[t], t, 0:4, :]))
        groups.append(([kq[:, 0, h, c] for h in range(4)], kd[0:ROWS[t], t, 0:4, :]))
        groups.append(([kq[:, 0, 4 + h, c] for h in range(4)], kd[0:ROWS[t], t, 4:8, :]))
    transpose_phase(K, groups)


def transpose_history(K, groups):
    nc = K.nc
    with K.phase("tr_full") as (block, full):
        @block.tensor
        def _(pe):
            for f, (srcs, dst) in enumerate(groups):
                last = nc.tensor.transpose(K.ps[f % 4][:, f // 4 * 24:f // 4 * 24 + 24], srcs[0],
                                           K.const("ident")[0:24, 0:24])
            last.then_inc(*full.up())

        @block.vector
        def _(dve):
            dve.wait_ge(*full.at(1))
            for f, (srcs, dst) in enumerate(groups):
                src = K.ps[f % 4][:, f // 4 * 24:f // 4 * 24 + 24].rearrange("p (a b j) -> p a b j", a=1, b=SEQS)
                nc.vector.tensor_copy(dst, src)


def ab_conv(K, st, raw, samples, cwT, kq, u_v):
    nc, O = K.nc, K.outs
    with contextlib.ExitStack() as tmp:
        last3 = K.sb(tmp, "last3", [128, 12, 32])
        tail = K.sb(tmp, "tail", [32, QKV])

        def place(f):
            return kq[:, 1, f, :] if f < 4 else kq[:, 0, f - 4, :] if f < 8 else u_v[:, f - 8, :]

        with K.phase("conv_done", "silu_done", "vector_step") as (block, conv, silu, step):
            @block.vector
            def _(dve):
                link = chain(dve, step)
                for f in range(12):
                    o = place(f)
                    os = o[:, SEQ:TOK].rearrange("p (b s) -> p b s", b=SEQS)
                    for j in range(CONV):
                        w = cwT[:, j, f:f + 1]
                        if j == 0:
                            nc.vector.tensor_scalar(o[:, 0:SEQ], raw[:, f, 0:SEQ], w, None, ALU.mult)
                            last = nc.vector.tensor_scalar(os, samples[:, f, :, 0:STEPS], w, None, ALU.mult)
                        else:
                            nc.vector.scalar_tensor_tensor(o[:, 0:SEQ], raw[:, f, j:j + SEQ], w, o[:, 0:SEQ],
                                                           ALU.mult, ALU.add)
                            last = nc.vector.scalar_tensor_tensor(os, samples[:, f, :, j:j + STEPS], w, os,
                                                                  ALU.mult, ALU.add)
                        if j < CONV - 1:
                            link(last)
                    last.then_inc(*conv.up())

            @block.gpsimd
            def _(pool):
                nc.gpsimd.tensor_copy(last3[:, :, 0:3], raw[:, :, SEQ:SEQ + 3])
                nc.gpsimd.tensor_copy(last3[:, :, 3:27].rearrange("p f (b j) -> p f b j", b=SEQS),
                                      samples[:, :, :, STEPS:STEPS + 3])

            @block.scalar
            def _(act):
                for f in range(12):
                    act.wait_ge(*conv.at(f + 1))
                    nc.scalar.activation(place(f), place(f), ACT.Silu)
        transpose_phase(K, [([last3[:, 4 * q + j, 0:27] for j in range(4)],
                             tail[0:27, 512 * q:512 * q + 512].rearrange("c (n p) -> c n p", n=4)) for q in range(3)])
        sq = K.sb(tmp, "sq", [128, 2, TOK])
        root = K.sb(tmp, "root", [128, 2, TOK])
        inv = K.sb(tmp, "inv", [128, 2, TOK])
        with K.phase("sq_done", "sum_done", "root_done", "inv_done", "scaled", "stored") as (
                block, sqd, summed, rooted, inved, scaled, stored):
            heads = [(i, h) for i in range(2) for h in range(4)]

            @block.sync
            def _(sp):
                sp.dma_start(O[4][0, 0], tail[0:3, :]).then_inc(*stored.up(16))
                sp.dma_start(O[9][0].rearrange("b j n -> (b j) n"), tail[3:27, :]).then_inc(*stored.up(16))
                sp.wait_ge(*stored.at(32))

            @block.gpsimd
            def _(pool):
                for n, (i, h) in enumerate(heads):
                    if n >= 2:
                        pool.wait_ge(*summed.at(n - 1))
                    nc.gpsimd.tensor_tensor(sq[:, n % 2, :], kq[:, i, h, :], kq[:, i, h, :], ALU.mult
                                            ).then_inc(*sqd.up())

            @block.tensor
            def _(pe):
                for n in range(8):
                    pe.wait_ge(*sqd.at(n + 1))
                    if n >= 2:
                        pe.wait_ge(*rooted.at(n - 1))
                    nc.tensor.matmul(K.ps[n % 2][:, 0:TOK], K.const("ones"), sq[:, n % 2, :], start=True, stop=True
                                     ).then_inc(*summed.up())

            @block.scalar
            def _(act):
                for n in range(8):
                    act.wait_ge(*summed.at(n + 1))
                    if n >= 2:
                        act.wait_ge(*inved.at(n - 1))
                    nc.scalar.activation(root[:, n % 2, :], K.ps[n % 2][:, 0:TOK], ACT.Sqrt, bias=K.eps6[:, 0:1]
                                         ).then_inc(*rooted.up())

            @block.vector
            def _(dve):
                for n, (i, h) in enumerate(heads):
                    dve.wait_ge(*rooted.at(n + 1))
                    if n >= 2:
                        dve.wait_ge(*scaled.at(n - 1))
                    nc.vector.reciprocal(inv[:, n % 2, :], root[:, n % 2, :]).then_inc(*inved.up())
                    dve.wait_ge(*inved.at(n + 1))
                    if i == 1:
                        nc.vector.scalar_tensor_tensor(kq[:, i, h, :], kq[:, i, h, :], 128.0 ** -0.5, inv[:, n % 2, :],
                                                       ALU.mult, ALU.mult).then_inc(*scaled.up())
                    else:
                        nc.vector.tensor_tensor(kq[:, i, h, :], kq[:, i, h, :], inv[:, n % 2, :], ALU.mult
                                                ).then_inc(*scaled.up())


def ab_rotary(K, st, qk, kq):
    nc = K.nc
    with contextlib.ExitStack() as tmp:
        t1 = K.sb(tmp, "t1", [128, 8, 64])
        t2 = K.sb(tmp, "t2", [128, 8, 64])
        with K.phase("rot_a", "vector_step") as (block, first, step):
            @block.vector
            def _(dve):
                link = chain(dve, step)
                for t in range(TILES):
                    r = slice(0, ROWS[t])
                    h = qk[r, t, :].rearrange("p (h d) -> p h d", h=8)
                    x1, x2 = h[:, :, 0:64], h[:, :, 64:128]
                    cos = K.const("cos")[r, t * 64:(t + 1) * 64].unsqueeze(1).broadcast_to([ROWS[t], 8, 64])
                    sin = K.const("sin")[r, t * 64:(t + 1) * 64].unsqueeze(1).broadcast_to([ROWS[t], 8, 64])
                    nc.vector.tensor_tensor(t1[r], x1, sin, ALU.mult)
                    link(nc.vector.tensor_tensor(t2[r], x2, sin, ALU.mult))
                    nc.vector.tensor_tensor(x1, x1, cos, ALU.mult)
                    link(nc.vector.tensor_tensor(x2, x2, cos, ALU.mult))
                    nc.vector.tensor_tensor(x1, x1, t2[r], ALU.subtract)
                    link(nc.vector.tensor_tensor(x2, x2, t1[r], ALU.add))
        groups = []
        for t in range(TILES):
            for i, o in ((1, 0), (0, 4)):
                groups.append(([qk[0:ROWS[t], t, (o + h) * 128:(o + h + 1) * 128] for h in range(4)],
                               kq[:, i, 4:8, cols_of(t)]))
        transpose_phase(K, groups)


def invert_phase(K, low, T, R, work, units, levels):
    nc = K.nc
    c, y = work
    with K.phase("inv_cut", "inv_y", "inv_yc", "inv_d", "inv_t", "inv_r") as (block, cut, ys, yc, ds, ts, rs):
        steps = [(s, n) for s in levels for n in range(len(units)) if s in units[n][2]]
        prior = {}
        for m, (s, n) in enumerate(steps):
            prior[m] = max([j for j in range(m) if steps[j][1] == n], default=-1)

        @block.gpsimd
        def _(pool):
            for m, (s, n) in enumerate(steps):
                i, rows, _ = units[n]
                if m >= 2:
                    pool.wait_ge(*ys.at(m - 1))
                mask = K.const(f"level{s}")[0:rows, 0:rows].unsqueeze(1).broadcast_to([rows, 4, rows])
                nc.gpsimd.tensor_tensor(c[0:rows, m % 2, :, 0:rows], low[0:rows, i, :, 0:rows], mask, ALU.mult
                                        ).then_inc(*cut.up())

        @block.tensor
        def _(pe):
            for m, (s, n) in enumerate(steps):
                i, rows, _ = units[n]
                b = m % 2
                pe.wait_ge(*cut.at(m + 1))
                if prior[m] >= 0:
                    pe.wait_ge(*ts.at(prior[m] + 1))
                    pe.wait_ge(*rs.at(prior[m] + 1))
                if m >= 2:
                    pe.wait_ge(*yc.at(m - 1))
                for h in range(4):
                    last = nc.tensor.matmul(K.ps[b][0:rows, h * rows:(h + 1) * rows], c[0:rows, b, h, 0:rows],
                                            R[0:rows, i, h, 0:rows], start=True, stop=True)
                last.then_inc(*ys.up())
                pe.wait_ge(*yc.at(m + 1))
                if m >= 2:
                    pe.wait_ge(*ts.at(m - 1))
                    pe.wait_ge(*rs.at(m - 1))
                for h in range(4):
                    nc.tensor.matmul(K.ps[2 + b][0:rows, h * rows:(h + 1) * rows], y[0:rows, b, h, 0:rows],
                                     T[0:rows, i, h, 0:rows], start=True, stop=True)
                for h in range(4):
                    last = nc.tensor.matmul(K.ps[4 + b][0:rows, h * rows:(h + 1) * rows], T[0:rows, i, h, 0:rows],
                                            y[0:rows, b, h, 0:rows], start=True, stop=True)
                last.then_inc(*ds.up())

        @block.scalar
        def _(act):
            for m, (s, n) in enumerate(steps):
                i, rows, _ = units[n]
                act.wait_ge(*ys.at(m + 1))
                if m >= 2:
                    act.wait_ge(*ds.at(m - 1))
                nc.scalar.copy(y[0:rows, m % 2, :, 0:rows],
                               K.ps[m % 2][0:rows, 0:4 * rows].rearrange("p (h n) -> p h n", h=4)).then_inc(*yc.up())

        @block.vector
        def _(dve):
            for m, (s, n) in enumerate(steps):
                i, rows, _ = units[n]
                dve.wait_ge(*ds.at(m + 1))
                for dst, bank, sig in ((T, 2, ts), (R, 4, rs)):
                    d = dst[0:rows, i, :, 0:rows]
                    nc.vector.tensor_tensor(d, d, K.ps[bank + m % 2][0:rows, 0:4 * rows].rearrange(
                        "p (h n) -> p h n", h=4), ALU.subtract).then_inc(*sig.up())


def first_level(K, low, T, R, units):
    nc = K.nc
    with K.phase("vector_step") as (block, step):
        @block.vector
        def _(dve):
            link = chain(dve, step)
            for i, rows, _ in units:
                d = T[0:rows, i, :, 0:rows]
                mask = K.const("level1")[0:rows, 0:rows].unsqueeze(1).broadcast_to([rows, 4, rows])
                ident = K.const("ident")[0:rows, 0:rows].unsqueeze(1).broadcast_to([rows, 4, rows])
                link(nc.vector.tensor_tensor(d, low[0:rows, i, :, 0:rows], mask, ALU.mult))
                link(nc.vector.tensor_tensor(d, ident, d, ALU.subtract))
    transpose_phase(K, [([T[0:rows, i, h, 0:rows] for h in range(4)], R[0:rows, i, :, 0:rows])
                        for i, rows, _ in units])


LEVELS = [2, 4, 8, 16, 32]


def ab_scan(K, st, kq, v, kd, ab, o):
    nc, I, O = K.nc, K.ins, K.outs
    qkd = K.sb(st, "qkd", [128, TILES, 8, 128])
    R = K.sb(st, "R", [128, TILES, 4, 128])
    beta = K.sb(st, "beta", [128, TILES, 4])
    gcol = K.sb(st, "gcol", [128, TILES, 8])
    egc = K.sb(st, "egc", [128, TILES, 8])
    ekd = K.sb(st, "ekd", [128, TILES, 8])
    nbeg = K.sb(st, "nbeg", [128, TILES, 4])
    total = K.sb(st, "total", [128, 4 + SEQS, 8])
    with contextlib.ExitStack() as tmp:
        arow = K.sb(tmp, "arow", [128, 8])
        g = K.sb(tmp, "g", [128, TILES, 4])
        s1 = K.sb(tmp, "s1", [128, TILES, 4])
        s2 = K.sb(tmp, "s2", [128, TILES, 4])
        gup = K.sb(tmp, "gup", [128, TILES, 4, 128])
        gp = K.sb(tmp, "gp", [128, 4, 4])
        gb = K.sb(tmp, "gb", [128, SEQS, 4])
        low = K.sb(tmp, "low", [128, TILES, 4, 128])
        T = K.sb(tmp, "T", [128, TILES, 4, 128])
        c = K.sb(tmp, "c", [128, 2, 4, 128])
        y = K.sb(tmp, "y", [128, 2, 4, 128])
        with K.phase("loaded", "scalar_step", "vector_step") as (block, loaded, by_act, by_dve):
            full = [(slice(0, 128), slice(0, 2)), (slice(0, SAMPLE), slice(2, 3))]

            @block.sync
            def _(sp):
                sp.dma_start(arow[:, 0:4], row_broadcast(I["ab_a_log"][0])).then_inc(*loaded.up(16))
                sp.dma_start(arow[:, 4:8], row_broadcast(I["ab_dt_bias"][0])).then_inc(*loaded.up(16))

            @block.scalar
            def _(act):
                link = chain(act, by_act)
                act.wait_ge(*loaded.at(32))
                link(nc.scalar.activation(arow[:, 0:4], arow[:, 0:4], ACT.Exp))
                act.wait_ge(*by_dve.at(2))
                for r, t in full:
                    nc.scalar.activation(beta[r, t, :], ab[r, t, 4:8], ACT.Sigmoid)
                for r, t in full:
                    last = nc.scalar.activation(s2[r, t, :], s1[r, t, :], ACT.Exp)
                link(last)
                for r, t in full:
                    last = nc.scalar.activation(s2[r, t, :], s2[r, t, :], ACT.Ln, bias=1.0)
                link(last)

            @block.vector
            def _(dve):
                link = chain(dve, by_dve)
                dve.wait_ge(*loaded.at(32))
                for r, t in full:
                    n = t.stop - t.start
                    last = nc.vector.tensor_tensor(g[r, t, :], ab[r, t, 0:4], arow[r, 4:8].unsqueeze(1).broadcast_to(
                        [r.stop, n, 4]), ALU.add)
                link(last)
                for r, t in full:
                    last = nc.vector.scalar_tensor_tensor(s1[r, t, :], g[r, t, :], -1.0, g[r, t, :], ALU.mult, ALU.min)
                link(last)
                dve.wait_ge(*by_act.at(3))
                for r, t in full:
                    last = nc.vector.scalar_tensor_tensor(g[r, t, :], g[r, t, :], 0.0, s2[r, t, :], ALU.max, ALU.add)
                link(last)
                for r, t in full:
                    n = t.stop - t.start
                    last = nc.vector.scalar_tensor_tensor(
                        g[r, t, :], g[r, t, :], -1.0, arow[r, 0:4].unsqueeze(1).broadcast_to([r.stop, n, 4]),
                        ALU.mult, ALU.mult)
                link(last)
                for t in range(TILES):
                    r = ROWS[t]
                    for h in range(4):
                        nc.vector.tensor_scalar(gup[0:r, t, h, 0:r], K.const("upto_" + tile_kind(t))[0:r, 0:r],
                                                g[0:r, t, h:h + 1], None, ALU.mult)
                for n in range(4):
                    nc.vector.tensor_scalar(gp[:, n, :], g[:, n // 2, :], K.const("of_chunk_p")[:, n % 2:n % 2 + 1],
                                            None, ALU.mult)
                nc.vector.tensor_tensor(
                    gb[0:SAMPLE], g[0:SAMPLE, 2, :].unsqueeze(1).broadcast_to([SAMPLE, SEQS, 4]),
                    K.const("of_chunk_s")[0:SAMPLE, :].unsqueeze(2).broadcast_to([SAMPLE, SEQS, 4]), ALU.mult)
        with K.phase("sum_full", "low_done", "scalar_step", "vector_step", "dec_pool") as (
                block, full, low_done, by_act, by_dve, by_pool):
            tot = K.ps[3][:, 32:80].rearrange("p (c h) -> p c h", h=4)

            @block.tensor
            def _(pe):
                for t in range(TILES):
                    r, kind = ROWS[t], tile_kind(t)
                    nc.tensor.matmul(K.ps[t][0:r, 0:4 * r], K.const("ones")[0:r, 0:r],
                                     gup[0:r, t, :, 0:r], start=True, stop=True)
                    nc.tensor.matmul(K.ps[3][0:r, 8 * t:8 * t + 4], K.const("upto_" + kind)[0:r, 0:r], g[0:r, t, :],
                                     start=True, stop=True)
                    nc.tensor.matmul(K.ps[3][0:r, 8 * t + 4:8 * t + 8], K.const("below_" + kind)[0:r, 0:r],
                                     g[0:r, t, :], start=True, stop=True)
                nc.tensor.matmul(tot[:, 0:4, :], K.const("ones"), gp[:, :, :], start=True, stop=True)
                nc.tensor.matmul(tot[:, 4:12, :], K.const("ones")[0:SAMPLE, :], gb[0:SAMPLE, :, :],
                                 start=True, stop=True).then_inc(*full.up())
                for t in range(TILES):
                    r = ROWS[t]
                    if t >= 1:
                        pe.wait_ge(*low_done.at(3 * t))
                    for h in range(4):
                        nc.tensor.matmul(K.ps[4][0:r, h * r:(h + 1) * r], kq[:, 0, h, cols_of(t)],
                                         kq[:, 0, h, cols_of(t)], start=True, stop=True)
                    for h in range(8):
                        last = nc.tensor.matmul(K.ps[5 + h // 4][0:r, h % 4 * r:(h % 4 + 1) * r],
                                                kq[:, 0, h, cols_of(t)], kq[:, 1, h, cols_of(t)],
                                                start=True, stop=True)
                    last.then_inc(*full.up())

            @block.vector
            def _(dve):
                link = chain(dve, by_dve)
                dve.wait_ge(*full.at(1))
                for t in range(TILES):
                    r = ROWS[t]
                    last = nc.vector.tensor_copy(gcol[0:r, t, :], K.ps[3][0:r, 8 * t:8 * t + 8])
                link(last)
                for t in range(TILES):
                    r = ROWS[t]
                    for h in range(4):
                        s = K.ps[t][0:r, h * r:(h + 1) * r]
                        gc = gcol[0:r, t, h:h + 1]
                        nc.vector.tensor_scalar(low[0:r, t, h, 0:r], s, gc, 0.0, ALU.subtract, ALU.max)
                        last = nc.vector.tensor_scalar(qkd[0:r, t, h, 0:r], s, gc, 0.0, ALU.subtract, ALU.min)
                link(last)
                dve.wait_ge(*by_act.at(1))
                for t in range(TILES):
                    r, kind = ROWS[t], tile_kind(t)
                    below = K.const("below_" + kind)[0:r, 0:r].unsqueeze(1).broadcast_to([r, 4, r])
                    upto = K.const("upto_" + kind)[0:r, 0:r].unsqueeze(1).broadcast_to([r, 4, r])
                    nc.vector.tensor_tensor(low[0:r, t, :, 0:r], low[0:r, t, :, 0:r], below, ALU.mult)
                    last = nc.vector.tensor_tensor(qkd[0:r, t, 0:4, 0:r], qkd[0:r, t, 0:4, 0:r], upto, ALU.mult)
                link(last)
                for t in range(TILES):
                    r, kind = ROWS[t], tile_kind(t)
                    dve.wait_ge(*full.at(t + 2))
                    for h in range(4):
                        last = nc.vector.scalar_tensor_tensor(
                            low[0:r, t, h, 0:r], K.ps[4][0:r, h * r:(h + 1) * r], beta[0:r, t, h:h + 1],
                            low[0:r, t, h, 0:r], ALU.mult, ALU.mult)
                    last.then_inc(*low_done.up())
                    nc.vector.tensor_tensor(qkd[0:r, t, 0:4, 0:r], qkd[0:r, t, 0:4, 0:r],
                                            K.ps[5][0:r, 0:4 * r].rearrange("p (h n) -> p h n", h=4), ALU.mult
                                            ).then_inc(*low_done.up())
                    ret = K.const("retdecay_" + kind)[0:r].rearrange("p (h n) -> p h n", h=4)[:, :, 0:r]
                    nc.vector.tensor_tensor(qkd[0:r, t, 4:8, 0:r], ret,
                                            K.ps[6][0:r, 0:4 * r].rearrange("p (h n) -> p h n", h=4), ALU.mult
                                            ).then_inc(*low_done.up())
                    nc.vector.tensor_copy(egc[0:r, t, 4:8], K.const("retq_" + kind)[0:r])
                    nc.vector.tensor_copy(ekd[0:r, t, 4:8], K.const("retk_" + kind)[0:r])
                    link(nc.vector.scalar_tensor_tensor(nbeg[0:r, t, :], egc[0:r, t, 0:4], -1.0, beta[0:r, t, :],
                                                   ALU.mult, ALU.mult))
                    for h in range(8):
                        nc.vector.tensor_scalar(kd[0:r, t, h, :], kd[0:r, t, h, :], ekd[0:r, t, h:h + 1], None,
                                                ALU.mult)
                        if h < 4:
                            nc.vector.tensor_scalar(v[0:r, t, h, :], v[0:r, t, h, :], beta[0:r, t, h:h + 1], None,
                                                    ALU.mult)
                for h in range(4):
                    nc.vector.memset(total[:, 0:4, 4 + h], CHUNK_DECAY[CHUNK][h])
                    nc.vector.memset(total[:, 4:12, 4 + h], CHUNK_DECAY[STEPS][h])

            @block.scalar
            def _(act):
                act.wait_ge(*by_dve.at(2))
                for t in range(TILES):
                    r = ROWS[t]
                    nc.scalar.activation(low[0:r, t, :, 0:r], low[0:r, t, :, 0:r], ACT.Exp, scale=-1.0)
                    nc.scalar.activation(qkd[0:r, t, 0:4, 0:r], qkd[0:r, t, 0:4, 0:r], ACT.Exp)
                    nc.scalar.activation(egc[0:r, t, 0:4], gcol[0:r, t, 0:4], ACT.Exp)
                    nc.scalar.activation(ekd[0:r, t, 0:4], gcol[0:r, t, 4:8], ACT.Exp)
                nc.scalar.activation(total[:, :, 0:4], tot, ACT.Exp).then_inc(*by_act.up())
        units = [(t, ROWS[t], LEVELS if t < 2 else [2, 4]) for t in range(TILES)]
        first_level(K, low, T, R, units)
        invert_phase(K, low, T, R, (c, y), units, LEVELS)
    ab_chunks(K, kq, v, kd, qkd, R, egc, nbeg, total, o)


def ab_chunks(K, kq, v, kd, qkd, R, egc, nbeg, total, o):
    nc, I, O = K.nc, K.ins, K.outs
    with contextlib.ExitStack() as tmp:
        S = K.sb(tmp, "S", [128, 8, 128])
        vn = K.sb(tmp, "vn", [128, 4, 128])
        r_ = K.sb(tmp, "r", [128, 4, 128])
        for n in range(5):
            ab_chunk(K, n, kq, v, kd, qkd, R, egc, nbeg, total, o, S, vn, r_)


def ab_chunk(K, n, kq, v, kd, qkd, R, egc, nbeg, total, o, S, vn, r_):
    nc, I, O = K.nc, K.ins, K.outs
    sample = n == 4
    t, off = (2, 0) if sample else (n // 2, 64 * (n % 2))
    sl = slice(off, off + 64)
    c = slice(AT[t] + off, AT[t] + off + 64)
    with contextlib.ExitStack() as tmp:
        if sample:
            ab_sample_states(K, tmp, kq)
        with K.phase("ks_full", "r_done", "vn_full", "vn_done", "o_full", "o_scaled", "o_done", "su_full",
                     "s_done", "stored") as (
                block, ks, rd, vf, vd, of, osc, od, sf, sd, out):
            @block.tensor
            def _(pe):
                if not sample and n:
                    for h in range(4):
                        nc.tensor.matmul(K.ps[0][sl, h * 128:(h + 1) * 128], kq[:, 0, h, c], S[:, h, :],
                                         start=True, stop=True)
                    for h in range(8):
                        last = nc.tensor.matmul(K.ps[1 + h // 4][sl, h % 4 * 128:(h % 4 + 1) * 128], kq[:, 1, h, c],
                                                S[:, h, :], start=True, stop=True)
                    last.then_inc(*ks.up())
                elif sample:
                    for h in range(4):
                        nc.tensor.matmul(K.ps[0][sl, h * 128:(h + 1) * 128], K.byst[:, h, 0, :], K.const("ident"),
                                         start=True, stop=True)
                    for h in range(8):
                        last = nc.tensor.matmul(K.ps[1 + h // 4][sl, h % 4 * 128:(h % 4 + 1) * 128],
                                                K.byst[:, h, 1, :], K.const("ident"), start=True, stop=True)
                    last.then_inc(*ks.up())
                if n:
                    pe.wait_ge(*rd.at(1))
                src = r_ if n else v[:, 0, 0:4, :]
                for h in range(4):
                    last = nc.tensor.matmul(K.ps[3][sl, h * 128:(h + 1) * 128], R[sl, t, h, sl], src[sl, h, :],
                                            start=True, stop=True)
                last.then_inc(*vf.up())
                pe.wait_ge(*vd.at(1))
                for h in range(8):
                    vals = vn[sl, h, :] if h < 4 else v[sl, t, h, :]
                    last = nc.tensor.matmul(K.ps[4 + h // 4][sl, h % 4 * 128:(h % 4 + 1) * 128], qkd[sl, t, h, sl],
                                            vals, start=True, stop=True)
                last.then_inc(*of.up())
                if not sample:
                    for h in range(8):
                        vals = vn[sl, h, :] if h < 4 else v[sl, t, h, :]
                        last = nc.tensor.matmul(K.ps[6 + h // 4][:, h % 4 * 128:(h % 4 + 1) * 128], kd[sl, t, h, :],
                                                vals, start=True, stop=True)
                    last.then_inc(*sf.up())

            @block.scalar
            def _(act):
                act.wait_ge(*vf.at(1))
                nc.scalar.copy(vn[sl, :, :], K.ps[3][sl, :].rearrange("p (h n) -> p h n", h=4)).then_inc(*vd.up())
                if n:
                    for h in range(8):
                        last = nc.scalar.mul(o[sl, t, h, :], K.ps[1 + h // 4][sl, h % 4 * 128:(h % 4 + 1) * 128],
                                             egc[sl, t, h:h + 1])
                    last.then_inc(*osc.up())

            @block.vector
            def _(dve):
                if n:
                    dve.wait_ge(*ks.at(1))
                    for h in range(4):
                        last = nc.vector.scalar_tensor_tensor(
                            r_[sl, h, :], K.ps[0][sl, h * 128:(h + 1) * 128], nbeg[sl, t, h:h + 1], v[sl, t, h, :],
                            ALU.mult, ALU.add)
                    last.then_inc(*rd.up())
                if not sample:
                    dve.wait_ge(*sf.at(1))
                    for h in range(8):
                        up = K.ps[6 + h // 4][:, h % 4 * 128:(h % 4 + 1) * 128]
                        if n:
                            last = nc.vector.scalar_tensor_tensor(S[:, h, :], S[:, h, :], total[:, n, h:h + 1], up,
                                                                  ALU.mult, ALU.add)
                        else:
                            last = nc.vector.tensor_copy(S[:, h, :], up)
                    last.then_inc(*sd.up())
                dve.wait_ge(*of.at(1))
                if n:
                    dve.wait_ge(*osc.at(1))
                for q in range(2):
                    ops = K.ps[4 + q][sl, :].rearrange("p (h n) -> p h n", h=4)
                    dst = o[sl, t, 4 * q:4 * q + 4, :]
                    if n:
                        nc.vector.tensor_tensor(dst, dst, ops, ALU.add)
                    else:
                        nc.vector.tensor_copy(dst, ops)

            if n == 3:
                @block.sync
                def _(sp):
                    sp.wait_ge(*sd.at(1))
                    for q, i in ((0, 5), (1, 6)):
                        sp.dma_start(O[i][0, 0].rearrange("h k v -> k h v"), S[:, 4 * q:4 * q + 4, :]
                                     ).then_inc(*out.up(16))
                    sp.wait_ge(*out.at(32))
        if sample:
            ab_sample_update(K, tmp, kd, v, vn, total)


def ab_sample_states(K, tmp, kq):
    nc, I = K.nc, K.ins
    K.byst = K.sb(tmp, "byst", [128, 8, 2, SAMPLE])
    K.state = K.sb(tmp, "state", [128, 2, SEQS, 128])
    with K.phase("st_in0", "st_in1", "st_full", "st_done") as (block, in0, in1, full, done):
        ins = (in0, in1)

        @block.sync
        def _(sp):
            for h in range(8):
                if h >= 2:
                    sp.wait_ge(*full.at(h - 1))
                src = I["state_delta" if h < 4 else "state_ret"][0, :, h % 4].rearrange("b k v -> k b v")
                sp.dma_start(K.state[:, h % 2, :, :], src).then_inc(*ins[h % 2].up(16))

        @block.tensor
        def _(pe):
            for h in range(8):
                pe.wait_ge(*ins[h % 2].at(16 * (h // 2 + 1)))
                if h >= 2:
                    pe.wait_ge(*done.at(h - 1))
                bank = K.ps[h % 2][:, 0:2 * SAMPLE].rearrange("p (i c) -> p i c", i=2)
                for b in range(SEQS):
                    c = slice(SEQ + 8 * b, SEQ + 8 * b + 8)
                    last = nc.tensor.matmul(bank[:, :, 8 * b:8 * b + 8], K.state[:, h % 2, b, :], kq[:, :, h, c],
                                            start=True, stop=True)
                last.then_inc(*full.up())

        @block.scalar
        def _(act):
            for h in range(8):
                act.wait_ge(*full.at(h + 1))
                nc.scalar.copy(K.byst[:, h, :, :], K.ps[h % 2][:, 0:2 * SAMPLE].rearrange("p (i c) -> p i c", i=2)
                               ).then_inc(*done.up())


def ab_sample_update(K, tmp, kd, v, vn, total):
    nc, I, O = K.nc, K.ins, K.outs
    spread = K.sb(tmp, "spread", [SAMPLE, 2, SEQS, 128])
    with K.phase("st_in0", "st_in1", "spread_done", "su_full", "su_done", "su_out0", "su_out1") as (
            block, in0, in1, sp_done, full, done, out0, out1):
        ins, outs = (in0, in1), (out0, out1)

        def store(sp, h):
            sp.wait_ge(*done.at(h + 1))
            dst = O[10 if h < 4 else 11][0, :, h % 4].rearrange("b k v -> k b v")
            sp.dma_start(dst, K.state[:, h % 2, :, :]).then_inc(*outs[h % 2].up(16))

        @block.sync
        def _(sp):
            for h in range(8):
                if h >= 2:
                    sp.wait_ge(*outs[h % 2].at(16 * (h // 2)))
                src = I["state_delta" if h < 4 else "state_ret"][0, :, h % 4].rearrange("b k v -> k b v")
                sp.dma_start(K.state[:, h % 2, :, :], src).then_inc(*ins[h % 2].up(16))
                if h >= 1:
                    store(sp, h - 1)
            store(sp, 7)
            for q in range(2):
                sp.wait_ge(*outs[q].at(64))

        @block.gpsimd
        def _(pool):
            for h in range(8):
                if h >= 2:
                    pool.wait_ge(*full.at(h - 1))
                vals = vn[0:SAMPLE, h, :] if h < 4 else v[0:SAMPLE, 2, h, :]
                nc.gpsimd.tensor_tensor(
                    spread[:, h % 2, :, :], vals.unsqueeze(1).broadcast_to([SAMPLE, SEQS, 128]),
                    K.const("of_chunk_s")[0:SAMPLE, :].unsqueeze(2).broadcast_to([SAMPLE, SEQS, 128]), ALU.mult
                ).then_inc(*sp_done.up())

        @block.tensor
        def _(pe):
            for h in range(8):
                pe.wait_ge(*sp_done.at(h + 1))
                if h >= 2:
                    pe.wait_ge(*done.at(h - 1))
                for q in range(2):
                    last = nc.tensor.matmul(K.ps[2 * (h % 2) + q][:, :], kd[0:SAMPLE, 2, h, :],
                                            spread[:, h % 2, 4 * q:4 * q + 4, :], start=True, stop=True)
                last.then_inc(*full.up())

        @block.vector
        def _(dve):
            for h in range(8):
                dve.wait_ge(*full.at(h + 1))
                dve.wait_ge(*ins[h % 2].at(16 * (h // 2 + 1)))
                for b in range(SEQS):
                    s = K.state[:, h % 2, b, :]
                    last = nc.vector.scalar_tensor_tensor(
                        s, s, total[:, 4 + b, h:h + 1], K.ps[2 * (h % 2) + b // 4][:, b % 4 * 128:(b % 4 + 1) * 128],
                        ALU.mult, ALU.add)
                last.then_inc(*done.up())


def ab_finish(K, o):
    nc, I = K.nc, K.ins
    with contextlib.ExitStack() as tmp:
        gate = K.sb(tmp, "gate", [128, TILES, D])
        nw = K.sb(tmp, "nw", [128, 128])
        sq = K.sb(tmp, "sq", [128, D])
        mean = K.sb(tmp, "mean", [128, TILES, 8])
        ms = K.sb(tmp, "ms", [128, TILES, 8])
        with K.phase("loaded", "ln_std", "ln_var", "vector_step", "fin_silu") as (block, loaded, std, var, step, silu):
            @block.sync
            def _(sp):
                for t in range(TILES):
                    sp.dma_start(gate[0:ROWS[t], t, :], K.scratch["gate"][cols_of(t), :]).then_inc(*loaded.up(16))
                sp.dma_start(nw[:, :], row_broadcast(I["ab_norm_w"][0])).then_inc(*loaded.up(16))

            @block.scalar
            def _(act):
                act.wait_ge(*loaded.at(64))
                for t in range(TILES):
                    nc.scalar.activation(gate[0:ROWS[t], t, :], gate[0:ROWS[t], t, :], ACT.Silu).then_inc(*silu.up())
                for t in range(TILES):
                    act.wait_ge(*var.at(t + 1))
                    r = ROWS[t]
                    nc.scalar.activation(ms[0:r, t, 0:4], ms[0:r, t, 0:4], ACT.Sqrt, scale=1.0 / 128,
                                         bias=K.eps6[0:r, 0:1])
                    nc.scalar.activation(ms[0:r, t, 4:8], ms[0:r, t, 4:8], ACT.Sqrt, scale=1.0 / 128,
                                         bias=K.eps5[0:r, 0:1]).then_inc(*std.up())

            @block.vector
            def _(dve):
                link = chain(dve, step)
                dve.wait_ge(*loaded.at(64))
                for t in range(TILES):
                    r = ROWS[t]
                    ot = o[0:r, t, :, :]
                    link(nc.vector.tensor_reduce(mean[0:r, t, 4:8], ot[:, 4:8, :], AX, ALU.add))
                    link(nc.vector.tensor_scalar(mean[0:r, t, 4:8], mean[0:r, t, 4:8], 1.0 / 128, None, ALU.mult))
                    link(nc.vector.tensor_tensor(ot[:, 4:8, :], ot[:, 4:8, :], mean[0:r, t, 4:8].unsqueeze(2
                                                 ).broadcast_to([r, 4, 128]), ALU.subtract))
                    sqv = sq[0:r, :].rearrange("p (h n) -> p h n", h=8)
                    link(nc.vector.tensor_tensor(sqv, ot, ot, ALU.mult))
                    nc.vector.tensor_reduce(ms[0:r, t, :], sqv, AX, ALU.add).then_inc(*var.up())
                    dve.wait_ge(*var.at(t + 1))
                for t in range(TILES):
                    r = ROWS[t]
                    ot = o[0:r, t, :, :]
                    dve.wait_ge(*std.at(t + 1))
                    link(nc.vector.reciprocal(ms[0:r, t, :], ms[0:r, t, :]))
                    link(nc.vector.tensor_tensor(ot, ot, ms[0:r, t, :].unsqueeze(2).broadcast_to([r, 8, 128]),
                                                 ALU.mult))
                    link(nc.vector.tensor_tensor(ot[:, 0:4, :], ot[:, 0:4, :], nw[0:r, :].unsqueeze(1).broadcast_to(
                        [r, 4, 128]), ALU.mult))
                    dve.wait_ge(*silu.at(t + 1))
                    link(nc.vector.tensor_tensor(ot, ot, gate[0:r, t, :].rearrange("p (h n) -> p h n", h=8),
                                                 ALU.mult))
        outT = K.sb(tmp, "outT", [128, KT, TOK])
        transpose_phase(K, [([o[0:ROWS[t], t, 4 * q + j, :] for j in range(4)],
                             outT[:, 4 * q:4 * q + 4, cols_of(t)]) for t in range(TILES) for q in range(2)])
        add_and_norm_phase(K, K.first["ab_out"], outT, 0, 0)



def cross_attention(K, layer):
    K.caches_in = [[K.sem(f"{n}_in{i}") for i in range(CACHES)] for n in ("keys", "values")]
    for sig in K.caches_in[0] + K.caches_in[1]:
        sig.base = sig.sent
    with contextlib.ExitStack() as st:
        oT = K.sb(st, "oT", [128, KT, TOK])
        with contextlib.ExitStack() as tmp:
            qT = K.sb(tmp, "qT", [128, KT, WIDE])
            caches = [K.sb(tmp, n, [128, CACHES, 2, D]) for n in ("kc", "vc")]
            with contextlib.ExitStack() as own:
                kT = K.sb(own, "kT", [128, KT, MEM])
                k, v = K.sb(own, "k", [128, 2, D]), K.sb(own, "v", [128, 2, D])
                stored = K.sem("kv_stored")
                stored.base = stored.sent
                project_memory(K, layer, kT, k, v, stored)
                feature_major_phase(K, K.first[f"x_q{layer}"], 2, K.xT, TOK,
                                    lambda f, bank: [(qT[:, f, 0:TOK], bank[:, 0:TOK])])
                attend_prompt(K, layer, qT, kT, v, oT, caches, stored)
            attend_samples(K, layer, qT, oT, caches)
        add_and_norm_phase(K, K.first[f"x_o{layer}"], oT, layer, 1)


def project_memory(K, layer, kT, k, v, stored):
    nc, I, O = K.nc, K.ins, K.outs
    with contextlib.ExitStack() as t1:
        mem = K.sb(t1, "mem", [128, 2, D])
        memT = K.sb(t1, "memT", [128, KT, MEM])
        with K.phase("loaded") as (block, loaded):
            @block.scalar
            def _(act):
                act.dma_start(mem[:, :, :], I["mem_prompt"][0].rearrange("(t p) n -> p t n", p=128)
                              ).then_inc(*loaded.up(16))
                act.wait_ge(*loaded.at(16))
        transpose_phase(K, [([mem[:, t, (4 * q + j) * 128:(4 * q + j + 1) * 128] for j in range(4)],
                             memT[:, 4 * q:4 * q + 4, t * 128:(t + 1) * 128])
                            for t in range(2) for q in range(2)])
        tiles = [(0, 128), (128, 128)]
        token_major_phase(
            K, K.first[f"x_k{layer}"], 4, memT, tiles,
            lambda g, t: (k, v)[g // 2][:, t, g % 2 * 512:g % 2 * 512 + 512],
            stores=[(O[2][layer, 0].rearrange("(t p) h d -> p t (h d)", p=128), k[:, :, :]),
                    (O[3][layer, 0].rearrange("(t p) h d -> p t (h d)", p=128), v[:, :, :])], stored_later=stored)
        transpose_phase(K, [([k[:, t, (4 * q + j) * 128:(4 * q + j + 1) * 128] for j in range(4)],
                             kT[:, 4 * q:4 * q + 4, t * 128:(t + 1) * 128])
                            for t in range(2) for q in range(2)])


XSCALE = float(D // XH) ** -0.5


CACHES = 2


def load_cache(K, sp, layer, b, which, caches, sig):
    src = K.ins[("cache_mem_k", "cache_mem_v")[which]][layer, b]
    sp.dma_start(caches[which][:, b % CACHES, :, :], src.rearrange("(t p) h d -> p t (h d)", p=128)
                 ).then_inc(*sig[b % CACHES].up(16))


def attend_prompt(K, layer, qT, kT, v, oT, caches, stored):
    nc = K.nc
    with contextlib.ExitStack() as tmp:
        p = K.sb(tmp, "p", [128, 8, MEM])
        pT = K.sb(tmp, "pT", [128, 2, 8, 128])
        col = K.sb(tmp, "col", [128, 3, 8])
        pairs = [(h, t) for h in range(XH) for t in range(2)]
        with K.phase("sc_full", "max_done", "exp_done", "vector_step") as (block, full, maxed, exped, step):
            @block.sync
            def _(sp):
                for b in range(CACHES):
                    for which in range(2):
                        load_cache(K, sp, layer, b, which, caches, K.caches_in[which])

            @block.gpsimd
            def _(pool):
                nc.gpsimd.memset(qT[:, :, TOK:WIDE], 0.0)

            @block.tensor
            def _(pe):
                for n, (h, t) in enumerate(pairs):
                    for j in range(2):
                        last = nc.tensor.matmul(K.ps[n][:, 0:MEM],
                                                qT[:, 2 * h + j, t * 128:(t + 1) * 128], kT[:, 2 * h + j, :],
                                                start=(j == 0), stop=(j == 1))
                    last.then_inc(*full.up())

            @block.vector
            def _(dve):
                link = chain(dve, step)
                for n in range(8):
                    dve.wait_ge(*full.at(n + 1))
                    link(nc.vector.reduce_max(col[:, 0, n:n + 1], K.ps[n][:, 0:MEM], AX))
                    nc.vector.tensor_scalar(col[:, 1, n:n + 1], col[:, 0, n:n + 1], -XSCALE, None, ALU.mult
                                            ).then_inc(*maxed.up())
                dve.wait_ge(*exped.at(8))
                link(nc.vector.reciprocal(col[:, 2, :], col[:, 2, :]))
                nc.vector.tensor_tensor(p[:, :, :], p[:, :, :], col[:, 2, :].unsqueeze(2).broadcast_to([128, 8, MEM]),
                                        ALU.mult)

            @block.scalar
            def _(act):
                for n in range(8):
                    act.wait_ge(*maxed.at(n + 1))
                    nc.scalar.activation(p[:, n, :], K.ps[n][:, 0:MEM], ACT.Exp,
                                         scale=XSCALE, bias=col[:, 1, n:n + 1], accum_out=col[:, 2, n:n + 1]
                                         ).then_inc(*exped.up())
        transpose_phase(K, [([p[:, 4 * q + j, m * 128:(m + 1) * 128] for j in range(4)],
                             pT[:, m, 4 * q:4 * q + 4, :]) for m in range(2) for q in range(2)])
        with K.phase("mm_full", "mm_act") as (block, full, by_act):
            @block.sync
            def _(sp):
                sp.wait_ge(*stored.at(32))

            @block.tensor
            def _(pe):
                for f in range(KT):
                    if f >= 4:
                        pe.wait_ge(*by_act.at(f - 3))
                    h = f // 2
                    for m in range(2):
                        last = nc.tensor.matmul(K.ps[f % 4][:, 0:SEQ], v[:, m, f * 128:(f + 1) * 128],
                                                pT[:, m, 2 * h:2 * h + 2, :], start=(m == 0), stop=(m == 1))
                    last.then_inc(*full.up())

            @block.scalar
            def _(act):
                for f in range(KT):
                    act.wait_ge(*full.at(f + 1))
                    nc.scalar.copy(oT[:, f, 0:SEQ], K.ps[f % 4][:, 0:SEQ]).then_inc(*by_act.up())


def attend_samples(K, layer, qT, oT, caches):
    nc = K.nc
    kc, vc = caches
    with contextlib.ExitStack() as tmp:
        kcT = K.sb(tmp, "kcT", [128, 2, KT, MEM])
        p = K.sb(tmp, "p", [128, 2, MEM])
        pT = K.sb(tmp, "pT", [128, 2, 2, 128])
        o = K.sb(tmp, "o", [128, 2, 256])
        col = K.sb(tmp, "col", [128, SEQS, 4])
        kin, vin = K.caches_in
        with K.phase("kt_full", "kt_act", "kt_dve", "sc_full", "max_done", "exp_done", "p_done", "pt_full",
                     "pt_done", "o_full", "o_act", "ot_full", "o_done", "vector_step") as (
                block, ktf, kta, ktd, scf, maxed, exped, pd, ptf, ptd, of, oa, otf, od, step):
            def arrived(sig, b):
                s = sig[b % CACHES]
                return s.sem, s.base + 16 * (b // CACHES + 1)

            @block.sync
            def _(sp):
                for b in range(CACHES, SEQS + 2):
                    if b < SEQS:
                        sp.wait_ge(*ktf.at(4 * (b - CACHES + 1)))
                        load_cache(K, sp, layer, b, 0, caches, kin)
                    if b - 2 >= CACHES:
                        sp.wait_ge(*of.at(b - 2 - CACHES + 1))
                        load_cache(K, sp, layer, b - 2, 1, caches, vin)

            @block.tensor
            def _(pe):
                def turn_keys(b):
                    pe.wait_ge(*arrived(kin, b))
                    for n in range(4):
                        t, q = n // 2, n % 2
                        if b:
                            pe.wait_ge(*(kta if n % 2 == 0 else ktd).at(2 * (b - 1) + n // 2 + 1))
                        for j in range(4):
                            f = 4 * q + j
                            last = nc.tensor.transpose(K.ps[n][:, j * 128:(j + 1) * 128],
                                                       kc[:, b % CACHES, t, f * 128:(f + 1) * 128], K.const("ident"))
                        last.then_inc(*ktf.up())

                def scores(b):
                    pe.wait_ge(*kta.at(2 * (b + 1)))
                    pe.wait_ge(*ktd.at(2 * (b + 1)))
                    c = slice(SEQ + 8 * b, SEQ + 8 * b + 32)
                    if b:
                        pe.wait_ge(*exped.at(b))
                    for h in range(XH):
                        for j in range(2):
                            last = nc.tensor.matmul(K.ps[4][32 * h:32 * h + 32, 0:MEM], qT[:, 2 * h + j, c],
                                                    kcT[:, b % 2, 2 * h + j, :], start=(j == 0), stop=(j == 1))
                    last.then_inc(*scf.up())

                def turn_probabilities(b):
                    pe.wait_ge(*pd.at(b + 1))
                    if b:
                        pe.wait_ge(*ptd.at(b))
                    for m in range(2):
                        last = nc.tensor.transpose(K.ps[5][:, m * 128:(m + 1) * 128],
                                                   p[:, b % 2, m * 128:(m + 1) * 128], K.const("ident"))
                    last.then_inc(*ptf.up())

                def outputs(b):
                    pe.wait_ge(*ptd.at(b + 1))
                    pe.wait_ge(*arrived(vin, b))
                    if b:
                        pe.wait_ge(*oa.at(b))
                    for h in range(XH):
                        for m in range(2):
                            last = nc.tensor.matmul(K.ps[6][32 * h:32 * h + 32, 0:256],
                                                    pT[:, b % 2, m, 32 * h:32 * h + 32],
                                                    vc[:, b % CACHES, m, h * 256:(h + 1) * 256],
                                                    start=(m == 0), stop=(m == 1))
                    last.then_inc(*of.up())

                def turn_outputs(b):
                    pe.wait_ge(*oa.at(b + 1))
                    if b:
                        pe.wait_ge(*od.at(b))
                    for j in range(2):
                        last = nc.tensor.transpose(K.ps[7][:, j * 128:(j + 1) * 128],
                                                   o[:, b % 2, j * 128:(j + 1) * 128], K.const("ident"))
                    last.then_inc(*otf.up())

                turn_keys(0)
                for b in range(SEQS):
                    scores(b)
                    if b >= 2:
                        turn_outputs(b - 2)
                    if b + 1 < SEQS:
                        turn_keys(b + 1)
                    if b:
                        outputs(b - 1)
                    turn_probabilities(b)
                turn_outputs(SEQS - 2)
                outputs(SEQS - 1)
                turn_outputs(SEQS - 1)

            @block.scalar
            def _(act):
                def copy_keys(b):
                    if b >= 2:
                        act.wait_ge(*scf.at(b - 1))
                    for n in (0, 2):
                        act.wait_ge(*ktf.at(4 * b + n + 1))
                        nc.scalar.copy(kcT[:, b % 2, 0:4, n // 2 * 128:(n // 2 + 1) * 128],
                                       K.ps[n][:, :].rearrange("p (j n) -> p j n", j=4)).then_inc(*kta.up())

                def copy_outputs(b):
                    act.wait_ge(*of.at(b + 1))
                    if b >= 2:
                        act.wait_ge(*otf.at(b - 1))
                    nc.scalar.copy(o[:, b % 2, :], K.ps[6][:, 0:256]).then_inc(*oa.up())

                copy_keys(0)
                for b in range(SEQS):
                    act.wait_ge(*maxed.at(b + 1))
                    if b >= 2:
                        act.wait_ge(*ptf.at(b - 1))
                    nc.scalar.activation(p[:, b % 2, :], K.ps[4][:, 0:MEM], ACT.Exp, scale=XSCALE,
                                         bias=col[:, b, 1:2], accum_out=col[:, b, 2:3]).then_inc(*exped.up())
                    if b + 1 < SEQS:
                        copy_keys(b + 1)
                    if b:
                        copy_outputs(b - 1)
                    act.wait_ge(*ptf.at(b + 1))
                    if b >= 2:
                        act.wait_ge(*of.at(b - 1))
                    nc.scalar.copy(pT[:, b % 2, :, :], K.ps[5][:, 0:2 * 128].rearrange("p (m n) -> p m n", m=2)
                                   ).then_inc(*ptd.up())
                copy_outputs(SEQS - 1)

            @block.vector
            def _(dve):
                link = chain(dve, step)

                def copy_keys(b):
                    if b >= 2:
                        dve.wait_ge(*scf.at(b - 1))
                    for n in (1, 3):
                        dve.wait_ge(*ktf.at(4 * b + n + 1))
                        nc.vector.tensor_copy(kcT[:, b % 2, 4:8, n // 2 * 128:(n // 2 + 1) * 128],
                                              K.ps[n][:, :].rearrange("p (j n) -> p j n", j=4)).then_inc(*ktd.up())

                def copy_outputs(b):
                    dve.wait_ge(*otf.at(b + 1))
                    turned = K.ps[7][:, 0:256].rearrange("p (j h q) -> p h j q", j=2, h=XH)
                    nc.vector.tensor_copy(oT[:, :, SEQ + 8 * b:SEQ + 8 * b + 8].rearrange("p (h j) q -> p h j q", j=2),
                                          turned[:, :, :, 0:8]).then_inc(*od.up())

                copy_keys(0)
                for b in range(SEQS):
                    dve.wait_ge(*scf.at(b + 1))
                    link(nc.vector.reduce_max(col[:, b, 0:1], K.ps[4][:, 0:MEM], AX))
                    nc.vector.tensor_scalar(col[:, b, 1:2], col[:, b, 0:1], -XSCALE, None, ALU.mult
                                            ).then_inc(*maxed.up())
                    dve.wait_ge(*exped.at(b + 1))
                    link(nc.vector.reciprocal(col[:, b, 3:4], col[:, b, 2:3]))
                    nc.vector.tensor_scalar(p[:, b % 2, :], p[:, b % 2, :], col[:, b, 3:4], None, ALU.mult
                                            ).then_inc(*pd.up())
                    if b >= 2:
                        copy_outputs(b - 2)
                    if b + 1 < SEQS:
                        copy_keys(b + 1)
                copy_outputs(SEQS - 2)
                copy_outputs(SEQS - 1)



CAP = 64
PAIRS = EXPERTS // 2


def moe(K, layer):
    with contextlib.ExitStack() as st:
        R = {"slot": K.sb(st, "slot", [128, TILES, 2]), "rows": K.sb(st, "rows", [128, 4, TOK]),
             "over": K.sb(st, "over", [1, 1], I32)}
        with contextlib.ExitStack() as tmp:
            route(K, tmp, layer, R)
        with contextlib.ExitStack() as tmp:
            experts(K, tmp, layer, R)
        moe_norm(K, st, layer)
    if layer == 0:
        transpose_x(K)


def route(K, tmp, layer, R):
    nc, I = K.nc, K.ins
    T = TILES
    w = K.sb(tmp, "w", [128, KT, 36])
    bias = K.sb(tmp, "bias", [128, 36])
    lg = K.sb(tmp, "lg", [128, T, 36])
    a = K.sb(tmp, "a", [128, T, 4])
    e8, o1, o2 = (K.sb(tmp, n, [128, T, 8]) for n in ("e8", "o1", "o2"))
    og = K.sb(tmp, "og", [128, T, 4])
    m = K.sb(tmp, "m", [128, 8, T])
    prod = K.sb(tmp, "prod", [128, T, 32])
    sel = [K.sb(tmp, "sel", [128, T, 32]) for _ in range(3)]
    gates = K.sb(tmp, "gates", [128, T, 32])
    cols = K.sb(tmp, "cols", [128, T, 4])
    gT = K.sb(tmp, "gT", [EXPERTS, TOK])
    cT = K.sb(tmp, "cT", [4, TOK])
    shape = lambda n: [128, T, n]
    by_group = lambda x: x.rearrange("p t (g e) -> p t g e", g=GROUPS)
    with K.phase("loaded", "ab_full", "r_exp", "vector_step", "r_sub", "r_sel", "r_pos", "r_cols", "r_rows", "r_copied",
                 "stored", "r_back") as (
            block, loaded, full, exped, step, sub, seld, pos, colsd, rowsd, copied, out, back):
        @block.sync
        def _(sp):
            sp.dma_start(w[:, :, 0:4], I["moe_w_grp"][layer].rearrange("(k p) n -> p k n", p=128)
                         ).then_inc(*loaded.up(16))
            for g in range(GROUPS):
                sp.dma_start(w[:, :, 4 + 8 * g:12 + 8 * g], I["moe_w_exp"][layer, g].rearrange(
                    "(k p) n -> p k n", p=128)).then_inc(*loaded.up(16))
            sp.dma_start(bias[:, 0:4], row_broadcast(I["moe_b_grp"][layer])).then_inc(*loaded.up(16))
            sp.dma_start(bias[:, 4:36], row_broadcast(I["moe_b_exp"][layer].rearrange("g e -> (g e)"))
                         ).then_inc(*loaded.up(16))
            for n in MOE_SIGNALS:
                sp.sem_clear(K.sem(n).sem)
            sp.wait_ge(*copied.at(1))
            sp.dma_start(K.scratch["gates"], gT[:, :]).then_inc(*out.up(16))
            sp.dma_start(K.scratch["cols"], cT[:, :]).then_inc(*out.up(16))
            sp.wait_ge(*out.at(32))
            for i in range(4):
                sp.dma_start(R["rows"][:, i, :], row_broadcast(K.scratch["cols"][i])).then_inc(*back.up(16))
            sp.wait_ge(*back.at(64))

        @block.tensor
        def _(pe):
            pe.wait_ge(*loaded.at(16 * 7))
            for t in range(T):
                for k in range(KT):
                    last = nc.tensor.matmul(K.ps[0][0:ROWS[t], 36 * t:36 * t + 36], K.xT[:, k, cols_of(t)], w[:, k, :],
                                            start=(k == 0), stop=(k == KT - 1))
            last.then_inc(*full.up())
            pe.wait_ge(*seld.at(1))
            for t in range(T + 1):
                rows = ROWS[t] if t < T else 128
                for s in range(min(t + 1, T)):
                    r = slice(0, ROWS[s])
                    last = nc.tensor.matmul(K.ps[1][0:rows, 32 * t:32 * t + 32],
                                            K.const("upto_all" if s == t else "ones")[r, 0:rows], sel[2][r, s, :],
                                            start=(s == 0), stop=(s == min(t, T - 1)))
            last.then_inc(*pos.up())
            pe.wait_ge(*colsd.at(1))
            for t in range(T):
                r = ROWS[t]
                nc.tensor.transpose(K.ps[2][0:EXPERTS, cols_of(t)], gates[0:r, t, :], K.const("ident")[0:r, 0:r])
                last = nc.tensor.transpose(K.ps[3][0:4, cols_of(t)], cols[0:r, t, :], K.const("ident")[0:r, 0:r])
            last.then_inc(*rowsd.up())

        @block.scalar
        def _(act):
            act.wait_ge(*sub.at(1))
            nc.scalar.activation(a[:, :, :], a[:, :, :], ACT.Exp)
            nc.scalar.activation(m[:, 5, :], m[:, 4, :], ACT.Exp).then_inc(*exped.up())

        @block.vector
        def _(dve):
            link = chain(dve, step)
            tt = nc.vector.tensor_tensor

            def wide(col, n):
                return m[:, col, :].unsqueeze(2).broadcast_to(shape(n))

            def first(val, mx, eq, n):
                descend = K.const("descend")[:, 0:n].unsqueeze(1).broadcast_to(shape(n))
                link(nc.vector.reduce_max(m[:, mx, :], val, AX))
                link(tt(eq, val, wide(mx, n), ALU.is_equal))
                link(tt(eq, eq, descend, ALU.mult))
                link(nc.vector.reduce_max(m[:, 0, :], eq, AX))
                link(tt(eq, descend, wide(0, n), ALU.is_equal))

            link(nc.vector.memset(lg[:, :, :], 0.0))
            dve.wait_ge(*loaded.at(16 * 7))
            dve.wait_ge(*full.at(1))
            for t in range(T):
                r = ROWS[t]
                last = tt(lg[0:r, t, :], K.ps[0][0:r, 36 * t:36 * t + 36], bias[0:r, :], ALU.add)
            link(last)
            first(lg[:, :, 0:4], 1, og[:, :, :], 4)
            tt(a[:, :, :], lg[:, :, 0:4], wide(1, 4), ALU.subtract)
            link(tt(by_group(prod[:, :, :]), by_group(lg[:, :, 4:36]),
                    og[:, :, :].unsqueeze(3).broadcast_to([128, T, 4, 8]), ALU.mult))
            link(tt(prod[:, :, 0:16], prod[:, :, 0:16], prod[:, :, 16:32], ALU.add))
            link(tt(e8[:, :, :], prod[:, :, 0:8], prod[:, :, 8:16], ALU.add))
            first(e8[:, :, :], 2, o1[:, :, :], 8)
            link(nc.vector.scalar_tensor_tensor(e8[:, :, :], o1[:, :, :], -1e30, e8[:, :, :], ALU.mult, ALU.add))
            first(e8[:, :, :], 3, o2[:, :, :], 8)
            tt(m[:, 4, :], m[:, 3, :], m[:, 2, :], ALU.subtract).then_inc(*sub.up())
            for i, o in enumerate((o1, o2)):
                last = tt(by_group(sel[i][:, :, :]), og[:, :, :].unsqueeze(3).broadcast_to([128, T, 4, 8]),
                          o[:, :, :].unsqueeze(2).broadcast_to([128, T, 4, 8]), ALU.mult)
            link(last)
            tt(sel[2][:, :, :], sel[0][:, :, :], sel[1][:, :, :], ALU.add).then_inc(*seld.up())
            dve.wait_ge(*exped.at(1))
            link(nc.vector.tensor_reduce(m[:, 6, :], a[:, :, :], AX, ALU.add))
            link(nc.vector.scalar_tensor_tensor(m[:, 6, :], m[:, 5, :], 1.0, m[:, 6, :], ALU.add, ALU.mult))
            link(nc.vector.reciprocal(cols[:, :, 2], m[:, 6, :]))
            link(tt(cols[:, :, 3], cols[:, :, 2], m[:, 5, :], ALU.mult))
            for i in range(2):
                last = tt((gates, prod)[i][:, :, :], sel[i][:, :, :],
                          cols[:, :, 2 + i:3 + i].broadcast_to(shape(32)), ALU.mult)
            link(last)
            link(tt(gates[:, :, :], gates[:, :, :], prod[:, :, :], ALU.add))
            dve.wait_ge(*pos.at(1))
            link(nc.vector.memset(prod[:, :, :], 0.0))
            for t in range(T):
                r = ROWS[t]
                last = tt(prod[0:r, t, :], K.ps[1][0:r, 32 * t:32 * t + 32], K.const("slot_base")[0:r, :], ALU.add)
            nc.vector.reduce_max(m[:, 7, 0:1], K.ps[1][:, 96:128], AX)
            link(last)
            for i in range(2):
                last = tt(sel[i][:, :, :], sel[i][:, :, :], prod[:, :, :], ALU.mult)
            link(last)
            for i in range(2):
                last = nc.vector.tensor_reduce(cols[:, :, i], sel[i][:, :, :], AX, ALU.add)
            link(last)
            nc.vector.tensor_scalar(R["over"][:, :], m[0:1, 7, 0:1], CAP + 0.5, None, ALU.is_gt)
            nc.vector.tensor_copy(R["slot"][:, :, :], cols[:, :, 0:2]).then_inc(*colsd.up())
            dve.wait_ge(*rowsd.at(1))
            nc.vector.tensor_copy(gT[:, :], K.ps[2][0:EXPERTS, 0:TOK])
            nc.vector.tensor_copy(cT[:, :], K.ps[3][0:4, 0:TOK]).then_inc(*copied.up())


def total_bank(K, t, half):
    return K.ps[2 * t + half][:, :] if t < 2 else K.ps[4][64 * half:64 * half + 64, :]


MOE_SIGNALS = ["e_sel", "e_sel_step", "e_gather_full", "e_gather_act", "e_gather_dve", "e_silu", "e_hidden", "e_turned", "e_ht",
               "e_y_act", "e_y_dve", "e_spread", "e_spread_step", "e_sum", "a_zeroed", "a_gate_in0", "a_gate_in1",
               "a_h_full", "a_silu", "a_h_read", "a_hidden", "a_y_full"]


class Experts:
    pass


def experts(K, tmp, layer, R):
    I = K.ins
    E = Experts()
    E.R = R
    E.first = K.first[f"moe{layer}"]
    E.slot = [(E.first + j) % RING for j in range(RING)]
    E.base = [K.arrival[E.first + j] for j in range(RING)]
    E.raised = [16 * len(K.chunks[E.first + j]) for j in range(RING)]
    w1 = I["moe_w1"][layer].rearrange("g e d f -> (g e) d f")
    w3 = I["moe_w3"][layer].rearrange("g e d f -> (g e) d f")
    w2 = I["moe_w2"][layer].rearrange("g e f d -> (g e) f d")
    E.up = [K.ring[:, E.slot[2 * j], :].rearrange("p (k i f) -> p k i f", k=KT, i=2) for j in range(2)]
    E.down = [K.ring[:, E.slot[2 * j + 1], 0:2 * D].rearrange("p (k n) -> p k n", k=2) for j in range(2)]
    E.sel = K.sb(tmp, "sel", [128, TILES, 128])
    E.xg = K.sb(tmp, "xg", [128, KT, 128])
    E.hs = K.sb(tmp, "hs", [128, FF])
    E.h = K.sb(tmp, "h", [128, FF])
    E.hT = K.sb(tmp, "hT", [128, 2, 128])
    E.y = K.sb(tmp, "y", [128, D])
    E.spread = K.sb(tmp, "spread", [128, 3, TOK])
    E.index = K.sb(tmp, "index", [128, 1])
    E.zero = K.sb(tmp, "zero", [128, 512])
    E.gate = K.sb(tmp, "gate", [128, 2, TOK])
    E.hs_all = K.sb(tmp, "hs_all", [128, 2, TOK])
    E.hT_all = K.sb(tmp, "hT_all", [128, 2, TOK])
    with K.phase("up_read", "down_read", *MOE_SIGNALS) as (block, up_read, down_read, *own):
        E.sig = dict(zip(MOE_SIGNALS, (s.sem for s in own)))
        E.up_read, E.down_read = up_read, down_read

        @block.sync
        def _(sp):
            with sp.Fori(0, PAIRS - 1) as it:
                for j in range(2):
                    sp.wait_ge(up_read.sem, it * 2 + (up_read.base + j + 1))
                    for i, w in enumerate((w1, w3)):
                        sp.dma_start(E.up[j][:, :, i, :], w[it * 2 + (2 + j)].rearrange("(k p) f -> p k f", p=128)
                                     ).then_inc(K.arrived[E.slot[2 * j]], 16)
                for j in range(2):
                    sp.wait_ge(down_read.sem, it * 2 + (down_read.base + j + 1))
                    sp.dma_start(E.down[j], w2[it * 2 + (2 + j)].rearrange("(k p) n -> p k n", p=128)
                                 ).then_inc(K.arrived[E.slot[2 * j + 1]], 16)
            for j in range(2):
                sp.wait_ge(*up_read.at(EXPERTS - 1 + j))
                load_chunk(K, sp, E.first + 2 * EXPERTS + 2 * j)
            for j in range(2):
                sp.wait_ge(*down_read.at(EXPERTS - 1 + j))
                load_chunk(K, sp, E.first + 2 * EXPERTS + 2 * j + 1)

        @block.tensor
        def _(pe):
            over = pe.value_load(R["over"][0:1, 0:1], min_val=0, max_val=1)
            with pe.If(over < 1):
                few_tensor(K, E, pe)
            with pe.Else():
                all_tensor(K, E, pe)

        @block.scalar
        def _(act):
            over = act.value_load(R["over"][0:1, 0:1], min_val=0, max_val=1)
            with act.If(over < 1):
                few_scalar(K, E, act)
            with act.Else():
                all_scalar(K, E, act)

        @block.vector
        def _(dve):
            over = dve.value_load(R["over"][0:1, 0:1], min_val=0, max_val=1)
            with dve.If(over < 1):
                few_vector(K, E, dve)
            with dve.Else():
                all_vector(K, E, dve)

        up_read.sent += EXPERTS
        down_read.sent += EXPERTS


def up_arrived(K, E, pe, pair, j):
    pe.wait_ge(K.arrived[E.slot[2 * j]], pair * E.raised[2 * j] + E.base[2 * j])


def down_arrived(K, E, pe, pair, j):
    pe.wait_ge(K.arrived[E.slot[2 * j + 1]], pair * E.raised[2 * j + 1] + E.base[2 * j + 1])



def few_tensor(K, E, pe):
    nc, sig = K.nc, E.sig

    def gather(p):
        pe.wait_ge(sig["e_sel"], p + 1)
        for q in range(2):
            for j in range(4):
                f = 4 * q + j
                for t in range(TILES):
                    r = slice(0, ROWS[t])
                    last = nc.tensor.matmul(K.ps[6 + q][:, j * 128:(j + 1) * 128], K.x[r, t, f * 128:(f + 1) * 128],
                                            E.sel[r, t, :], start=(t == 0), stop=(t == TILES - 1))
            last.then_inc(sig["e_gather_full"], 1)

    def hidden(p):
        pe.wait_ge(sig["e_gather_act"], p + 1)
        pe.wait_ge(sig["e_gather_dve"], p + 1)
        for j in range(2):
            up_arrived(K, E, pe, p, j)
            for k in range(KT):
                last = nc.tensor.matmul(K.ps[5][CAP * j:CAP * (j + 1), :], E.xg[:, k, CAP * j:CAP * (j + 1)],
                                        E.up[j][:, k, :, :], start=(k == 0), stop=(k == KT - 1))
            last.then_inc(E.up_read.sem, 1)

    def turn(p):
        pe.wait_ge(sig["e_hidden"], p + 1)
        for f in range(2):
            last = nc.tensor.transpose(K.ps[5][:, f * 128:(f + 1) * 128], E.h[:, f * 128:(f + 1) * 128],
                                       K.const("ident"))
        last.then_inc(sig["e_turned"], 1)

    def add(p, start, stop):
        pe.wait_ge(sig["e_y_act"], p + 1)
        pe.wait_ge(sig["e_y_dve"], p + 1)
        pe.wait_ge(sig["e_spread"], p + 1)
        for t in range(TILES):
            for half in range(2):
                last = nc.tensor.matmul(total_bank(K, t, half), E.spread[:, 0, cols_of(t)],
                                        E.y[:, 512 * half:512 * half + 512], start=start, stop=stop,
                                        skip_group_check=True)
        last.then_inc(sig["e_sum"], 1)

    def output(p):
        pe.wait_ge(sig["e_ht"], p + 1)
        for j in range(2):
            down_arrived(K, E, pe, p, j)
            for half in range(2):
                for f in range(2):
                    last = nc.tensor.matmul(K.ps[6 + half][CAP * j:CAP * (j + 1), :], E.hT[:, f, CAP * j:CAP * (j + 1)],
                                            E.down[j][:, f, 512 * half:512 * half + 512],
                                            start=(f == 0), stop=(f == 1))
            last.then_inc(E.down_read.sem, 1)

    def copied(p):
        pe.wait_ge(sig["e_gather_act"], p + 1)
        pe.wait_ge(sig["e_gather_dve"], p + 1)

    def stored(p):
        pe.wait_ge(sig["e_y_act"], p + 1)
        pe.wait_ge(sig["e_y_dve"], p + 1)

    gather(0)
    hidden(0)
    gather(1)
    turn(0)
    copied(1)
    output(0)
    hidden(1)
    stored(0)
    gather(2)
    turn(1)
    add(0, True, False)
    copied(2)
    output(1)
    with pe.Fori(2, PAIRS - 1) as p:
        hidden(p)
        stored(p - 1)
        gather(p + 1)
        turn(p)
        add(p - 1, False, False)
        copied(p + 1)
        output(p)
    hidden(PAIRS - 1)
    turn(PAIRS - 1)
    add(PAIRS - 2, False, False)
    output(PAIRS - 1)
    add(PAIRS - 1, False, True)


def few_scalar(K, E, act):
    nc, sig = K.nc, E.sig

    def columns(p):
        act.wait_ge(sig["e_gather_full"], p * 2 + 1)
        nc.scalar.copy(E.xg[:, 0:4, :], K.ps[6][:, :].rearrange("p (f s) -> p f s", f=4)
                       ).then_inc(sig["e_gather_act"], 1)

    def silu(p):
        act.wait_ge(E.up_read.sem, p * 2 + (E.up_read.base + 2))
        nc.scalar.activation(E.hs[:, :], K.ps[5][:, 0:FF], ACT.Silu).then_inc(sig["e_silu"], 1)

    def turned(p):
        act.wait_ge(sig["e_turned"], p + 1)
        nc.scalar.copy(E.hT[:, :, :], K.ps[5][:, 0:FF].rearrange("p (f s) -> p f s", f=2)).then_inc(sig["e_ht"], 1)

    def rows(p):
        act.wait_ge(E.down_read.sem, p * 2 + (E.down_read.base + 2))
        nc.scalar.copy(E.y[:, 0:512], K.ps[6][:, :]).then_inc(sig["e_y_act"], 1)

    columns(0)
    silu(0)
    columns(1)
    turned(0)
    rows(0)
    with act.Fori(1, PAIRS - 1) as p:
        act.wait_ge(sig["e_hidden"], p)
        silu(p)
        columns(p + 1)
        turned(p)
        act.wait_ge(sig["e_sum"], p)
        rows(p)
    act.wait_ge(sig["e_hidden"], PAIRS - 1)
    silu(PAIRS - 1)
    turned(PAIRS - 1)
    act.wait_ge(sig["e_sum"], PAIRS - 1)
    rows(PAIRS - 1)


def few_vector(K, E, dve):
    nc, sig, R = K.nc, E.sig, E.R
    v = nc.vector

    def select(p):
        slots = K.const("slots")
        for t in range(TILES):
            r = slice(0, ROWS[t])
            last = v.tensor_scalar(E.sel[r, t, :], slots[r, :], R["slot"][r, t, 0:1], None, ALU.is_equal)
        last.then_inc(sig["e_sel_step"], 1)
        dve.wait_ge(sig["e_sel_step"], p * 2 + 1)
        for t in range(TILES):
            r = slice(0, ROWS[t])
            last = v.scalar_tensor_tensor(E.sel[r, t, :], slots[r, :], R["slot"][r, t, 1:2], E.sel[r, t, :],
                                          ALU.is_equal, ALU.add)
        last.then_inc(sig["e_sel"], 1)
        dve.wait_ge(sig["e_sel"], p + 1)
        v.tensor_scalar(R["slot"][:, :, :], R["slot"][:, :, :], -128.0, None, ALU.add).then_inc(sig["e_sel_step"], 1)
        dve.wait_ge(sig["e_sel_step"], p * 2 + 2)

    def columns(p):
        dve.wait_ge(sig["e_gather_full"], p * 2 + 2)
        v.tensor_copy(E.xg[:, 4:8, :], K.ps[7][:, :].rearrange("p (f s) -> p f s", f=4)
                      ).then_inc(sig["e_gather_dve"], 1)

    def product(p):
        dve.wait_ge(sig["e_silu"], p + 1)
        v.tensor_tensor(E.h[:, :], E.hs[:, :], K.ps[5][:, FF:2 * FF], ALU.mult).then_inc(sig["e_hidden"], 1)

    def spread(p, wait):
        for i in range(2):
            last = v.scalar_tensor_tensor(E.spread[:, 1 + i, :], R["rows"][:, i, :], E.index[:, 0:1],
                                          R["rows"][:, 2 + i, :], ALU.is_equal, ALU.mult)
        last.then_inc(sig["e_spread_step"], 1)
        dve.wait_ge(sig["e_spread_step"], p * 2 + 2)
        if wait:
            dve.wait_ge(sig["e_sum"], p)
        v.tensor_tensor(E.spread[:, 0, :], E.spread[:, 1, :], E.spread[:, 2, :], ALU.add).then_inc(sig["e_spread"], 1)
        v.tensor_scalar(E.index[:, :], E.index[:, :], 128.0, None, ALU.add).then_inc(sig["e_spread_step"], 1)
        dve.wait_ge(sig["e_spread_step"], p * 2 + 3)

    def rows(p):
        dve.wait_ge(E.down_read.sem, p * 2 + (E.down_read.base + 2))
        v.tensor_copy(E.y[:, 512:1024], K.ps[7][:, :]).then_inc(sig["e_y_dve"], 1)

    v.tensor_copy(E.index[:, :], K.const("row")).then_inc(sig["e_spread_step"], 1)
    dve.wait_ge(sig["e_spread_step"], 1)
    select(0)
    columns(0)
    select(1)
    product(0)
    columns(1)
    spread(0, False)
    rows(0)
    with dve.Fori(1, PAIRS - 1) as p:
        select(p + 1)
        product(p)
        columns(p + 1)
        spread(p, True)
        rows(p)
    product(PAIRS - 1)
    spread(PAIRS - 1, True)
    rows(PAIRS - 1)



def all_tensor(K, E, pe):
    nc, sig = K.nc, E.sig
    zero = E.zero
    pe.sem_inc(sig["a_y_full"], 1)
    pe.wait_ge(sig["a_zeroed"], 1)
    for t in range(TILES):
        for half in range(2):
            nc.tensor.matmul(total_bank(K, t, half), zero[:, 0:ROWS[t]], zero[:, :], start=True, stop=False,
                             skip_group_check=True)
    with pe.Fori(0, PAIRS) as it:
        for j in range(2):
            up_arrived(K, E, pe, it, j)
            for f in range(2):
                pe.wait_ge(sig["a_h_read"], it * 4 + (1 + 2 * j + f))
                for i in range(2):
                    for k in range(KT):
                        last = nc.tensor.matmul(K.ps[6 + i][:, 0:TOK], E.up[j][:, k, i, f * 128:(f + 1) * 128],
                                                K.xT[:, k, 0:TOK], start=(k == 0), stop=(k == KT - 1))
                last.then_inc(sig["a_h_full"], 1)
            pe.wait_ge(sig["a_h_full"], it * 4 + (2 * j + 2))
            pe.sem_inc(E.up_read.sem, 1)
            down_arrived(K, E, pe, it, j)
            pe.wait_ge(sig["a_hidden"], it * 4 + (1 + 2 * j + 2))
            for t in range(TILES):
                for half in range(2):
                    for f in range(2):
                        last = nc.tensor.matmul(total_bank(K, t, half), E.hT_all[:, f, cols_of(t)],
                                                E.down[j][:, f, 512 * half:512 * half + 512],
                                                start=False, stop=False, skip_group_check=True)
            last.then_inc(sig["a_y_full"], 1)
            pe.wait_ge(sig["a_y_full"], it * 2 + (1 + j + 1))
            pe.sem_inc(E.down_read.sem, 1)
    for t in range(TILES):
        for half in range(2):
            nc.tensor.matmul(total_bank(K, t, half), zero[:, 0:ROWS[t]], zero[:, :], start=False, stop=True,
                             skip_group_check=True)


def all_scalar(K, E, act):
    nc, sig = K.nc, E.sig
    with act.Fori(0, PAIRS) as it:
        for j in range(2):
            act.wait_ge(sig["a_hidden"], it * 4 + (1 + 2 * j))
            act.dma_start(E.gate[:, j, :], K.scratch["gates"][bass.ds(it * 2 + j, 1), :].broadcast_to([128, TOK])
                          ).then_inc(sig[f"a_gate_in{j}"], 16)
            for f in range(2):
                act.wait_ge(sig["a_h_full"], it * 4 + (2 * j + f + 1))
                nc.scalar.activation(E.hs_all[:, f, :], K.ps[6][:, 0:TOK], ACT.Silu).then_inc(sig["a_silu"], 1)


def all_vector(K, E, dve):
    nc, sig = K.nc, E.sig
    nc.vector.memset(E.zero[:, :], 0.0).then_inc(sig["a_zeroed"], 1)
    dve.sem_inc(sig["a_h_read"], 1)
    dve.sem_inc(sig["a_hidden"], 1)
    with dve.Fori(0, PAIRS) as it:
        for j in range(2):
            dve.wait_ge(sig[f"a_gate_in{j}"], it * 16 + 16)
            dve.wait_ge(sig["a_y_full"], it * 2 + (1 + j))
            for f in range(2):
                dve.wait_ge(sig["a_silu"], it * 4 + (2 * j + f + 1))
                nc.vector.tensor_tensor(E.hT_all[:, f, :], E.hs_all[:, f, :], K.ps[7][:, 0:TOK], ALU.mult
                                        ).then_inc(sig["a_h_read"], 1)
                dve.wait_ge(sig["a_h_read"], it * 4 + (1 + 2 * j + f + 1))
                nc.vector.tensor_tensor(E.hT_all[:, f, :], E.hT_all[:, f, :], E.gate[:, j, :], ALU.mult
                                        ).then_inc(sig["a_hidden"], 1)


def moe_norm(K, st, layer):
    nc, I = K.nc, K.ins
    with contextlib.ExitStack() as tmp:
        lnw, lnb = K.sb(tmp, "lnw", [128, D]), K.sb(tmp, "lnb", [128, D])
        stats, mv = K.sb(tmp, "stats", [128, 2, 6]), K.sb(tmp, "mv", [128, TILES, 4])
        late = K.sb(tmp, "late", [SAMPLE, 512])
        with K.phase("loaded", "ln_var", "ln_std", "vector_step", "late_copied") as (
                block, rows_in, var, std, step, copied):
            @block.sync
            def _(sp):
                sp.dma_start(lnw[:, :], row_broadcast(I["ln_w"][layer, 2])).then_inc(*rows_in.up(16))
                sp.dma_start(lnb[:, :], row_broadcast(I["ln_b"][layer, 2])).then_inc(*rows_in.up(16))

            @block.scalar
            def _(act):
                nc.scalar.copy(late[:, :], total_bank(K, 2, 1)).then_inc(*copied.up())
                for t in range(TILES):
                    act.wait_ge(*var.at(t + 1))
                    nc.scalar.activation(mv[0:ROWS[t], t, 2:3], mv[0:ROWS[t], t, 1:2], ACT.Sqrt).then_inc(*std.up())

            @block.vector
            def _(dve):
                link = chain(dve, step)
                for t in range(TILES):
                    if t == 2:
                        dve.wait_ge(*copied.at(1))
                    for g in range(2):
                        xs = K.x[0:ROWS[t], t, g * 512:(g + 1) * 512]
                        src = late[:, :] if t == 2 and g else total_bank(K, t, g)
                        last = nc.vector.scalar_tensor_tensor(xs, xs, ALPHA, src, ALU.mult, ALU.add)
                    link(last)
                    if t == 0:
                        dve.wait_ge(*rows_in.at(32))
                    norm_tile(K, dve, link, std, var, t, ROWS[t], stats, mv, lnw, lnb)



C_HEADS = 16


def rwkv_mixer(K):
    nc, I, O = K.nc, K.ins, K.outs
    rwkv_project(K)
    with contextlib.ExitStack() as st:
        yT = K.sb(st, "yT", [128, KT, TOK])
        H = K.sb(st, "H", [128, KT, 128])
        for t in range(TILES):
            with contextlib.ExitStack() as tt:
                rwkv_tile(K, tt, t, H, yT)
        add_and_norm_phase(K, K.first["c_out"], yT, 1, 0)


def rwkv_project(K):
    nc, I, O = K.nc, K.ins, K.outs
    tiles = [(AT[t], ROWS[t]) for t in range(TILES)]
    with contextlib.ExitStack() as st:
        shift = K.sb(st, "shift", [SEQS, D])
        cols = K.sb(st, "cols", [48, 128])
        shT = K.sb(st, "shT", [128, KT, SEQS])
        mu = K.sb(st, "mu", [128, 6, KT])
        xx = K.sb(st, "xx", [128, KT, TOK])
        mixes = K.sb(st, "mix", [128, 2, KT, TOK])
        outs = K.sb(st, "out", [128, 2, TILES, D])
        hT = K.sb(st, "hT", [128, TOK])
        l1 = {"w": K.sb(st, "w1", [128, KT, 64]), "a": K.sb(st, "a1", [128, KT, 64]),
              "g": K.sb(st, "g1", [128, KT, 128])}
        l2 = {"w": K.sb(st, "w2", [64, D]), "a": K.sb(st, "a2", [64, D]), "g": K.sb(st, "g2", [128, D])}
        row = {"w": K.sb(st, "w0", [128, D]), "a": K.sb(st, "a0", [128, D])}
        with K.phase("loaded", "stored") as (block, loaded, shifted):
            @block.sync
            def _(sp):
                sp.dma_start(shift[:, :], I["state_shift_c"][0]).then_inc(*loaded.up(16))
                sp.dma_start(cols[:, :], I["c_mu"][0].rearrange("i (k p) -> (i k) p", p=128)).then_inc(*loaded.up(16))
                for n in "wag":
                    sp.dma_start(l1[n][:, :, :], I[f"c_w_{n}1"][0].rearrange("(k p) n -> p k n", p=128)
                                 ).then_inc(*loaded.up(16))
                    sp.dma_start(l2[n][:, :], I[f"c_w_{n}2"][0]).then_inc(*loaded.up(16))
                sp.dma_start(row["w"][:, :], row_broadcast(I["c_w0"][0])).then_inc(*loaded.up(16))
                sp.dma_start(row["a"][:, :], row_broadcast(I["c_a0"][0])).then_inc(*loaded.up(16))
                sp.dma_start(O[7][0], K.x[127:128, 1, :]).then_inc(*shifted.up(16))
                for b in range(SEQS):
                    sp.dma_start(O[12][0, b:b + 1], K.x[8 * b + 7:8 * b + 8, 2, :]).then_inc(*shifted.up(16))
                sp.wait_ge(*loaded.at(160))
                sp.wait_ge(*shifted.at(16 * 9))
        transpose_phase(K, [([shift[:, (4 * q + j) * 128:(4 * q + j + 1) * 128] for j in range(4)],
                             shT[:, 4 * q:4 * q + 4, :]) for q in range(2)]
                        + [([cols[:, :]], mu[:, :, :].rearrange("p i k -> p (i k)").unsqueeze(1))])
        with K.phase("z_done") as (block, done):
            @block.vector
            def _(dve):
                x = K.xT
                nc.vector.tensor_tensor(xx[:, :, 1:SEQ], x[:, :, 0:SEQ - 1], x[:, :, 1:SEQ], ALU.subtract)
                nc.vector.tensor_scalar(xx[:, :, 0:1], x[:, :, 0:1], -1.0, None, ALU.mult)
                xs = x[:, :, SEQ:TOK].rearrange("p k (b s) -> p k b s", b=SEQS)
                ds = xx[:, :, SEQ:TOK].rearrange("p k (b s) -> p k b s", b=SEQS)
                for k in range(KT):
                    nc.vector.tensor_tensor(ds[:, k, :, 1:8], xs[:, k, :, 0:7], xs[:, k, :, 1:8], ALU.subtract)
                nc.vector.tensor_tensor(ds[:, :, :, 0], shT[:, :, :], xs[:, :, :, 0], ALU.subtract)

        order = ((0, "r"), (2, "k"), (3, "v"), (1, "w"), (4, "a"), (5, "g"))
        kept = [K.sem(f"mix_stored{j}") for j in range(2)]
        for sig in kept:
            sig.base = sig.sent

        def mixture(n):
            for k in range(KT):
                nc.vector.scalar_tensor_tensor(mixes[:, n % 2, k, :], xx[:, k, :], mu[:, order[n][0], k:k + 1],
                                               K.xT[:, k, 0:TOK], ALU.mult, ALU.add)

        def aside(n):
            if n + 1 == len(order):
                return None

            def work(pool, scaled):
                m = mixes[:, (n + 1) % 2, :, :]
                for k in range(KT):
                    last = nc.gpsimd.tensor_scalar(m[:, k, :], xx[:, k, :], mu[:, order[n + 1][0], k:k + 1], None,
                                                   ALU.mult)
                last.then_inc(*scaled.up())
                pool.wait_ge(*scaled.at(1))
                nc.gpsimd.tensor_tensor(m, m, K.xT[:, :, 0:TOK], ALU.add)

            return work

        def stores(n):
            return [(K.scratch[order[n][1]][cols_of(t), :], outs[0:ROWS[t], n % 2, t, :]) for t in range(TILES)]

        def before(sp, n):
            if n:
                sp.wait_ge(*kept[(n - 1) % 2].at(16 * TILES * ((n - 1) // 2 + 1)))

        with K.phase("z_done") as (block, done):
            @block.vector
            def _(dve):
                mixture(0)
        for n in range(3):
            token_major_phase(K, K.first["c_" + order[n][1]], 2, mixes[:, n % 2, :, :], tiles,
                              lambda g, t: outs[0:ROWS[t], n % 2, t, g * 512:(g + 1) * 512], stores=stores(n),
                              stored_later=kept[n % 2], aside=aside(n), last_wait=lambda sp: before(sp, n))
        for n, inner in ((3, ACT.Tanh), (4, ACT.Copy), (5, ACT.Sigmoid)):
            rwkv_low_rank(K, n, order[n][1], inner, mixes[:, n % 2, :, :], outs[:, n % 2, :, :], hT, l1, l2, row,
                          stores(n), kept[n % 2], aside(n), before)


def rwkv_low_rank(K, index, n, inner, mix, out, hT, l1, l2, row, stores, stored, aside, before):
    nc = K.nc
    m = 128 if n == "g" else 64
    with K.phase("l1_full", "l1_done", "l2_full", "l2_done", "l2_step", "aside_step") as (
            block, f1, d1, f2, d2, step, scaled):
        if aside:
            @block.gpsimd
            def _(pool):
                aside(pool, scaled)

        @block.tensor
        def _(pe):
            for k in range(KT):
                last = nc.tensor.matmul(K.ps[0][0:m, 0:TOK], l1[n][:, k, :], mix[:, k, :],
                                        start=(k == 0), stop=(k == KT - 1))
            last.then_inc(*f1.up())
            pe.wait_ge(*d1.at(1))
            for t in range(TILES):
                for g in range(2):
                    last = nc.tensor.matmul(K.ps[1 + 2 * t + g][0:ROWS[t], :], hT[0:m, cols_of(t)],
                                            l2[n][:, g * 512:(g + 1) * 512], start=True, stop=True)
                last.then_inc(*f2.up())

        @block.scalar
        def _(act):
            act.wait_ge(*f1.at(1))
            nc.scalar.activation(hT[0:m, :], K.ps[0][0:m, 0:TOK], inner).then_inc(*d1.up())
            for t in range(TILES):
                r = ROWS[t]
                if n == "g":
                    act.wait_ge(*f2.at(t + 1))
                    for g in range(2):
                        last = nc.scalar.copy(out[0:r, t, g * 512:(g + 1) * 512], K.ps[1 + 2 * t + g][0:r, :])
                    last.then_inc(*d2.up())
                else:
                    act.wait_ge(*step.at(t + 1))
                    nc.scalar.activation(out[0:r, t, :], out[0:r, t, :], ACT.Sigmoid).then_inc(*d2.up())

        if n != "g":
            @block.vector
            def _(dve):
                for t in range(TILES):
                    r = ROWS[t]
                    dve.wait_ge(*f2.at(t + 1))
                    for g in range(2):
                        c = slice(g * 512, (g + 1) * 512)
                        last = nc.vector.tensor_tensor(out[0:r, t, c], K.ps[1 + 2 * t + g][0:r, :],
                                                       row[n][0:r, c], ALU.add)
                    last.then_inc(*step.up())

        @block.sync
        def _(sp):
            sp.wait_ge(*d2.at(TILES))
            for dst, src in stores:
                sp.dma_start(dst, src).then_inc(*stored.up(16))
            before(sp, index)
            if n == "g":
                before(sp, index + 1)


def rwkv_tile(K, st, t, H, yT):
    nc, I, O = K.nc, K.ins, K.outs
    rows, kind = ROWS[t], tile_kind(t)
    r = slice(0, rows)
    names = ["r", "k", "v", "w", "a"]
    d = {n: K.sb(st, "in_" + n, [128, D]) for n in names}
    bonus = K.sb(st, "bonus", [128, C_HEADS])
    ec = K.sb(st, "ec", [128, KT, 8])
    y = K.sb(st, "y", [128, D])
    with contextlib.ExitStack() as outer:
        ktr = K.sb(outer, "ktr", [128, KT, 2, rows])
        bkn = K.sb(outer, "bkn", [128, KT, 2, rows])
        with contextlib.ExitStack() as tmp:
            rwkv_factors(K, tmp, t, d, bonus, ec, ktr, bkn)
        if t == 2:
            byst, S = rwkv_sample_states(K, outer, ktr)
        for half in range(2):
            with contextlib.ExitStack() as tmp:
                rwkv_half(K, tmp, t, half, d, ec, ktr, bkn, H, y, byst if t == 2 else None)
        if t == 2:
            rwkv_sample_update(K, outer, d, ec, S)
    if t == 1:
        rwkv_prompt_state(K, H)
    rwkv_output(K, t, d, bonus, y, yT)


def rwkv_factors(K, tmp, t, d, bonus, ec, ktr, bkn):
    nc, I = K.nc, K.ins
    rows, kind = ROWS[t], tile_kind(t)
    r = slice(0, rows)
    kt = K.sb(tmp, "kt", [128, D])
    t1 = K.sb(tmp, "t1", [128, D])
    t2 = K.sb(tmp, "t2", [128, D])
    vec = {n: K.sb(tmp, "vec_" + n, [128, D]) for n in ("k_k", "k_a", "r_k")}
    ss = K.sb(tmp, "ss", [128, 3, C_HEADS])
    y_neg, y_pos = K.sb(tmp, "neg", [128, D]), K.sb(tmp, "pos", [128, D])
    h3 = lambda a: a[r, :].rearrange("p (h n) -> p h n", h=C_HEADS)
    with K.phase("loaded", "f_lw", "sum_full", "f_kk", "scalar_step", "vector_step", "f_root") as (
            block, loaded, lw, summed, kkd, by_act, by_dve, rooted):
        @block.sync
        def _(sp):
            for n in d:
                sp.dma_start(d[n][r, :], K.scratch[n][cols_of(t), :]).then_inc(*loaded.up(16))
            for n, src in (("k_k", I["c_k_k"][0]), ("k_a", I["c_k_a"][0]),
                           ("r_k", I["c_r_k"][0].rearrange("h n -> (h n)"))):
                sp.dma_start(vec[n][:, :], row_broadcast(src)).then_inc(*loaded.up(16))

        @block.tensor
        def _(pe):
            pe.wait_ge(*lw.at(1))
            for g in range(2):
                nc.tensor.matmul(K.ps[g][r, :], K.const("upto_" + kind)[r, 0:rows], d["w"][r, g * 512:(g + 1) * 512],
                                 start=True, stop=True)
            for f in range(KT):
                last = nc.tensor.matmul(K.ps[2][:, 8 * f:8 * f + 8], d["w"][r, f * 128:(f + 1) * 128],
                                        K.const("of_chunk_" + kind)[r, :], start=True, stop=True)
            last.then_inc(*summed.up())

        @block.scalar
        def _(act):
            act.wait_ge(*rooted.at(1))
            nc.scalar.activation(ss[r, 1, :], ss[r, 0, :], ACT.Sqrt, bias=K.eps6[r, 0:1]).then_inc(*by_act.up())
            act.wait_ge(*summed.at(1))
            nc.scalar.activation(ec[:, :, :], K.ps[2][:, 0:64].rearrange("p (f c) -> p f c", f=KT), ACT.Exp
                                 ).then_inc(*by_act.up())
            for g in range(2):
                c = slice(g * 512, (g + 1) * 512)
                nc.scalar.activation(y_neg[r, c], K.ps[g][r, :], ACT.Exp, scale=-1.0)
                last = nc.scalar.activation(y_pos[r, c], K.ps[g][r, :], ACT.Exp)
            last.then_inc(*by_act.up())
            act.wait_ge(*kkd.at(1))
            nc.scalar.activation(d["w"][r, :], d["w"][r, :], ACT.Exp).then_inc(*by_act.up())

        @block.vector
        def _(dve):
            link = chain(dve, by_dve)
            dve.wait_ge(*loaded.at(128))
            nc.vector.tensor_scalar(d["w"][r, :], d["w"][r, :], -float(np.exp(-0.5)), None, ALU.mult
                                    ).then_inc(*lw.up())
            link(nc.vector.tensor_tensor(kt[r, :], d["k"][r, :], vec["k_k"][r, :], ALU.mult))
            link(nc.vector.tensor_tensor(t1[r, :], kt[r, :], kt[r, :], ALU.mult))
            nc.vector.tensor_reduce(ss[r, 0, :], h3(t1), AX, ALU.add).then_inc(*rooted.up())
            nc.vector.scalar_tensor_tensor(t2[r, :], d["a"][r, :], -1.0, vec["k_a"][r, :], ALU.add, ALU.mult)
            dve.wait_ge(*by_act.at(1))
            link(nc.vector.reciprocal(ss[r, 2, :], ss[r, 1, :]))
            link(nc.vector.scalar_tensor_tensor(d["k"][r, :], t2[r, :], 1.0, d["k"][r, :], ALU.add, ALU.mult))
            link(nc.vector.tensor_tensor(h3(kt), h3(kt), ss[r, 2, :].unsqueeze(2).broadcast_to([rows, C_HEADS, 64]),
                                         ALU.mult))
            link(nc.vector.tensor_tensor(t1[r, :], d["r"][r, :], d["k"][r, :], ALU.mult))
            link(nc.vector.tensor_tensor(t1[r, :], t1[r, :], vec["r_k"][r, :], ALU.mult))
            nc.vector.tensor_reduce(bonus[r, :], h3(t1), AX, ALU.add)
            link(nc.vector.scalar_tensor_tensor(d["a"][r, :], d["a"][r, :], -1.0, kt[r, :], ALU.mult, ALU.mult))
            dve.wait_ge(*by_act.at(3))
            for g in range(2):
                c = slice(g * 512, (g + 1) * 512)
                last = nc.vector.scalar_tensor_tensor(d["w"][r, c], d["w"][r, c], -1.0, K.ps[g][r, :],
                                                      ALU.mult, ALU.add)
            last.then_inc(*kkd.up())
            nc.vector.tensor_tensor(d["a"][r, :], d["a"][r, :], y_neg[r, :], ALU.mult)
            nc.vector.tensor_tensor(d["k"][r, :], d["k"][r, :], y_neg[r, :], ALU.mult)
            nc.vector.tensor_tensor(d["r"][r, :], d["r"][r, :], y_pos[r, :], ALU.mult)
            dve.wait_ge(*by_act.at(4))
            nc.vector.tensor_tensor(kt[r, :], kt[r, :], d["w"][r, :], ALU.mult)
    groups = []
    for q in range(2):
        for src, dst, i in ((kt, ktr, 0), (d["r"], ktr, 1), (d["a"], bkn, 0), (d["k"], bkn, 1)):
            groups.append(([src[r, (4 * q + j) * 128:(4 * q + j + 1) * 128] for j in range(4)],
                           dst[:, 4 * q:4 * q + 4, i, :]))
    transpose_phase(K, groups)


def rwkv_half(K, tmp, t, half, d, ec, ktr, bkn, H, y, byst):
    nc = K.nc
    rows, kind = ROWS[t], tile_kind(t)
    r = slice(0, rows)
    mats = {n: K.sb(tmp, "m_" + n, [128, 2, 4, rows]) for n in ("low", "n", "rb", "rk", "T", "R")}
    with contextlib.ExitStack() as t2:
        work = (K.sb(t2, "c", [128, 2, 4, rows]), K.sb(t2, "y", [128, 2, 4, rows]))
        with K.phase("int_full", "int_done") as (block, full, done):
            @block.tensor
            def _(pe):
                for i in range(2):
                    if i:
                        pe.wait_ge(*done.at(4))
                    for h in range(4):
                        f = 4 * half + 2 * i + h // 2
                        k = slice(64 * (h % 2), 64 * (h % 2) + 64)
                        c = slice(h * rows, (h + 1) * rows)
                        kt, rt, bn, kn = ktr[k, f, 0, :], ktr[k, f, 1, :], bkn[k, f, 0, :], bkn[k, f, 1, :]
                        nc.tensor.matmul(K.ps[h % 2 * 4 + 0][r, h // 2 * rows:(h // 2 + 1) * rows], kt, bn, start=True, stop=True)
                        nc.tensor.matmul(K.ps[h % 2 * 4 + 1][r, h // 2 * rows:(h // 2 + 1) * rows], kn, kt, start=True, stop=True)
                        nc.tensor.matmul(K.ps[h % 2 * 4 + 2][r, h // 2 * rows:(h // 2 + 1) * rows], bn, rt, start=True, stop=True)
                        last = nc.tensor.matmul(K.ps[h % 2 * 4 + 3][r, h // 2 * rows:(h // 2 + 1) * rows], kn, rt, start=True, stop=True)
                    last.then_inc(*full.up())

            @block.vector
            def _(dve):
                for i in range(2):
                    dve.wait_ge(*full.at(i + 1))
                    for b, (n, mask) in enumerate((("low", "below_"), ("n", "above_"), ("rb", "upto_"),
                                                   ("rk", "upto_"))):
                        m = K.const(mask + kind)[r, 0:rows].unsqueeze(1).broadcast_to([rows, 2, rows])
                        for e in range(2):
                            src = K.ps[4 * e + b][r, 0:2 * rows].rearrange("p (h n) -> p h n", h=2)
                            dst = mats[n][r, i, e::2, 0:rows]
                            if b == 0:
                                last = nc.vector.scalar_tensor_tensor(dst, src, -1.0, m, ALU.mult, ALU.mult)
                            else:
                                last = nc.vector.tensor_tensor(dst, src, m, ALU.mult)
                        last.then_inc(*done.up())
        units = [(i, rows, LEVELS if t < 2 else [2, 4]) for i in range(2)]
        first_level(K, mats["low"], mats["T"], mats["R"], units)
        invert_phase(K, mats["low"], mats["T"], mats["R"], work, units, LEVELS)
    for chunk in range(2 if t < 2 else 1):
        rwkv_chunk(K, tmp, t, half, chunk, d, ec, ktr, mats, H, y, byst)


def rwkv_chunk(K, tmp, t, half, chunk, d, ec, ktr, mats, H, y, byst):
    nc = K.nc
    first = t == 0 and chunk == 0
    o = 64 * chunk
    sl = slice(o, o + 64)
    fs = slice(4 * half, 4 * half + 4)
    hs = slice(512 * half, 512 * half + 512)
    with contextlib.ExitStack() as t2:
        u = K.sb(t2, "u", [128, 512])
        s = K.s_all if t == 2 else K.sb(t2, "s", [128, D])
        change = K.sb(t2, "change", [128, 4, 128])
        with K.phase("u_full", "u_done", "s_full", "s_done", "y_full", "h_full", "vector_step", "h_done") as (
                block, uf, ud, sf, sd, yf, hf, step, hdone):
            def from_state(bank, p, i):
                f = 4 * half + p
                out = bank[sl, p * 128:(p + 1) * 128]
                if byst is not None:
                    nc.tensor.matmul(out, byst[:, f, i, :], K.const("ident"), start=True, stop=False,
                                     skip_group_check=True)
                elif not first:
                    nc.tensor.matmul(out, ktr[:, f, i, sl], H[:, f, :], start=True, stop=False,
                                     skip_group_check=True)

            def head(h):
                return mats_at(h), slice(512 * half + 64 * h, 512 * half + 64 * h + 64)

            def mats_at(h):
                return h // 4, h % 4

            @block.tensor
            def _(pe):
                for p in range(4):
                    from_state(K.ps[0], p, 0)
                    for h in (2 * p, 2 * p + 1):
                        (i, j), c = head(h)
                        last = nc.tensor.matmul(K.ps[0][sl, h * 64:h * 64 + 64], mats["n"][sl, i, j, sl],
                                                d["v"][sl, c], start=first, stop=True, skip_group_check=True)
                last.then_inc(*uf.up())
                pe.wait_ge(*ud.at(1))
                for h in range(8):
                    (i, j), c = head(h)
                    last = nc.tensor.matmul(K.ps[1][sl, h * 64:h * 64 + 64], mats["R"][sl, i, j, sl],
                                            u[sl, h * 64:h * 64 + 64], start=True, stop=True)
                last.then_inc(*sf.up())
                pe.wait_ge(*sd.at(1))
                if t < 2:
                    for p in range(4):
                        c = slice(512 * half + p * 128, 512 * half + p * 128 + 128)
                        nc.tensor.matmul(K.ps[3][:, p * 128:(p + 1) * 128], d["a"][sl, c], s[sl, c],
                                         start=True, stop=False)
                        last = nc.tensor.matmul(K.ps[3][:, p * 128:(p + 1) * 128], d["k"][sl, c], d["v"][sl, c],
                                                start=False, stop=True)
                    last.then_inc(*hf.up())
                for p in range(4):
                    from_state(K.ps[2], p, 1)
                    for h in (2 * p, 2 * p + 1):
                        (i, j), c = head(h)
                        nc.tensor.matmul(K.ps[2][sl, h * 64:h * 64 + 64], mats["rb"][sl, i, j, sl], s[sl, c],
                                         start=first, stop=False, skip_group_check=True)
                        last = nc.tensor.matmul(K.ps[2][sl, h * 64:h * 64 + 64], mats["rk"][sl, i, j, sl],
                                                d["v"][sl, c], start=False, stop=True, skip_group_check=True)
                last.then_inc(*yf.up())

            @block.scalar
            def _(act):
                act.wait_ge(*uf.at(1))
                nc.scalar.copy(u[sl, :], K.ps[0][sl, :]).then_inc(*ud.up())
                act.wait_ge(*sf.at(1))
                nc.scalar.copy(s[sl, hs], K.ps[1][sl, :]).then_inc(*sd.up())
                act.wait_ge(*yf.at(1))
                nc.scalar.copy(y[sl, hs], K.ps[2][sl, :])

            if t < 2:
                @block.vector
                def _(dve):
                    link = chain(dve, step)
                    dve.wait_ge(*hf.at(1))
                    pair = K.const("pair").unsqueeze(1).broadcast_to([128, 4, 128])
                    link(nc.vector.tensor_tensor(change[:, :, :], K.ps[3][:, :].rearrange("p (f n) -> p f n", f=4),
                                                 pair, ALU.mult))
                    if not first:
                        link(nc.vector.tensor_tensor(change[:, :, :], change[:, :, :], H[:, fs, :], ALU.add))
                    dve.wait_ge(*yf.at(1))
                    nc.vector.tensor_tensor(H[:, fs, :], change[:, :, :],
                                            ec[:, fs, chunk:chunk + 1].broadcast_to([128, 4, 128]), ALU.mult)


def load_states(K, sp, buf, b, sig):
    for e in range(2):
        src = K.ins["state_wkv"][0, b].rearrange("(f e) v k -> e v f k", e=2)[e]
        sp.dma_start(buf[64 * e:64 * e + 64, :, 64 * e:64 * e + 64], src).then_inc(*sig.up(16))


def rwkv_sample_states(K, outer, ktr):
    nc = K.nc
    byst = K.sb(outer, "byst", [128, KT, 2, SAMPLE])
    K.s_all = K.sb(outer, "s_all", [128, D])
    S = K.sb(outer, "S", [128, SEQS, KT, 128])
    with contextlib.ExitStack() as tmp:
        HT = K.sb(tmp, "HT", [128, 2, KT, 128])
        with K.phase("zero_low", "zero_high", "st_full", "st_act", "st_dve", "by_full", "by_done",
                     *(f"state_in{i}" for i in range(2))) as (
                block, zlow, zhigh, full, by_act, by_dve, byf, byd, *arrived):
            @block.sync
            def _(sp):
                for b in range(SEQS):
                    if b >= 2:
                        sp.wait_ge(*arrived[b % 2].at(32 * (b // 2)))
                    load_states(K, sp, S[:, b, :, :], b, arrived[b % 2])

            @block.gpsimd
            def _(pool):
                nc.gpsimd.memset(S[0:64, :, :, 64:128], 0.0).then_inc(*zlow.up())

            @block.tensor
            def _(pe):
                pe.wait_ge(*zlow.at(1))
                pe.wait_ge(*zhigh.at(1))

                def turn(b):
                    pe.wait_ge(*arrived[b % 2].at(32 * (b // 2 + 1)))
                    if b >= 2:
                        pe.wait_ge(*by_act.at(b - 1))
                        pe.wait_ge(*by_dve.at(b - 1))
                    for q in range(2):
                        for j in range(4):
                            last = nc.tensor.transpose(K.ps[2 * (b % 2) + q][:, j * 128:(j + 1) * 128],
                                                       S[:, b, 4 * q + j, :], K.const("ident"))
                        last.then_inc(*full.up())

                turn(0)
                for b in range(SEQS):
                    if b + 1 < SEQS:
                        turn(b + 1)
                    pe.wait_ge(*by_act.at(b + 1))
                    pe.wait_ge(*by_dve.at(b + 1))
                    if b >= 2:
                        pe.wait_ge(*byd.at(b - 1))
                    for f in range(KT):
                        last = nc.tensor.matmul(K.ps[4 + b % 2][:, 16 * f:16 * f + 16], HT[:, b % 2, f, :],
                                                ktr[:, f, :, 8 * b:8 * b + 8], start=True, stop=True)
                    last.then_inc(*byf.up())

            @block.scalar
            def _(act):
                for b in range(SEQS):
                    act.wait_ge(*full.at(2 * b + 1))
                    if b >= 2:
                        act.wait_ge(*byf.at(b - 1))
                    nc.scalar.copy(HT[:, b % 2, 0:4, :], K.ps[2 * (b % 2)][:, :].rearrange("p (f n) -> p f n", f=4)
                                   ).then_inc(*by_act.up())

            @block.vector
            def _(dve):
                def copy_products(b):
                    dve.wait_ge(*byf.at(b + 1))
                    nc.vector.tensor_copy(byst[:, :, :, 8 * b:8 * b + 8],
                                          K.ps[4 + b % 2][:, 0:128].rearrange("p (f i s) -> p f i s", f=KT, i=2)
                                          ).then_inc(*byd.up())

                nc.vector.memset(S[64:128, :, :, 0:64], 0.0).then_inc(*zhigh.up())
                for b in range(SEQS):
                    dve.wait_ge(*full.at(2 * b + 2))
                    if b >= 2:
                        dve.wait_ge(*byf.at(b - 1))
                    nc.vector.tensor_copy(HT[:, b % 2, 4:8, :],
                                          K.ps[2 * (b % 2) + 1][:, :].rearrange("p (f n) -> p f n", f=4)
                                          ).then_inc(*by_dve.up())
                    if b:
                        copy_products(b - 1)
                copy_products(SEQS - 1)
    return byst, S


def rwkv_sample_update(K, outer, d, ec, S):
    nc, I, O = K.nc, K.ins, K.outs
    with contextlib.ExitStack() as tmp:
        cut = K.sb(tmp, "cut", [SAMPLE, 2, 2, D])
        with K.phase("cut_done", "ch_full", "ch_done", "stored", "vector_step") as (block, cd, chf, chd, stored, step):
            @block.sync
            def _(sp):
                for b in range(SEQS):
                    sp.wait_ge(*chd.at(b + 1))
                    for e in range(2):
                        dst = O[13][0, b].rearrange("(f e) v k -> e v f k", e=2)[e]
                        sp.dma_start(dst, S[64 * e:64 * e + 64, b, :, 64 * e:64 * e + 64]).then_inc(*stored.up(16))
                sp.wait_ge(*stored.at(32 * SEQS))

            @block.scalar
            def _(act):
                for b in range(SEQS):
                    if b >= 2:
                        act.wait_ge(*chf.at(b - 1))
                    m = K.const("of_chunk_s")[0:SAMPLE, b:b + 1]
                    nc.scalar.activation(cut[:, b % 2, 0, :], K.s_all[0:SAMPLE, :], ACT.Copy, scale=m)
                    nc.scalar.activation(cut[:, b % 2, 1, :], d["v"][0:SAMPLE, :], ACT.Copy, scale=m
                                         ).then_inc(*cd.up())

            @block.tensor
            def _(pe):
                r = slice(0, SAMPLE)
                for b in range(SEQS):
                    if b >= 2:
                        pe.wait_ge(*chd.at(b - 1))
                    o = 4 * (b % 2)
                    for f in range(KT):
                        q, j = f // 4, f % 4
                        nc.tensor.matmul(K.ps[o + q][:, j * 128:(j + 1) * 128],
                                         ec[:, f, b:b + 1].broadcast_to([128, 128]), K.const("ident"),
                                         start=True, stop=True)
                    pe.wait_ge(*cd.at(b + 1))
                    for f in range(KT):
                        q, j = f // 4, f % 4
                        c = slice(f * 128, (f + 1) * 128)
                        out = K.ps[o + 2 + q][:, j * 128:(j + 1) * 128]
                        nc.tensor.matmul(out, cut[:, b % 2, 0, c], d["a"][r, c], start=True, stop=False)
                        last = nc.tensor.matmul(out, cut[:, b % 2, 1, c], d["k"][r, c], start=False, stop=True)
                    last.then_inc(*chf.up())

            @block.vector
            def _(dve):
                link = chain(dve, step)
                for b in range(SEQS):
                    dve.wait_ge(*chf.at(b + 1))
                    for op, i in ((ALU.add, 2), (ALU.mult, 0)):
                        for q in range(2):
                            h = S[:, b, 4 * q:4 * q + 4, :]
                            last = nc.vector.tensor_tensor(
                                h, h, K.ps[4 * (b % 2) + i + q][:, :].rearrange("p (f n) -> p f n", f=4), op)
                        if i:
                            link(last)
                    last.then_inc(*chd.up())


def rwkv_prompt_state(K, H):
    nc, O = K.nc, K.outs
    with contextlib.ExitStack() as tmp:
        S = K.sb(tmp, "S", [128, KT, 128])
        transpose_phase(K, [([H[:, 4 * q + j, :] for j in range(4)], S[:, 4 * q:4 * q + 4, :]) for q in range(2)])
        with K.phase("su_out0") as (block, out):
            @block.sync
            def _(sp):
                for e in range(2):
                    dst = O[8][0, 0].rearrange("(f e) v k -> e v f k", e=2)[e]
                    sp.dma_start(dst, S[64 * e:64 * e + 64, :, 64 * e:64 * e + 64]).then_inc(*out.up(16))
                sp.wait_ge(*out.at(32))


def rwkv_output(K, t, d, bonus, y, yT):
    nc, I = K.nc, K.ins
    rows = ROWS[t]
    r = slice(0, rows)
    h3 = lambda a: a[r, :].rearrange("p (h n) -> p h n", h=C_HEADS)
    bc = lambda a: a.unsqueeze(2).broadcast_to([rows, C_HEADS, 64])
    with contextlib.ExitStack() as tmp:
        g, w, b, sq = (K.sb(tmp, n, [128, D]) for n in ("g", "lw", "lb", "sq"))
        s = K.sb(tmp, "s", [128, 3, C_HEADS])
        with K.phase("loaded", "ln_var", "ln_std", "vector_step") as (block, loaded, var, std, step):
            @block.sync
            def _(sp):
                sp.dma_start(g[r, :], K.scratch["g"][cols_of(t), :]).then_inc(*loaded.up(16))
                sp.dma_start(w[:, :], row_broadcast(I["c_ln_w"][0])).then_inc(*loaded.up(16))
                sp.dma_start(b[:, :], row_broadcast(I["c_ln_b"][0])).then_inc(*loaded.up(16))

            @block.scalar
            def _(act):
                act.wait_ge(*var.at(1))
                nc.scalar.activation(s[r, 1, :], s[r, 1, :], ACT.Sqrt, scale=1.0 / 64, bias=K.epsg[r, 0:1]
                                     ).then_inc(*std.up())

            @block.vector
            def _(dve):
                link = chain(dve, step)
                link(nc.vector.tensor_reduce(s[r, 0, :], h3(y), AX, ALU.add))
                link(nc.vector.tensor_scalar(s[r, 0, :], s[r, 0, :], 1.0 / 64, None, ALU.mult))
                link(nc.vector.tensor_tensor(h3(y), h3(y), bc(s[r, 0, :]), ALU.subtract))
                link(nc.vector.tensor_tensor(sq[r, :], y[r, :], y[r, :], ALU.mult))
                nc.vector.tensor_reduce(s[r, 1, :], h3(sq), AX, ALU.add).then_inc(*var.up())
                dve.wait_ge(*std.at(1))
                link(nc.vector.reciprocal(s[r, 2, :], s[r, 1, :]))
                link(nc.vector.tensor_tensor(h3(y), h3(y), bc(s[r, 2, :]), ALU.mult))
                dve.wait_ge(*loaded.at(48))
                link(nc.vector.tensor_tensor(y[r, :], y[r, :], w[r, :], ALU.mult))
                link(nc.vector.tensor_tensor(y[r, :], y[r, :], b[r, :], ALU.add))
                link(nc.vector.tensor_tensor(h3(sq), h3(d["v"]), bc(bonus[r, :]), ALU.mult))
                link(nc.vector.tensor_tensor(y[r, :], y[r, :], sq[r, :], ALU.add))
                link(nc.vector.tensor_tensor(y[r, :], y[r, :], g[r, :], ALU.mult))
        transpose_phase(K, [([y[r, (4 * q + j) * 128:(4 * q + j + 1) * 128] for j in range(4)],
                             yT[:, 4 * q:4 * q + 4, cols_of(t)]) for q in range(2)])



INPUTS = ["x_prompt", "x_sample", "mem_prompt", "cache_mem_k", "cache_mem_v", "state_conv_a", "state_delta",
          "state_ret", "state_shift_c", "state_wkv", "ab_w_in", "ab_conv_w", "ab_a_log", "ab_dt_bias", "ab_norm_w",
          "ab_w_out", "c_mu", "c_w_r", "c_w_k", "c_w_v", "c_w0", "c_w_w1", "c_w_w2", "c_a0", "c_w_a1", "c_w_a2",
          "c_w_g1", "c_w_g2", "c_k_k", "c_k_a", "c_r_k", "c_ln_w", "c_ln_b", "c_w_out", "x_w_q", "x_w_k", "x_w_v",
          "x_w_o", "moe_w_grp", "moe_b_grp", "moe_w_exp", "moe_b_exp", "moe_w1", "moe_w3", "moe_w2", "ln_w", "ln_b"]
OUTPUTS = [(1, 256, 1024), (8, 8, 1024), (2, 1, 256, 4, 256), (2, 1, 256, 4, 256), (1, 1, 3, 1536),
           (1, 1, 4, 128, 128), (1, 1, 4, 128, 128), (1, 1, 1024), (1, 1, 16, 64, 64), (1, 8, 3, 1536),
           (1, 8, 4, 128, 128), (1, 8, 4, 128, 128), (1, 8, 1024), (1, 8, 16, 64, 64)]


def inference_step(nc, ins, outs, at, probe=None):
    stack = contextlib.ExitStack()
    with stack:
        K = Kernel(nc, ins, outs, at, stack)
        K.scratch = {n: nc.dram_tensor("scratch_" + n, (TOK, D), F32, kind="Internal").ap()
                     for n in ("gate", "r", "k", "v", "w", "a", "g")}
        K.scratch["gates"] = nc.dram_tensor("scratch_gates", (EXPERTS, TOK), F32, kind="Internal").ap()
        K.scratch["cols"] = nc.dram_tensor("scratch_cols", (4, TOK), F32, kind="Internal").ap()
        K.cst = K.sb(stack, "cst", [128, ins["constants"].shape[1]])
        K.x = K.sb(stack, "x", [128, TILES, D])
        K.xT = K.sb(stack, "xT", [128, KT, TOK])
        K.ring = K.sb(stack, "ring", [128, RING, SLOT])
        K.eps6, K.eps5, K.epsg = (K.sb(stack, "eps", [128, 1]) for _ in range(3))
        K.ps = [stack.enter_context(nc.psum_tensor(f"bank{b}", [128, 512], F32)) for b in range(8)]
        K.arrived = [stack.enter_context(nc.semaphore(f"weights_arrived{b}")) for b in range(RING)]
        K.chunks, K.first = weight_chunks(K)
        total = [0] * RING
        K.arrival = []
        for g, chunk in enumerate(K.chunks):
            total[g % RING] += 16 * len(chunk)
            K.arrival.append(total[g % RING])
        with K.phase("loaded") as (block, loaded):
            @block.sync
            def _(sp):
                sp.dma_start(K.cst[:, :], ins["constants"]).then_inc(*loaded.up(16))
                for t in range(2):
                    sp.dma_start(K.x[:, t, :], ins["x_prompt"][0, t * 128:(t + 1) * 128, :]).then_inc(*loaded.up(16))
                sp.dma_start(K.x[0:SAMPLE, 2, :], ins["x_sample"].rearrange("b s d -> (b s) d")
                             ).then_inc(*loaded.up(16))
                for g in range(RING):
                    load_chunk(K, sp, g)
                sp.wait_ge(*loaded.at(64))

            @block.vector
            def _(dve):
                nc.vector.memset(K.eps6[:, :], 1e-6)
                nc.vector.memset(K.eps5[:, :], LN_EPS)
                nc.vector.memset(K.epsg[:, :], GN_EPS)
        transpose_x(K)
        ab_mixer(K)
        if probe == "ab":
            return finish(K)
        cross_attention(K, 0)
        if probe == "x0":
            return finish(K)
        moe(K, 0)
        if probe == "moe0":
            return finish(K)
        rwkv_mixer(K)
        if probe == "c":
            return finish(K)
        cross_attention(K, 1)
        moe(K, 1)
        finish(K)


def finish(K):
    with K.phase("stored") as (block, out):
        @block.sync
        def _(sp):
            for t in range(2):
                sp.dma_start(K.outs[0][0, t * 128:(t + 1) * 128, :], K.x[:, t, :]).then_inc(*out.up(16))
            sp.dma_start(K.outs[1].rearrange("b s d -> (b s) d"), K.x[0:SAMPLE, 2, :]).then_inc(*out.up(16))
            sp.wait_ge(*out.at(48))


def kernel(**inputs):
    import concourse.bacc as bacc
    from concourse.bass_utils import run_bass_kernel_spmd

    nc = bacc.Bacc("TRN2", target_bir_lowering=False, num_devices=1)
    table, at = constants()
    arrays = {"in_" + n: np.ascontiguousarray(inputs[n]) for n in INPUTS}
    arrays["in_constants"] = table
    ins = {n[3:]: nc.dram_tensor(n, a.shape, F32, kind="ExternalInput").ap() for n, a in arrays.items()}
    outs = [nc.dram_tensor(f"out_{i}", s, F32, kind="ExternalOutput").ap() for i, s in enumerate(OUTPUTS)]
    inference_step(nc, ins, outs, at)
    r = run_bass_kernel_spmd(nc, [arrays], core_ids=[0])
    return tuple(r.results[0][f"out_{i}"] for i in range(len(OUTPUTS)))
```

```python
import contextlib

import numpy as np

import concourse.bass as bass
from concourse import mybir

F32 = mybir.dt.float32
I32 = mybir.dt.int32
ALU = mybir.AluOpType
ACT = mybir.ActivationFunctionType
AX = mybir.AxisListType.X

D = 1024
KT = D // 128
SEQ, SEQS, STEPS = 256, 8, 8
SAMPLE = SEQS * STEPS
TOK = SEQ + SAMPLE
TILES = 3
ROWS = [128, 128, SAMPLE]
AT = [0, 128, 256]
MEM = 256
CONV = 4
QKV = 1536
XH = 4
GROUPS, PER_GROUP, FF = 4, 8, 256
EXPERTS = GROUPS * PER_GROUP
CHUNK = 64
ALPHA = 4.0 ** 0.25
LN_EPS, RMS_EPS, GN_EPS = 1e-5, 1e-6, 64e-5
WIDE = TOK + 24
RING, SLOT = 4, 4096
PAST = 2048


def constants():
    i = np.arange(128)
    parts = {}
    parts["ident"] = np.eye(128)
    parts["ones"] = np.ones((128, 128))
    for kind, c in (("p", CHUNK), ("s", STEPS)):
        same = i[:, None] // c == i[None, :] // c
        parts["upto_" + kind] = same & (i[:, None] <= i[None, :])
        parts["below_" + kind] = same & (i[:, None] > i[None, :])
        parts["above_" + kind] = same & (i[:, None] < i[None, :])
        parts["of_chunk_" + kind] = i[:, None] // c == np.arange(8)[None, :]
    for s in (1, 2, 4, 8, 16, 32):
        same = i[:, None] // (2 * s) == i[None, :] // (2 * s)
        parts[f"level{s}"] = same & (i[:, None] // s % 2 == 1) & (i[None, :] // s % 2 == 0)
        parts[f"upper{s}"] = np.tile(parts[f"level{s}"][0:64, 0:64].T, (2, 1))
    for kind in "ps":
        for n in ("upto", "above"):
            parts[f"{n}_chunk_{kind}"] = np.tile(parts[f"{n}_{kind}"][0:64, 0:64], (2, 1))
    parts["ident_chunk"] = np.tile(np.eye(64), (2, 1))
    parts["pair"] = i[:, None] // 64 == i[None, :] // 64
    half = 64
    inv = np.float32(10000.0) ** (-np.linspace(0.0, 1.0, half, dtype=np.float32))
    pos = np.concatenate([np.arange(256), PAST + np.arange(64) % 8, np.zeros(64)]).astype(np.float32)
    ang = (pos[:, None] * inv[None, :]).astype(np.float32).reshape(3, 128, half)
    parts["cos"] = np.cos(ang).transpose(1, 0, 2).reshape(128, -1)
    parts["sin"] = np.sin(ang).transpose(1, 0, 2).reshape(128, -1)
    lg = np.log(1.0 - 2.0 ** (-5.0 - np.arange(4)))
    scale = 128.0 ** -0.5
    for kind, c in (("p", CHUNK), ("s", STEPS)):
        d = i[None, :] - i[:, None]
        same = (i[:, None] // c == i[None, :] // c) & (d >= 0)
        dec = np.exp(lg[None, :, None] * np.maximum(d, 0)[:, None, :]) * same[:, None, :] * scale
        parts["retdecay_" + kind] = dec.reshape(128, -1)
        parts["retq_" + kind] = np.exp(lg[None, :] * (i[:, None] % c + 1.0))
        parts["retk_" + kind] = np.exp(lg[None, :] * (c - 1.0 - i[:, None] % c)) * scale
    parts["descend"] = np.tile(8.0 - np.arange(8), (128, 1))
    parts["upto_all"] = i[:, None] <= i[None, :]
    parts["slot_base"] = np.tile(64.0 * np.arange(32) - 1.0, (128, 1))
    parts["slots"] = np.tile(i, (128, 1))
    parts["row"] = i[:, None]
    at, cols = {}, 0
    for name, a in parts.items():
        a = np.asarray(a, np.float32).reshape(128, -1)
        parts[name] = a
        at[name] = (cols, a.shape[1])
        cols += a.shape[1]
    return np.concatenate(list(parts.values()), 1), at


CHUNK_DECAY = {c: [float((1.0 - 2.0 ** (-5.0 - h)) ** c) for h in range(4)] for c in (CHUNK, STEPS)}


class Signal:

    def __init__(self, sem):
        self.sem, self.sent, self.base = sem, 0, 0

    def up(self, by=1):
        self.sent += by
        return self.sem, by

    def at(self, n):
        return self.sem, self.base + n


class Kernel:

    def __init__(self, nc, ins, outs, at, stack):
        self.nc, self.ins, self.outs, self.at, self.stack = nc, ins, outs, at, stack
        self.signals = {}
        self.uid = 0

    def sem(self, name):
        if name not in self.signals:
            self.signals[name] = Signal(self.stack.enter_context(self.nc.semaphore(name)))
        return self.signals[name]

    @contextlib.contextmanager
    def phase(self, *names):
        got = [self.sem(n) for n in names]
        for s in got:
            s.base = s.sent
        with self.nc.Block() as block:
            yield (block, *got)

    def sb(self, stack, name, shape, dt=F32):
        self.uid += 1
        return stack.enter_context(self.nc.sbuf_tensor(f"{name}_{self.uid}", shape, dt))

    def const(self, name, rows=128):
        a, n = self.at[name]
        return self.cst[0:rows, a:a + n]


def chain(eng, sig):

    def link(ins):
        ins.then_inc(*sig.up())
        eng.wait_ge(sig.sem, sig.sent)

    return link


def tile_kind(t):
    return "p" if t < 2 else "s"


def cols_of(t):
    return slice(AT[t], AT[t] + ROWS[t])



def weight_chunks(K):
    I = K.ins
    chunks, first = [], {}

    def dense(name, w, c0s):
        first[name] = len(chunks)
        for c0 in c0s:
            chunks.append([(lambda s: s.rearrange("p (k n) -> p k n", k=KT),
                            w[:, c0:c0 + 512].rearrange("(k p) n -> p k n", p=128))])

    def experts(name, layer):
        first[name] = len(chunks)
        for e in range(EXPERTS):
            for c in expert_chunks(K, layer, e // PER_GROUP, e % PER_GROUP):
                chunks.append(c)

    w_in = I["ab_w_in"][0]
    dense("ab_qkv", w_in, [0, 512, 1024])
    dense("ab_rest", w_in, [1544 + 512 * n for n in (0, 4, 1, 2, 3)])
    dense("ab_out", I["ab_w_out"][0], [0, 512])
    for layer in range(2):
        if layer:
            for n in ("r", "k", "v"):
                dense("c_" + n, I["c_w_" + n][0], [0, 512])
            dense("c_out", I["c_w_out"][0], [0, 512])
        for n in ("k", "v", "q", "o"):
            dense(f"x_{n}{layer}", I["x_w_" + n][layer], [0, 512])
        experts(f"moe{layer}", layer)
    return chunks, first


def expert_chunks(K, layer, g, e):
    I = K.ins
    up = [(lambda s, j=j: s.rearrange("p (k j f) -> p k j f", k=KT, j=2)[:, :, j, :],
           I[w][layer, g, e].rearrange("(k p) f -> p k f", p=128)) for j, w in enumerate(("moe_w1", "moe_w3"))]
    down = [(lambda s: s[:, 0:2 * D].rearrange("p (k n) -> p k n", k=2),
             I["moe_w2"][layer, g, e].rearrange("(k p) n -> p k n", p=128))]
    return [up, down]


def load_chunk(K, sp, g):
    if g >= len(K.chunks):
        return
    for view, src in K.chunks[g]:
        sp.dma_start(view(K.ring[:, g % RING, :]), src).then_inc(K.arrived[g % RING], 16)


def run_ahead(K, sp, first, full, counts):
    for n, count in enumerate(counts):
        sp.wait_ge(*full.at(count))
        load_chunk(K, sp, first + n + RING)


def await_chunk(K, pe, g):
    pe.wait_ge(K.arrived[g % RING], K.arrival[g])


def slot8(K, g):
    return K.ring[:, g % RING, :].rearrange("p (k n) -> p k n", k=KT)



def transpose_phase(K, groups):
    nc = K.nc
    with K.phase("tr_full", "tr_act", "tr_dve") as (block, full, by_act, by_dve):
        def view(n):
            srcs, dst = groups[n]
            p, c = srcs[0].shape[0], srcs[0].shape[1]
            return K.ps[n % 4][0:c, 0:len(srcs) * p].rearrange("c (n p) -> c n p", p=p)

        @block.tensor
        def _(pe):
            for n, (srcs, dst) in enumerate(groups):
                if n >= 4:
                    pe.wait_ge(*(by_act if n % 2 == 0 else by_dve).at((n - 4) // 2 + 1))
                for j, s in enumerate(srcs):
                    last = nc.tensor.transpose(view(n)[:, j, :], s, K.const("ident")[0:s.shape[0], 0:s.shape[0]])
                last.then_inc(*full.up())

        @block.scalar
        def _(act):
            for n in range(0, len(groups), 2):
                act.wait_ge(*full.at(n + 1))
                nc.scalar.copy(groups[n][1], view(n)).then_inc(*by_act.up())

        @block.vector
        def _(dve):
            for n in range(1, len(groups), 2):
                dve.wait_ge(*full.at(n + 1))
                nc.vector.tensor_copy(groups[n][1], view(n)).then_inc(*by_dve.up())


def token_major_phase(K, first, n_chunks, xT, tiles, dest, stores=(), stored_later=None,
                      aside=None, last_wait=None, between=None, stores_after=None):
    nc = K.nc
    units = [(g, t) for g in range(n_chunks) for t in range(len(tiles))]
    with K.phase("mm_full", "mm_act", "mm_dve", "stored", "aside_step", "vector_step", "conv_done") as (
            block, full, by_act, by_dve, stored, scaled, step, conv):
        @block.sync
        def _(sp):
            ready = stores_after or n_chunks
            run_ahead(K, sp, first, full, [len(tiles) * (g + 1) for g in range(ready)])
            for n, (dst, src) in enumerate(stores):
                if n == 0:
                    sp.wait_ge(*by_act.at((len(tiles) * ready + 1) // 2))
                    sp.wait_ge(*by_dve.at(len(tiles) * ready // 2))
                sp.dma_start(dst, src).then_inc(*(stored_later or stored).up(16))
            run_ahead(K, sp, first + ready, full, [len(tiles) * (g + 1) for g in range(ready, n_chunks)])
            if stores and not stored_later:
                sp.wait_ge(*stored.at(16 * len(stores)))
            if last_wait:
                last_wait(sp)

        if aside:
            @block.gpsimd
            def _(pool):
                aside(pool, scaled)

        @block.tensor
        def _(pe):
            for n, (g, t) in enumerate(units):
                if t == 0:
                    await_chunk(K, pe, first + g)
                if n >= 4:
                    pe.wait_ge(*(by_act if n % 2 == 0 else by_dve).at((n - 4) // 2 + 1))
                c, rows = tiles[t]
                w = slot8(K, first + g)
                for k in range(KT):
                    last = nc.tensor.matmul(K.ps[n % 4][0:rows, :], xT[:, k, c:c + rows], w[:, k, :],
                                            start=(k == 0), stop=(k == KT - 1))
                last.then_inc(*full.up())

        @block.scalar
        def _(act):
            for n in range(0, len(units), 2):
                act.wait_ge(*full.at(n + 1))
                g, t = units[n]
                nc.scalar.copy(dest(g, t), K.ps[n % 4][0:tiles[t][1], :]).then_inc(*by_act.up())
                if between:
                    between[1](act, n // 2, conv)

        @block.vector
        def _(dve):
            for n in range(1, len(units), 2):
                dve.wait_ge(*full.at(n + 1))
                g, t = units[n]
                nc.vector.tensor_copy(dest(g, t), K.ps[n % 4][0:tiles[t][1], :]).then_inc(*by_dve.up())
                if between:
                    between[0](dve, n // 2, step, conv, by_act)


def feature_major_phase(K, first, n_chunks, xT, n_tok, dest):
    nc = K.nc
    with K.phase("mm_full", "mm_act", "mm_dve") as (block, full, by_act, by_dve):
        @block.sync
        def _(sp):
            run_ahead(K, sp, first, full, [4 * (g + 1) for g in range(n_chunks)])

        @block.tensor
        def _(pe):
            for f in range(4 * n_chunks):
                g = first + f // 4
                if f % 4 == 0:
                    await_chunk(K, pe, g)
                if f >= 4:
                    pe.wait_ge(*(by_act if f % 2 == 0 else by_dve).at((f - 4) // 2 + 1))
                w = slot8(K, g)
                for k in range(KT):
                    last = nc.tensor.matmul(K.ps[f % 4][:, 0:n_tok], w[:, k, (f % 4) * 128:(f % 4 + 1) * 128],
                                            xT[:, k, 0:n_tok], start=(k == 0), stop=(k == KT - 1))
                last.then_inc(*full.up())

        @block.scalar
        def _(act):
            for f in range(0, 4 * n_chunks, 2):
                act.wait_ge(*full.at(f + 1))
                for dst, src in dest(f, K.ps[f % 4]):
                    last = nc.scalar.copy(dst, src)
                last.then_inc(*by_act.up())

        @block.vector
        def _(dve):
            for f in range(1, 4 * n_chunks, 2):
                dve.wait_ge(*full.at(f + 1))
                for dst, src in dest(f, K.ps[f % 4]):
                    last = nc.vector.tensor_copy(dst, src)
                last.then_inc(*by_dve.up())


def transpose_x(K):
    groups = []
    for t in range(TILES):
        for q in range(2):
            groups.append(([K.x[0:ROWS[t], t, (4 * q + j) * 128:(4 * q + j + 1) * 128] for j in range(4)],
                           K.xT[:, 4 * q:4 * q + 4, cols_of(t)]))
    transpose_phase(K, groups)


def row_broadcast(ap, rows=128):
    return ap.rearrange("(a n) -> a n", a=1).broadcast_to([rows, ap.shape[0]])


def turn_tile(K, pe, t, banks, normed, full, copied):
    pe.wait_ge(*normed.at(t + 1))
    rows = ROWS[t]
    for q in range(2):
        n = 2 * t + q
        if n >= len(banks):
            pe.wait_ge(*copied.at(n - len(banks) + 1))
        for j in range(4):
            last = K.nc.tensor.transpose(K.ps[banks[n % len(banks)]][:, j * rows:(j + 1) * rows],
                                         K.x[0:rows, t, (4 * q + j) * 128:(4 * q + j + 1) * 128],
                                         K.const("ident")[0:rows, 0:rows])
        last.then_inc(*full.up())


def copy_turned(K, act, t, banks, full, copied):
    for q in range(2):
        n = 2 * t + q
        act.wait_ge(*full.at(n + 1))
        src = K.ps[banks[n % len(banks)]][:, 0:4 * ROWS[t]].rearrange("c (n p) -> c n p", n=4)
        K.nc.scalar.copy(K.xT[:, 4 * q:4 * q + 4, cols_of(t)], src).then_inc(*copied.up())


def norm_tile(K, dve, link, act_sig, sq, normed, t, rows, stats, mv, lnw, lnb):
    nc = K.nc
    x = K.x[0:rows, t, :]
    for h in range(2):
        last = nc.vector.bn_stats(stats[0:rows, h, :], K.x[0:rows, t, h * 512:(h + 1) * 512])
    link(last)
    link(nc.vector.bn_aggr(mv[0:rows, t, 0:2], stats[0:rows, :, :].rearrange("p a b -> p (a b)")))
    nc.vector.tensor_scalar(mv[0:rows, t, 1:2], mv[0:rows, t, 1:2], LN_EPS, None, ALU.add).then_inc(*sq.up())
    dve.wait_ge(*act_sig.at(t + 1))
    link(nc.vector.reciprocal(mv[0:rows, t, 3:4], mv[0:rows, t, 2:3]))
    link(nc.vector.tensor_scalar(x, x, mv[0:rows, t, 0:1], mv[0:rows, t, 3:4], ALU.subtract, ALU.mult))
    link(nc.vector.tensor_tensor(x, x, lnw[0:rows, :], ALU.mult))
    link(nc.vector.tensor_tensor(x, x, lnb[0:rows, :], ALU.add))
    dve.sem_inc(*normed.up())


def add_and_norm_phase(K, first, srcT, layer, which):
    nc = K.nc
    with contextlib.ExitStack() as st:
        lnw, lnb = K.sb(st, "lnw", [128, D]), K.sb(st, "lnb", [128, D])
        stats, mv = K.sb(st, "stats", [128, 2, 6]), K.sb(st, "mv", [128, TILES, 4])
        with K.phase("mm_full", "loaded", "ln_free", "ln_var", "ln_std", "vector_step", "normed", "tr_full",
                     "tr_act") as (block, full, rows_in, free, var, std, step, normed, turned, copied):
            @block.sync
            def _(sp):
                sp.dma_start(lnw[:, :], row_broadcast(K.ins["ln_w"][layer, which])).then_inc(*rows_in.up(16))
                sp.dma_start(lnb[:, :], row_broadcast(K.ins["ln_b"][layer, which])).then_inc(*rows_in.up(16))
                run_ahead(K, sp, first, full, [TILES, TILES])

            @block.tensor
            def _(pe):
                for g in range(2):
                    await_chunk(K, pe, first + g)
                for t in range(TILES):
                    if t == 2:
                        pe.wait_ge(*free.at(1))
                    for g in range(2):
                        w = slot8(K, first + g)
                        for k in range(KT):
                            last = nc.tensor.matmul(K.ps[2 * (t % 2) + g][0:ROWS[t], :], srcT[:, k, cols_of(t)],
                                                    w[:, k, :], start=(k == 0), stop=(k == KT - 1))
                    last.then_inc(*full.up())
                for t in range(TILES):
                    turn_tile(K, pe, t, [4, 5, 6, 7], normed, turned, copied)

            @block.scalar
            def _(act):
                for t in range(TILES):
                    act.wait_ge(*var.at(t + 1))
                    nc.scalar.activation(mv[0:ROWS[t], t, 2:3], mv[0:ROWS[t], t, 1:2], ACT.Sqrt).then_inc(*std.up())
                for t in range(TILES):
                    copy_turned(K, act, t, [4, 5, 6, 7], turned, copied)

            @block.vector
            def _(dve):
                link = chain(dve, step)
                for t in range(TILES):
                    rows = ROWS[t]
                    dve.wait_ge(*full.at(t + 1))
                    for g in range(2):
                        xs = K.x[0:rows, t, g * 512:(g + 1) * 512]
                        last = nc.vector.scalar_tensor_tensor(xs, xs, ALPHA, K.ps[2 * (t % 2) + g][0:rows, :],
                                                              ALU.mult, ALU.add)
                    last.then_inc(*free.up())
                    dve.wait_ge(*free.at(t + 1))
                    if t == 0:
                        dve.wait_ge(*rows_in.at(32))
                    norm_tile(K, dve, link, std, var, normed, t, rows, stats, mv, lnw, lnb)



def hist(b):
    return 3 + SEQ + b * (CONV - 1 + STEPS)


RAW = 3 + SEQ + SEQS * (CONV - 1 + STEPS)


def ab_mixer(K):
    with contextlib.ExitStack() as outer:
        o = K.sb(outer, "o", [128, TILES, 8, 128])
        ab_heads(K, o)
        ab_finish(K, o)


def ab_heads(K, o):
    with contextlib.ExitStack() as st:
        kq = K.sb(st, "kq", [128, 2, 8, TOK])
        v = K.sb(st, "v", [128, TILES, 8, 128])
        kd = K.sb(st, "kd", [128, TILES, 8, 128])
        ab = K.sb(st, "ab", [128, TILES, 8])
        with contextlib.ExitStack() as s1:
            ab_project(K, s1, kq, v, kd, ab)
        ab_scan(K, st, kq, v, kd, ab, o)


def ab_project(K, st, kq, v, kd, ab):
    nc, I, O = K.nc, K.ins, K.outs
    raw = K.sb(st, "raw", [128, 12, RAW])
    u_v = K.sb(st, "u_v", [128, 4, TOK])
    cwT = K.sb(st, "cwT", [128, CONV, 12])
    small = contextlib.ExitStack()
    past = K.sb(small, "past", [24, QKV])
    cw = K.sb(small, "cw", [48, 128])
    wab = K.sb(small, "wab", [128, KT, 8])
    with K.phase("loaded", "ab_full") as (block, loaded, full):
        @block.sync
        def _(sp):
            sp.dma_start(past[:, :], I["state_conv_a"][0].rearrange("b j n -> (b j) n")).then_inc(*loaded.up(16))
            sp.dma_start(cw[:, :], I["ab_conv_w"][0].rearrange("j (k p) -> (j k) p", p=128)).then_inc(*loaded.up(16))
            sp.dma_start(wab[:, :, :], I["ab_w_in"][0][:, QKV:QKV + 8].rearrange("(k p) n -> p k n", p=128)
                         ).then_inc(*loaded.up(16))
            for g in range(RING):
                load_chunk(K, sp, g)

        @block.scalar
        def _(act):
            act.wait_ge(*full.at(1))
            for t in range(TILES):
                last = nc.scalar.copy(ab[0:ROWS[t], t, :], K.ps[4][0:ROWS[t], 8 * t:8 * t + 8])

        @block.vector
        def _(dve):
            nc.vector.memset(raw[:, :, 0:3], 0.0)

        @block.tensor
        def _(pe):
            pe.wait_ge(*loaded.at(48))
            for t in range(TILES):
                for k in range(KT):
                    last = nc.tensor.matmul(K.ps[4][0:ROWS[t], 8 * t:8 * t + 8], K.xT[:, k, cols_of(t)],
                                            wab[:, k, :], start=(k == 0), stop=(k == KT - 1))
            last.then_inc(*full.up())
    samples = raw[:, :, hist(0):RAW].rearrange("p f (b j) -> p f b j", b=SEQS)
    groups = [([past[:, f * 128:(f + 1) * 128]],
               samples[:, f:f + 1, :, 0:3]) for f in range(12)]
    transpose_history(K, groups)
    transpose_phase(K, [([cw[:, :]], cwT[:, :, :].rearrange("p j f -> p (j f)").unsqueeze(1))])
    small.close()
    qk = K.sb(st, "qk", [128, TILES, D])
    gates = contextlib.ExitStack()
    gate = K.sb(gates, "gate", [128, TILES, D])

    def raw_dest(f, bank):
        return [(raw[:, f, 3:3 + SEQ], bank[:, 0:SEQ]),
                (samples[:, f, :, 3:3 + STEPS], bank[:, SEQ:TOK].rearrange("p (b s) -> p b s", b=SEQS))]

    feature_major_phase(K, K.first["ab_qkv"], 3, K.xT, TOK, raw_dest)
    tiles = [(AT[t], ROWS[t]) for t in range(TILES)]

    def rest_dest(g, t):
        r = slice(0, ROWS[t])
        if g < 2:
            return gate[r, t, g * 512:(g + 1) * 512]
        if g < 4:
            return qk[r, t, (g - 2) * 512:(g - 1) * 512]
        return v[r, t, 4:8, :].rearrange("p h d -> p (h d)")

    last3 = K.sb(gates, "last3", [128, 12, 32])

    def place(f):
        return kq[:, 1, f, :] if f < 4 else kq[:, 0, f - 4, :] if f < 8 else u_v[:, f - 8, :]

    def convolve(dve, f, step, conv):
        link = chain(dve, step)
        o = place(f)
        os = o[:, SEQ:TOK].rearrange("p (b s) -> p b s", b=SEQS)
        for j in range(CONV):
            w = cwT[:, j, f:f + 1]
            if j == 0:
                nc.vector.tensor_scalar(o[:, 0:SEQ], raw[:, f, 0:SEQ], w, None, ALU.mult)
                last = nc.vector.tensor_scalar(os, samples[:, f, :, 0:STEPS], w, None, ALU.mult)
            else:
                nc.vector.scalar_tensor_tensor(o[:, 0:SEQ], raw[:, f, j:j + SEQ], w, o[:, 0:SEQ], ALU.mult, ALU.add)
                last = nc.vector.scalar_tensor_tensor(os, samples[:, f, :, j:j + STEPS], w, os, ALU.mult, ALU.add)
            if j < CONV - 1:
                link(last)
        last.then_inc(*conv.up())

    free = kq[:, 0, 4:8, :].rearrange("p h n -> p (h n)")
    parts = [free[:, 512 * j:512 * j + 512].rearrange("p (h d) -> p h d", h=8) for j in range(2)]

    def dve_between(dve, i, step, conv, by_act):
        for f in range(2 * i, min(2 * i + 2, 12)):
            convolve(dve, f, step, conv)
        if i == 5:
            dve.wait_ge(*by_act.at(6))
            rotate(K, chain(dve, step), qk, *parts)

    def act_between(act, i, conv):
        for f in range(2 * i - 2, min(2 * i, 12)):
            if f >= 0:
                act.wait_ge(*conv.at(f + 1))
                nc.scalar.activation(place(f), place(f), ACT.Silu)

    def last_tokens(pool, _):
        nc.gpsimd.tensor_copy(last3[:, :, 0:3], raw[:, :, SEQ:SEQ + 3])
        nc.gpsimd.tensor_copy(last3[:, :, 3:27].rearrange("p f (b j) -> p f b j", b=SEQS),
                              samples[:, :, :, STEPS:STEPS + 3])

    token_major_phase(K, K.first["ab_rest"], 5, K.xT, tiles, rest_dest,
                      stores=[(K.scratch["gate"][cols_of(t), :], gate[0:ROWS[t], t, :]) for t in range(TILES)],
                      stores_after=2, aside=last_tokens, between=(dve_between, act_between))
    tail = raw[0:32, :, 0:128]
    transpose_phase(K, [([last3[:, 4 * q + j, 0:27] for j in range(4)],
                         tail[0:27, 4 * q:4 * q + 4, :]) for q in range(3)])
    gates.close()
    ab_norms(K, kq, qk, tail)
    groups = []
    for t in range(TILES):
        c = cols_of(t)
        groups.append(([u_v[:, h, c] for h in range(4)], v[0:ROWS[t], t, 0:4, :]))
        groups.append(([kq[:, 0, h, c] for h in range(4)], kd[0:ROWS[t], t, 0:4, :]))
        groups.append(([kq[:, 0, 4 + h, c] for h in range(4)], kd[0:ROWS[t], t, 4:8, :]))
    transpose_phase(K, groups)


def transpose_history(K, groups):
    nc = K.nc
    with K.phase("tr_full") as (block, full):
        @block.tensor
        def _(pe):
            for f, (srcs, dst) in enumerate(groups):
                last = nc.tensor.transpose(K.ps[f % 4][:, f // 4 * 24:f // 4 * 24 + 24], srcs[0],
                                           K.const("ident")[0:24, 0:24])
            last.then_inc(*full.up())

        @block.vector
        def _(dve):
            dve.wait_ge(*full.at(1))
            for f, (srcs, dst) in enumerate(groups):
                src = K.ps[f % 4][:, f // 4 * 24:f // 4 * 24 + 24].rearrange("p (a b j) -> p a b j", a=1, b=SEQS)
                nc.vector.tensor_copy(dst, src)


def ab_norms(K, kq, qk, tail):
    nc, O = K.nc, K.outs
    with contextlib.ExitStack() as tmp:
        sq = K.sb(tmp, "sq", [128, 2, TOK])
        root = K.sb(tmp, "root", [128, 2, TOK])
        inv = K.sb(tmp, "inv", [128, 2, TOK])
        turns = [(t, i, o) for t in range(TILES) for i, o in ((1, 0), (0, 4))]
        with K.phase("sq_done", "sum_done", "root_done", "inv_done", "scaled", "stored", "tr_full") as (
                block, sqd, summed, rooted, inved, scaled, stored, turned):
            heads = [(i, h) for i in range(2) for h in range(4)]

            @block.sync
            def _(sp):
                sp.dma_start(O[4][0, 0].rearrange("j (f p) -> j f p", f=12), tail[0:3]).then_inc(*stored.up(16))
                sp.dma_start(O[9][0].rearrange("b j (f p) -> (b j) f p", f=12), tail[3:27]).then_inc(*stored.up(16))
                sp.wait_ge(*stored.at(32))

            @block.gpsimd
            def _(pool):
                for n, (i, h) in enumerate(heads):
                    if n >= 2:
                        pool.wait_ge(*summed.at(n - 1))
                    nc.gpsimd.tensor_tensor(sq[:, n % 2, :], kq[:, i, h, :], kq[:, i, h, :], ALU.mult
                                            ).then_inc(*sqd.up())

            @block.tensor
            def _(pe):
                for n in range(8):
                    pe.wait_ge(*sqd.at(n + 1))
                    if n >= 2:
                        pe.wait_ge(*rooted.at(n - 1))
                    nc.tensor.matmul(K.ps[n % 2][:, 0:TOK], K.const("ones"), sq[:, n % 2, :], start=True, stop=True
                                     ).then_inc(*summed.up())
                    if n < len(turns):
                        t, i, o = turns[n]
                        r = ROWS[t]
                        for h in range(4):
                            last = nc.tensor.transpose(K.ps[2 + n][:, h * r:(h + 1) * r],
                                                       qk[0:r, t, (o + h) * 128:(o + h + 1) * 128],
                                                       K.const("ident")[0:r, 0:r])
                        last.then_inc(*turned.up())

            @block.scalar
            def _(act):
                for n in range(8):
                    act.wait_ge(*summed.at(n + 1))
                    if n >= 2:
                        act.wait_ge(*inved.at(n - 1))
                    nc.scalar.activation(root[:, n % 2, :], K.ps[n % 2][:, 0:TOK], ACT.Sqrt, bias=K.eps6[:, 0:1]
                                         ).then_inc(*rooted.up())
                    if n < len(turns):
                        act.wait_ge(*turned.at(n + 1))
                        t, i, _ = turns[n]
                        nc.scalar.copy(kq[:, i, 4:8, cols_of(t)],
                                       K.ps[2 + n][:, 0:4 * ROWS[t]].rearrange("c (n p) -> c n p", n=4))

            @block.vector
            def _(dve):
                for n, (i, h) in enumerate(heads):
                    dve.wait_ge(*rooted.at(n + 1))
                    if n >= 2:
                        dve.wait_ge(*scaled.at(n - 1))
                    nc.vector.reciprocal(inv[:, n % 2, :], root[:, n % 2, :]).then_inc(*inved.up())
                    dve.wait_ge(*inved.at(n + 1))
                    if i == 1:
                        nc.vector.scalar_tensor_tensor(kq[:, i, h, :], kq[:, i, h, :], 128.0 ** -0.5, inv[:, n % 2, :],
                                                       ALU.mult, ALU.mult).then_inc(*scaled.up())
                    else:
                        nc.vector.tensor_tensor(kq[:, i, h, :], kq[:, i, h, :], inv[:, n % 2, :], ALU.mult
                                                ).then_inc(*scaled.up())


def rotate(K, link, qk, t1, t2):
    nc = K.nc
    for t in range(TILES):
        r = slice(0, ROWS[t])
        h = qk[r, t, :].rearrange("p (h d) -> p h d", h=8)
        x1, x2 = h[:, :, 0:64], h[:, :, 64:128]
        cos = K.const("cos")[r, t * 64:(t + 1) * 64].unsqueeze(1).broadcast_to([ROWS[t], 8, 64])
        sin = K.const("sin")[r, t * 64:(t + 1) * 64].unsqueeze(1).broadcast_to([ROWS[t], 8, 64])
        nc.vector.tensor_tensor(t1[r], x1, sin, ALU.mult)
        link(nc.vector.tensor_tensor(t2[r], x2, sin, ALU.mult))
        nc.vector.tensor_tensor(x1, x1, cos, ALU.mult)
        link(nc.vector.tensor_tensor(x2, x2, cos, ALU.mult))
        nc.vector.tensor_tensor(x1, x1, t2[r], ALU.subtract)
        link(nc.vector.tensor_tensor(x2, x2, t1[r], ALU.add))


def invert_phase(K, low, T, R, work, units, levels):
    nc = K.nc
    c, y = work
    with K.phase("inv_cut", "inv_y", "inv_yc", "inv_d", "inv_t", "inv_r") as (block, cut, ys, yc, ds, ts, rs):
        steps = [(s, n) for s in levels for n in range(len(units)) if s in units[n][2]]
        prior = {}
        for m, (s, n) in enumerate(steps):
            prior[m] = max([j for j in range(m) if steps[j][1] == n], default=-1)

        @block.gpsimd
        def _(pool):
            for m, (s, n) in enumerate(steps):
                i, rows, _ = units[n]
                if m >= 2:
                    pool.wait_ge(*ys.at(m - 1))
                mask = K.const(f"level{s}")[0:rows, 0:rows].unsqueeze(1).broadcast_to([rows, 4, rows])
                nc.gpsimd.tensor_tensor(c[0:rows, m % 2, :, 0:rows], low[0:rows, i, :, 0:rows], mask, ALU.mult
                                        ).then_inc(*cut.up())

        @block.tensor
        def _(pe):
            for m, (s, n) in enumerate(steps):
                i, rows, _ = units[n]
                b = m % 2
                pe.wait_ge(*cut.at(m + 1))
                if prior[m] >= 0:
                    pe.wait_ge(*ts.at(prior[m] + 1))
                    pe.wait_ge(*rs.at(prior[m] + 1))
                if m >= 2:
                    pe.wait_ge(*yc.at(m - 1))
                for h in range(4):
                    last = nc.tensor.matmul(K.ps[b][0:rows, h * rows:(h + 1) * rows], c[0:rows, b, h, 0:rows],
                                            R[0:rows, i, h, 0:rows], start=True, stop=True)
                last.then_inc(*ys.up())
                pe.wait_ge(*yc.at(m + 1))
                if m >= 2:
                    pe.wait_ge(*ts.at(m - 1))
                    pe.wait_ge(*rs.at(m - 1))
                for h in range(4):
                    nc.tensor.matmul(K.ps[2 + b][0:rows, h * rows:(h + 1) * rows], y[0:rows, b, h, 0:rows],
                                     T[0:rows, i, h, 0:rows], start=True, stop=True)
                for h in range(4):
                    last = nc.tensor.matmul(K.ps[4 + b][0:rows, h * rows:(h + 1) * rows], T[0:rows, i, h, 0:rows],
                                            y[0:rows, b, h, 0:rows], start=True, stop=True)
                last.then_inc(*ds.up())

        @block.scalar
        def _(act):
            for m, (s, n) in enumerate(steps):
                i, rows, _ = units[n]
                act.wait_ge(*ys.at(m + 1))
                if m >= 2:
                    act.wait_ge(*ds.at(m - 1))
                nc.scalar.copy(y[0:rows, m % 2, :, 0:rows],
                               K.ps[m % 2][0:rows, 0:4 * rows].rearrange("p (h n) -> p h n", h=4)).then_inc(*yc.up())

        @block.vector
        def _(dve):
            for m, (s, n) in enumerate(steps):
                i, rows, _ = units[n]
                dve.wait_ge(*ds.at(m + 1))
                for dst, bank, sig in ((T, 2, ts), (R, 4, rs)):
                    d = dst[0:rows, i, :, 0:rows]
                    nc.vector.tensor_tensor(d, d, K.ps[bank + m % 2][0:rows, 0:4 * rows].rearrange(
                        "p (h n) -> p h n", h=4), ALU.subtract).then_inc(*sig.up())


def first_level(K, low, T, R, units):
    nc = K.nc
    with K.phase("vector_step") as (block, step):
        @block.vector
        def _(dve):
            link = chain(dve, step)
            for i, rows, _ in units:
                d = T[0:rows, i, :, 0:rows]
                mask = K.const("level1")[0:rows, 0:rows].unsqueeze(1).broadcast_to([rows, 4, rows])
                ident = K.const("ident")[0:rows, 0:rows].unsqueeze(1).broadcast_to([rows, 4, rows])
                link(nc.vector.tensor_tensor(d, low[0:rows, i, :, 0:rows], mask, ALU.mult))
                link(nc.vector.tensor_tensor(d, ident, d, ALU.subtract))
    transpose_phase(K, [([T[0:rows, i, h, 0:rows] for h in range(4)], R[0:rows, i, :, 0:rows])
                        for i, rows, _ in units])


LEVELS = [2, 4, 8, 16, 32]


def ab_scan(K, st, kq, v, kd, ab, o):
    nc, I, O = K.nc, K.ins, K.outs
    qkd = K.sb(st, "qkd", [128, TILES, 8, 128])
    R = K.sb(st, "R", [128, TILES, 4, 128])
    beta = K.sb(st, "beta", [128, TILES, 4])
    gcol = K.sb(st, "gcol", [128, TILES, 8])
    egc = K.sb(st, "egc", [128, TILES, 8])
    ekd = K.sb(st, "ekd", [128, TILES, 8])
    nbeg = K.sb(st, "nbeg", [128, TILES, 4])
    total = K.sb(st, "total", [128, 4 + SEQS, 8])
    with contextlib.ExitStack() as tmp:
        arow = K.sb(tmp, "arow", [128, 8])
        g = K.sb(tmp, "g", [128, TILES, 4])
        s1 = K.sb(tmp, "s1", [128, TILES, 4])
        s2 = K.sb(tmp, "s2", [128, TILES, 4])
        gup = K.sb(tmp, "gup", [128, TILES, 4, 128])
        gp = K.sb(tmp, "gp", [128, 4, 4])
        gb = K.sb(tmp, "gb", [128, SEQS, 4])
        low = K.sb(tmp, "low", [128, TILES, 4, 128])
        T = K.sb(tmp, "T", [128, TILES, 4, 128])
        c = K.sb(tmp, "c", [128, 2, 4, 128])
        y = K.sb(tmp, "y", [128, 2, 4, 128])
        with K.phase("loaded", "scalar_step", "vector_step") as (block, loaded, by_act, by_dve):
            full = [(slice(0, 128), slice(0, 2)), (slice(0, SAMPLE), slice(2, 3))]

            @block.sync
            def _(sp):
                sp.dma_start(arow[:, 0:4], row_broadcast(I["ab_a_log"][0])).then_inc(*loaded.up(16))
                sp.dma_start(arow[:, 4:8], row_broadcast(I["ab_dt_bias"][0])).then_inc(*loaded.up(16))

            @block.scalar
            def _(act):
                link = chain(act, by_act)
                act.wait_ge(*loaded.at(32))
                link(nc.scalar.activation(arow[:, 0:4], arow[:, 0:4], ACT.Exp))
                act.wait_ge(*by_dve.at(2))
                for r, t in full:
                    nc.scalar.activation(beta[r, t, :], ab[r, t, 4:8], ACT.Sigmoid)
                for r, t in full:
                    last = nc.scalar.activation(s2[r, t, :], s1[r, t, :], ACT.Exp)
                link(last)
                for r, t in full:
                    last = nc.scalar.activation(s2[r, t, :], s2[r, t, :], ACT.Ln, bias=1.0)
                link(last)

            @block.vector
            def _(dve):
                link = chain(dve, by_dve)
                dve.wait_ge(*loaded.at(32))
                for r, t in full:
                    n = t.stop - t.start
                    last = nc.vector.tensor_tensor(g[r, t, :], ab[r, t, 0:4], arow[r, 4:8].unsqueeze(1).broadcast_to(
                        [r.stop, n, 4]), ALU.add)
                link(last)
                for r, t in full:
                    last = nc.vector.scalar_tensor_tensor(s1[r, t, :], g[r, t, :], -1.0, g[r, t, :], ALU.mult, ALU.min)
                link(last)
                dve.wait_ge(*by_act.at(3))
                for r, t in full:
                    last = nc.vector.scalar_tensor_tensor(g[r, t, :], g[r, t, :], 0.0, s2[r, t, :], ALU.max, ALU.add)
                link(last)
                for r, t in full:
                    n = t.stop - t.start
                    last = nc.vector.scalar_tensor_tensor(
                        g[r, t, :], g[r, t, :], -1.0, arow[r, 0:4].unsqueeze(1).broadcast_to([r.stop, n, 4]),
                        ALU.mult, ALU.mult)
                link(last)
                for t in range(TILES):
                    r = ROWS[t]
                    for h in range(4):
                        nc.vector.tensor_scalar(gup[0:r, t, h, 0:r], K.const("upto_" + tile_kind(t))[0:r, 0:r],
                                                g[0:r, t, h:h + 1], None, ALU.mult)
                for n in range(4):
                    nc.vector.tensor_scalar(gp[:, n, :], g[:, n // 2, :], K.const("of_chunk_p")[:, n % 2:n % 2 + 1],
                                            None, ALU.mult)
                nc.vector.tensor_tensor(
                    gb[0:SAMPLE], g[0:SAMPLE, 2, :].unsqueeze(1).broadcast_to([SAMPLE, SEQS, 4]),
                    K.const("of_chunk_s")[0:SAMPLE, :].unsqueeze(2).broadcast_to([SAMPLE, SEQS, 4]), ALU.mult)
        with K.phase("sum_full", "low_done", "scalar_step", "vector_step", "dec_pool") as (
                block, full, low_done, by_act, by_dve, by_pool):
            tot = K.ps[3][:, 32:80].rearrange("p (c h) -> p c h", h=4)

            @block.tensor
            def _(pe):
                for t in range(TILES):
                    r, kind = ROWS[t], tile_kind(t)
                    nc.tensor.matmul(K.ps[t][0:r, 0:4 * r], K.const("ones")[0:r, 0:r],
                                     gup[0:r, t, :, 0:r], start=True, stop=True)
                    nc.tensor.matmul(K.ps[3][0:r, 8 * t:8 * t + 4], K.const("upto_" + kind)[0:r, 0:r], g[0:r, t, :],
                                     start=True, stop=True)
                    nc.tensor.matmul(K.ps[3][0:r, 8 * t + 4:8 * t + 8], K.const("below_" + kind)[0:r, 0:r],
                                     g[0:r, t, :], start=True, stop=True)
                nc.tensor.matmul(tot[:, 0:4, :], K.const("ones"), gp[:, :, :], start=True, stop=True)
                nc.tensor.matmul(tot[:, 4:12, :], K.const("ones")[0:SAMPLE, :], gb[0:SAMPLE, :, :],
                                 start=True, stop=True).then_inc(*full.up())
                for t in range(TILES):
                    r = ROWS[t]
                    if t >= 1:
                        pe.wait_ge(*low_done.at(3 * t))
                    for h in range(4):
                        nc.tensor.matmul(K.ps[4][0:r, h * r:(h + 1) * r], kq[:, 0, h, cols_of(t)],
                                         kq[:, 0, h, cols_of(t)], start=True, stop=True)
                    for h in range(8):
                        last = nc.tensor.matmul(K.ps[5 + h // 4][0:r, h % 4 * r:(h % 4 + 1) * r],
                                                kq[:, 0, h, cols_of(t)], kq[:, 1, h, cols_of(t)],
                                                start=True, stop=True)
                    last.then_inc(*full.up())

            @block.vector
            def _(dve):
                link = chain(dve, by_dve)
                dve.wait_ge(*full.at(1))
                for t in range(TILES):
                    r = ROWS[t]
                    last = nc.vector.tensor_copy(gcol[0:r, t, :], K.ps[3][0:r, 8 * t:8 * t + 8])
                link(last)
                for t in range(TILES):
                    r = ROWS[t]
                    for h in range(4):
                        s = K.ps[t][0:r, h * r:(h + 1) * r]
                        gc = gcol[0:r, t, h:h + 1]
                        nc.vector.tensor_scalar(low[0:r, t, h, 0:r], s, gc, 0.0, ALU.subtract, ALU.max)
                        last = nc.vector.tensor_scalar(qkd[0:r, t, h, 0:r], s, gc, 0.0, ALU.subtract, ALU.min)
                link(last)
                dve.wait_ge(*by_act.at(1))
                for t in range(TILES):
                    r, kind = ROWS[t], tile_kind(t)
                    below = K.const("below_" + kind)[0:r, 0:r].unsqueeze(1).broadcast_to([r, 4, r])
                    upto = K.const("upto_" + kind)[0:r, 0:r].unsqueeze(1).broadcast_to([r, 4, r])
                    nc.vector.tensor_tensor(low[0:r, t, :, 0:r], low[0:r, t, :, 0:r], below, ALU.mult)
                    last = nc.vector.tensor_tensor(qkd[0:r, t, 0:4, 0:r], qkd[0:r, t, 0:4, 0:r], upto, ALU.mult)
                link(last)
                for t in range(TILES):
                    r, kind = ROWS[t], tile_kind(t)
                    dve.wait_ge(*full.at(t + 2))
                    for h in range(4):
                        last = nc.vector.scalar_tensor_tensor(
                            low[0:r, t, h, 0:r], K.ps[4][0:r, h * r:(h + 1) * r], beta[0:r, t, h:h + 1],
                            low[0:r, t, h, 0:r], ALU.mult, ALU.mult)
                    last.then_inc(*low_done.up())
                    nc.vector.tensor_tensor(qkd[0:r, t, 0:4, 0:r], qkd[0:r, t, 0:4, 0:r],
                                            K.ps[5][0:r, 0:4 * r].rearrange("p (h n) -> p h n", h=4), ALU.mult
                                            ).then_inc(*low_done.up())
                    ret = K.const("retdecay_" + kind)[0:r].rearrange("p (h n) -> p h n", h=4)[:, :, 0:r]
                    nc.vector.tensor_tensor(qkd[0:r, t, 4:8, 0:r], ret,
                                            K.ps[6][0:r, 0:4 * r].rearrange("p (h n) -> p h n", h=4), ALU.mult
                                            ).then_inc(*low_done.up())
                    nc.vector.tensor_copy(egc[0:r, t, 4:8], K.const("retq_" + kind)[0:r])
                    nc.vector.tensor_copy(ekd[0:r, t, 4:8], K.const("retk_" + kind)[0:r])
                    link(nc.vector.scalar_tensor_tensor(nbeg[0:r, t, :], egc[0:r, t, 0:4], -1.0, beta[0:r, t, :],
                                                   ALU.mult, ALU.mult))
                    for h in range(8):
                        nc.vector.tensor_scalar(kd[0:r, t, h, :], kd[0:r, t, h, :], ekd[0:r, t, h:h + 1], None,
                                                ALU.mult)
                        if h < 4:
                            nc.vector.tensor_scalar(v[0:r, t, h, :], v[0:r, t, h, :], beta[0:r, t, h:h + 1], None,
                                                    ALU.mult)
                for h in range(4):
                    nc.vector.memset(total[:, 0:4, 4 + h], CHUNK_DECAY[CHUNK][h])
                    nc.vector.memset(total[:, 4:12, 4 + h], CHUNK_DECAY[STEPS][h])

            @block.scalar
            def _(act):
                act.wait_ge(*by_dve.at(2))
                for t in range(TILES):
                    r = ROWS[t]
                    nc.scalar.activation(low[0:r, t, :, 0:r], low[0:r, t, :, 0:r], ACT.Exp, scale=-1.0)
                    nc.scalar.activation(qkd[0:r, t, 0:4, 0:r], qkd[0:r, t, 0:4, 0:r], ACT.Exp)
                    nc.scalar.activation(egc[0:r, t, 0:4], gcol[0:r, t, 0:4], ACT.Exp)
                    nc.scalar.activation(ekd[0:r, t, 0:4], gcol[0:r, t, 4:8], ACT.Exp)
                nc.scalar.activation(total[:, :, 0:4], tot, ACT.Exp).then_inc(*by_act.up())
        units = [(t, ROWS[t], LEVELS if t < 2 else [2, 4]) for t in range(TILES)]
        first_level(K, low, T, R, units)
        invert_phase(K, low, T, R, (c, y), units, LEVELS)
    ab_chunks(K, kq, v, kd, qkd, R, egc, nbeg, total, o)


def ab_chunks(K, kq, v, kd, qkd, R, egc, nbeg, total, o):
    nc, I, O = K.nc, K.ins, K.outs
    with contextlib.ExitStack() as tmp:
        S = K.sb(tmp, "S", [128, 8, 128])
        vn = K.sb(tmp, "vn", [128, 4, 128])
        r_ = K.sb(tmp, "r", [128, 4, 128])
        K.state = K.sb(tmp, "state", [128, HELD, SEQS, 128])
        K.state_in = [K.sem(f"state_in{i}") for i in range(HELD)]
        for sig in K.state_in:
            sig.base = sig.sent
        for n in range(5):
            ab_chunk(K, n, kq, v, kd, qkd, R, egc, nbeg, total, o, S, vn, r_)


def ab_chunk(K, n, kq, v, kd, qkd, R, egc, nbeg, total, o, S, vn, r_):
    nc, I, O = K.nc, K.ins, K.outs
    sample = n == 4
    t, off = (2, 0) if sample else (n // 2, 64 * (n % 2))
    sl = slice(off, off + 64)
    c = slice(AT[t] + off, AT[t] + off + 64)
    with contextlib.ExitStack() as tmp:
        if sample:
            ab_sample_states(K, tmp, kq)
        with K.phase("ks_full", "r_done", "vn_full", "vn_done", "o_full", "o_scaled", "o_done", "su_full",
                     "s_done", "stored") as (
                block, ks, rd, vf, vd, of, osc, od, sf, sd, out):
            @block.tensor
            def _(pe):
                if not sample and n:
                    for h in range(4):
                        nc.tensor.matmul(K.ps[0][sl, h * 128:(h + 1) * 128], kq[:, 0, h, c], S[:, h, :],
                                         start=True, stop=True)
                    for h in range(8):
                        last = nc.tensor.matmul(K.ps[1 + h // 4][sl, h % 4 * 128:(h % 4 + 1) * 128], kq[:, 1, h, c],
                                                S[:, h, :], start=True, stop=True)
                    last.then_inc(*ks.up())
                elif sample:
                    for h in range(4):
                        nc.tensor.matmul(K.ps[0][sl, h * 128:(h + 1) * 128], K.byst[:, h, 0, :], K.const("ident"),
                                         start=True, stop=True)
                    for h in range(8):
                        last = nc.tensor.matmul(K.ps[1 + h // 4][sl, h % 4 * 128:(h % 4 + 1) * 128],
                                                K.byst[:, h, 1, :], K.const("ident"), start=True, stop=True)
                    last.then_inc(*ks.up())
                if n:
                    pe.wait_ge(*rd.at(1))
                src = r_ if n else v[:, 0, 0:4, :]
                for h in range(4):
                    last = nc.tensor.matmul(K.ps[3][sl, h * 128:(h + 1) * 128], R[sl, t, h, sl], src[sl, h, :],
                                            start=True, stop=True)
                last.then_inc(*vf.up())
                pe.wait_ge(*vd.at(1))
                for h in range(8):
                    vals = vn[sl, h, :] if h < 4 else v[sl, t, h, :]
                    last = nc.tensor.matmul(K.ps[4 + h // 4][sl, h % 4 * 128:(h % 4 + 1) * 128], qkd[sl, t, h, sl],
                                            vals, start=True, stop=True)
                last.then_inc(*of.up())
                if not sample:
                    for h in range(8):
                        vals = vn[sl, h, :] if h < 4 else v[sl, t, h, :]
                        last = nc.tensor.matmul(K.ps[6 + h // 4][:, h % 4 * 128:(h % 4 + 1) * 128], kd[sl, t, h, :],
                                                vals, start=True, stop=True)
                    last.then_inc(*sf.up())

            @block.scalar
            def _(act):
                act.wait_ge(*vf.at(1))
                nc.scalar.copy(vn[sl, :, :], K.ps[3][sl, :].rearrange("p (h n) -> p h n", h=4)).then_inc(*vd.up())
                if n:
                    for h in range(8):
                        last = nc.scalar.mul(o[sl, t, h, :], K.ps[1 + h // 4][sl, h % 4 * 128:(h % 4 + 1) * 128],
                                             egc[sl, t, h:h + 1])
                    last.then_inc(*osc.up())

            @block.vector
            def _(dve):
                if n:
                    dve.wait_ge(*ks.at(1))
                    for h in range(4):
                        last = nc.vector.scalar_tensor_tensor(
                            r_[sl, h, :], K.ps[0][sl, h * 128:(h + 1) * 128], nbeg[sl, t, h:h + 1], v[sl, t, h, :],
                            ALU.mult, ALU.add)
                    last.then_inc(*rd.up())
                if not sample:
                    dve.wait_ge(*sf.at(1))
                    for h in range(8):
                        up = K.ps[6 + h // 4][:, h % 4 * 128:(h % 4 + 1) * 128]
                        if n:
                            last = nc.vector.scalar_tensor_tensor(S[:, h, :], S[:, h, :], total[:, n, h:h + 1], up,
                                                                  ALU.mult, ALU.add)
                        else:
                            last = nc.vector.tensor_copy(S[:, h, :], up)
                    last.then_inc(*sd.up())
                dve.wait_ge(*of.at(1))
                if n:
                    dve.wait_ge(*osc.at(1))
                for q in range(2):
                    ops = K.ps[4 + q][sl, :].rearrange("p (h n) -> p h n", h=4)
                    dst = o[sl, t, 4 * q:4 * q + 4, :]
                    if n:
                        nc.vector.tensor_tensor(dst, dst, ops, ALU.add)
                    else:
                        nc.vector.tensor_copy(dst, ops)

            if n == 0:
                @block.sync
                def _(sp):
                    for h in range(HELD):
                        load_head(K, sp, h)

            if n == 3:
                @block.sync
                def _(sp):
                    sp.wait_ge(*sd.at(1))
                    for q, i in ((0, 5), (1, 6)):
                        sp.dma_start(O[i][0, 0].rearrange("h k v -> k h v"), S[:, 4 * q:4 * q + 4, :]
                                     ).then_inc(*out.up(16))
                    sp.wait_ge(*out.at(32))
        if sample:
            ab_sample_update(K, kd, v, vn, total, S)


HELD = 4


def load_head(K, sp, h):
    src = K.ins["state_delta" if h < 4 else "state_ret"][0, :, h % 4].rearrange("b k v -> k b v")
    sp.dma_start(K.state[:, h % HELD, :, :], src).then_inc(*K.state_in[h % HELD].up(16))


def ab_sample_states(K, tmp, kq):
    nc, I = K.nc, K.ins
    K.byst = K.sb(tmp, "byst", [128, 8, 2, SAMPLE])
    with K.phase("st_full", "st_done") as (block, full, done):
        @block.sync
        def _(sp):
            for h in range(HELD, 8):
                sp.wait_ge(*full.at(h - HELD + 1))
                load_head(K, sp, h)

        @block.tensor
        def _(pe):
            for h in range(8):
                pe.wait_ge(*K.state_in[h % HELD].at(16 * (h // HELD + 1)))
                if h >= 2:
                    pe.wait_ge(*done.at(h - 1))
                bank = K.ps[h % 2][:, 0:2 * SAMPLE].rearrange("p (i c) -> p i c", i=2)
                for b in range(SEQS):
                    c = slice(SEQ + 8 * b, SEQ + 8 * b + 8)
                    last = nc.tensor.matmul(bank[:, :, 8 * b:8 * b + 8], K.state[:, h % HELD, b, :], kq[:, :, h, c],
                                            start=True, stop=True)
                last.then_inc(*full.up())

        @block.scalar
        def _(act):
            for h in range(8):
                act.wait_ge(*full.at(h + 1))
                nc.scalar.copy(K.byst[:, h, :, :], K.ps[h % 2][:, 0:2 * SAMPLE].rearrange("p (i c) -> p i c", i=2)
                               ).then_inc(*done.up())


def ab_sample_update(K, kd, v, vn, total, S):
    nc, O = K.nc, K.outs
    order = [4, 5, 6, 7, 0, 1, 2, 3]
    spread = [K.byst[0:SAMPLE].rearrange("p h i c -> p (h i c)").rearrange("p (b n) -> p b n", n=128), S[0:SAMPLE]]
    with K.phase("spread_done", "su_full", "su_done", *(f"state_out{i}" for i in range(HELD))) as (
            block, sp_done, full, done, *outs):
        def store(sp, n):
            h = order[n]
            sp.wait_ge(*done.at(n + 1))
            dst = O[10 if h < 4 else 11][0, :, h % 4].rearrange("b k v -> k b v")
            sp.dma_start(dst, K.state[:, h % HELD, :, :]).then_inc(*outs[h % HELD].up(16))

        @block.sync
        def _(sp):
            for n in range(8):
                store(sp, n)
                if 1 <= n <= HELD:
                    h = order[n - 1 + HELD]
                    sp.wait_ge(*outs[h % HELD].at(16))
                    load_head(K, sp, h)
            for out in outs:
                sp.wait_ge(*out.at(32))

        @block.gpsimd
        def _(pool):
            for n, h in enumerate(order):
                if n >= 2:
                    pool.wait_ge(*full.at(n - 1))
                vals = vn[0:SAMPLE, h, :] if h < 4 else v[0:SAMPLE, 2, h, :]
                nc.gpsimd.tensor_tensor(
                    spread[n % 2], vals.unsqueeze(1).broadcast_to([SAMPLE, SEQS, 128]),
                    K.const("of_chunk_s")[0:SAMPLE, :].unsqueeze(2).broadcast_to([SAMPLE, SEQS, 128]), ALU.mult
                ).then_inc(*sp_done.up())

        @block.tensor
        def _(pe):
            for n, h in enumerate(order):
                pe.wait_ge(*sp_done.at(n + 1))
                if n >= 2:
                    pe.wait_ge(*done.at(n - 1))
                for q in range(2):
                    last = nc.tensor.matmul(K.ps[2 * (n % 2) + q][:, :], kd[0:SAMPLE, 2, h, :],
                                            spread[n % 2][:, 4 * q:4 * q + 4, :], start=True, stop=True)
                last.then_inc(*full.up())

        @block.vector
        def _(dve):
            for n, h in enumerate(order):
                dve.wait_ge(*full.at(n + 1))
                dve.wait_ge(*K.state_in[h % HELD].at(16 * (2 if n < HELD else 3)))
                for b in range(SEQS):
                    s = K.state[:, h % HELD, b, :]
                    last = nc.vector.scalar_tensor_tensor(
                        s, s, total[:, 4 + b, h:h + 1], K.ps[2 * (n % 2) + b // 4][:, b % 4 * 128:(b % 4 + 1) * 128],
                        ALU.mult, ALU.add)
                last.then_inc(*done.up())


def ab_finish(K, o):
    nc, I = K.nc, K.ins
    with contextlib.ExitStack() as tmp:
        gate = K.sb(tmp, "gate", [128, TILES, D])
        nw = K.sb(tmp, "nw", [128, 128])
        sq = K.sb(tmp, "sq", [128, D])
        mean = K.sb(tmp, "mean", [128, TILES, 8])
        ms = K.sb(tmp, "ms", [128, TILES, 8])
        with K.phase("loaded", "ln_std", "ln_var", "vector_step", "fin_silu") as (block, loaded, std, var, step, silu):
            @block.sync
            def _(sp):
                for t in range(TILES):
                    sp.dma_start(gate[0:ROWS[t], t, :], K.scratch["gate"][cols_of(t), :]).then_inc(*loaded.up(16))
                sp.dma_start(nw[:, :], row_broadcast(I["ab_norm_w"][0])).then_inc(*loaded.up(16))

            @block.scalar
            def _(act):
                act.wait_ge(*loaded.at(64))
                for t in range(TILES):
                    nc.scalar.activation(gate[0:ROWS[t], t, :], gate[0:ROWS[t], t, :], ACT.Silu).then_inc(*silu.up())
                for t in range(TILES):
                    act.wait_ge(*var.at(t + 1))
                    r = ROWS[t]
                    nc.scalar.activation(ms[0:r, t, 0:4], ms[0:r, t, 0:4], ACT.Sqrt, scale=1.0 / 128,
                                         bias=K.eps6[0:r, 0:1])
                    nc.scalar.activation(ms[0:r, t, 4:8], ms[0:r, t, 4:8], ACT.Sqrt, scale=1.0 / 128,
                                         bias=K.eps5[0:r, 0:1]).then_inc(*std.up())

            @block.vector
            def _(dve):
                link = chain(dve, step)
                dve.wait_ge(*loaded.at(64))
                for t in range(TILES):
                    r = ROWS[t]
                    ot = o[0:r, t, :, :]
                    link(nc.vector.tensor_reduce(mean[0:r, t, 4:8], ot[:, 4:8, :], AX, ALU.add))
                    link(nc.vector.tensor_scalar(mean[0:r, t, 4:8], mean[0:r, t, 4:8], 1.0 / 128, None, ALU.mult))
                    link(nc.vector.tensor_tensor(ot[:, 4:8, :], ot[:, 4:8, :], mean[0:r, t, 4:8].unsqueeze(2
                                                 ).broadcast_to([r, 4, 128]), ALU.subtract))
                    sqv = sq[0:r, :].rearrange("p (h n) -> p h n", h=8)
                    link(nc.vector.tensor_tensor(sqv, ot, ot, ALU.mult))
                    nc.vector.tensor_reduce(ms[0:r, t, :], sqv, AX, ALU.add).then_inc(*var.up())
                    dve.wait_ge(*var.at(t + 1))
                for t in range(TILES):
                    r = ROWS[t]
                    ot = o[0:r, t, :, :]
                    dve.wait_ge(*std.at(t + 1))
                    link(nc.vector.reciprocal(ms[0:r, t, :], ms[0:r, t, :]))
                    link(nc.vector.tensor_tensor(ot, ot, ms[0:r, t, :].unsqueeze(2).broadcast_to([r, 8, 128]),
                                                 ALU.mult))
                    link(nc.vector.tensor_tensor(ot[:, 0:4, :], ot[:, 0:4, :], nw[0:r, :].unsqueeze(1).broadcast_to(
                        [r, 4, 128]), ALU.mult))
                    dve.wait_ge(*silu.at(t + 1))
                    link(nc.vector.tensor_tensor(ot, ot, gate[0:r, t, :].rearrange("p (h n) -> p h n", h=8),
                                                 ALU.mult))
        outT = K.sb(tmp, "outT", [128, KT, TOK])
        transpose_phase(K, [([o[0:ROWS[t], t, 4 * q + j, :] for j in range(4)],
                             outT[:, 4 * q:4 * q + 4, cols_of(t)]) for t in range(TILES) for q in range(2)])
        add_and_norm_phase(K, K.first["ab_out"], outT, 0, 0)



def cross_attention(K, layer):
    K.caches_in = [[K.sem(f"{n}_in{i}") for i in range(CACHES)] for n in ("keys", "values")]
    for sig in K.caches_in[0] + K.caches_in[1]:
        sig.base = sig.sent
    with contextlib.ExitStack() as st:
        oT = K.sb(st, "oT", [128, KT, TOK])
        with contextlib.ExitStack() as tmp:
            qT = K.sb(tmp, "qT", [128, KT, WIDE])
            caches = [K.sb(tmp, n, [128, CACHES, 2, D]) for n in ("kc", "vc")]
            with contextlib.ExitStack() as own:
                kT = K.sb(own, "kT", [128, KT, MEM])
                k, v = K.sb(own, "k", [128, 2, D]), K.sb(own, "v", [128, 2, D])
                stored = K.sem("kv_stored")
                stored.base = stored.sent
                project_memory(K, layer, kT, k, v, stored)
                feature_major_phase(K, K.first[f"x_q{layer}"], 2, K.xT, TOK,
                                    lambda f, bank: [(qT[:, f, 0:TOK], bank[:, 0:TOK])])
                attend_prompt(K, layer, qT, kT, v, oT, caches, stored)
            attend_samples(K, layer, qT, oT, caches)
        add_and_norm_phase(K, K.first[f"x_o{layer}"], oT, layer, 1)


def project_memory(K, layer, kT, k, v, stored):
    nc, I, O = K.nc, K.ins, K.outs
    with contextlib.ExitStack() as t1:
        mem = K.sb(t1, "mem", [128, 2, D])
        memT = K.sb(t1, "memT", [128, KT, MEM])
        with K.phase("loaded") as (block, loaded):
            @block.scalar
            def _(act):
                act.dma_start(mem[:, :, :], I["mem_prompt"][0].rearrange("(t p) n -> p t n", p=128)
                              ).then_inc(*loaded.up(16))
                act.wait_ge(*loaded.at(16))
        transpose_phase(K, [([mem[:, t, (4 * q + j) * 128:(4 * q + j + 1) * 128] for j in range(4)],
                             memT[:, 4 * q:4 * q + 4, t * 128:(t + 1) * 128])
                            for t in range(2) for q in range(2)])
        tiles = [(0, 128), (128, 128)]
        token_major_phase(
            K, K.first[f"x_k{layer}"], 4, memT, tiles,
            lambda g, t: (k, v)[g // 2][:, t, g % 2 * 512:g % 2 * 512 + 512],
            stores=[(O[2][layer, 0].rearrange("(t p) h d -> p t (h d)", p=128), k[:, :, :]),
                    (O[3][layer, 0].rearrange("(t p) h d -> p t (h d)", p=128), v[:, :, :])], stored_later=stored)
        transpose_phase(K, [([k[:, t, (4 * q + j) * 128:(4 * q + j + 1) * 128] for j in range(4)],
                             kT[:, 4 * q:4 * q + 4, t * 128:(t + 1) * 128])
                            for t in range(2) for q in range(2)])


XSCALE = float(D // XH) ** -0.5


CACHES = 2


def load_cache(K, sp, layer, b, which, caches, sig):
    src = K.ins[("cache_mem_k", "cache_mem_v")[which]][layer, b]
    sp.dma_start(caches[which][:, b % CACHES, :, :], src.rearrange("(t p) h d -> p t (h d)", p=128)
                 ).then_inc(*sig[b % CACHES].up(16))


def attend_prompt(K, layer, qT, kT, v, oT, caches, stored):
    nc = K.nc
    with contextlib.ExitStack() as tmp:
        p = K.sb(tmp, "p", [128, 8, MEM])
        pT = K.sb(tmp, "pT", [128, 2, 8, 128])
        col = K.sb(tmp, "col", [128, 3, 8])
        pairs = [(h, t) for h in range(XH) for t in range(2)]
        with K.phase("sc_full", "max_done", "exp_done", "vector_step") as (block, full, maxed, exped, step):
            @block.sync
            def _(sp):
                for b in range(CACHES):
                    for which in range(2):
                        load_cache(K, sp, layer, b, which, caches, K.caches_in[which])

            @block.gpsimd
            def _(pool):
                nc.gpsimd.memset(qT[:, :, TOK:WIDE], 0.0)

            @block.tensor
            def _(pe):
                for n, (h, t) in enumerate(pairs):
                    for j in range(2):
                        last = nc.tensor.matmul(K.ps[n][:, 0:MEM],
                                                qT[:, 2 * h + j, t * 128:(t + 1) * 128], kT[:, 2 * h + j, :],
                                                start=(j == 0), stop=(j == 1))
                    last.then_inc(*full.up())

            @block.vector
            def _(dve):
                link = chain(dve, step)
                for n in range(8):
                    dve.wait_ge(*full.at(n + 1))
                    link(nc.vector.reduce_max(col[:, 0, n:n + 1], K.ps[n][:, 0:MEM], AX))
                    nc.vector.tensor_scalar(col[:, 1, n:n + 1], col[:, 0, n:n + 1], -XSCALE, None, ALU.mult
                                            ).then_inc(*maxed.up())
                dve.wait_ge(*exped.at(8))
                link(nc.vector.reciprocal(col[:, 2, :], col[:, 2, :]))
                nc.vector.tensor_tensor(p[:, :, :], p[:, :, :], col[:, 2, :].unsqueeze(2).broadcast_to([128, 8, MEM]),
                                        ALU.mult)

            @block.scalar
            def _(act):
                for n in range(8):
                    act.wait_ge(*maxed.at(n + 1))
                    nc.scalar.activation(p[:, n, :], K.ps[n][:, 0:MEM], ACT.Exp,
                                         scale=XSCALE, bias=col[:, 1, n:n + 1], accum_out=col[:, 2, n:n + 1]
                                         ).then_inc(*exped.up())
        transpose_phase(K, [([p[:, 4 * q + j, m * 128:(m + 1) * 128] for j in range(4)],
                             pT[:, m, 4 * q:4 * q + 4, :]) for m in range(2) for q in range(2)])
        with K.phase("mm_full", "mm_act") as (block, full, by_act):
            @block.sync
            def _(sp):
                sp.wait_ge(*stored.at(32))

            @block.tensor
            def _(pe):
                for f in range(KT):
                    if f >= 4:
                        pe.wait_ge(*by_act.at(f - 3))
                    h = f // 2
                    for m in range(2):
                        last = nc.tensor.matmul(K.ps[f % 4][:, 0:SEQ], v[:, m, f * 128:(f + 1) * 128],
                                                pT[:, m, 2 * h:2 * h + 2, :], start=(m == 0), stop=(m == 1))
                    last.then_inc(*full.up())

            @block.scalar
            def _(act):
                for f in range(KT):
                    act.wait_ge(*full.at(f + 1))
                    nc.scalar.copy(oT[:, f, 0:SEQ], K.ps[f % 4][:, 0:SEQ]).then_inc(*by_act.up())


def attend_samples(K, layer, qT, oT, caches):
    nc = K.nc
    kc, vc = caches
    with contextlib.ExitStack() as tmp:
        kcT = K.sb(tmp, "kcT", [128, 2, KT, MEM])
        p = K.sb(tmp, "p", [128, 2, MEM])
        pT = K.sb(tmp, "pT", [128, 2, 2, 128])
        o = K.sb(tmp, "o", [128, 2, 256])
        col = K.sb(tmp, "col", [128, SEQS, 4])
        kin, vin = K.caches_in
        with K.phase("kt_full", "kt_act", "kt_dve", "sc_full", "max_done", "exp_done", "p_done", "pt_full",
                     "pt_done", "o_full", "o_act", "ot_full", "o_done", "vector_step") as (
                block, ktf, kta, ktd, scf, maxed, exped, pd, ptf, ptd, of, oa, otf, od, step):
            def arrived(sig, b):
                s = sig[b % CACHES]
                return s.sem, s.base + 16 * (b // CACHES + 1)

            @block.sync
            def _(sp):
                for b in range(CACHES, SEQS + 2):
                    if b < SEQS:
                        sp.wait_ge(*ktf.at(4 * (b - CACHES + 1)))
                        load_cache(K, sp, layer, b, 0, caches, kin)
                    if b - 2 >= CACHES:
                        sp.wait_ge(*of.at(b - 2 - CACHES + 1))
                        load_cache(K, sp, layer, b - 2, 1, caches, vin)

            @block.tensor
            def _(pe):
                def turn_keys(b):
                    pe.wait_ge(*arrived(kin, b))
                    for n in range(4):
                        t, q = n // 2, n % 2
                        if b:
                            pe.wait_ge(*(kta if n % 2 == 0 else ktd).at(2 * (b - 1) + n // 2 + 1))
                        for j in range(4):
                            f = 4 * q + j
                            last = nc.tensor.transpose(K.ps[n][:, j * 128:(j + 1) * 128],
                                                       kc[:, b % CACHES, t, f * 128:(f + 1) * 128], K.const("ident"))
                        last.then_inc(*ktf.up())

                def scores(b):
                    pe.wait_ge(*kta.at(2 * (b + 1)))
                    pe.wait_ge(*ktd.at(2 * (b + 1)))
                    c = slice(SEQ + 8 * b, SEQ + 8 * b + 32)
                    if b:
                        pe.wait_ge(*exped.at(b))
                    for h in range(XH):
                        for j in range(2):
                            last = nc.tensor.matmul(K.ps[4][32 * h:32 * h + 32, 0:MEM], qT[:, 2 * h + j, c],
                                                    kcT[:, b % 2, 2 * h + j, :], start=(j == 0), stop=(j == 1))
                    last.then_inc(*scf.up())

                def turn_probabilities(b):
                    pe.wait_ge(*pd.at(b + 1))
                    if b:
                        pe.wait_ge(*ptd.at(b))
                    for m in range(2):
                        last = nc.tensor.transpose(K.ps[5][:, m * 128:(m + 1) * 128],
                                                   p[:, b % 2, m * 128:(m + 1) * 128], K.const("ident"))
                    last.then_inc(*ptf.up())

                def outputs(b):
                    pe.wait_ge(*ptd.at(b + 1))
                    pe.wait_ge(*arrived(vin, b))
                    if b:
                        pe.wait_ge(*oa.at(b))
                    for h in range(XH):
                        for m in range(2):
                            last = nc.tensor.matmul(K.ps[6][32 * h:32 * h + 32, 0:256],
                                                    pT[:, b % 2, m, 32 * h:32 * h + 32],
                                                    vc[:, b % CACHES, m, h * 256:(h + 1) * 256],
                                                    start=(m == 0), stop=(m == 1))
                    last.then_inc(*of.up())

                def turn_outputs(b):
                    pe.wait_ge(*oa.at(b + 1))
                    if b:
                        pe.wait_ge(*od.at(b))
                    for j in range(2):
                        last = nc.tensor.transpose(K.ps[7][:, j * 128:(j + 1) * 128],
                                                   o[:, b % 2, j * 128:(j + 1) * 128], K.const("ident"))
                    last.then_inc(*otf.up())

                turn_keys(0)
                for b in range(SEQS):
                    scores(b)
                    if b >= 2:
                        turn_outputs(b - 2)
                    if b + 1 < SEQS:
                        turn_keys(b + 1)
                    if b:
                        outputs(b - 1)
                    turn_probabilities(b)
                turn_outputs(SEQS - 2)
                outputs(SEQS - 1)
                turn_outputs(SEQS - 1)

            @block.scalar
            def _(act):
                def copy_keys(b):
                    if b >= 2:
                        act.wait_ge(*scf.at(b - 1))
                    for n in (0, 2):
                        act.wait_ge(*ktf.at(4 * b + n + 1))
                        nc.scalar.copy(kcT[:, b % 2, 0:4, n // 2 * 128:(n // 2 + 1) * 128],
                                       K.ps[n][:, :].rearrange("p (j n) -> p j n", j=4)).then_inc(*kta.up())

                def copy_outputs(b):
                    act.wait_ge(*of.at(b + 1))
                    if b >= 2:
                        act.wait_ge(*otf.at(b - 1))
                    nc.scalar.copy(o[:, b % 2, :], K.ps[6][:, 0:256]).then_inc(*oa.up())

                copy_keys(0)
                for b in range(SEQS):
                    act.wait_ge(*maxed.at(b + 1))
                    if b >= 2:
                        act.wait_ge(*ptf.at(b - 1))
                    nc.scalar.activation(p[:, b % 2, :], K.ps[4][:, 0:MEM], ACT.Exp, scale=XSCALE,
                                         bias=col[:, b, 1:2], accum_out=col[:, b, 2:3]).then_inc(*exped.up())
                    if b + 1 < SEQS:
                        copy_keys(b + 1)
                    if b:
                        copy_outputs(b - 1)
                    act.wait_ge(*ptf.at(b + 1))
                    if b >= 2:
                        act.wait_ge(*of.at(b - 1))
                    nc.scalar.copy(pT[:, b % 2, :, :], K.ps[5][:, 0:2 * 128].rearrange("p (m n) -> p m n", m=2)
                                   ).then_inc(*ptd.up())
                copy_outputs(SEQS - 1)

            @block.vector
            def _(dve):
                link = chain(dve, step)

                def copy_keys(b):
                    if b >= 2:
                        dve.wait_ge(*scf.at(b - 1))
                    for n in (1, 3):
                        dve.wait_ge(*ktf.at(4 * b + n + 1))
                        nc.vector.tensor_copy(kcT[:, b % 2, 4:8, n // 2 * 128:(n // 2 + 1) * 128],
                                              K.ps[n][:, :].rearrange("p (j n) -> p j n", j=4)).then_inc(*ktd.up())

                def copy_outputs(b):
                    dve.wait_ge(*otf.at(b + 1))
                    turned = K.ps[7][:, 0:256].rearrange("p (j h q) -> p h j q", j=2, h=XH)
                    nc.vector.tensor_copy(oT[:, :, SEQ + 8 * b:SEQ + 8 * b + 8].rearrange("p (h j) q -> p h j q", j=2),
                                          turned[:, :, :, 0:8]).then_inc(*od.up())

                copy_keys(0)
                for b in range(SEQS):
                    dve.wait_ge(*scf.at(b + 1))
                    link(nc.vector.reduce_max(col[:, b, 0:1], K.ps[4][:, 0:MEM], AX))
                    nc.vector.tensor_scalar(col[:, b, 1:2], col[:, b, 0:1], -XSCALE, None, ALU.mult
                                            ).then_inc(*maxed.up())
                    dve.wait_ge(*exped.at(b + 1))
                    link(nc.vector.reciprocal(col[:, b, 3:4], col[:, b, 2:3]))
                    nc.vector.tensor_scalar(p[:, b % 2, :], p[:, b % 2, :], col[:, b, 3:4], None, ALU.mult
                                            ).then_inc(*pd.up())
                    if b >= 2:
                        copy_outputs(b - 2)
                    if b + 1 < SEQS:
                        copy_keys(b + 1)
                copy_outputs(SEQS - 2)
                copy_outputs(SEQS - 1)



CAP = 64
PAIRS = EXPERTS // 2


def moe(K, layer):
    with contextlib.ExitStack() as st:
        R = {"slot": K.sb(st, "slot", [128, TILES, 2]), "rows": K.sb(st, "rows", [128, 4, TOK]),
             "over": K.sb(st, "over", [1, 1], I32),
             "lnw": K.sb(st, "lnw", [128, D]), "lnb": K.sb(st, "lnb", [128, D])}
        with contextlib.ExitStack() as tmp:
            route(K, tmp, layer, R)
        with contextlib.ExitStack() as tmp:
            experts(K, tmp, layer, R)
        moe_norm(K, layer, R)


def route(K, tmp, layer, R):
    nc, I = K.nc, K.ins
    T = TILES
    w = K.sb(tmp, "w", [128, KT, 36])
    bias = K.sb(tmp, "bias", [128, 36])
    lg = K.sb(tmp, "lg", [128, T, 36])
    a = K.sb(tmp, "a", [128, T, 4])
    e8, o1, o2 = (K.sb(tmp, n, [128, T, 8]) for n in ("e8", "o1", "o2"))
    og = K.sb(tmp, "og", [128, T, 4])
    m = K.sb(tmp, "m", [128, 8, T])
    prod = K.sb(tmp, "prod", [128, T, 32])
    sel = [K.sb(tmp, "sel", [128, T, 32]) for _ in range(3)]
    gates = K.sb(tmp, "gates", [128, T, 32])
    cols = K.sb(tmp, "cols", [128, T, 4])
    gT = K.sb(tmp, "gT", [EXPERTS, TOK])
    cT = K.sb(tmp, "cT", [4, TOK])
    shape = lambda n: [128, T, n]
    by_group = lambda x: x.rearrange("p t (g e) -> p t g e", g=GROUPS)
    with K.phase("loaded", "ab_full", "r_exp", "vector_step", "r_sub", "r_sel", "r_pos", "r_cols", "r_rows", "r_copied",
                 "stored", "r_back") as (
            block, loaded, full, exped, step, sub, seld, pos, colsd, rowsd, copied, out, back):
        @block.sync
        def _(sp):
            sp.dma_start(w[:, :, 0:4], I["moe_w_grp"][layer].rearrange("(k p) n -> p k n", p=128)
                         ).then_inc(*loaded.up(16))
            for g in range(GROUPS):
                sp.dma_start(w[:, :, 4 + 8 * g:12 + 8 * g], I["moe_w_exp"][layer, g].rearrange(
                    "(k p) n -> p k n", p=128)).then_inc(*loaded.up(16))
            sp.dma_start(bias[:, 0:4], row_broadcast(I["moe_b_grp"][layer])).then_inc(*loaded.up(16))
            sp.dma_start(bias[:, 4:36], row_broadcast(I["moe_b_exp"][layer].rearrange("g e -> (g e)"))
                         ).then_inc(*loaded.up(16))
            for i, n in enumerate(("ln_w", "ln_b")):
                sp.dma_start(R["lnw" if i == 0 else "lnb"][:, :], row_broadcast(I[n][layer, 2])).then_inc(*back.up(16))
            for n in MOE_SIGNALS:
                sp.sem_clear(K.sem(n).sem)
            sp.wait_ge(*copied.at(1))
            sp.dma_start(K.scratch["gates"], gT[:, :]).then_inc(*out.up(16))
            sp.dma_start(K.scratch["cols"], cT[:, :]).then_inc(*out.up(16))
            sp.wait_ge(*out.at(32))
            for i in range(4):
                sp.dma_start(R["rows"][:, i, :], row_broadcast(K.scratch["cols"][i])).then_inc(*back.up(16))
            sp.wait_ge(*back.at(96))

        @block.tensor
        def _(pe):
            pe.wait_ge(*loaded.at(16 * 7))
            for t in range(T):
                for k in range(KT):
                    last = nc.tensor.matmul(K.ps[0][0:ROWS[t], 36 * t:36 * t + 36], K.xT[:, k, cols_of(t)], w[:, k, :],
                                            start=(k == 0), stop=(k == KT - 1))
            last.then_inc(*full.up())
            pe.wait_ge(*seld.at(1))
            for t in range(T + 1):
                rows = ROWS[t] if t < T else 128
                for s in range(min(t + 1, T)):
                    r = slice(0, ROWS[s])
                    last = nc.tensor.matmul(K.ps[1][0:rows, 32 * t:32 * t + 32],
                                            K.const("upto_all" if s == t else "ones")[r, 0:rows], sel[2][r, s, :],
                                            start=(s == 0), stop=(s == min(t, T - 1)))
            last.then_inc(*pos.up())
            pe.wait_ge(*colsd.at(1))
            for t in range(T):
                r = ROWS[t]
                nc.tensor.transpose(K.ps[2][0:EXPERTS, cols_of(t)], gates[0:r, t, :], K.const("ident")[0:r, 0:r])
                last = nc.tensor.transpose(K.ps[3][0:4, cols_of(t)], cols[0:r, t, :], K.const("ident")[0:r, 0:r])
            last.then_inc(*rowsd.up())

        @block.scalar
        def _(act):
            act.wait_ge(*sub.at(1))
            nc.scalar.activation(a[:, :, :], a[:, :, :], ACT.Exp)
            nc.scalar.activation(m[:, 5, :], m[:, 4, :], ACT.Exp).then_inc(*exped.up())

        @block.vector
        def _(dve):
            link = chain(dve, step)
            tt = nc.vector.tensor_tensor

            def wide(col, n):
                return m[:, col, :].unsqueeze(2).broadcast_to(shape(n))

            def first(val, mx, eq, n):
                descend = K.const("descend")[:, 0:n].unsqueeze(1).broadcast_to(shape(n))
                link(nc.vector.reduce_max(m[:, mx, :], val, AX))
                link(tt(eq, val, wide(mx, n), ALU.is_equal))
                link(tt(eq, eq, descend, ALU.mult))
                link(nc.vector.reduce_max(m[:, 0, :], eq, AX))
                link(tt(eq, descend, wide(0, n), ALU.is_equal))

            link(nc.vector.memset(lg[:, :, :], 0.0))
            dve.wait_ge(*loaded.at(16 * 7))
            dve.wait_ge(*full.at(1))
            for t in range(T):
                r = ROWS[t]
                last = tt(lg[0:r, t, :], K.ps[0][0:r, 36 * t:36 * t + 36], bias[0:r, :], ALU.add)
            link(last)
            first(lg[:, :, 0:4], 1, og[:, :, :], 4)
            tt(a[:, :, :], lg[:, :, 0:4], wide(1, 4), ALU.subtract)
            link(tt(by_group(prod[:, :, :]), by_group(lg[:, :, 4:36]),
                    og[:, :, :].unsqueeze(3).broadcast_to([128, T, 4, 8]), ALU.mult))
            link(tt(prod[:, :, 0:16], prod[:, :, 0:16], prod[:, :, 16:32], ALU.add))
            link(tt(e8[:, :, :], prod[:, :, 0:8], prod[:, :, 8:16], ALU.add))
            first(e8[:, :, :], 2, o1[:, :, :], 8)
            link(nc.vector.scalar_tensor_tensor(e8[:, :, :], o1[:, :, :], -1e30, e8[:, :, :], ALU.mult, ALU.add))
            first(e8[:, :, :], 3, o2[:, :, :], 8)
            tt(m[:, 4, :], m[:, 3, :], m[:, 2, :], ALU.subtract).then_inc(*sub.up())
            for i, o in enumerate((o1, o2)):
                last = tt(by_group(sel[i][:, :, :]), og[:, :, :].unsqueeze(3).broadcast_to([128, T, 4, 8]),
                          o[:, :, :].unsqueeze(2).broadcast_to([128, T, 4, 8]), ALU.mult)
            link(last)
            tt(sel[2][:, :, :], sel[0][:, :, :], sel[1][:, :, :], ALU.add).then_inc(*seld.up())
            dve.wait_ge(*exped.at(1))
            link(nc.vector.tensor_reduce(m[:, 6, :], a[:, :, :], AX, ALU.add))
            link(nc.vector.scalar_tensor_tensor(m[:, 6, :], m[:, 5, :], 1.0, m[:, 6, :], ALU.add, ALU.mult))
            link(nc.vector.reciprocal(cols[:, :, 2], m[:, 6, :]))
            link(tt(cols[:, :, 3], cols[:, :, 2], m[:, 5, :], ALU.mult))
            for i in range(2):
                last = tt((gates, prod)[i][:, :, :], sel[i][:, :, :],
                          cols[:, :, 2 + i:3 + i].broadcast_to(shape(32)), ALU.mult)
            link(last)
            link(tt(gates[:, :, :], gates[:, :, :], prod[:, :, :], ALU.add))
            dve.wait_ge(*pos.at(1))
            link(nc.vector.memset(prod[:, :, :], 0.0))
            for t in range(T):
                r = ROWS[t]
                last = tt(prod[0:r, t, :], K.ps[1][0:r, 32 * t:32 * t + 32], K.const("slot_base")[0:r, :], ALU.add)
            nc.vector.reduce_max(m[:, 7, 0:1], K.ps[1][:, 96:128], AX)
            link(last)
            for i in range(2):
                last = tt(sel[i][:, :, :], sel[i][:, :, :], prod[:, :, :], ALU.mult)
            link(last)
            for i in range(2):
                last = nc.vector.tensor_reduce(cols[:, :, i], sel[i][:, :, :], AX, ALU.add)
            link(last)
            nc.vector.tensor_scalar(R["over"][:, :], m[0:1, 7, 0:1], CAP + 0.5, None, ALU.is_gt)
            nc.vector.tensor_copy(R["slot"][:, :, :], cols[:, :, 0:2]).then_inc(*colsd.up())
            dve.wait_ge(*rowsd.at(1))
            nc.vector.tensor_copy(gT[:, :], K.ps[2][0:EXPERTS, 0:TOK])
            nc.vector.tensor_copy(cT[:, :], K.ps[3][0:4, 0:TOK]).then_inc(*copied.up())


def total_bank(K, t, half):
    return K.ps[2 * t + half][:, :] if t < 2 else K.ps[4][64 * half:64 * half + 64, :]


MOE_SIGNALS = ["e_sel", "e_sel_step", "e_gather_full", "e_gather_act", "e_gather_dve", "e_silu", "e_hidden",
               "e_turned", "e_ht", "e_y_act", "e_y_dve", "e_spread", "e_spread_step", "e_sum", "a_zeroed", "a_gate_in0", "a_gate_in1",
               "a_h_full", "a_silu", "a_h_read", "a_hidden", "a_y_full"]


class Experts:
    pass


def experts(K, tmp, layer, R):
    I = K.ins
    E = Experts()
    E.R = R
    E.first = K.first[f"moe{layer}"]
    E.slot = [(E.first + j) % RING for j in range(RING)]
    E.base = [K.arrival[E.first + j] for j in range(RING)]
    E.raised = [16 * len(K.chunks[E.first + j]) for j in range(RING)]
    w1 = I["moe_w1"][layer].rearrange("g e d f -> (g e) d f")
    w3 = I["moe_w3"][layer].rearrange("g e d f -> (g e) d f")
    w2 = I["moe_w2"][layer].rearrange("g e f d -> (g e) f d")
    E.up = [K.ring[:, E.slot[2 * j], :].rearrange("p (k i f) -> p k i f", k=KT, i=2) for j in range(2)]
    E.down = [K.ring[:, E.slot[2 * j + 1], 0:2 * D].rearrange("p (k n) -> p k n", k=2) for j in range(2)]
    E.sel = K.sb(tmp, "sel", [128, TILES, 128])
    E.xg = K.sb(tmp, "xg", [128, KT, 128])
    E.hs = K.sb(tmp, "hs", [128, FF])
    E.h = K.sb(tmp, "h", [128, FF])
    E.hT = K.sb(tmp, "hT", [128, 2, 128])
    E.y = K.sb(tmp, "y", [128, D])
    E.spread = K.sb(tmp, "spread", [128, 3, TOK])
    E.index = K.sb(tmp, "index", [128, 1])
    E.zero = K.sb(tmp, "zero", [128, 512])
    E.gate = K.sb(tmp, "gate", [128, 2, TOK])
    E.hs_all = K.sb(tmp, "hs_all", [128, 2, TOK])
    E.hT_all = K.sb(tmp, "hT_all", [128, 2, TOK])
    with K.phase("up_read", "down_read", *MOE_SIGNALS) as (block, up_read, down_read, *own):
        E.sig = dict(zip(MOE_SIGNALS, (s.sem for s in own)))
        E.up_read, E.down_read = up_read, down_read

        @block.sync
        def _(sp):
            with sp.Fori(0, PAIRS - 1) as it:
                for j in range(2):
                    sp.wait_ge(up_read.sem, it * 2 + (up_read.base + j + 1))
                    for i, w in enumerate((w1, w3)):
                        sp.dma_start(E.up[j][:, :, i, :], w[it * 2 + (2 + j)].rearrange("(k p) f -> p k f", p=128)
                                     ).then_inc(K.arrived[E.slot[2 * j]], 16)
                for j in range(2):
                    sp.wait_ge(down_read.sem, it * 2 + (down_read.base + j + 1))
                    sp.dma_start(E.down[j], w2[it * 2 + (2 + j)].rearrange("(k p) n -> p k n", p=128)
                                 ).then_inc(K.arrived[E.slot[2 * j + 1]], 16)
            for j in range(2):
                sp.wait_ge(*up_read.at(EXPERTS - 1 + j))
                load_chunk(K, sp, E.first + 2 * EXPERTS + 2 * j)
            for j in range(2):
                sp.wait_ge(*down_read.at(EXPERTS - 1 + j))
                load_chunk(K, sp, E.first + 2 * EXPERTS + 2 * j + 1)

        @block.tensor
        def _(pe):
            over = pe.value_load(R["over"][0:1, 0:1], min_val=0, max_val=1)
            with pe.If(over < 1):
                few_tensor(K, E, pe)
            with pe.Else():
                all_tensor(K, E, pe)

        @block.scalar
        def _(act):
            over = act.value_load(R["over"][0:1, 0:1], min_val=0, max_val=1)
            with act.If(over < 1):
                few_scalar(K, E, act)
            with act.Else():
                all_scalar(K, E, act)

        @block.vector
        def _(dve):
            over = dve.value_load(R["over"][0:1, 0:1], min_val=0, max_val=1)
            with dve.If(over < 1):
                few_vector(K, E, dve)
            with dve.Else():
                all_vector(K, E, dve)

        up_read.sent += EXPERTS
        down_read.sent += EXPERTS


def up_arrived(K, E, pe, pair, j):
    pe.wait_ge(K.arrived[E.slot[2 * j]], pair * E.raised[2 * j] + E.base[2 * j])


def down_arrived(K, E, pe, pair, j):
    pe.wait_ge(K.arrived[E.slot[2 * j + 1]], pair * E.raised[2 * j + 1] + E.base[2 * j + 1])



def few_tensor(K, E, pe):
    nc, sig = K.nc, E.sig

    def gather(p):
        pe.wait_ge(sig["e_sel"], p + 1)
        for q in range(2):
            for j in range(4):
                f = 4 * q + j
                for t in range(TILES):
                    r = slice(0, ROWS[t])
                    last = nc.tensor.matmul(K.ps[6 + q][:, j * 128:(j + 1) * 128], K.x[r, t, f * 128:(f + 1) * 128],
                                            E.sel[r, t, :], start=(t == 0), stop=(t == TILES - 1))
            last.then_inc(sig["e_gather_full"], 1)

    def hidden(p):
        pe.wait_ge(sig["e_gather_act"], p + 1)
        pe.wait_ge(sig["e_gather_dve"], p + 1)
        for j in range(2):
            up_arrived(K, E, pe, p, j)
            for k in range(KT):
                last = nc.tensor.matmul(K.ps[5][CAP * j:CAP * (j + 1), :], E.xg[:, k, CAP * j:CAP * (j + 1)],
                                        E.up[j][:, k, :, :], start=(k == 0), stop=(k == KT - 1))
            last.then_inc(E.up_read.sem, 1)

    def turn(p):
        pe.wait_ge(sig["e_hidden"], p + 1)
        for f in range(2):
            last = nc.tensor.transpose(K.ps[5][:, f * 128:(f + 1) * 128], E.h[:, f * 128:(f + 1) * 128],
                                       K.const("ident"))
        last.then_inc(sig["e_turned"], 1)

    def add(p, start, stop):
        pe.wait_ge(sig["e_y_act"], p + 1)
        pe.wait_ge(sig["e_y_dve"], p + 1)
        pe.wait_ge(sig["e_spread"], p + 1)
        for t in range(TILES):
            for half in range(2):
                last = nc.tensor.matmul(total_bank(K, t, half), E.spread[:, 0, cols_of(t)],
                                        E.y[:, 512 * half:512 * half + 512], start=start, stop=stop,
                                        skip_group_check=True)
        last.then_inc(sig["e_sum"], 1)

    def output(p):
        pe.wait_ge(sig["e_ht"], p + 1)
        for j in range(2):
            down_arrived(K, E, pe, p, j)
            for half in range(2):
                for f in range(2):
                    last = nc.tensor.matmul(K.ps[6 + half][CAP * j:CAP * (j + 1), :], E.hT[:, f, CAP * j:CAP * (j + 1)],
                                            E.down[j][:, f, 512 * half:512 * half + 512],
                                            start=(f == 0), stop=(f == 1))
            last.then_inc(E.down_read.sem, 1)

    def copied(p):
        pe.wait_ge(sig["e_gather_act"], p + 1)
        pe.wait_ge(sig["e_gather_dve"], p + 1)

    def stored(p):
        pe.wait_ge(sig["e_y_act"], p + 1)
        pe.wait_ge(sig["e_y_dve"], p + 1)

    gather(0)
    hidden(0)
    gather(1)
    turn(0)
    copied(1)
    output(0)
    hidden(1)
    stored(0)
    gather(2)
    turn(1)
    add(0, True, False)
    copied(2)
    output(1)
    with pe.Fori(2, PAIRS - 1) as p:
        hidden(p)
        stored(p - 1)
        gather(p + 1)
        turn(p)
        add(p - 1, False, False)
        copied(p + 1)
        output(p)
    hidden(PAIRS - 1)
    turn(PAIRS - 1)
    add(PAIRS - 2, False, False)
    output(PAIRS - 1)
    add(PAIRS - 1, False, True)


def few_scalar(K, E, act):
    nc, sig = K.nc, E.sig

    def columns(p):
        act.wait_ge(sig["e_gather_full"], p * 2 + 1)
        nc.scalar.copy(E.xg[:, 0:4, :], K.ps[6][:, :].rearrange("p (f s) -> p f s", f=4)
                       ).then_inc(sig["e_gather_act"], 1)

    def silu(p):
        act.wait_ge(E.up_read.sem, p * 2 + (E.up_read.base + 2))
        nc.scalar.activation(E.hs[:, :], K.ps[5][:, 0:FF], ACT.Silu).then_inc(sig["e_silu"], 1)

    def turned(p):
        act.wait_ge(sig["e_turned"], p + 1)
        nc.scalar.copy(E.hT[:, :, :], K.ps[5][:, 0:FF].rearrange("p (f s) -> p f s", f=2)).then_inc(sig["e_ht"], 1)

    def rows(p):
        act.wait_ge(E.down_read.sem, p * 2 + (E.down_read.base + 2))
        nc.scalar.copy(E.y[:, 0:512], K.ps[6][:, :]).then_inc(sig["e_y_act"], 1)

    columns(0)
    silu(0)
    columns(1)
    turned(0)
    rows(0)
    with act.Fori(1, PAIRS - 1) as p:
        act.wait_ge(sig["e_hidden"], p)
        silu(p)
        columns(p + 1)
        turned(p)
        act.wait_ge(sig["e_sum"], p)
        rows(p)
    act.wait_ge(sig["e_hidden"], PAIRS - 1)
    silu(PAIRS - 1)
    turned(PAIRS - 1)
    act.wait_ge(sig["e_sum"], PAIRS - 1)
    rows(PAIRS - 1)


def few_vector(K, E, dve):
    nc, sig, R = K.nc, E.sig, E.R
    v = nc.vector

    def select(p):
        slots = K.const("slots")
        for t in range(TILES):
            r = slice(0, ROWS[t])
            last = v.tensor_scalar(E.sel[r, t, :], slots[r, :], R["slot"][r, t, 0:1], None, ALU.is_equal)
        last.then_inc(sig["e_sel_step"], 1)
        dve.wait_ge(sig["e_sel_step"], p * 2 + 1)
        for t in range(TILES):
            r = slice(0, ROWS[t])
            last = v.scalar_tensor_tensor(E.sel[r, t, :], slots[r, :], R["slot"][r, t, 1:2], E.sel[r, t, :],
                                          ALU.is_equal, ALU.add)
        last.then_inc(sig["e_sel"], 1)
        dve.wait_ge(sig["e_sel"], p + 1)
        v.tensor_scalar(R["slot"][:, :, :], R["slot"][:, :, :], -128.0, None, ALU.add).then_inc(sig["e_sel_step"], 1)
        dve.wait_ge(sig["e_sel_step"], p * 2 + 2)

    def columns(p):
        dve.wait_ge(sig["e_gather_full"], p * 2 + 2)
        v.tensor_copy(E.xg[:, 4:8, :], K.ps[7][:, :].rearrange("p (f s) -> p f s", f=4)
                      ).then_inc(sig["e_gather_dve"], 1)

    def product(p):
        dve.wait_ge(sig["e_silu"], p + 1)
        v.tensor_tensor(E.h[:, :], E.hs[:, :], K.ps[5][:, FF:2 * FF], ALU.mult).then_inc(sig["e_hidden"], 1)

    def spread(p, wait):
        for i in range(2):
            last = v.scalar_tensor_tensor(E.spread[:, 1 + i, :], R["rows"][:, i, :], E.index[:, 0:1],
                                          R["rows"][:, 2 + i, :], ALU.is_equal, ALU.mult)
        last.then_inc(sig["e_spread_step"], 1)
        dve.wait_ge(sig["e_spread_step"], p * 2 + 2)
        if wait:
            dve.wait_ge(sig["e_sum"], p)
        v.tensor_tensor(E.spread[:, 0, :], E.spread[:, 1, :], E.spread[:, 2, :], ALU.add).then_inc(sig["e_spread"], 1)
        v.tensor_scalar(E.index[:, :], E.index[:, :], 128.0, None, ALU.add).then_inc(sig["e_spread_step"], 1)
        dve.wait_ge(sig["e_spread_step"], p * 2 + 3)

    def rows(p):
        dve.wait_ge(E.down_read.sem, p * 2 + (E.down_read.base + 2))
        v.tensor_copy(E.y[:, 512:1024], K.ps[7][:, :]).then_inc(sig["e_y_dve"], 1)

    v.tensor_copy(E.index[:, :], K.const("row")).then_inc(sig["e_spread_step"], 1)
    dve.wait_ge(sig["e_spread_step"], 1)
    select(0)
    columns(0)
    select(1)
    product(0)
    columns(1)
    spread(0, False)
    rows(0)
    with dve.Fori(1, PAIRS - 1) as p:
        select(p + 1)
        product(p)
        columns(p + 1)
        spread(p, True)
        rows(p)
    product(PAIRS - 1)
    spread(PAIRS - 1, True)
    rows(PAIRS - 1)



def all_tensor(K, E, pe):
    nc, sig = K.nc, E.sig
    zero = E.zero
    pe.sem_inc(sig["a_y_full"], 1)
    pe.wait_ge(sig["a_zeroed"], 1)
    for t in range(TILES):
        for half in range(2):
            nc.tensor.matmul(total_bank(K, t, half), zero[:, 0:ROWS[t]], zero[:, :], start=True, stop=False,
                             skip_group_check=True)
    with pe.Fori(0, PAIRS) as it:
        for j in range(2):
            up_arrived(K, E, pe, it, j)
            for f in range(2):
                pe.wait_ge(sig["a_h_read"], it * 4 + (1 + 2 * j + f))
                for i in range(2):
                    for k in range(KT):
                        last = nc.tensor.matmul(K.ps[6 + i][:, 0:TOK], E.up[j][:, k, i, f * 128:(f + 1) * 128],
                                                K.xT[:, k, 0:TOK], start=(k == 0), stop=(k == KT - 1))
                last.then_inc(sig["a_h_full"], 1)
            pe.wait_ge(sig["a_h_full"], it * 4 + (2 * j + 2))
            pe.sem_inc(E.up_read.sem, 1)
            down_arrived(K, E, pe, it, j)
            pe.wait_ge(sig["a_hidden"], it * 4 + (1 + 2 * j + 2))
            for t in range(TILES):
                for half in range(2):
                    for f in range(2):
                        last = nc.tensor.matmul(total_bank(K, t, half), E.hT_all[:, f, cols_of(t)],
                                                E.down[j][:, f, 512 * half:512 * half + 512],
                                                start=False, stop=False, skip_group_check=True)
            last.then_inc(sig["a_y_full"], 1)
            pe.wait_ge(sig["a_y_full"], it * 2 + (1 + j + 1))
            pe.sem_inc(E.down_read.sem, 1)
    for t in range(TILES):
        for half in range(2):
            nc.tensor.matmul(total_bank(K, t, half), zero[:, 0:ROWS[t]], zero[:, :], start=False, stop=True,
                             skip_group_check=True)


def all_scalar(K, E, act):
    nc, sig = K.nc, E.sig
    with act.Fori(0, PAIRS) as it:
        for j in range(2):
            act.wait_ge(sig["a_hidden"], it * 4 + (1 + 2 * j))
            act.dma_start(E.gate[:, j, :], K.scratch["gates"][bass.ds(it * 2 + j, 1), :].broadcast_to([128, TOK])
                          ).then_inc(sig[f"a_gate_in{j}"], 16)
            for f in range(2):
                act.wait_ge(sig["a_h_full"], it * 4 + (2 * j + f + 1))
                nc.scalar.activation(E.hs_all[:, f, :], K.ps[6][:, 0:TOK], ACT.Silu).then_inc(sig["a_silu"], 1)


def all_vector(K, E, dve):
    nc, sig = K.nc, E.sig
    nc.vector.memset(E.zero[:, :], 0.0).then_inc(sig["a_zeroed"], 1)
    dve.sem_inc(sig["a_h_read"], 1)
    dve.sem_inc(sig["a_hidden"], 1)
    with dve.Fori(0, PAIRS) as it:
        for j in range(2):
            dve.wait_ge(sig[f"a_gate_in{j}"], it * 16 + 16)
            dve.wait_ge(sig["a_y_full"], it * 2 + (1 + j))
            for f in range(2):
                dve.wait_ge(sig["a_silu"], it * 4 + (2 * j + f + 1))
                nc.vector.tensor_tensor(E.hT_all[:, f, :], E.hs_all[:, f, :], K.ps[7][:, 0:TOK], ALU.mult
                                        ).then_inc(sig["a_h_read"], 1)
                dve.wait_ge(sig["a_h_read"], it * 4 + (1 + 2 * j + f + 1))
                nc.vector.tensor_tensor(E.hT_all[:, f, :], E.hT_all[:, f, :], E.gate[:, j, :], ALU.mult
                                        ).then_inc(sig["a_hidden"], 1)


def moe_norm(K, layer, R):
    nc = K.nc
    with contextlib.ExitStack() as tmp:
        stats, mv = K.sb(tmp, "stats", [128, 2, 6]), K.sb(tmp, "mv", [128, TILES, 4])
        late = K.sb(tmp, "late", [SAMPLE, 512])
        banks = [5, 6, 7]
        with K.phase("ln_var", "ln_std", "vector_step", "late_copied", "normed", "tr_full", "tr_act", "stored") as (
                block, var, std, step, copied, normed, turned, in_xT, stored):
            if layer == 0:
                @block.tensor
                def _(pe):
                    for t in range(TILES):
                        turn_tile(K, pe, t, banks, normed, turned, in_xT)
            else:
                @block.sync
                def _(sp):
                    for t in range(TILES):
                        sp.wait_ge(*normed.at(t + 1))
                        dst = (K.outs[0][0, t * 128:(t + 1) * 128, :] if t < 2 else
                               K.outs[1].rearrange("b s d -> (b s) d"))
                        sp.dma_start(dst, K.x[0:ROWS[t], t, :]).then_inc(*stored.up(16))
                    sp.wait_ge(*stored.at(16 * TILES))

            @block.scalar
            def _(act):
                nc.scalar.copy(late[:, :], total_bank(K, 2, 1)).then_inc(*copied.up())
                for t in range(TILES):
                    act.wait_ge(*var.at(t + 1))
                    nc.scalar.activation(mv[0:ROWS[t], t, 2:3], mv[0:ROWS[t], t, 1:2], ACT.Sqrt).then_inc(*std.up())
                    if layer == 0 and t:
                        copy_turned(K, act, t - 1, banks, turned, in_xT)
                if layer == 0:
                    copy_turned(K, act, TILES - 1, banks, turned, in_xT)

            @block.vector
            def _(dve):
                link = chain(dve, step)
                for t in range(TILES):
                    if t == 2:
                        dve.wait_ge(*copied.at(1))
                    for g in range(2):
                        xs = K.x[0:ROWS[t], t, g * 512:(g + 1) * 512]
                        src = late[:, :] if t == 2 and g else total_bank(K, t, g)
                        last = nc.vector.scalar_tensor_tensor(xs, xs, ALPHA, src, ALU.mult, ALU.add)
                    link(last)
                    norm_tile(K, dve, link, std, var, normed, t, ROWS[t], stats, mv, R["lnw"], R["lnb"])



C_HEADS = 16


def rwkv_mixer(K):
    nc, I, O = K.nc, K.ins, K.outs
    rwkv_project(K)
    with contextlib.ExitStack() as st:
        yT = K.sb(st, "yT", [128, KT, TOK])
        prompt = contextlib.ExitStack()
        H = K.sb(prompt, "H", [128, KT, 128])
        wide = {n: K.sb(prompt, "wide_" + n, [128, 2, 8, 128]) for n in ("cut", "R")}
        with K.phase() as (block,):
            @block.gpsimd
            def _(pool):
                nc.gpsimd.memset(wide["cut"][0:64, :, :, 64:128], 0.0)
                nc.gpsimd.memset(wide["cut"][64:128, :, :, 0:64], 0.0)

            @block.vector
            def _(dve):
                nc.vector.memset(wide["R"][0:64, :, :, 64:128], 0.0)
                nc.vector.memset(wide["R"][64:128, :, :, 0:64], 0.0)
        for t in range(TILES):
            if t == 2:
                prompt.close()
                wide = {"R": K.sb(st, "R", [SAMPLE, 2, 8, 64])}
            with contextlib.ExitStack() as tt:
                rwkv_tile(K, tt, t, H, yT, wide)
        add_and_norm_phase(K, K.first["c_out"], yT, 1, 0)


def rwkv_project(K):
    nc, I, O = K.nc, K.ins, K.outs
    tiles = [(AT[t], ROWS[t]) for t in range(TILES)]
    with contextlib.ExitStack() as st:
        shift = K.sb(st, "shift", [SEQS, D])
        cols = K.sb(st, "cols", [48, 128])
        shT = K.sb(st, "shT", [128, KT, SEQS])
        mu = K.sb(st, "mu", [128, 6, KT])
        xx = K.sb(st, "xx", [128, KT, TOK])
        mixes = K.sb(st, "mix", [128, 2, KT, TOK])
        outs = K.sb(st, "out", [128, 2, TILES, D])
        hT = K.sb(st, "hT", [128, TOK])
        l1 = {"w": K.sb(st, "w1", [128, KT, 64]), "a": K.sb(st, "a1", [128, KT, 64]),
              "g": K.sb(st, "g1", [128, KT, 128])}
        l2 = {"w": K.sb(st, "w2", [64, D]), "a": K.sb(st, "a2", [64, D]), "g": K.sb(st, "g2", [128, D])}
        row = {"w": K.sb(st, "w0", [128, D]), "a": K.sb(st, "a0", [128, D])}
        later, shifted = K.sem("small_in"), K.sem("shift_stored")
        later.base, shifted.base = later.sent, shifted.sent
        with K.phase("loaded") as (block, loaded):
            @block.sync
            def _(sp):
                sp.dma_start(shift[:, :], I["state_shift_c"][0]).then_inc(*loaded.up(16))
                sp.dma_start(cols[:, :], I["c_mu"][0].rearrange("i (k p) -> (i k) p", p=128)).then_inc(*loaded.up(16))
                for n in "wag":
                    sp.dma_start(l1[n][:, :, :], I[f"c_w_{n}1"][0].rearrange("(k p) n -> p k n", p=128)
                                 ).then_inc(*later.up(16))
                    sp.dma_start(l2[n][:, :], I[f"c_w_{n}2"][0]).then_inc(*later.up(16))
                sp.dma_start(row["w"][:, :], row_broadcast(I["c_w0"][0])).then_inc(*later.up(16))
                sp.dma_start(row["a"][:, :], row_broadcast(I["c_a0"][0])).then_inc(*later.up(16))
                sp.dma_start(O[7][0], K.x[127:128, 1, :]).then_inc(*shifted.up(16))
                for b in range(SEQS):
                    sp.dma_start(O[12][0, b:b + 1], K.x[8 * b + 7:8 * b + 8, 2, :]).then_inc(*shifted.up(16))
                sp.wait_ge(*loaded.at(32))
        transpose_phase(K, [([shift[:, (4 * q + j) * 128:(4 * q + j + 1) * 128] for j in range(4)],
                             shT[:, 4 * q:4 * q + 4, :]) for q in range(2)]
                        + [([cols[:, :]], mu[:, :, :].rearrange("p i k -> p (i k)").unsqueeze(1))])
        with K.phase("z_done") as (block, done):
            @block.vector
            def _(dve):
                x = K.xT
                nc.vector.tensor_tensor(xx[:, :, 1:SEQ], x[:, :, 0:SEQ - 1], x[:, :, 1:SEQ], ALU.subtract)
                nc.vector.tensor_scalar(xx[:, :, 0:1], x[:, :, 0:1], -1.0, None, ALU.mult)
                xs = x[:, :, SEQ:TOK].rearrange("p k (b s) -> p k b s", b=SEQS)
                ds = xx[:, :, SEQ:TOK].rearrange("p k (b s) -> p k b s", b=SEQS)
                for k in range(KT):
                    nc.vector.tensor_tensor(ds[:, k, :, 1:8], xs[:, k, :, 0:7], xs[:, k, :, 1:8], ALU.subtract)
                nc.vector.tensor_tensor(ds[:, :, :, 0], shT[:, :, :], xs[:, :, :, 0], ALU.subtract)

        order = ((0, "r"), (2, "k"), (3, "v"), (1, "w"), (4, "a"), (5, "g"))
        kept = [K.sem(f"mix_stored{j}") for j in range(2)]
        for sig in kept:
            sig.base = sig.sent

        def mixture(n):
            for k in range(KT):
                nc.vector.scalar_tensor_tensor(mixes[:, n % 2, k, :], xx[:, k, :], mu[:, order[n][0], k:k + 1],
                                               K.xT[:, k, 0:TOK], ALU.mult, ALU.add)

        def aside(n):
            if n + 1 == len(order):
                return None

            def work(pool, scaled):
                m = mixes[:, (n + 1) % 2, :, :]
                for k in range(KT):
                    last = nc.gpsimd.tensor_scalar(m[:, k, :], xx[:, k, :], mu[:, order[n + 1][0], k:k + 1], None,
                                                   ALU.mult)
                last.then_inc(*scaled.up())
                pool.wait_ge(*scaled.at(1))
                nc.gpsimd.tensor_tensor(m, m, K.xT[:, :, 0:TOK], ALU.add)

            return work

        def stores(n):
            return [(K.scratch[order[n][1]][cols_of(t), :], outs[0:ROWS[t], n % 2, t, :]) for t in range(TILES)]

        def before(sp, n):
            if n == 0:
                sp.wait_ge(*later.at(16 * 8))
                sp.wait_ge(*shifted.at(16 * 9))
            if n:
                sp.wait_ge(*kept[(n - 1) % 2].at(16 * TILES * ((n - 1) // 2 + 1)))

        with K.phase("z_done") as (block, done):
            @block.vector
            def _(dve):
                mixture(0)
        for n in range(3):
            token_major_phase(K, K.first["c_" + order[n][1]], 2, mixes[:, n % 2, :, :], tiles,
                              lambda g, t: outs[0:ROWS[t], n % 2, t, g * 512:(g + 1) * 512], stores=stores(n),
                              stored_later=kept[n % 2], aside=aside(n), last_wait=lambda sp: before(sp, n))
        for n, inner in ((3, ACT.Tanh), (4, ACT.Copy), (5, ACT.Sigmoid)):
            rwkv_low_rank(K, n, order[n][1], inner, mixes[:, n % 2, :, :], outs[:, n % 2, :, :], hT, l1, l2, row,
                          stores(n), kept[n % 2], aside(n), before)


def rwkv_low_rank(K, index, n, inner, mix, out, hT, l1, l2, row, stores, stored, aside, before):
    nc = K.nc
    m = 128 if n == "g" else 64
    with K.phase("l1_full", "l1_done", "l2_full", "l2_done", "l2_step", "aside_step") as (
            block, f1, d1, f2, d2, step, scaled):
        if aside:
            @block.gpsimd
            def _(pool):
                aside(pool, scaled)

        @block.tensor
        def _(pe):
            for k in range(KT):
                last = nc.tensor.matmul(K.ps[0][0:m, 0:TOK], l1[n][:, k, :], mix[:, k, :],
                                        start=(k == 0), stop=(k == KT - 1))
            last.then_inc(*f1.up())
            pe.wait_ge(*d1.at(1))
            for t in range(TILES):
                for g in range(2):
                    last = nc.tensor.matmul(K.ps[1 + 2 * t + g][0:ROWS[t], :], hT[0:m, cols_of(t)],
                                            l2[n][:, g * 512:(g + 1) * 512], start=True, stop=True)
                last.then_inc(*f2.up())

        @block.scalar
        def _(act):
            act.wait_ge(*f1.at(1))
            nc.scalar.activation(hT[0:m, :], K.ps[0][0:m, 0:TOK], inner).then_inc(*d1.up())
            for t in range(TILES):
                r = ROWS[t]
                if n == "g":
                    act.wait_ge(*f2.at(t + 1))
                    for g in range(2):
                        last = nc.scalar.copy(out[0:r, t, g * 512:(g + 1) * 512], K.ps[1 + 2 * t + g][0:r, :])
                    last.then_inc(*d2.up())
                else:
                    act.wait_ge(*step.at(t + 1))
                    nc.scalar.activation(out[0:r, t, :], out[0:r, t, :], ACT.Sigmoid).then_inc(*d2.up())

        if n != "g":
            @block.vector
            def _(dve):
                for t in range(TILES):
                    r = ROWS[t]
                    dve.wait_ge(*f2.at(t + 1))
                    for g in range(2):
                        c = slice(g * 512, (g + 1) * 512)
                        last = nc.vector.tensor_tensor(out[0:r, t, c], K.ps[1 + 2 * t + g][0:r, :],
                                                       row[n][0:r, c], ALU.add)
                    last.then_inc(*step.up())

        @block.sync
        def _(sp):
            sp.wait_ge(*d2.at(TILES))
            for dst, src in stores:
                sp.dma_start(dst, src).then_inc(*stored.up(16))
            before(sp, index)
            if n == "g":
                before(sp, index + 1)


def rwkv_tile(K, st, t, H, yT, wide):
    nc, I, O = K.nc, K.ins, K.outs
    rows, kind = ROWS[t], tile_kind(t)
    r = slice(0, rows)
    names = ["r", "k", "v", "w", "a"]
    d = {n: K.sb(st, "in_" + n, [128, D]) for n in names}
    bonus = K.sb(st, "bonus", [128, C_HEADS])
    ec = K.sb(st, "ec", [128, KT, 8])
    y = d["w"]
    with contextlib.ExitStack() as outer:
        ktr = K.sb(outer, "ktr", [128, KT, 2, rows])
        bkn = K.sb(outer, "bkn", [128, KT, 2, rows])
        with contextlib.ExitStack() as tmp:
            rwkv_factors(K, tmp, t, d, bonus, ec, ktr, bkn)
        with contextlib.ExitStack() as tmp:
            mats = rwkv_matrices(K, tmp, t, ktr, bkn, wide)
            if t == 2:
                byst, S = rwkv_sample_states(K, tmp, ktr)
            for chunk in range(2 if t < 2 else 1):
                rwkv_chunk(K, tmp, t, chunk, d, ec, ktr, mats, H, y, byst if t == 2 else None)
            if t == 2:
                rwkv_sample_update(K, d, ec, S, mats)
    if t == 1:
        rwkv_prompt_state(K, H)
    rwkv_output(K, t, d, bonus, y, yT)


def rwkv_factors(K, tmp, t, d, bonus, ec, ktr, bkn):
    nc, I = K.nc, K.ins
    rows, kind = ROWS[t], tile_kind(t)
    r = slice(0, rows)
    kt = K.sb(tmp, "kt", [128, D])
    t1 = K.sb(tmp, "t1", [128, D])
    t2 = K.sb(tmp, "t2", [128, D])
    vec = {n: K.sb(tmp, "vec_" + n, [128, D]) for n in ("k_k", "k_a", "r_k")}
    ss = K.sb(tmp, "ss", [128, 3, C_HEADS])
    y_neg, y_pos = vec["k_k"], K.sb(tmp, "pos", [128, D])
    h3 = lambda a: a[r, :].rearrange("p (h n) -> p h n", h=C_HEADS)
    turned = ((d["a"], bkn, 0), (d["k"], bkn, 1), (d["r"], ktr, 1), (kt, ktr, 0))

    def group(n):
        src, dst, i = turned[n // 2]
        q = n % 2
        bank = K.ps[3 + n % 4][:, 0:4 * rows].rearrange("c (n p) -> c n p", n=4)
        return [src[r, (4 * q + j) * 128:(4 * q + j + 1) * 128] for j in range(4)], bank, dst[:, 4 * q:4 * q + 4, i, :]

    groups = (["w"], ["k", "k_k"], ["a", "k_a"], ["r", "r_k", "v"])
    with K.phase("f_lw", "sum_full", "f_kk", "scalar_step", "vector_step", "f_root", "normed", "tr_full", "tr_act",
                 "state_in0", "state_in1", "state_in2", "state_in3") as (
            block, lw, summed, kkd, by_act, by_dve, rooted, ended, full, copied, *arrived):
        @block.sync
        def _(sp):
            rows_of = {"k_k": I["c_k_k"][0], "k_a": I["c_k_a"][0], "r_k": I["c_r_k"][0].rearrange("h n -> (h n)")}
            for group, sig in zip(groups, arrived):
                for n in group:
                    if n in d:
                        sp.dma_start(d[n][r, :], K.scratch[n][cols_of(t), :]).then_inc(*sig.up(16))
                    else:
                        sp.dma_start(vec[n][:, :], row_broadcast(rows_of[n])).then_inc(*sig.up(16))

        @block.tensor
        def _(pe):
            pe.wait_ge(*lw.at(1))
            for g in range(2):
                nc.tensor.matmul(K.ps[g][r, :], K.const("upto_" + kind)[r, 0:rows], d["w"][r, g * 512:(g + 1) * 512],
                                 start=True, stop=True)
            for f in range(KT):
                last = nc.tensor.matmul(K.ps[2][:, 8 * f:8 * f + 8], d["w"][r, f * 128:(f + 1) * 128],
                                        K.const("of_chunk_" + kind)[r, :], start=True, stop=True)
            last.then_inc(*summed.up())
            for n in range(8):
                pe.wait_ge(*ended.at(n // 2 + 1))
                if n >= 4:
                    pe.wait_ge(*copied.at(n - 3))
                srcs, bank, _ = group(n)
                for j in range(4):
                    last = nc.tensor.transpose(bank[:, j, :], srcs[j], K.const("ident")[r, 0:rows])
                last.then_inc(*full.up())

        @block.scalar
        def _(act):
            act.wait_ge(*rooted.at(1))
            nc.scalar.activation(ss[r, 1, :], ss[r, 0, :], ACT.Sqrt, bias=K.eps6[r, 0:1]).then_inc(*by_act.up())
            act.wait_ge(*summed.at(1))
            nc.scalar.activation(ec[:, :, :], K.ps[2][:, 0:64].rearrange("p (f c) -> p f c", f=KT), ACT.Exp
                                 ).then_inc(*by_act.up())
            for g in range(2):
                c = slice(g * 512, (g + 1) * 512)
                nc.scalar.activation(y_neg[r, c], K.ps[g][r, :], ACT.Exp, scale=-1.0)
                last = nc.scalar.activation(y_pos[r, c], K.ps[g][r, :], ACT.Exp)
            last.then_inc(*by_act.up())
            act.wait_ge(*kkd.at(1))
            nc.scalar.activation(d["w"][r, :], d["w"][r, :], ACT.Exp).then_inc(*by_act.up())
            for n in range(8):
                act.wait_ge(*full.at(n + 1))
                _, bank, place = group(n)
                nc.scalar.copy(place, bank).then_inc(*copied.up())

        @block.vector
        def _(dve):
            link = chain(dve, by_dve)
            dve.wait_ge(*arrived[0].at(16))
            nc.vector.tensor_scalar(d["w"][r, :], d["w"][r, :], -float(np.exp(-0.5)), None, ALU.mult
                                    ).then_inc(*lw.up())
            dve.wait_ge(*arrived[1].at(32))
            link(nc.vector.tensor_tensor(kt[r, :], d["k"][r, :], vec["k_k"][r, :], ALU.mult))
            link(nc.vector.tensor_tensor(t1[r, :], kt[r, :], kt[r, :], ALU.mult))
            nc.vector.tensor_reduce(ss[r, 0, :], h3(t1), AX, ALU.add).then_inc(*rooted.up())
            dve.wait_ge(*arrived[2].at(32))
            nc.vector.scalar_tensor_tensor(t2[r, :], d["a"][r, :], -1.0, vec["k_a"][r, :], ALU.add, ALU.mult)
            dve.wait_ge(*by_act.at(1))
            link(nc.vector.reciprocal(ss[r, 2, :], ss[r, 1, :]))
            link(nc.vector.scalar_tensor_tensor(d["k"][r, :], t2[r, :], 1.0, d["k"][r, :], ALU.add, ALU.mult))
            link(nc.vector.tensor_tensor(h3(kt), h3(kt), ss[r, 2, :].unsqueeze(2).broadcast_to([rows, C_HEADS, 64]),
                                         ALU.mult))
            dve.wait_ge(*arrived[3].at(48))
            link(nc.vector.tensor_tensor(t1[r, :], d["r"][r, :], d["k"][r, :], ALU.mult))
            link(nc.vector.tensor_tensor(t1[r, :], t1[r, :], vec["r_k"][r, :], ALU.mult))
            nc.vector.tensor_reduce(bonus[r, :], h3(t1), AX, ALU.add)
            link(nc.vector.scalar_tensor_tensor(d["a"][r, :], d["a"][r, :], -1.0, kt[r, :], ALU.mult, ALU.mult))
            dve.wait_ge(*by_act.at(3))
            for g in range(2):
                c = slice(g * 512, (g + 1) * 512)
                last = nc.vector.scalar_tensor_tensor(d["w"][r, c], d["w"][r, c], -1.0, K.ps[g][r, :],
                                                      ALU.mult, ALU.add)
            last.then_inc(*kkd.up())
            nc.vector.tensor_tensor(d["a"][r, :], d["a"][r, :], y_neg[r, :], ALU.mult).then_inc(*ended.up())
            nc.vector.tensor_tensor(d["k"][r, :], d["k"][r, :], y_neg[r, :], ALU.mult).then_inc(*ended.up())
            nc.vector.tensor_tensor(d["r"][r, :], d["r"][r, :], y_pos[r, :], ALU.mult).then_inc(*ended.up())
            dve.wait_ge(*by_act.at(4))
            nc.vector.tensor_tensor(kt[r, :], kt[r, :], d["w"][r, :], ALU.mult).then_inc(*ended.up())


def rwkv_matrices(K, tmp, t, ktr, bkn, wide):
    nc = K.nc
    rows, kind = ROWS[t], tile_kind(t)
    r = slice(0, rows)
    chunks = [slice(64 * c, 64 * c + 64) for c in range(rows // 64)]
    mats = {n: K.sb(tmp, "m_" + n, [128, 2, 8, 64]) for n in ("n", "rb", "rk")}
    mats["R"] = wide["R"]
    with contextlib.ExitStack() as t2:
        up = K.sb(t2, "up", [128, 2, 8, 64])
        T = K.sb(t2, "T", [128, 2, 8, rows])
        y = K.sb(t2, "y", [128, 2, 8, rows])
        cut = wide["cut"] if t < 2 else K.sb(t2, "cut", [SAMPLE, 2, 8, 64])
        with K.phase("int_full") as (block, full):
            @block.tensor
            def _(pe):
                for half in range(2):
                    for h in range(8):
                        f = 4 * half + h // 2
                        k = slice(64 * (h % 2), 64 * (h % 2) + 64)
                        c = slice(h // 2 * 128, h // 2 * 128 + 128)
                        for sl in chunks:
                            for i in range(2):
                                last = nc.tensor.matmul(K.ps[4 * half + 2 * (h % 2) + i][sl, c], bkn[k, f, i, sl],
                                                        ktr[k, f, :, sl], start=True, stop=True)
                    last.then_inc(*full.up())

            @block.vector
            def _(dve):
                for half in range(2):
                    dve.wait_ge(*full.at(half + 1))
                    for i, j, dst, mask in ((0, 0, up, "above"), (0, 1, mats["rb"], "upto"),
                                            (1, 0, mats["n"], "above"), (1, 1, mats["rk"], "upto")):
                        m = K.const(f"{mask}_chunk_{kind}")[r, :].unsqueeze(1).broadcast_to([rows, 4, 64])
                        for e in range(2):
                            src = K.ps[4 * half + 2 * e + i][r, :].rearrange("p (h j n) -> p h j n", h=4, j=2)
                            if dst is up:
                                nc.vector.scalar_tensor_tensor(dst[r, half, e::2, :], src[:, :, j, :], -1.0, m,
                                                               ALU.mult, ALU.mult)
                            else:
                                nc.vector.tensor_tensor(dst[r, half, e::2, :], src[:, :, j, :], m, ALU.mult)
        rwkv_invert(K, t, up, T, mats["R"], cut, y)
    return mats


def rwkv_invert(K, t, up, T, R, cut, y):
    nc = K.nc
    rows = ROWS[t]
    r = slice(0, rows)
    levels = [2, 4, 8, 16, 32] if t < 2 else [2, 4]
    steps = [(s, half) for s in levels for half in range(2)]
    diagonal = [slice(64 * c, 64 * c + 64) for c in range(rows // 64)]
    last_level = lambda m: m >= len(steps) - 2

    def bank(b, q):
        return K.ps[b + q][r, 0:4 * rows].rearrange("p (h n) -> p h n", h=4)

    with K.phase("inv_cut", "inv_y", "inv_yc", "inv_dr", "inv_dt", "inv_t", "inv_r", "vector_step") as (
            block, cutd, ys, yc, drs, dts, ts, rs, step):
        def product(b, lhsT, rhs):
            for h in range(8):
                last = nc.tensor.matmul(bank(b, h // 4)[:, h % 4, :], lhsT(h), rhs(h), start=True, stop=True)
            return last

        @block.gpsimd
        def _(pool):
            for m, (s, half) in enumerate(steps):
                if m >= 2:
                    pool.wait_ge(*ys.at(m - 1))
                for c in diagonal:
                    mask = K.const(f"upper{s}")[c, :].unsqueeze(1).broadcast_to([64, 8, 64])
                    last = nc.gpsimd.tensor_tensor(cut[c, half, :, c], up[c, half], mask, ALU.mult)
                last.then_inc(*cutd.up())

        @block.tensor
        def _(pe):
            for half in range(2):
                pe.wait_ge(*rs.at(half + 1))
                product(2 * half, lambda h: R[r, half, h, r], lambda h: K.const("ident")[r, r]).then_inc(*dts.up())
            for level in range(len(levels)):
                for half in range(2):
                    m = 2 * level + half
                    pe.wait_ge(*cutd.at(m + 1))
                    pe.wait_ge(*ts.at(m + 1))
                    product(2 * half, lambda h: cut[r, half, h, r], lambda h: T[r, half, h, r]).then_inc(*ys.up())
                for half in range(2):
                    m = 2 * level + half
                    pe.wait_ge(*yc.at(m + 1))
                    pe.wait_ge(*rs.at(m + 1))
                    if not last_level(m):
                        pe.wait_ge(*ts.at(m + 2))
                        product(4, lambda h: R[r, half, h, r], lambda h: y[r, half, h, r]).then_inc(*dts.up())
                    if m >= 1:
                        pe.wait_ge(*rs.at(m + 2))
                    product(6, lambda h: y[r, half, h, r], lambda h: R[r, half, h, r]).then_inc(*drs.up())

        @block.scalar
        def _(act):
            for m, (s, half) in enumerate(steps):
                act.wait_ge(*ys.at(m + 1))
                if m >= 2:
                    act.wait_ge(*drs.at(m - 1))
                for q in range(2):
                    last = nc.scalar.copy(y[r, half, 4 * q:4 * q + 4, r], bank(2 * half, q))
                last.then_inc(*yc.up())

        @block.vector
        def _(dve):
            link = chain(dve, step)
            for half in range(2):
                for c in diagonal:
                    mask = K.const("upper1")[c, :].unsqueeze(1).broadcast_to([64, 8, 64])
                    last = nc.vector.tensor_tensor(R[c, half, :, c], up[c, half], mask, ALU.mult)
                link(last)
                for c in diagonal:
                    ident = K.const("ident_chunk")[c, :].unsqueeze(1).broadcast_to([64, 8, 64])
                    last = nc.vector.tensor_tensor(R[c, half, :, c], ident, R[c, half, :, c], ALU.subtract)
                last.then_inc(*rs.up())
            for half in range(2):
                dve.wait_ge(*dts.at(half + 1))
                for q in range(2):
                    last = nc.vector.tensor_copy(T[r, half, 4 * q:4 * q + 4, r], bank(2 * half, q))
                last.then_inc(*ts.up())
            for m, (s, half) in enumerate(steps):
                for dst, b, done, sig in ((T, 4, dts.at(m + 3), ts), (R, 6, drs.at(m + 1), rs)):
                    if dst is T and last_level(m):
                        continue
                    dve.wait_ge(*done)
                    for q in range(2):
                        d = dst[r, half, 4 * q:4 * q + 4, r]
                        last = nc.vector.tensor_tensor(d, d, bank(b, q), ALU.subtract)
                    last.then_inc(*sig.up())


def rwkv_chunk(K, tmp, t, chunk, d, ec, ktr, mats, H, y, byst):
    nc = K.nc
    first = t == 0 and chunk == 0
    sl = slice(64 * chunk, 64 * chunk + 64)
    with contextlib.ExitStack() as t2:
        u = K.sb(t2, "u", [128, D])
        s = K.s_all if t == 2 else K.sb(t2, "s", [128, D])
        change = K.sb(t2, "change", [128, KT, 128])
        with K.phase("u_full", "u_act", "u_dve", "s_full", "s_act", "s_dve", "y_full", "h_full", "vector_step") as (
                block, uf, ua, ud, sf, sa, sd, yf, hf, step):
            def from_state(bank, half, p, i):
                f = 4 * half + p
                out = bank[sl, p * 128:(p + 1) * 128]
                if byst is not None:
                    nc.tensor.matmul(out, byst[:, f, i, :], K.const("ident"), start=True, stop=False,
                                     skip_group_check=True)
                elif not first:
                    nc.tensor.matmul(out, ktr[:, f, i, sl], H[:, f, :], start=True, stop=False,
                                     skip_group_check=True)

            def columns(half, h):
                return slice(512 * half + 64 * h, 512 * half + 64 * h + 64)

            @block.tensor
            def _(pe):
                for half in range(2):
                    bank = K.ps[4 * half]
                    for p in range(4):
                        from_state(bank, half, p, 0)
                        for h in (2 * p, 2 * p + 1):
                            last = nc.tensor.matmul(bank[sl, h * 64:h * 64 + 64], mats["n"][sl, half, h, :],
                                                    d["v"][sl, columns(half, h)], start=first, stop=True,
                                                    skip_group_check=True)
                    last.then_inc(*uf.up())
                for half in range(2):
                    pe.wait_ge(*(ud if half else ua).at(1))
                    for h in range(8):
                        last = nc.tensor.matmul(K.ps[4 * half + 1][sl, h * 64:h * 64 + 64],
                                                mats["R"][sl, half, h, sl], u[sl, columns(half, h)],
                                                start=True, stop=True)
                    last.then_inc(*sf.up())
                for half in range(2):
                    pe.wait_ge(*(sd if half else sa).at(1))
                    if t < 2:
                        for p in range(4):
                            c = slice(512 * half + p * 128, 512 * half + p * 128 + 128)
                            out = K.ps[4 * half + 3][:, p * 128:(p + 1) * 128]
                            nc.tensor.matmul(out, d["a"][sl, c], s[sl, c], start=True, stop=False)
                            last = nc.tensor.matmul(out, d["k"][sl, c], d["v"][sl, c], start=False, stop=True)
                        last.then_inc(*hf.up())
                    bank = K.ps[4 * half + 2]
                    for p in range(4):
                        from_state(bank, half, p, 1)
                        for h in (2 * p, 2 * p + 1):
                            out, c = bank[sl, h * 64:h * 64 + 64], columns(half, h)
                            nc.tensor.matmul(out, mats["rb"][sl, half, h, :], s[sl, c], start=first, stop=False,
                                             skip_group_check=True)
                            last = nc.tensor.matmul(out, mats["rk"][sl, half, h, :], d["v"][sl, c], start=False,
                                                    stop=True, skip_group_check=True)
                    last.then_inc(*yf.up())

            @block.scalar
            def _(act):
                act.wait_ge(*uf.at(1))
                nc.scalar.copy(u[sl, 0:512], K.ps[0][sl, :]).then_inc(*ua.up())
                act.wait_ge(*sf.at(1))
                nc.scalar.copy(s[sl, 0:512], K.ps[1][sl, :]).then_inc(*sa.up())
                for half in range(2):
                    act.wait_ge(*yf.at(half + 1))
                    nc.scalar.copy(y[sl, 512 * half:512 * half + 512], K.ps[4 * half + 2][sl, :])

            @block.vector
            def _(dve):
                link = chain(dve, step)
                dve.wait_ge(*uf.at(2))
                nc.vector.tensor_copy(u[sl, 512:D], K.ps[4][sl, :]).then_inc(*ud.up())
                dve.wait_ge(*sf.at(2))
                nc.vector.tensor_copy(s[sl, 512:D], K.ps[5][sl, :]).then_inc(*sd.up())
                if t < 2:
                    pair = K.const("pair").unsqueeze(1).broadcast_to([128, 4, 128])
                    for half in range(2):
                        fs = slice(4 * half, 4 * half + 4)
                        dve.wait_ge(*hf.at(half + 1))
                        link(nc.vector.tensor_tensor(change[:, fs, :], K.ps[4 * half + 3][:, :].rearrange(
                            "p (f n) -> p f n", f=4), pair, ALU.mult))
                        if not first:
                            link(nc.vector.tensor_tensor(change[:, fs, :], change[:, fs, :], H[:, fs, :], ALU.add))
                        dve.wait_ge(*yf.at(half + 1))
                        nc.vector.tensor_tensor(H[:, fs, :], change[:, fs, :],
                                                ec[:, fs, chunk:chunk + 1].broadcast_to([128, 4, 128]), ALU.mult)


def load_states(K, sp, buf, b, sig):
    for e in range(2):
        src = K.ins["state_wkv"][0, b].rearrange("(f e) v k -> e v f k", e=2)[e]
        sp.dma_start(buf[64 * e:64 * e + 64, :, 64 * e:64 * e + 64], src).then_inc(*sig.up(16))


def rwkv_sample_states(K, outer, ktr):
    nc = K.nc
    byst = K.sb(outer, "byst", [128, KT, 2, SAMPLE])
    K.s_all = K.sb(outer, "s_all", [128, D])
    S = K.sb(outer, "S", [128, SEQS, KT, 128])
    with contextlib.ExitStack() as tmp:
        HT = K.sb(tmp, "HT", [128, 2, KT, 128])
        with K.phase("zero_low", "zero_high", "st_full", "st_act", "st_dve", "by_full", "by_done",
                     *(f"state_in{i}" for i in range(2))) as (
                block, zlow, zhigh, full, by_act, by_dve, byf, byd, *arrived):
            @block.sync
            def _(sp):
                for b in range(SEQS):
                    if b >= 2:
                        sp.wait_ge(*arrived[b % 2].at(32 * (b // 2)))
                    load_states(K, sp, S[:, b, :, :], b, arrived[b % 2])

            @block.gpsimd
            def _(pool):
                nc.gpsimd.memset(S[0:64, :, :, 64:128], 0.0).then_inc(*zlow.up())

            @block.tensor
            def _(pe):
                pe.wait_ge(*zlow.at(1))
                pe.wait_ge(*zhigh.at(1))

                def turn(b):
                    pe.wait_ge(*arrived[b % 2].at(32 * (b // 2 + 1)))
                    if b >= 2:
                        pe.wait_ge(*by_act.at(b - 1))
                        pe.wait_ge(*by_dve.at(b - 1))
                    for q in range(2):
                        for j in range(4):
                            last = nc.tensor.transpose(K.ps[2 * (b % 2) + q][:, j * 128:(j + 1) * 128],
                                                       S[:, b, 4 * q + j, :], K.const("ident"))
                        last.then_inc(*full.up())

                turn(0)
                for b in range(SEQS):
                    if b + 1 < SEQS:
                        turn(b + 1)
                    pe.wait_ge(*by_act.at(b + 1))
                    pe.wait_ge(*by_dve.at(b + 1))
                    if b >= 2:
                        pe.wait_ge(*byd.at(b - 1))
                    for f in range(KT):
                        last = nc.tensor.matmul(K.ps[4 + b % 2][:, 16 * f:16 * f + 16], HT[:, b % 2, f, :],
                                                ktr[:, f, :, 8 * b:8 * b + 8], start=True, stop=True)
                    last.then_inc(*byf.up())

            @block.scalar
            def _(act):
                for b in range(SEQS):
                    act.wait_ge(*full.at(2 * b + 1))
                    if b >= 2:
                        act.wait_ge(*byf.at(b - 1))
                    nc.scalar.copy(HT[:, b % 2, 0:4, :], K.ps[2 * (b % 2)][:, :].rearrange("p (f n) -> p f n", f=4)
                                   ).then_inc(*by_act.up())

            @block.vector
            def _(dve):
                def copy_products(b):
                    dve.wait_ge(*byf.at(b + 1))
                    nc.vector.tensor_copy(byst[:, :, :, 8 * b:8 * b + 8],
                                          K.ps[4 + b % 2][:, 0:128].rearrange("p (f i s) -> p f i s", f=KT, i=2)
                                          ).then_inc(*byd.up())

                nc.vector.memset(S[64:128, :, :, 0:64], 0.0).then_inc(*zhigh.up())
                for b in range(SEQS):
                    dve.wait_ge(*full.at(2 * b + 2))
                    if b >= 2:
                        dve.wait_ge(*byf.at(b - 1))
                    nc.vector.tensor_copy(HT[:, b % 2, 4:8, :],
                                          K.ps[2 * (b % 2) + 1][:, :].rearrange("p (f n) -> p f n", f=4)
                                          ).then_inc(*by_dve.up())
                    if b:
                        copy_products(b - 1)
                copy_products(SEQS - 1)
    return byst, S


def rwkv_sample_update(K, d, ec, S, mats):
    nc, I, O = K.nc, K.ins, K.outs
    cut = [[mats[n][0:SAMPLE].rearrange("p a h n -> p (a h n)") for n in pair] for pair in (("n", "rb"), ("rk", "R"))]
    with K.phase("cut_done", "ch_full", "ch_done", "stored", "vector_step") as (block, cd, chf, chd, stored, step):
        @block.sync
        def _(sp):
            for b in range(SEQS):
                sp.wait_ge(*chd.at(b + 1))
                for e in range(2):
                    dst = O[13][0, b].rearrange("(f e) v k -> e v f k", e=2)[e]
                    sp.dma_start(dst, S[64 * e:64 * e + 64, b, :, 64 * e:64 * e + 64]).then_inc(*stored.up(16))
            sp.wait_ge(*stored.at(32 * SEQS))

        @block.scalar
        def _(act):
            for b in range(SEQS):
                if b >= 2:
                    act.wait_ge(*chf.at(b - 1))
                m = K.const("of_chunk_s")[0:SAMPLE, b:b + 1]
                nc.scalar.activation(cut[b % 2][0][0:SAMPLE, :], K.s_all[0:SAMPLE, :], ACT.Copy, scale=m)
                nc.scalar.activation(cut[b % 2][1][0:SAMPLE, :], d["v"][0:SAMPLE, :], ACT.Copy, scale=m
                                     ).then_inc(*cd.up())

        @block.tensor
        def _(pe):
            r = slice(0, SAMPLE)
            for b in range(SEQS):
                if b >= 2:
                    pe.wait_ge(*chd.at(b - 1))
                o = 4 * (b % 2)
                for f in range(KT):
                    q, j = f // 4, f % 4
                    nc.tensor.matmul(K.ps[o + q][:, j * 128:(j + 1) * 128],
                                     ec[:, f, b:b + 1].broadcast_to([128, 128]), K.const("ident"),
                                     start=True, stop=True)
                pe.wait_ge(*cd.at(b + 1))
                for f in range(KT):
                    q, j = f // 4, f % 4
                    c = slice(f * 128, (f + 1) * 128)
                    out = K.ps[o + 2 + q][:, j * 128:(j + 1) * 128]
                    nc.tensor.matmul(out, cut[b % 2][0][r, c], d["a"][r, c], start=True, stop=False)
                    last = nc.tensor.matmul(out, cut[b % 2][1][r, c], d["k"][r, c], start=False, stop=True)
                last.then_inc(*chf.up())

        @block.vector
        def _(dve):
            link = chain(dve, step)
            for b in range(SEQS):
                dve.wait_ge(*chf.at(b + 1))
                for op, i in ((ALU.add, 2), (ALU.mult, 0)):
                    for q in range(2):
                        h = S[:, b, 4 * q:4 * q + 4, :]
                        last = nc.vector.tensor_tensor(
                            h, h, K.ps[4 * (b % 2) + i + q][:, :].rearrange("p (f n) -> p f n", f=4), op)
                    if i:
                        link(last)
                last.then_inc(*chd.up())


def rwkv_prompt_state(K, H):
    nc, O = K.nc, K.outs
    with contextlib.ExitStack() as tmp:
        S = K.sb(tmp, "S", [128, KT, 128])
        transpose_phase(K, [([H[:, 4 * q + j, :] for j in range(4)], S[:, 4 * q:4 * q + 4, :]) for q in range(2)])
        with K.phase("su_out0") as (block, out):
            @block.sync
            def _(sp):
                for e in range(2):
                    dst = O[8][0, 0].rearrange("(f e) v k -> e v f k", e=2)[e]
                    sp.dma_start(dst, S[64 * e:64 * e + 64, :, 64 * e:64 * e + 64]).then_inc(*out.up(16))
                sp.wait_ge(*out.at(32))


def rwkv_output(K, t, d, bonus, y, yT):
    nc, I = K.nc, K.ins
    rows = ROWS[t]
    r = slice(0, rows)
    h3 = lambda a: a[r, :].rearrange("p (h n) -> p h n", h=C_HEADS)
    bc = lambda a: a.unsqueeze(2).broadcast_to([rows, C_HEADS, 64])
    with contextlib.ExitStack() as tmp:
        g, w, b, sq, bv = (K.sb(tmp, n, [128, D]) for n in ("g", "lw", "lb", "sq", "bv"))
        s = K.sb(tmp, "s", [128, 3, C_HEADS])
        with K.phase("loaded", "ln_var", "ln_std", "vector_step", "aside_step") as (
                block, loaded, var, std, step, added):
            @block.sync
            def _(sp):
                sp.dma_start(g[r, :], K.scratch["g"][cols_of(t), :]).then_inc(*loaded.up(16))
                sp.dma_start(w[:, :], row_broadcast(I["c_ln_w"][0])).then_inc(*loaded.up(16))
                sp.dma_start(b[:, :], row_broadcast(I["c_ln_b"][0])).then_inc(*loaded.up(16))

            @block.scalar
            def _(act):
                act.wait_ge(*var.at(1))
                nc.scalar.activation(s[r, 1, :], s[r, 1, :], ACT.Sqrt, scale=1.0 / 64, bias=K.epsg[r, 0:1]
                                     ).then_inc(*std.up())

            @block.gpsimd
            def _(pool):
                nc.gpsimd.tensor_tensor(h3(bv), h3(d["v"]), bc(bonus[r, :]), ALU.mult).then_inc(*added.up())
                pool.wait_ge(*added.at(1))
                pool.wait_ge(*loaded.at(48))
                nc.gpsimd.tensor_tensor(bv[r, :], bv[r, :], b[r, :], ALU.add).then_inc(*added.up())

            @block.vector
            def _(dve):
                link = chain(dve, step)
                link(nc.vector.tensor_reduce(s[r, 0, :], h3(y), AX, ALU.add))
                link(nc.vector.tensor_scalar(s[r, 0, :], s[r, 0, :], 1.0 / 64, None, ALU.mult))
                link(nc.vector.tensor_tensor(h3(y), h3(y), bc(s[r, 0, :]), ALU.subtract))
                link(nc.vector.tensor_tensor(sq[r, :], y[r, :], y[r, :], ALU.mult))
                nc.vector.tensor_reduce(s[r, 1, :], h3(sq), AX, ALU.add).then_inc(*var.up())
                dve.wait_ge(*std.at(1))
                link(nc.vector.reciprocal(s[r, 2, :], s[r, 1, :]))
                link(nc.vector.tensor_tensor(h3(y), h3(y), bc(s[r, 2, :]), ALU.mult))
                dve.wait_ge(*loaded.at(48))
                link(nc.vector.tensor_tensor(y[r, :], y[r, :], w[r, :], ALU.mult))
                dve.wait_ge(*added.at(2))
                link(nc.vector.tensor_tensor(y[r, :], y[r, :], bv[r, :], ALU.add))
                link(nc.vector.tensor_tensor(y[r, :], y[r, :], g[r, :], ALU.mult))
        transpose_phase(K, [([y[r, (4 * q + j) * 128:(4 * q + j + 1) * 128] for j in range(4)],
                             yT[:, 4 * q:4 * q + 4, cols_of(t)]) for q in range(2)])



INPUTS = ["x_prompt", "x_sample", "mem_prompt", "cache_mem_k", "cache_mem_v", "state_conv_a", "state_delta",
          "state_ret", "state_shift_c", "state_wkv", "ab_w_in", "ab_conv_w", "ab_a_log", "ab_dt_bias", "ab_norm_w",
          "ab_w_out", "c_mu", "c_w_r", "c_w_k", "c_w_v", "c_w0", "c_w_w1", "c_w_w2", "c_a0", "c_w_a1", "c_w_a2",
          "c_w_g1", "c_w_g2", "c_k_k", "c_k_a", "c_r_k", "c_ln_w", "c_ln_b", "c_w_out", "x_w_q", "x_w_k", "x_w_v",
          "x_w_o", "moe_w_grp", "moe_b_grp", "moe_w_exp", "moe_b_exp", "moe_w1", "moe_w3", "moe_w2", "ln_w", "ln_b"]
OUTPUTS = [(1, 256, 1024), (8, 8, 1024), (2, 1, 256, 4, 256), (2, 1, 256, 4, 256), (1, 1, 3, 1536),
           (1, 1, 4, 128, 128), (1, 1, 4, 128, 128), (1, 1, 1024), (1, 1, 16, 64, 64), (1, 8, 3, 1536),
           (1, 8, 4, 128, 128), (1, 8, 4, 128, 128), (1, 8, 1024), (1, 8, 16, 64, 64)]


def inference_step(nc, ins, outs, at, probe=None):
    stack = contextlib.ExitStack()
    with stack:
        K = Kernel(nc, ins, outs, at, stack)
        K.scratch = {n: nc.dram_tensor("scratch_" + n, (TOK, D), F32, kind="Internal").ap()
                     for n in ("gate", "r", "k", "v", "w", "a", "g")}
        K.scratch["gates"] = nc.dram_tensor("scratch_gates", (EXPERTS, TOK), F32, kind="Internal").ap()
        K.scratch["cols"] = nc.dram_tensor("scratch_cols", (4, TOK), F32, kind="Internal").ap()
        K.cst = K.sb(stack, "cst", [128, ins["constants"].shape[1]])
        K.x = K.sb(stack, "x", [128, TILES, D])
        K.xT = K.sb(stack, "xT", [128, KT, TOK])
        K.ring = K.sb(stack, "ring", [128, RING, SLOT])
        K.eps6, K.eps5, K.epsg = (K.sb(stack, "eps", [128, 1]) for _ in range(3))
        K.ps = [stack.enter_context(nc.psum_tensor(f"bank{b}", [128, 512], F32)) for b in range(8)]
        K.arrived = [stack.enter_context(nc.semaphore(f"weights_arrived{b}")) for b in range(RING)]
        K.chunks, K.first = weight_chunks(K)
        total = [0] * RING
        K.arrival = []
        for g, chunk in enumerate(K.chunks):
            total[g % RING] += 16 * len(chunk)
            K.arrival.append(total[g % RING])
        with K.phase("loaded") as (block, loaded):
            @block.sync
            def _(sp):
                sp.dma_start(K.cst[:, :], ins["constants"]).then_inc(*loaded.up(16))
                for t in range(2):
                    sp.dma_start(K.x[:, t, :], ins["x_prompt"][0, t * 128:(t + 1) * 128, :]).then_inc(*loaded.up(16))
                sp.dma_start(K.x[0:SAMPLE, 2, :], ins["x_sample"].rearrange("b s d -> (b s) d")
                             ).then_inc(*loaded.up(16))
                sp.wait_ge(*loaded.at(64))

            @block.vector
            def _(dve):
                nc.vector.memset(K.eps6[:, :], 1e-6)
                nc.vector.memset(K.eps5[:, :], LN_EPS)
                nc.vector.memset(K.epsg[:, :], GN_EPS)
        transpose_x(K)
        ab_mixer(K)
        if probe == "ab":
            return finish(K)
        cross_attention(K, 0)
        if probe == "x0":
            return finish(K)
        moe(K, 0)
        if probe == "moe0":
            return finish(K)
        rwkv_mixer(K)
        if probe == "c":
            return finish(K)
        cross_attention(K, 1)
        moe(K, 1)


def finish(K):
    with K.phase("stored") as (block, out):
        @block.sync
        def _(sp):
            for t in range(2):
                sp.dma_start(K.outs[0][0, t * 128:(t + 1) * 128, :], K.x[:, t, :]).then_inc(*out.up(16))
            sp.dma_start(K.outs[1].rearrange("b s d -> (b s) d"), K.x[0:SAMPLE, 2, :]).then_inc(*out.up(16))
            sp.wait_ge(*out.at(48))


def kernel(**inputs):
    import concourse.bacc as bacc
    from concourse.bass_utils import run_bass_kernel_spmd

    nc = bacc.Bacc("TRN2", target_bir_lowering=False, num_devices=1)
    table, at = constants()
    arrays = {"in_" + n: np.ascontiguousarray(inputs[n]) for n in INPUTS}
    arrays["in_constants"] = table
    ins = {n[3:]: nc.dram_tensor(n, a.shape, F32, kind="ExternalInput").ap() for n, a in arrays.items()}
    outs = [nc.dram_tensor(f"out_{i}", s, F32, kind="ExternalOutput").ap() for i, s in enumerate(OUTPUTS)]
    inference_step(nc, ins, outs, at)
    r = run_bass_kernel_spmd(nc, [arrays], core_ids=[0])
    return tuple(r.results[0][f"out_{i}"] for i in range(len(OUTPUTS)))
```
